# Optimizing a Trainium2 kernel written in Bass

```python
import math
import jax
import jax.numpy as jnp
from jax import lax
import numpy as np

D_MODEL = 1024
BATCH = 1
SEQ = 1024
DEPTH = 1
DEC_BATCH = 8
DEC_SEQ = 4
PAST_LEN = 4096
PAGE_SIZE = 128

N_Q_HEADS = 8
N_KV_HEADS = 2
Q_PER_KV = N_Q_HEADS // N_KV_HEADS
HEAD_DIM = 64
ATTN_WIDTH = N_Q_HEADS * HEAD_DIM
KV_WIDTH = N_KV_HEADS * HEAD_DIM
CMP_BLOCK = 32
CMP_STRIDE = 16
CMP_RATIO = CMP_BLOCK // CMP_STRIDE
SLC_BLOCK = 64
N_SELECT = 16
WINDOW = 512
WIN_Q_BLOCK = 128
SLC_Q_BLOCK = 64
SSM_WIDTH = D_MODEL // 2
SSM_GROUP = 16
N_SSM_GROUPS = SSM_WIDTH // SSM_GROUP
SSM_STATE = 64
DT_MIN = 1e-3
DT_MAX = 1e-1
N_BUCKETS = 32
MAX_DISTANCE = 128
D_FF = 4 * D_MODEL
IN_SPLITS = (ATTN_WIDTH,) + (KV_WIDTH,) * 6 + (3 * N_Q_HEADS, SSM_WIDTH, D_MODEL, D_MODEL)
IN_WIDTH = sum(IN_SPLITS)
RMS_EPS = 1e-6
NEG_INF = -1e30
TINY = 1e-30

kernel_name = 'nsa_s5_parallel_hybrid_step'

def rms_norm(x, g):
    xf = x.astype(jnp.float32)
    y = xf * lax.rsqrt(jnp.mean(xf * xf, axis=-1, keepdims=True) + RMS_EPS)
    return (y * g.astype(jnp.float32)).astype(x.dtype)

def t5_bucket(dist):
    n = jnp.maximum(dist, 0)
    exact = N_BUCKETS // 2
    nf = jnp.maximum(n, exact).astype(jnp.float32)
    large = exact + (jnp.log(nf / exact) / math.log(MAX_DISTANCE / exact) * (N_BUCKETS - exact)).astype(jnp.int32)
    return jnp.where(n < exact, n, jnp.minimum(large, N_BUCKETS - 1))

def shared_bias(table, dist):
    b = jnp.moveaxis(table[t5_bucket(dist)].astype(jnp.float32), -1, 0)
    return b.reshape((N_KV_HEADS, Q_PER_KV) + dist.shape)

def gathered_bias(table, dist):
    table_g = table.T.reshape(N_KV_HEADS, Q_PER_KV, N_BUCKETS)
    g_idx = jnp.arange(N_KV_HEADS)[None, :, None, None]
    b = table_g[g_idx, :, t5_bucket(dist)]
    return jnp.moveaxis(b, -1, 2).astype(jnp.float32)

def masked_softmax(s, mask):
    s = jnp.where(mask, s, NEG_INF)
    p = jnp.where(mask, jnp.exp(s - jnp.max(s, axis=-1, keepdims=True)), 0.0)
    return p / jnp.maximum(jnp.sum(p, axis=-1, keepdims=True), TINY)

def attend_shared(q, k, v, dist, mask, table):
    s = jnp.einsum('ngrtd,nsgd->ngrts', q, k).astype(jnp.float32) + shared_bias(table, dist)
    p = masked_softmax(s, mask)
    return jnp.einsum('ngrts,nsgd->ngrtd', p.astype(v.dtype), v), p

def slc_attend(q, kg, vg, kpos, kok, q_pos, table):
    dist = q_pos[None, None, :, None] - kpos
    mask = kok & (dist >= 0)
    s = jnp.einsum('ngrtd,ngtsd->ngrts', q, kg).astype(jnp.float32) + gathered_bias(table, dist)
    p = masked_softmax(s, mask[:, :, None])
    return jnp.einsum('ngrts,ngtsd->ngrtd', p.astype(vg.dtype), vg)

def compress(x, pe, w1, b1, w2):
    n, length, g, hd = x.shape
    n_chunks = -(-length // CMP_STRIDE)
    x = jnp.pad(x, ((0, 0), (0, n_chunks * CMP_STRIDE - length), (0, 0), (0, 0)))
    x = x.reshape(n, n_chunks, CMP_STRIDE, g, hd)
    w1c = w1.reshape(CMP_RATIO, CMP_STRIDE, hd, hd)
    pec = pe.reshape(CMP_RATIO, CMP_STRIDE, hd)
    part = jnp.einsum('ncsgd,jsde->jncge', x, w1c)
    n_cmp = n_chunks - CMP_RATIO + 1
    hid = b1 + jnp.einsum('jsd,jsde->e', pec, w1c)
    for j in range(CMP_RATIO):
        hid = hid + part[j, :, j:j + n_cmp]
    return jnp.einsum('ncge,ef->ncgf', jax.nn.silu(hid), w2)

def cmp_ends(n_cmp):
    return jnp.arange(n_cmp) * CMP_STRIDE + CMP_BLOCK - 1

def select_blocks(imp, q_pos, n_slc):
    n_cmp = imp.shape[-1]
    chunk = jnp.arange(n_cmp)[:, None] + jnp.arange(CMP_RATIO)[None, :]
    chunk_blk = chunk // (SLC_BLOCK // CMP_STRIDE)
    blk = jnp.arange(n_slc)
    overlap = jnp.sum(chunk_blk[:, :, None] == blk[None, None, :], axis=1).astype(jnp.float32)
    score = jnp.einsum('ngtc,cj->ngtj', imp.astype(jnp.float32), overlap)
    cur = (q_pos // SLC_BLOCK)[:, None]
    forced = (blk[None, :] == 0) | (blk[None, :] == cur) | (blk[None, :] == cur - 1)
    avail = blk[None, :] * SLC_BLOCK <= q_pos[:, None]
    score = jnp.where(forced, jnp.inf, jnp.where(avail, score, -jnp.inf))
    top, idx = lax.top_k(score, min(N_SELECT, n_slc))
    return idx, top > -jnp.inf

def slc_prompt(q, k, v, idx, ok, table):
    n, g, r, t, hd = q.shape
    n_slc = t // SLC_BLOCK
    kb = k.reshape(n, n_slc, SLC_BLOCK, g, hd).transpose(0, 3, 1, 2, 4)
    vb = v.reshape(n, n_slc, SLC_BLOCK, g, hd).transpose(0, 3, 1, 2, 4)
    nqb = t // SLC_Q_BLOCK
    kk = idx.shape[-1]
    n_ar = jnp.arange(n)[:, None, None, None]
    g_ar = jnp.arange(g)[None, :, None, None]
    s_ar = jnp.arange(SLC_BLOCK)

    def block(args):
        qb, ib, okb, pb = args
        kg = kb[n_ar, g_ar, ib].reshape(n, g, SLC_Q_BLOCK, kk * SLC_BLOCK, hd)
        vg = vb[n_ar, g_ar, ib].reshape(n, g, SLC_Q_BLOCK, kk * SLC_BLOCK, hd)
        kpos = (ib[..., None] * SLC_BLOCK + s_ar).reshape(n, g, SLC_Q_BLOCK, -1)
        kok = jnp.broadcast_to(okb[..., None], ib.shape + (SLC_BLOCK,)).reshape(n, g, SLC_Q_BLOCK, -1)
        return slc_attend(qb, kg, vg, kpos, kok, pb, table)

    xs = (q.reshape(n, g, r, nqb, SLC_Q_BLOCK, hd).transpose(3, 0, 1, 2, 4, 5),
          idx.reshape(n, g, nqb, SLC_Q_BLOCK, kk).transpose(2, 0, 1, 3, 4),
          ok.reshape(n, g, nqb, SLC_Q_BLOCK, kk).transpose(2, 0, 1, 3, 4),
          jnp.arange(t).reshape(nqb, SLC_Q_BLOCK))
    o = lax.map(block, xs)
    return o.transpose(1, 2, 3, 0, 4, 5).reshape(n, g, r, t, hd)

def slc_sample(q, k_new, v_new, idx, ok, q_pos, cache_k, cache_v, layer, page_table, table):
    n, g, r, t, hd = q.shape
    kk = idx.shape[-1]
    past_blk = page_table.shape[1] * PAGE_SIZE // SLC_BLOCK
    pb = PAGE_SIZE // SLC_BLOCK
    n_ar = jnp.arange(n)[:, None, None, None]
    g5 = jnp.arange(g)[None, :, None, None, None]
    s_ar = jnp.arange(SLC_BLOCK)
    jc = jnp.minimum(idx, past_blk - 1)
    phys = page_table[n_ar, jc // pb]
    rows = (jc % pb)[..., None] * SLC_BLOCK + s_ar
    kg = cache_k[layer, phys[..., None], rows, g5].reshape(n, g, t, kk * SLC_BLOCK, hd)
    vg = cache_v[layer, phys[..., None], rows, g5].reshape(n, g, t, kk * SLC_BLOCK, hd)
    kpos_past = (idx[..., None] * SLC_BLOCK + s_ar).reshape(n, g, t, -1)
    kok_past = jnp.broadcast_to((ok & (idx < past_blk))[..., None], idx.shape + (SLC_BLOCK,)).reshape(n, g, t, -1)
    new_blk = q_pos // SLC_BLOCK
    chosen = jnp.any((idx[..., None] == new_blk) & ok[..., None], axis=3)
    k_nb = jnp.broadcast_to(k_new.transpose(0, 2, 1, 3)[:, :, None], (n, g, t, t, hd)).astype(kg.dtype)
    v_nb = jnp.broadcast_to(v_new.transpose(0, 2, 1, 3)[:, :, None], (n, g, t, t, hd)).astype(vg.dtype)
    kg = jnp.concatenate([kg, k_nb], axis=3)
    vg = jnp.concatenate([vg, v_nb], axis=3)
    kpos = jnp.concatenate([kpos_past, jnp.broadcast_to(q_pos, (n, g, t, t))], axis=3)
    kok = jnp.concatenate([kok_past, chosen], axis=3)
    return slc_attend(q, kg, vg, kpos, kok, q_pos, table)

def win_prompt(q, k, v, table):
    n, g, r, t, hd = q.shape
    nb = t // WIN_Q_BLOCK
    nprev = -(-WINDOW // WIN_Q_BLOCK)
    pad = ((0, 0), (nprev * WIN_Q_BLOCK, 0), (0, 0), (0, 0))
    kp = jnp.pad(k, pad).reshape(n, nb + nprev, WIN_Q_BLOCK, g, hd)
    vp = jnp.pad(v, pad).reshape(n, nb + nprev, WIN_Q_BLOCK, g, hd)
    kband = jnp.concatenate([kp[:, j:j + nb] for j in range(nprev + 1)], axis=2)
    vband = jnp.concatenate([vp[:, j:j + nb] for j in range(nprev + 1)], axis=2)
    qpos = jnp.arange(t).reshape(nb, WIN_Q_BLOCK)
    kpos = (jnp.arange(nb)[:, None] - nprev) * WIN_Q_BLOCK + jnp.arange((nprev + 1) * WIN_Q_BLOCK)[None, :]
    dist = qpos[:, :, None] - kpos[:, None, :]
    mask = (dist >= 0) & (dist <= WINDOW) & (kpos >= 0)[:, None, :]
    qb = q.reshape(n, g, r, nb, WIN_Q_BLOCK, hd)
    s = jnp.einsum('ngrbid,nbjgd->ngrbij', qb, kband).astype(jnp.float32) + shared_bias(table, dist)
    p = masked_softmax(s, mask)
    o = jnp.einsum('ngrbij,nbjgd->ngrbid', p.astype(vband.dtype), vband)
    return o.reshape(n, g, r, t, hd)

def win_sample(q, k_new, v_new, buf_k, buf_v, q_pos, past_len, table):
    w_buf = buf_k.shape[1]
    keys = jnp.concatenate([buf_k, k_new.astype(buf_k.dtype)], axis=1)
    vals = jnp.concatenate([buf_v, v_new.astype(buf_v.dtype)], axis=1)
    kpos = past_len - w_buf + jnp.arange(keys.shape[1])
    dist = q_pos[:, None] - kpos[None, :]
    mask = (dist >= 0) & (dist <= WINDOW)
    o, _ = attend_shared(q, keys, vals, dist, mask, table)
    return o, keys[:, -w_buf:], vals[:, -w_buf:]

def s5_ssm(u, x0_re, x0_im, lam_re, lam_im, log_dt, b_re, b_im, c_re, c_im, d, w_glu):
    n, t, _ = u.shape
    f32 = jnp.float32
    uf = u.astype(f32).reshape(n, t, N_SSM_GROUPS, SSM_GROUP)
    dt = jnp.exp(log_dt.astype(f32))[:, None]
    lr = jnp.minimum(lam_re.astype(f32), -1e-4)
    li = lam_im.astype(f32)
    mag = jnp.exp(lr * dt)
    ar, ai = mag * jnp.cos(li * dt), mag * jnp.sin(li * dt)
    den = lr * lr + li * li
    fr = ((ar - 1.0) * lr + ai * li) / den
    fi = (ai * lr - (ar - 1.0) * li) / den
    br, bi = b_re.astype(f32), b_im.astype(f32)
    bbr = fr[..., None] * br - fi[..., None] * bi
    bbi = fr[..., None] * bi + fi[..., None] * br
    bu_r = jnp.einsum('ntgi,gpi->ntgp', uf, bbr)
    bu_i = jnp.einsum('ntgi,gpi->ntgp', uf, bbi)
    x0r, x0i = x0_re.astype(f32), x0_im.astype(f32)
    bu_r = bu_r.at[:, 0].add(ar * x0r - ai * x0i)
    bu_i = bu_i.at[:, 0].add(ar * x0i + ai * x0r)
    a_r = jnp.broadcast_to(ar, bu_r.shape)
    a_i = jnp.broadcast_to(ai, bu_i.shape)

    def combine(e1, e2):
        a1r, a1i, b1r, b1i = e1
        a2r, a2i, b2r, b2i = e2
        return (a2r * a1r - a2i * a1i, a2r * a1i + a2i * a1r,
                a2r * b1r - a2i * b1i + b2r, a2r * b1i + a2i * b1r + b2i)

    _, _, hr, hi = lax.associative_scan(combine, (a_r, a_i, bu_r, bu_i), axis=1)
    y = jnp.einsum('ntgp,gip->ntgi', hr, c_re.astype(f32)) - jnp.einsum('ntgp,gip->ntgi', hi, c_im.astype(f32))
    y = y.reshape(n, t, SSM_WIDTH) + d.astype(f32) * uf.reshape(n, t, SSM_WIDTH)
    z = jax.nn.gelu(y)
    out = z * jax.nn.sigmoid(z @ w_glu.astype(f32))
    return out.astype(u.dtype), hr[:, -1], hi[:, -1]

def ada_mods(c, w_ada, b_ada):
    m = jax.nn.silu(c) @ w_ada + b_ada
    return [mm[:, None, :] for mm in jnp.split(m, 6, axis=-1)]

def mixer_inputs(x, c, lw):
    mods = ada_mods(c, lw['w_ada'], lw['b_ada'])
    h = rms_norm(x, lw['g_norm_mix']) * (1 + mods[1]) + mods[0]
    n, t, _ = h.shape
    proj = jnp.einsum('ntd,de->nte', h, lw['w_in'])
    offs = [int(o) for o in np.cumsum(IN_SPLITS)[:-1]]
    q, kc, vc, ks, vs, kw, vw, g_nsa, u, g_a, g_s = jnp.split(proj, offs, axis=-1)
    q = (q * HEAD_DIM ** -0.5).reshape(n, t, N_KV_HEADS, Q_PER_KV, HEAD_DIM).transpose(0, 2, 3, 1, 4)
    kvs = [a.reshape(n, t, N_KV_HEADS, HEAD_DIM) for a in (kc, vc, ks, vs, kw, vw)]
    g_nsa = jax.nn.sigmoid(g_nsa.reshape(n, t, 3, N_Q_HEADS)).transpose(2, 0, 3, 1)
    g_nsa = g_nsa.reshape(3, n, N_KV_HEADS, Q_PER_KV, t)[..., None]
    return mods, q, kvs, g_nsa, u, g_a, g_s

def finish_layer(x, mods, o_cmp, o_slc, o_win, g_nsa, o_ssm, g_a, g_s, lw):
    n, g, r, t, hd = o_cmp.shape
    o = g_nsa[0] * o_cmp + g_nsa[1] * o_slc + g_nsa[2] * o_win
    o_attn = o.transpose(0, 3, 1, 2, 4).reshape(n, t, ATTN_WIDTH)
    mixed = jax.nn.sigmoid(g_a) * (o_attn @ lw['w_br_attn']) + jax.nn.sigmoid(g_s) * (o_ssm @ lw['w_br_ssm'])
    x = x + mods[2] * (mixed @ lw['w_out'])
    h = rms_norm(x, lw['g_norm_mlp']) * (1 + mods[4]) + mods[3]
    return x + mods[5] * (jnp.square(jax.nn.relu(h @ lw['w_ff1'])) @ lw['w_ff2'])

def ssm_args(lw):
    return (lw['ssm_lambda_re'], lw['ssm_lambda_im'], lw['ssm_log_dt'], lw['ssm_b_re'], lw['ssm_b_im'],
            lw['ssm_c_re'], lw['ssm_c_im'], lw['ssm_d'], lw['w_glu'])

def prompt_layer(x, c, lw, table):
    mods, q, (k_cmp, v_cmp, k_slc, v_slc, k_win, v_win), g_nsa, u, g_a, g_s = mixer_inputs(x, c, lw)
    n, t, _ = x.shape
    q_pos = jnp.arange(t)
    kc = compress(k_cmp, lw['cmp_pe'][0], lw['cmp_w1'][0], lw['cmp_b1'][0], lw['cmp_w2'][0])
    vc = compress(v_cmp, lw['cmp_pe'][1], lw['cmp_w1'][1], lw['cmp_b1'][1], lw['cmp_w2'][1])
    dist = q_pos[:, None] - cmp_ends(kc.shape[1])[None, :]
    o_cmp, p_cmp = attend_shared(q, kc, vc, dist, dist >= 0, table)
    idx, ok = select_blocks(jnp.sum(p_cmp, axis=2), q_pos, -(-t // SLC_BLOCK))
    o_slc = slc_prompt(q, k_slc, v_slc, idx, ok, table)
    o_win = win_prompt(q, k_win, v_win, table)
    zeros = jnp.zeros((n, N_SSM_GROUPS, SSM_STATE), jnp.float32)
    o_ssm, s_re, s_im = s5_ssm(u, zeros, zeros, *ssm_args(lw))
    y = finish_layer(x, mods, o_cmp, o_slc, o_win, g_nsa, o_ssm, g_a, g_s, lw)
    keep = min(WINDOW, t)
    return y, (k_cmp, v_cmp, k_slc, v_slc, k_win[:, t - keep:], v_win[:, t - keep:], s_re, s_im)

def sample_layer(x, c, lw, layer, cache_k_cmp, cache_v_cmp, cache_k_slc, cache_v_slc,
                 cache_k_win, cache_v_win, state_ssm_re, state_ssm_im, page_table, table):
    mods, q, (k_cmp, v_cmp, k_slc, v_slc, k_win, v_win), g_nsa, u, g_a, g_s = mixer_inputs(x, c, lw)
    n, t, _ = x.shape
    past_len = page_table.shape[1] * PAGE_SIZE
    q_pos = past_len + jnp.arange(t)
    k_past = cache_k_cmp[layer, page_table].reshape(n, past_len, N_KV_HEADS, HEAD_DIM)
    v_past = cache_v_cmp[layer, page_table].reshape(n, past_len, N_KV_HEADS, HEAD_DIM)
    k_all = jnp.concatenate([k_past, k_cmp.astype(k_past.dtype)], axis=1)
    v_all = jnp.concatenate([v_past, v_cmp.astype(v_past.dtype)], axis=1)
    kc = compress(k_all, lw['cmp_pe'][0], lw['cmp_w1'][0], lw['cmp_b1'][0], lw['cmp_w2'][0])
    vc = compress(v_all, lw['cmp_pe'][1], lw['cmp_w1'][1], lw['cmp_b1'][1], lw['cmp_w2'][1])
    dist = q_pos[:, None] - cmp_ends(kc.shape[1])[None, :]
    o_cmp, p_cmp = attend_shared(q, kc, vc, dist, dist >= 0, table)
    idx, ok = select_blocks(jnp.sum(p_cmp, axis=2), q_pos, -(-(past_len + t) // SLC_BLOCK))
    o_slc = slc_sample(q, k_slc, v_slc, idx, ok, q_pos, cache_k_slc, cache_v_slc, layer, page_table, table)
    o_win, nbk, nbv = win_sample(q, k_win, v_win, cache_k_win[layer], cache_v_win[layer], q_pos, past_len, table)
    o_ssm, s_re, s_im = s5_ssm(u, state_ssm_re[layer], state_ssm_im[layer], *ssm_args(lw))
    y = finish_layer(x, mods, o_cmp, o_slc, o_win, g_nsa, o_ssm, g_a, g_s, lw)
    return y, (k_cmp, v_cmp, k_slc, v_slc, nbk, nbv, s_re, s_im)

def setup_inputs(seed: int = 0) -> dict:
    key = jax.random.key(seed)
    ks = iter(jax.random.split(key, 64))

    def normal(shape, scale):
        return scale * jax.random.normal(next(ks), shape, jnp.float32)

    n_pages = PAST_LEN // PAGE_SIZE
    n_phys = (5 * DEC_BATCH * n_pages) // 4
    w_buf = min(WINDOW, PAST_LEN)
    page_shape = (DEPTH, n_phys, PAGE_SIZE, N_KV_HEADS, HEAD_DIM)
    win_shape = (DEPTH, DEC_BATCH, w_buf, N_KV_HEADS, HEAD_DIM)
    ssm_shape = (DEPTH, DEC_BATCH, N_SSM_GROUPS, SSM_STATE)
    page_table = jax.random.permutation(next(ks), n_phys)[:DEC_BATCH * n_pages]
    page_table = page_table.reshape(DEC_BATCH, n_pages).astype(jnp.int32)
    lam_im = jnp.pi * jnp.arange(SSM_STATE, dtype=jnp.float32)
    log_dt = jax.random.uniform(next(ks), (DEPTH, N_SSM_GROUPS), jnp.float32,
                                math.log(DT_MIN), math.log(DT_MAX))
    return {
        'x_prompt': normal((BATCH, SEQ, D_MODEL), 1.0),
        'x_sample': normal((DEC_BATCH, DEC_SEQ, D_MODEL), 1.0),
        'cache_k_cmp': normal(page_shape, 1.0),
        'cache_v_cmp': normal(page_shape, 1.0),
        'cache_k_slc': normal(page_shape, 1.0),
        'cache_v_slc': normal(page_shape, 1.0),
        'cache_k_win': normal(win_shape, 1.0),
        'cache_v_win': normal(win_shape, 1.0),
        'state_ssm_re': normal(ssm_shape, 0.3),
        'state_ssm_im': normal(ssm_shape, 0.3),
        'page_table': page_table,
        'c_prompt': normal((BATCH, D_MODEL), 1.0),
        'c_sample': normal((DEC_BATCH, D_MODEL), 1.0),
        'rel_bias': normal((N_BUCKETS, N_Q_HEADS), 0.5),
        'w_ada': normal((DEPTH, D_MODEL, 6 * D_MODEL), 0.5 * D_MODEL ** -0.5),
        'b_ada': normal((DEPTH, 6 * D_MODEL), 0.02),
        'g_norm_mix': 1.0 + normal((DEPTH, D_MODEL), 0.02),
        'g_norm_mlp': 1.0 + normal((DEPTH, D_MODEL), 0.02),
        'w_in': normal((DEPTH, D_MODEL, IN_WIDTH), D_MODEL ** -0.5),
        'cmp_pe': normal((DEPTH, 2, CMP_BLOCK, HEAD_DIM), 0.02),
        'cmp_w1': normal((DEPTH, 2, CMP_BLOCK, HEAD_DIM, HEAD_DIM), (CMP_BLOCK * HEAD_DIM) ** -0.5),
        'cmp_b1': normal((DEPTH, 2, HEAD_DIM), 0.02),
        'cmp_w2': normal((DEPTH, 2, HEAD_DIM, HEAD_DIM), HEAD_DIM ** -0.5),
        'ssm_lambda_re': -0.5 + normal((DEPTH, N_SSM_GROUPS, SSM_STATE), 0.01),
        'ssm_lambda_im': lam_im + normal((DEPTH, N_SSM_GROUPS, SSM_STATE), 0.01),
        'ssm_log_dt': log_dt,
        'ssm_b_re': normal((DEPTH, N_SSM_GROUPS, SSM_STATE, SSM_GROUP), (2 * SSM_GROUP) ** -0.5),
        'ssm_b_im': normal((DEPTH, N_SSM_GROUPS, SSM_STATE, SSM_GROUP), (2 * SSM_GROUP) ** -0.5),
        'ssm_c_re': normal((DEPTH, N_SSM_GROUPS, SSM_GROUP, SSM_STATE), (2 * SSM_STATE) ** -0.5),
        'ssm_c_im': normal((DEPTH, N_SSM_GROUPS, SSM_GROUP, SSM_STATE), (2 * SSM_STATE) ** -0.5),
        'ssm_d': normal((DEPTH, SSM_WIDTH), 0.5),
        'w_glu': normal((DEPTH, SSM_WIDTH, SSM_WIDTH), SSM_WIDTH ** -0.5),
        'w_br_attn': normal((DEPTH, ATTN_WIDTH, D_MODEL), ATTN_WIDTH ** -0.5),
        'w_br_ssm': normal((DEPTH, SSM_WIDTH, D_MODEL), SSM_WIDTH ** -0.5),
        'w_out': normal((DEPTH, D_MODEL, D_MODEL), D_MODEL ** -0.5),
        'w_ff1': normal((DEPTH, D_MODEL, D_FF), D_MODEL ** -0.5),
        'w_ff2': normal((DEPTH, D_FF, D_MODEL), D_FF ** -0.5),
        'g_final': 1.0 + normal((D_MODEL,), 0.02),
    }

def reference(x_prompt, x_sample, cache_k_cmp, cache_v_cmp, cache_k_slc, cache_v_slc, cache_k_win,
              cache_v_win, state_ssm_re, state_ssm_im, page_table, c_prompt, c_sample, rel_bias,
              w_ada, b_ada, g_norm_mix, g_norm_mlp, w_in, cmp_pe, cmp_w1, cmp_b1, cmp_w2,
              ssm_lambda_re, ssm_lambda_im, ssm_log_dt, ssm_b_re, ssm_b_im, ssm_c_re, ssm_c_im,
              ssm_d, w_glu, w_br_attn, w_br_ssm, w_out, w_ff1, w_ff2, g_final):
    hp, hs = x_prompt, x_sample
    p_states, s_states = [], []
    for l in range(DEPTH):
        lw = dict(w_ada=w_ada[l], b_ada=b_ada[l], g_norm_mix=g_norm_mix[l], g_norm_mlp=g_norm_mlp[l],
                  w_in=w_in[l], cmp_pe=cmp_pe[l], cmp_w1=cmp_w1[l], cmp_b1=cmp_b1[l], cmp_w2=cmp_w2[l],
                  ssm_lambda_re=ssm_lambda_re[l], ssm_lambda_im=ssm_lambda_im[l], ssm_log_dt=ssm_log_dt[l],
                  ssm_b_re=ssm_b_re[l], ssm_b_im=ssm_b_im[l], ssm_c_re=ssm_c_re[l], ssm_c_im=ssm_c_im[l],
                  ssm_d=ssm_d[l], w_glu=w_glu[l], w_br_attn=w_br_attn[l], w_br_ssm=w_br_ssm[l],
                  w_out=w_out[l], w_ff1=w_ff1[l], w_ff2=w_ff2[l])
        hp, st = prompt_layer(hp, c_prompt, lw, rel_bias)
        p_states.append(st)
        hs, st = sample_layer(hs, c_sample, lw, l, cache_k_cmp, cache_v_cmp, cache_k_slc, cache_v_slc,
                              cache_k_win, cache_v_win, state_ssm_re, state_ssm_im, page_table, rel_bias)
        s_states.append(st)
    p_k_cmp, p_v_cmp, p_k_slc, p_v_slc, p_k_win, p_v_win, p_ssm_re, p_ssm_im = [jnp.stack(a) for a in zip(*p_states)]
    s_k_cmp, s_v_cmp, s_k_slc, s_v_slc, s_k_win, s_v_win, s_ssm_re, s_ssm_im = [jnp.stack(a) for a in zip(*s_states)]
    y_prompt = rms_norm(hp, g_final)
    y_sample = rms_norm(hs, g_final)
    return (y_prompt, y_sample,
            p_k_cmp, p_v_cmp, p_k_slc, p_v_slc, p_k_win, p_v_win, p_ssm_re, p_ssm_im,
            s_k_cmp, s_v_cmp, s_k_slc, s_v_slc, s_k_win, s_v_win, s_ssm_re, s_ssm_im)


_drawn_inputs = setup_inputs


def setup_inputs(seed=0):
    import zlib

    import numpy as np

    out = dict(_drawn_inputs(seed))
    spreads = {}
    factors = {'cache_k_cmp': 8.0,
     'cache_v_cmp': 8.0,
     'cache_k_slc': 8.0,
     'cache_v_slc': 8.0,
     'rel_bias': 6.197,
     'g_norm_mix': 2.878,
     'g_norm_mlp': 6.388,
     'cmp_pe': 8.0,
     'cmp_b1': 8.0,
     'ssm_lambda_re': 3.346,
     'ssm_c_re': 5.068,
     'ssm_c_im': 5.26,
     'w_glu': 7.858,
     'g_final': 2.71}
    for name, (base, spread) in spreads.items():
        noise = np.random.default_rng([zlib.crc32(name.encode()), seed]).standard_normal(out[name].shape)
        drawn = base * np.exp(spread * noise) if base else spread * noise
        out[name] = jnp.asarray(drawn.astype(out[name].dtype))
    for name, factor in factors.items():
        out[name] = (out[name] * factor).astype(out[name].dtype)
    return out
```

```python
from contextlib import ExitStack

import numpy as np

import concourse.bass as bass
from concourse import mybir

ALU = mybir.AluOpType
ACT = mybir.ActivationFunctionType
F32 = mybir.dt.float32
I32 = mybir.dt.int32
U32 = mybir.dt.uint32
AXX = mybir.AxisListType.X

P = 128
D = 1024
KD = D // P
T = 1024
TB = T // P
NSEQ, TS = 8, 4
NS = NSEQ * TS
NT = T + NS
SL = NT // 3
HQ, G, R, HD = 8, 2, 4, 64
KVW = G * HD
PAST, PAGE = 4096, 128
NPAGE = PAST // PAGE
NPHYS = 5 * NSEQ * NPAGE // 4
CHK = 16
WIN = 512
F = 4 * D
SSM = D // 2
SG, SI, SP = 32, 16, 64
LC = 8
NCH = T // LC
NB = 32
EPS = 1e-6
NEG = -1e30
BIG = 1e30
Q0 = 0
KV0 = HQ * HD
GN0 = KV0 + 6 * KVW
U0 = GN0 + 3 * HQ
GA0 = U0 + SSM
GS0 = GA0 + D
INW = GS0 + D
TWO_PI = 2.0 * np.pi


class Env:
    pass


def load_wait(eng, sem, n):
    eng.wait_ge(sem, 16 * n)


def stage_semaphores(nc, c, stage):
    taken = []

    def give_back():
        nc.clear_and_free_semaphores(taken)
        nc.all_engine_barrier()

    def sem(name):
        taken.append(nc.alloc_semaphore(name=f"{name}_{stage}"))
        return taken[-1]

    c.callback(give_back)
    return sem


def stage_inputs(nc, e):
    NC9 = 1 + NSEQ
    with ExitStack() as c:
        sb = lambda n, s, d=F32: c.enter_context(nc.sbuf_tensor(n, s, d))
        sem = stage_semaphores(nc, c, "in")
        xrow = sb("xrow", [P, 3, D])
        crow = sb("crow", [NC9, D])
        srow = sb("srow", [NC9, D])
        scT = sb("scT", [P, KD, NC9])
        vrow = sb("vrow", [3 * KD, P])
        brow = sb("brow", [1, 6 * D])
        one9 = sb("one9", [1, NC9])
        wada = sb("wada", [P, 2, KD, 512])
        modrow = sb("modrow", [NC9, 2, 512])
        s_const, s_cond, s_vec, s_bada = sem("s_const"), sem("s_cond"), sem("s_vec"), sem("s_bada")
        s_x = [sem(f"s_x{i}") for i in range(3)]
        s_wada = [sem(f"s_wada{i}") for i in range(2)]
        s_silu, s_one, s_cT, s_cTc, s_vT, s_vTc = (sem(n) for n in ("s_silu", "s_one", "s_cT", "s_cTc", "s_vT", "s_vTc"))
        s_xT, s_xTc, s_mod, s_modc, s_mT, s_mTc = (sem(n) for n in ("s_xT", "s_xTc", "s_mod", "s_modc", "s_mT", "s_mTc"))
        block = c.enter_context(nc.Block())
        wview = e.w_ada[0].rearrange("(k p) n -> p k n", p=P)
        NBLK = 6 * D // 512

        def tokens(tb):
            return P if tb < TB else NS

        @block.sync
        def _(sp):
            sp.dma_start(crow[0:1, :], e.c_prompt).then_inc(s_cond, 16)
            sp.dma_start(crow[1:NC9, :], e.c_sample).then_inc(s_cond, 16)
            sp.dma_start(e.consts[:, :], e.consts_in).then_inc(s_const, 16)
            sp.dma_start(brow[:, :], e.b_ada).then_inc(s_bada, 16)
            for i in range(NBLK):
                if i >= 2:
                    sp.wait_ge(s_mod, i - 1)
                sp.dma_start(wada[:, i % 2], wview[:, :, i * 512:(i + 1) * 512]).then_inc(s_wada[i % 2], 16)

        @block.gpsimd
        def _(pool):
            pool.memset(one9[:, :], 1.0).then_inc(s_one, 1)

        @block.scalar
        def _(act):
            for i, g in enumerate((e.g_norm_mix, e.g_norm_mlp, e.g_final)):
                act.dma_start(vrow[i * KD:(i + 1) * KD, :], g).then_inc(s_vec, 16)
            for tb in range(TB + 1):
                if tb >= 3:
                    act.wait_ge(s_xT, 2 * (tb - 2))
                n = tokens(tb)
                src = e.x_prompt[0, tb * P:(tb + 1) * P, :] if tb < TB else e.x_sample.rearrange("n t d -> (n t) d")
                act.dma_start(xrow[0:n, tb % 3, :], src).then_inc(s_x[tb % 3], 16)
                if tb == 2:
                    load_wait(act, s_cond, 2)
                    act.activation(srow[:, :], crow[:, :], ACT.Silu).then_inc(s_silu, 1)

        @block.tensor
        def _(pe):
            load_wait(pe, s_const, 1)
            pe.wait_ge(s_silu, 1)
            for k in range(KD):
                mm = pe.transpose(e.bank[0][:, k * NC9:(k + 1) * NC9], srow[:, k * P:(k + 1) * P], e.ident[0:NC9, 0:NC9])
            mm.then_inc(s_cT, 1)
            load_wait(pe, s_vec, 3)
            pe.transpose(e.bank[1][:, 0:3 * KD], vrow[:, :], e.ident[0:3 * KD, 0:3 * KD]).then_inc(s_vT, 1)
            for tb in range(TB + 1):
                n = tokens(tb)
                load_wait(pe, s_x[tb % 3], tb // 3 + 1)
                for h in range(2):
                    j = 2 * tb + h
                    if j >= 2:
                        pe.wait_ge(s_xTc, j - 1)
                    for k in range(4):
                        kk = 4 * h + k
                        mm = pe.transpose(e.bank[2 + h][:, k * P:k * P + n], xrow[0:n, tb % 3, kk * P:(kk + 1) * P],
                                          e.ident[0:n, 0:n])
                    mm.then_inc(s_xT, 1)
            pe.wait_ge(s_cTc, 1)
            pe.wait_ge(s_one, 1)
            load_wait(pe, s_bada, 1)

            def turn(i):
                pe.wait_ge(s_modc, i + 1)
                if i >= 2:
                    pe.wait_ge(s_mTc, i - 1)
                for q in range(4):
                    mm = pe.transpose(e.bank[6 + i % 2][:, q * NC9:(q + 1) * NC9], modrow[:, i % 2, q * P:(q + 1) * P],
                                      e.ident[0:NC9, 0:NC9])
                mm.then_inc(s_mT, 1)

            for i in range(NBLK):
                load_wait(pe, s_wada[i % 2], i // 2 + 1)
                if i >= 2:
                    pe.wait_ge(s_modc, i - 1)
                out = e.bank[4 + i % 2][0:NC9, :]
                for k in range(KD):
                    pe.matmul(out, scT[:, k, :], wada[:, i % 2, k, :], start=(k == 0), stop=False)
                pe.matmul(out, one9[:, :], brow[:, i * 512:(i + 1) * 512], start=False, stop=True).then_inc(s_mod, 1)
                if i >= 1:
                    turn(i - 1)
            turn(NBLK - 1)

        @block.vector
        def _(dve):
            dve.wait_ge(s_cT, 1)
            dve.tensor_copy(scT[:, :, :], e.bank[0][:, 0:KD * NC9].rearrange("p (k n) -> p k n", k=KD)).then_inc(s_cTc, 1)
            dve.wait_ge(s_vT, 1)
            dve.tensor_copy(e.vec[:, :], e.bank[1][:, 0:3 * KD]).then_inc(s_vTc, 1)
            for tb in range(TB + 1):
                n = tokens(tb)
                for h in range(2):
                    dve.wait_ge(s_xT, 2 * tb + h + 1)
                    dve.tensor_copy(e.xT[:, 4 * h:4 * h + 4, tb * P:tb * P + n],
                                    e.bank[2 + h][:, :].rearrange("p (k n) -> p k n", k=4)[:, :, 0:n]).then_inc(s_xTc, 1)

            def keep(i):
                dve.wait_ge(s_mT, i + 1)
                dve.tensor_copy(e.mod[:, 4 * i:4 * i + 4, :],
                                e.bank[6 + i % 2][:, 0:4 * NC9].rearrange("p (q n) -> p q n", q=4)).then_inc(s_mTc, 1)

            for i in range(NBLK):
                dve.wait_ge(s_mod, i + 1)
                if i >= 2:
                    dve.wait_ge(s_mT, i - 1)
                dve.tensor_copy(modrow[:, i % 2, :], e.bank[4 + i % 2][0:NC9, :]).then_inc(s_modc, 1)
                if i >= 1:
                    keep(i - 1)
            keep(NBLK - 1)


def stage_norm(nc, e, tag, src, dst, gain, shift=None, scale=None):
    NC9 = 1 + NSEQ
    with ExitStack() as c:
        sb = lambda n, s, d=F32: c.enter_context(nc.sbuf_tensor(n + tag, s, d))
        sem = stage_semaphores(nc, c, "norm" + tag)
        sq = sb("sq", [P, 4, SL])
        rstd = sb("rstd", [P, NT])
        amp = sb("amp", [P, KD, NC9])
        s_sq, s_ssq, s_sqrt, s_amp, s_r, s_n, s_h = (sem(n) for n in ("s_sq", "s_ssq", "s_sqrt", "s_amp", "s_r", "s_n", "s_h"))
        block = c.enter_context(nc.Block())
        NU = 3 * KD

        @block.scalar
        def _(act):
            for i in range(NU):
                s, k = i // KD, i % KD
                if i >= 4:
                    act.wait_ge(s_ssq, i - 3)
                act.activation(sq[:, i % 4, :], src[:, k, s * SL:(s + 1) * SL], ACT.Square).then_inc(s_sq, 1)
            act.wait_ge(s_ssq, NU)
            for s in range(3):
                act.activation(rstd[:, s * SL:(s + 1) * SL], e.bank[s][:, 0:SL], ACT.Sqrt, bias=e.eps, scale=1.0 / D)\
                   .then_inc(s_sqrt, 1)

        @block.tensor
        def _(pe):
            for i in range(NU):
                s, k = i // KD, i % KD
                pe.wait_ge(s_sq, i + 1)
                pe.matmul(e.bank[s][:, 0:SL], e.ones[:, :], sq[:, i % 4, :], start=(k == 0), stop=(k == KD - 1))\
                  .then_inc(s_ssq, 1)

        @block.vector
        def _(dve):
            g = e.vec[:, gain * KD:(gain + 1) * KD]
            if scale is not None:
                dve.tensor_scalar(amp[:, :, :], e.mod[:, scale * KD:(scale + 1) * KD, :], 1.0, None, ALU.add).then_inc(s_amp, 1)
                dve.wait_ge(s_amp, 1)
                dve.tensor_tensor(amp[:, :, :], amp[:, :, :], g.unsqueeze(2).to_broadcast([P, KD, NC9]), ALU.mult)\
                   .then_inc(s_amp, 1)
            for s in range(3):
                dve.wait_ge(s_sqrt, s + 1)
                dve.reciprocal(rstd[:, s * SL:(s + 1) * SL], rstd[:, s * SL:(s + 1) * SL]).then_inc(s_r, 1)
            dve.wait_ge(s_r, 3)
            if scale is not None:
                dve.wait_ge(s_amp, 2)
            for k in range(KD):
                dve.tensor_tensor(dst[:, k, :], src[:, k, :], rstd[:, :], ALU.mult).then_inc(s_n, 1)
                dve.wait_ge(s_n, k + 1)
                if scale is None:
                    dve.tensor_scalar(dst[:, k, :], dst[:, k, :], g[:, k:k + 1], None, ALU.mult).then_inc(s_h, 1)
                    continue
                dve.tensor_scalar(dst[:, k, 0:T], dst[:, k, 0:T], amp[:, k, 0:1], e.mod[:, shift * KD + k, 0:1],
                                  ALU.mult, ALU.add).then_inc(s_h, 1)
                ds = dst[:, k, T:NT].rearrange("p (n t) -> p n t", t=TS)
                dve.tensor_tensor(ds, ds, amp[:, k, 1:NC9].unsqueeze(2).to_broadcast([P, NSEQ, TS]), ALU.mult)\
                   .then_inc(s_h, 1)
                dve.wait_ge(s_h, 3 * k + 2)
                dve.tensor_tensor(ds, ds, e.mod[:, shift * KD + k, 1:NC9].unsqueeze(2).to_broadcast([P, NSEQ, TS]),
                                  ALU.add).then_inc(s_h, 1)


NJ = SG // 2
E1 = NCH + 1


def stage_ssm(nc, e):
    MAGIC = float(1.5 * 2 ** 23)
    PI2 = float(np.nextafter(np.float32(TWO_PI), np.float32(0)))
    NP = 2 * LC + 1
    with ExitStack() as c:
        sb = lambda n, s, d=F32: c.enter_context(nc.sbuf_tensor(n, s, d))
        sem = stage_semaphores(nc, c, "ssm")
        U = sb("U", [P, SG, LC, SI])
        small = sb("small", [SI, SG * LC * SI])
        Us = small[0:NSEQ, :].rearrange("p (g k i) -> p g k i", g=SG, k=LC)
        hall = small[:, :].rearrange("p (g k i) -> p g k i", g=SG, k=LC)
        Y = U[:, :, :, :].rearrange("p g k i -> p (g k i)").rearrange("p (k g i) -> p k g i", k=LC, g=SG)
        Ys = small[0:NSEQ, 0:SG * TS * SI].rearrange("p (k g i) -> p k g i", g=SG, k=TS)
        UT = sb("UT", [P, SG, NCH + NSEQ])
        wu = sb("wu", [P, KD, SSM])
        Gre = wu[:, 0:4, :].rearrange("p a (b k i) -> p (a b) k i", b=4, k=LC)
        Gim = wu[:, 4:8, :].rearrange("p a (b k i) -> p (a b) k i", b=4, k=LC)
        wglu = wu[:, 0:4, :]
        big = sb("big", [P, 4 * NT])
        ET = big[:, 0:2 * NJ * P].rearrange("p (c j m) -> p c j m", c=2, j=NJ)
        Tm = big[:, 0:SG * P].rearrange("p (g k o) -> p g k o", g=SG, k=LC)
        zT = big[:, :].rearrange("p (q t) -> p q t", q=4)
        Fre = sb("Fre", [P, NJ, LC + 1, SI])
        Fim = sb("Fim", [P, NJ, LC + 1, SI])
        rtab = e.ossmT[:, :, :].rearrange("p q t -> p (q t)")
        Rre = rtab[:, 0:NJ * E1].rearrange("p (j n) -> p j n", j=NJ)
        Rim = rtab[:, NJ * E1:2 * NJ * E1].rearrange("p (j n) -> p j n", j=NJ)
        Sre = sb("Sre", [P, NJ, E1])
        Sim = sb("Sim", [P, NJ, E1])
        H8 = NJ // 2
        M = sb("M", [P, H8, E1])
        t0 = sb("t0", [P, H8, E1])
        t1 = sb("t1", [P, H8, E1])
        Bre = sb("Bre", [P, NJ, SI])
        Bim = sb("Bim", [P, NJ, SI])
        BBre = sb("BBre", [P, NJ, SI])
        BBim = sb("BBim", [P, NJ, SI])
        cdup = big[:, 0:16 * SP].rearrange("p (c q d s) -> p c q d s", c=2, q=4, d=2)
        CT = sb("CT", [P, 2, NJ, SI])
        lamrow = sb("lamrow", [NJ, 2, P])
        ldt = sb("ldt", [1, SG])
        x0 = sb("x0", [P, 2, NSEQ, NJ])
        xs = sb("xs", [P, 2, NSEQ, NJ])
        xt = sb("xt", [P, NSEQ, NJ])
        dtb = sb("dtb", [P, SG])
        dtj = sb("dtj", [P, NJ])
        lam = sb("lam", [P, 2, NJ])
        dT = sb("dT", [SI, SG])
        dI = sb("dI", [SI, SG, SI])
        v = sb("v", [P, 8, NJ])
        w1 = sb("w1", [P, 4, NJ])
        w2 = sb("w2", [P, 4, NJ])
        angles = lambda m: m[:, :, :].rearrange("p j n -> p (j n)")[:, 0:2 * NJ * NP].rearrange("p (c j n) -> p c j n", c=2, j=NJ)
        ang, rnd = angles(M), angles(t1)
        trig = sb("trig", [P, 2, NJ, NP])
        mag = sb("mag", [P, NJ, NP])
        pw = sb("pw", [P, 2, NJ, NP])
        finrow = sb("finrow", [P, 4, P])
        x0row = finrow[:, 0:2, :]
        names = ("s_wu s_lam s_ldt s_b s_c s_x0 s_d s_glu s_ut s_um s_uc s_uT s_uTc s_zero s_lamT s_dt s_x0T s_cT s_exp"
                 " s_mag s_trig s_ptr s_gT s_gTc s_h s_hc s_tm s_et s_bu s_sc s_y s_yc s_ys s_fin s_finc s_zT s_zTc"
                 " s_gl s_sig s_glc s_r s_pchain s_dchain s_ready s_ask s_ttz s_hz s_trot s_setr s_bs s_hall").split()
        S = {n: sem(n) for n in names}
        block = c.enter_context(nc.Block())
        ident = e.ident
        NU = LC + TS
        NG3 = -(-SG // 3)
        bank = e.bank

        @block.sync
        def _(sp):
            sp.dma_start(wu[:, :, :], e.w_in[0].rearrange("(k p) n -> p k n", p=P)[:, :, U0:U0 + SSM]).then_inc(S["s_wu"], 16)
            for i, l in enumerate((e.lam_re, e.lam_im)):
                sp.dma_start(lamrow[:, i, :], l[0].rearrange("(j g) p -> j (g p)", g=2)).then_inc(S["s_lam"], 16)
            sp.dma_start(ldt[:, :], e.log_dt).then_inc(S["s_ldt"], 16)
            for b, s in ((Bre, e.b_re), (Bim, e.b_im)):
                sp.dma_start(b[:, :, :], s[0].rearrange("(j g) p i -> (g p) j i", g=2)).then_inc(S["s_b"], 16)
            for i, s in enumerate((e.c_re, e.c_im)):
                for q in range(4):
                    for d in range(2):
                        sp.dma_start(cdup[:, i, q, d, :], s[0, 8 * q:8 * q + 8].rearrange("g o p -> (g o) p")).then_inc(S["s_c"], 16)
            for i, s in enumerate((e.state_re, e.state_im)):
                sp.dma_start(x0row[:, i, :], s[0].rearrange("n (j g) p -> (n j) (g p)", g=2)).then_inc(S["s_x0"], 16)
            sp.dma_start(dT[:, :], e.ssm_d[0].rearrange("(g i) -> i g", i=SI), allow_slow_non_contiguous=True).then_inc(S["s_d"], 16)
            sp.wait_ge(S["s_hall"], 1)
            sp.wait_ge(S["s_ttz"], 1)
            for k in range(LC):
                sp.dma_start(Tm[SI * k:SI * (k + 1), :, k:LC, :], hall[:, :, 0:LC - k, :]).then_inc(S["s_tm"], 16)
            sp.wait_ge(S["s_gT"], 8)
            sp.dma_start(wglu, e.w_glu[0].rearrange("(k p) n -> p k n", p=P)).then_inc(S["s_glu"], 16)
            sp.wait_ge(S["s_finc"], 1)
            for i, o in enumerate((e.p_re, e.p_im)):
                sp.dma_start(o[0, 0].rearrange("(j g) p -> j (g p)", g=2), finrow[0:NJ, i, :]).then_inc(e.states_stored, 16)
            for i, o in enumerate((e.s_re, e.s_im)):
                sp.dma_start(o[0].rearrange("n (j g) p -> (n j) (g p)", g=2), finrow[:, 2 + i, :]).then_inc(e.states_stored, 16)
            load_wait(sp, e.states_stored, 4)

        @block.gpsimd
        def _(pool):
            n = [0]

            def link(ins):
                n[0] += 1
                ins.then_inc(S["s_pchain"], 1)
                pool.wait_ge(S["s_pchain"], n[0])

            pool.memset(small[0:NSEQ, :], 0.0).then_inc(S["s_zero"], 1)
            link(pool.memset(Rre[:, :, 0:2], 1.0))
            link(pool.memset(Rim[:, :, 0:2], 0.0))
            pool.wait_ge(S["s_ptr"], 1)
            wr, wi, wr2, wi2 = w1[:, 0, :], w1[:, 1, :], w2[:, 0, :], w2[:, 1, :]
            link(pool.tensor_copy(wr, trig[:, 0, :, LC]))
            link(pool.tensor_copy(wi, trig[:, 1, :, LC]))
            m = 1
            while m < NCH:
                wrb = wr.unsqueeze(2).to_broadcast([P, NJ, m])
                wib = wi.unsqueeze(2).to_broadcast([P, NJ, m])
                ar, ai = Rre[:, :, 1:1 + m], Rim[:, :, 1:1 + m]
                br, bi = Rre[:, :, 1 + m:1 + 2 * m], Rim[:, :, 1 + m:1 + 2 * m]
                tt = Sre[:, :, 0:m]
                t2 = Sim[:, :, 0:m]
                link(pool.tensor_tensor(br, ar, wrb, ALU.mult))
                link(pool.tensor_tensor(tt, ai, wib, ALU.mult))
                link(pool.tensor_tensor(br, br, tt, ALU.subtract))
                link(pool.tensor_tensor(bi, ar, wib, ALU.mult))
                link(pool.tensor_tensor(t2, ai, wrb, ALU.mult))
                link(pool.tensor_tensor(bi, bi, t2, ALU.add))
                if 2 * m < NCH:
                    link(pool.tensor_tensor(wr2, wr, wr, ALU.mult))
                    link(pool.tensor_tensor(wi2, wi, wi, ALU.mult))
                    link(pool.tensor_tensor(wi, wr, wi, ALU.mult))
                    link(pool.tensor_tensor(wr, wr2, wi2, ALU.subtract))
                    link(pool.tensor_tensor(wi, wi, wi, ALU.add))
                m *= 2
            pool.sem_inc(S["s_r"], 1)

        @block.tensor
        def _(pe):
            load_wait(pe, S["s_lam"], 2)
            for i in range(2):
                mm = pe.transpose(bank[0][:, i * NJ:(i + 1) * NJ], lamrow[:, i, :], ident[0:NJ, 0:NJ])
            mm.then_inc(S["s_lamT"], 1)
            load_wait(pe, S["s_ldt"], 1)
            pe.matmul(bank[1][:, 0:SG], e.ones[0:1, :], ldt[:, :], start=True, stop=True).then_inc(S["s_dt"], 1)
            load_wait(pe, S["s_x0"], 2)
            for i in range(2):
                mm = pe.transpose(bank[2][:, i * P:(i + 1) * P], x0row[:, i, :], ident[:, :])
            mm.then_inc(S["s_x0T"], 1)
            load_wait(pe, S["s_c"], 16)
            for i in range(2):
                for q in range(4):
                    mm = pe.transpose(bank[3 + i][:, q * P:(q + 1) * P], cdup[:, i, q, :, :].rearrange("p d s -> p (d s)"), ident[:, :])
            mm.then_inc(S["s_cT"], 1)
            load_wait(pe, S["s_wu"], 1)
            for i in range(NU):
                m = P if i < LC else NSEQ
                if i >= 2:
                    pe.wait_ge(S["s_uc"], i - 1)
                for k in range(KD):
                    lhs = e.hT[:, k, 0:T].rearrange("p (c k) -> p c k", k=LC)[:, :, i] if i < LC else \
                        e.hT[:, k, T:NT].rearrange("p (n t) -> p n t", t=TS)[:, :, i - LC]
                    mm = pe.matmul(bank[6 + i % 2][0:m, :], lhs, wu[:, k, :], start=(k == 0), stop=(k == KD - 1))
                mm.then_inc(S["s_um"], 1)
            pe.wait_ge(S["s_uc"], NU)
            for b in range(NG3):
                if b >= 2:
                    pe.wait_ge(S["s_uTc"], b - 1)
                for g in range(3 * b, min(3 * b + 3, SG)):
                    o = (g - 3 * b) * (NCH + NSEQ)
                    pe.transpose(bank[6 + b % 2][:, o:o + NCH], U[:, g, :, :].rearrange("p k i -> p (k i)"), ident[:, :])
                    mm = pe.transpose(bank[6 + b % 2][:, o + NCH:o + NCH + NSEQ], Us[:, g, :, :].rearrange("p k i -> p (k i)"),
                                      ident[0:NSEQ, 0:NSEQ])
                mm.then_inc(S["s_uT"], 1)
            pe.wait_ge(S["s_ask"], 1)
            for b in range(8):
                if b >= 2:
                    pe.wait_ge(S["s_gTc"], b - 1)
                elif b == 0:
                    pe.wait_ge(S["s_uTc"], NG3)
                for q in range(4):
                    x = 4 * b + q
                    Gx = (Gre, Gim)[x // NJ]
                    mm = pe.transpose(bank[6 + b % 2][:, q * P:(q + 1) * P], Gx[:, x % NJ, :, :].rearrange("p k i -> p (k i)"), ident[:, :])
                    if q == 3:
                        mm.then_inc(S["s_gT"], 1)
            for b in range(4):
                pe.wait_ge(S["s_hc"], 2 * b - 2) if b >= 2 else pe.wait_ge(S["s_gTc"], 8)
                for q in range(8):
                    g = 8 * b + q
                    j, h = g // 2, 64 * (g % 2)
                    o = bank[4 + 2 * (b % 2) + g % 2][0:SI, q // 2 * P:(q // 2 + 1) * P]
                    pe.matmul(o, BBre[h:h + SP, j, :], Fre[h:h + SP, j, 0:LC, :].rearrange("p l o -> p (l o)"), start=True, stop=False)
                    mm = pe.matmul(o, BBim[h:h + SP, j, :], Fim[h:h + SP, j, 0:LC, :].rearrange("p l o -> p (l o)"), start=False, stop=True)
                    if q >= 6:
                        mm.then_inc(S["s_h"], 1)
            for half in range(2):
                if half:
                    pe.wait_ge(S["s_sc"], 1)
                else:
                    pe.wait_ge(S["s_gTc"], 8)
                for ci in range(2):
                    for jj in range(H8):
                        j = half * H8 + jj
                        for h in range(2):
                            mm = pe.matmul(bank[2 * ci + jj // 4][64 * h:64 * h + 64, (jj % 4) * P:(jj % 4 + 1) * P],
                                           ET[:, ci, j, 64 * h:64 * h + 64], UT[:, 2 * j + h, 0:NCH], start=True, stop=True)
                mm.then_inc(S["s_bu"], 1)
            for ci in range(2):
                for j in range(NJ):
                    for h in range(2):
                        o = ci * P + j * NSEQ
                        mm = pe.matmul(bank[4][64 * h:64 * h + 64, o:o + NSEQ], ET[:, ci, j, 64 * h:64 * h + 64],
                                       UT[:, 2 * j + h, NCH:NCH + NSEQ], start=True, stop=True)
            mm.then_inc(S["s_bs"], 1)
            pe.wait_ge(S["s_fin"], 1)
            for i, s in enumerate((Sre, Sim)):
                pe.transpose(bank[0][0:NJ, i * P:(i + 1) * P], s[:, :, NCH], ident[:, :])
            for i in range(2):
                mm = pe.transpose(bank[0][:, (2 + i) * P:(3 + i) * P], xs[:, i, :, :].rearrange("p n j -> p (n j)"), ident[:, :])
            mm.then_inc(S["s_setr"], 1)
            load_wait(pe, S["s_tm"], LC)
            pe.wait_ge(S["s_hc"], 8)
            for b in range(4):
                if b >= 2:
                    pe.wait_ge(S["s_yc"], 2 * b - 2)
                for q in range(8):
                    g = 8 * b + q
                    j, h = g // 2, 64 * (g % 2)
                    o = bank[4 + 2 * (b % 2) + g % 2][:, q // 2 * P:(q // 2 + 1) * P]
                    pe.matmul(o, UT[:, g, 0:NCH], Tm[:, g, :, :].rearrange("p k o -> p (k o)"), start=True, stop=False)
                    pe.matmul(o, Sre[h:h + SP, j, 0:NCH], Fre[h:h + SP, j, 1:LC + 1, :].rearrange("p l o -> p (l o)"), start=False, stop=False)
                    mm = pe.matmul(o, Sim[h:h + SP, j, 0:NCH], Fim[h:h + SP, j, 1:LC + 1, :].rearrange("p l o -> p (l o)"), start=False, stop=True)
                    if q >= 6:
                        mm.then_inc(S["s_y"], 1)
            for b in range(4):
                if b >= 2:
                    pe.wait_ge(S["s_ys"], 2 * b - 2)
                if b == 1:
                    pe.wait_ge(S["s_finc"], 1)
                for q in range(8):
                    g = 8 * b + q
                    j, h = g // 2, 64 * (g % 2)
                    o = bank[2 - 2 * (b % 2) + g % 2][0:NSEQ, q // 2 * 64:(q // 2 + 1) * 64]
                    pe.matmul(o, UT[:, g, NCH:NCH + NSEQ], Tm[:, g, TS:LC, :].rearrange("p k o -> p (k o)"), start=True, stop=False)
                    pe.matmul(o, x0[h:h + SP, 0, :, j], Fre[h:h + SP, j, 1:TS + 1, :].rearrange("p l o -> p (l o)"), start=False, stop=False)
                    mm = pe.matmul(o, x0[h:h + SP, 1, :, j], Fim[h:h + SP, j, 1:TS + 1, :].rearrange("p l o -> p (l o)"), start=False, stop=True)
                    if q >= 6:
                        mm.then_inc(S["s_y"], 1)
            pe.wait_ge(S["s_yc"], 8)
            pe.wait_ge(S["s_ys"], 8)
            for b in range(LC):
                if b >= 2:
                    pe.wait_ge(S["s_zTc"], b - 1)
                for q in range(4):
                    mm = pe.transpose(bank[6 + b % 2][:, q * P:(q + 1) * P], Y[:, b, 8 * q:8 * q + 8, :].rearrange("p g i -> p (g i)"), ident[:, :])
                mm.then_inc(S["s_zT"], 1)
            pe.wait_ge(S["s_zTc"], 7)
            for k in range(TS):
                for q in range(4):
                    o = (k * 4 + q) * NSEQ
                    mm = pe.transpose(bank[6][:, o:o + NSEQ], Ys[:, k, 8 * q:8 * q + 8, :].rearrange("p g i -> p (g i)"), ident[0:NSEQ, 0:NSEQ])
            mm.then_inc(S["s_zT"], 1)
            pe.wait_ge(S["s_zTc"], LC + 1)
            load_wait(pe, S["s_glu"], 1)
            for f in range(4):
                for s in range(3):
                    i = 3 * f + s
                    if i >= 4:
                        pe.wait_ge(S["s_sig"], i - 3)
                    for k in range(4):
                        mm = pe.matmul(bank[i % 4][:, 0:SL], wglu[:, k, f * P:(f + 1) * P], zT[:, k, s * SL:(s + 1) * SL],
                                       start=(k == 0), stop=(k == 3))
                    mm.then_inc(S["s_gl"], 1)

        @block.scalar
        def _(act):
            act.wait_ge(S["s_dt"], 1)
            act.activation(dtb[:, :], bank[1][:, 0:SG], ACT.Exp).then_inc(S["s_exp"], 1)
            act.wait_ge(S["s_zero"], 1)
            for i in range(NU):
                act.wait_ge(S["s_um"], i + 1)
                m, dst, k = (P, U, i) if i < LC else (NSEQ, Us, TS + i - LC)
                act.activation(dst[:, :, k, :], bank[6 + i % 2][0:m, :].rearrange("p (g i) -> p g i", g=SG), ACT.Copy)\
                   .then_inc(S["s_uc"], 1)
            for b in range(NG3):
                g0, g1 = 3 * b, min(3 * b + 3, SG)
                act.wait_ge(S["s_uT"], b + 1)
                act.activation(UT[:, g0:g1, :], bank[6 + b % 2][:, 0:(g1 - g0) * (NCH + NSEQ)].rearrange("p (g n) -> p g n", g=g1 - g0),
                               ACT.Copy).then_inc(S["s_uTc"], 1)
            act.wait_ge(S["s_mag"], 1)
            act.activation(mag[:, :, :], mag[:, :, :], ACT.Exp).then_inc(S["s_exp"], 1)
            act.wait_ge(S["s_trig"], 1)
            act.activation(trig[:, :, :, :], ang[:, :, :, :], ACT.Sin, scale=PI2).then_inc(S["s_ptr"], 1)
            for b in range(8):
                act.wait_ge(S["s_gT"], b + 1)
                x = 4 * b
                act.activation(ET[:, x // NJ, x % NJ:x % NJ + 4, :], bank[6 + b % 2][:, :].rearrange("p (q m) -> p q m", q=4), ACT.Copy)\
                   .then_inc(S["s_gTc"], 1)
            act.wait_ge(S["s_uT"], NG3)
            for x in range(8):
                b, h = x // 2, x % 2
                act.wait_ge(S["s_h"], x + 1)
                act.activation(hall[:, 8 * b + h:8 * b + 8:2, :, :], bank[4 + 2 * (b % 2) + h][0:SI, :].rearrange("p (g k o) -> p g k o", g=4, k=LC),
                               ACT.Copy).then_inc(S["s_hc"], 1)
            for x in range(8):
                b, h = x // 2, x % 2
                act.wait_ge(S["s_y"], x + 1)
                act.activation(Y[:, :, 8 * b + h:8 * b + 8:2, :], bank[4 + 2 * (b % 2) + h][:, :].rearrange("p (g k o) -> p k g o", g=4, k=LC),
                               ACT.Gelu_apprx_tanh).then_inc(S["s_yc"], 1)
            for x in range(8):
                b, h = x // 2, x % 2
                act.wait_ge(S["s_y"], 8 + x + 1)
                act.activation(Ys[:, :, 8 * b + h:8 * b + 8:2, :], bank[2 - 2 * (b % 2) + h][0:NSEQ, 0:256].rearrange("p (g k o) -> p k g o", g=4, k=TS),
                               ACT.Gelu_apprx_tanh).then_inc(S["s_ys"], 1)
            for b in range(LC):
                act.wait_ge(S["s_zT"], b + 1)
                act.activation(zT[:, :, 0:T].rearrange("p q (c k) -> p q c k", k=LC)[:, :, :, b],
                               bank[6 + b % 2][:, :].rearrange("p (q c) -> p q c", q=4), ACT.Copy).then_inc(S["s_zTc"], 1)
            act.wait_ge(S["s_zT"], LC + 1)
            for k in range(TS):
                ins = act.activation(zT[:, :, T:NT].rearrange("p q (n t) -> p q n t", t=TS)[:, :, :, k],
                                     bank[6][:, k * 32:(k + 1) * 32].rearrange("p (q n) -> p q n", q=4), ACT.Copy)
            ins.then_inc(S["s_zTc"], 1)
            for i in range(12):
                f, s = i // 3, i % 3
                act.wait_ge(S["s_gl"], i + 1)
                act.activation(e.ossmT[:, f, s * SL:(s + 1) * SL], bank[i % 4][:, 0:SL], ACT.Sigmoid).then_inc(S["s_sig"], 1)

        @block.vector
        def _(dve):
            n = [0]

            def link(ins):
                n[0] += 1
                ins.then_inc(S["s_dchain"], 1)
                dve.wait_ge(S["s_dchain"], n[0])

            tt, ts_ = dve.tensor_tensor, dve.tensor_scalar
            dve.wait_ge(S["s_exp"], 1)
            link(dve.tensor_copy(dtj[0:64, :], dtb[0:64, :].rearrange("p (j g) -> p j g", g=2)[:, :, 0]))
            link(dve.tensor_copy(dtj[64:128, :], dtb[64:128, :].rearrange("p (j g) -> p j g", g=2)[:, :, 1]))
            dve.wait_ge(S["s_lamT"], 1)
            link(ts_(lam[:, 0, :], bank[0][:, 0:NJ], -1e-4, None, ALU.min))
            link(dve.tensor_copy(lam[:, 1, :], bank[0][:, NJ:2 * NJ]))
            lr, li = lam[:, 0, :], lam[:, 1, :]
            a1, th = v[:, 0, :], v[:, 1, :]
            link(tt(a1, lr, dtj[:, :], ALU.mult))
            link(tt(th, li, dtj[:, :], ALU.mult))
            link(ts_(th, th, float(1.0 / TWO_PI), None, ALU.mult))
            pows = e.consts[:, C_POW:C_POW + NP].unsqueeze(1).to_broadcast([P, NJ, NP])
            wide = lambda a: a.unsqueeze(2).to_broadcast([P, NJ, NP])
            tt(mag[:, :, :], wide(a1), pows, ALU.mult).then_inc(S["s_mag"], 1)
            link(tt(ang[:, 1, :, :], wide(th), pows, ALU.mult))
            link(ts_(ang[:, 0, :, :], ang[:, 1, :, :], 0.25, None, ALU.add))
            link(ts_(rnd[:, :, :, :], ang[:, :, :, :], MAGIC, None, ALU.add))
            link(ts_(rnd[:, :, :, :], rnd[:, :, :, :], MAGIC, None, ALU.subtract))
            link(tt(ang[:, :, :, :], ang[:, :, :, :], rnd[:, :, :, :], ALU.subtract))
            dve.sem_inc(S["s_trig"], 1)
            dve.wait_ge(S["s_ptr"], 1)
            dve.wait_ge(S["s_exp"], 2)
            for i in range(2):
                link(tt(pw[:, i, :, :], mag[:, :, :], trig[:, i, :, :], ALU.mult))
            pr, pi = pw[:, 0, :, :], pw[:, 1, :, :]
            am, den, fr, fi, x = v[:, 2, :], v[:, 3, :], v[:, 4, :], v[:, 5, :], v[:, 6, :]
            link(ts_(am, pr[:, :, 1], -1.0, None, ALU.add))
            link(tt(den, lr, lr, ALU.mult))
            link(tt(x, li, li, ALU.mult))
            link(tt(den, den, x, ALU.add))
            link(dve.reciprocal(den, den))
            link(tt(fr, am, lr, ALU.mult))
            link(tt(x, pi[:, :, 1], li, ALU.mult))
            link(tt(fr, fr, x, ALU.add))
            link(tt(fr, fr, den, ALU.mult))
            link(tt(fi, pi[:, :, 1], lr, ALU.mult))
            link(tt(x, am, li, ALU.mult))
            link(tt(fi, fi, x, ALU.subtract))
            link(tt(fi, fi, den, ALU.mult))
            load_wait(dve, S["s_b"], 2)
            frb, fib = (a.unsqueeze(2).to_broadcast([P, NJ, SI]) for a in (fr, fi))
            tb = t0[:, :, :].rearrange("p j n -> p (j n)")[:, 0:NJ * SI].rearrange("p (j i) -> p j i", i=SI)
            link(tt(BBre[:, :, :], Bre[:, :, :], frb, ALU.mult))
            link(tt(tb, Bim[:, :, :], fib, ALU.mult))
            link(tt(BBre[:, :, :], BBre[:, :, :], tb, ALU.subtract))
            link(tt(BBim[:, :, :], Bim[:, :, :], frb, ALU.mult))
            link(tt(tb, Bre[:, :, :], fib, ALU.mult))
            link(tt(BBim[:, :, :], BBim[:, :, :], tb, ALU.add))
            dve.wait_ge(S["s_cT"], 1)
            for i in range(2):
                src = bank[3 + i][:, :].rearrange("p (j g o) -> p j g o", g=2, o=SI)
                for h in range(2):
                    link(dve.tensor_copy(CT[64 * h:64 * h + 64, i, :, :], src[64 * h:64 * h + 64, :, h, :]))
            dve.wait_ge(S["s_x0T"], 1)
            link(dve.tensor_copy(x0[:, :, :, :], bank[2][:, 0:2 * P].rearrange("p (c n j) -> p c n j", c=2, n=NSEQ)))
            dve.wait_ge(S["s_um"], NU)
            tG = lambda a, k, s: a[:, :, k].unsqueeze(2).to_broadcast([P, NJ, s])
            tg = t0[:, :, :].rearrange("p j n -> p (j n)")[:, 0:NJ * SI].rearrange("p (j i) -> p j i", i=SI)
            for k in range(LC):
                q = LC + 1 + k
                link(tt(Gre[:, :, k, :], BBre[:, :, :], tG(pr, q, SI), ALU.mult))
                link(tt(tg, BBim[:, :, :], tG(pi, q, SI), ALU.mult))
                link(tt(Gre[:, :, k, :], Gre[:, :, k, :], tg, ALU.subtract))
                link(tt(Gim[:, :, k, :], BBim[:, :, :], tG(pr, q, SI), ALU.mult))
                link(tt(tg, BBre[:, :, :], tG(pi, q, SI), ALU.mult))
                link(tt(Gim[:, :, k, :], Gim[:, :, k, :], tg, ALU.add))
            for l in range(LC + 1):
                cr, cim = CT[:, 0, :, :], CT[:, 1, :, :]
                link(tt(Fre[:, :, l, :], cr, tG(pr, l, SI), ALU.mult))
                link(tt(tg, cim, tG(pi, l, SI), ALU.mult))
                link(tt(Fre[:, :, l, :], Fre[:, :, l, :], tg, ALU.subtract))
                link(tt(Fim[:, :, l, :], cr, tG(pi, l, SI), ALU.mult))
                link(tt(tg, cim, tG(pr, l, SI), ALU.mult))
                link(dve.scalar_tensor_tensor(out=Fim[:, :, l, :], in0=Fim[:, :, l, :], scalar=-1.0, in1=tg,
                                              op0=ALU.mult, op1=ALU.subtract))
            dve.sem_inc(S["s_ask"], 1)
            load_wait(dve, S["s_d"], 1)
            link(tt(dI[:, :, :], dT[:, :].unsqueeze(2).to_broadcast([SI, SG, SI]),
                    ident[0:SI, 0:SI].unsqueeze(1).to_broadcast([SI, SG, SI]), ALU.mult))
            dve.wait_ge(S["s_hc"], 8)
            tt(hall[:, :, 0, :], hall[:, :, 0, :], dI[:, :, :], ALU.add).then_inc(S["s_hall"], 1)
            dve.wait_ge(S["s_r"], 1)
            for half in range(2):
                j0 = half * H8
                jj = slice(j0, j0 + H8)
                link(dve.tensor_copy(M[:, :, :], mag[:, jj, LC].unsqueeze(2).to_broadcast([P, H8, E1])))
                link(dve.memset(M[:, :, 0], 0.0))
                link(dve.memset(Sre[:, jj, 0], 0.0))
                link(dve.memset(Sim[:, jj, 0], 0.0))
                dve.wait_ge(S["s_bu"], half + 1)
                for q in range(2):
                    qq = slice(j0 + 4 * q, j0 + 4 * q + 4)
                    br = bank[q][:, :].rearrange("p (j n) -> p j n", j=4)
                    bi = bank[2 + q][:, :].rearrange("p (j n) -> p j n", j=4)
                    rr, ri = Rre[:, qq, 1:E1], Rim[:, qq, 1:E1]
                    sr, si = Sre[:, qq, 1:E1], Sim[:, qq, 1:E1]
                    a, b = t0[:, 0:4, 1:E1], t1[:, 0:4, 1:E1]
                    link(tt(sr, br, rr, ALU.mult))
                    link(tt(a, bi, ri, ALU.mult))
                    link(tt(si, bi, rr, ALU.mult))
                    link(tt(b, br, ri, ALU.mult))
                    link(tt(sr, sr, a, ALU.add))
                    link(tt(si, si, b, ALU.subtract))
                Mf = M[:, :, :].rearrange("p j n -> p (j n)")
                for s in (Sre, Sim):
                    f = s[:, jj, :].rearrange("p j n -> p (j n)")
                    link(dve.tensor_tensor_scan(f, Mf, f, 0.0, ALU.mult, ALU.add))
                rr, ri, sr, si = Rre[:, jj, :], Rim[:, jj, :], Sre[:, jj, :], Sim[:, jj, :]
                link(tt(t0[:, :, :], sr, ri, ALU.mult))
                link(tt(t1[:, :, :], si, ri, ALU.mult))
                link(tt(sr, sr, rr, ALU.mult))
                link(tt(si, si, rr, ALU.mult))
                link(tt(sr, sr, t1[:, :, :], ALU.subtract))
                tt(si, si, t0[:, :, :], ALU.add).then_inc(S["s_sc"], 1)
                dve.wait_ge(S["s_sc"], half + 1)
            dve.wait_ge(S["s_bs"], 1)
            p4r = pr[:, :, TS].unsqueeze(1).to_broadcast([P, NSEQ, NJ])
            p4i = pi[:, :, TS].unsqueeze(1).to_broadcast([P, NSEQ, NJ])
            bs = bank[4][:, 0:2 * P].rearrange("p (c j n) -> p c n j", c=2, n=NSEQ)
            link(tt(xs[:, 0, :, :], x0[:, 0, :, :], p4r, ALU.mult))
            link(tt(xt[:, :, :], x0[:, 1, :, :], p4i, ALU.mult))
            link(tt(xs[:, 0, :, :], xs[:, 0, :, :], xt[:, :, :], ALU.subtract))
            link(tt(xs[:, 0, :, :], bs[:, 0], xs[:, 0, :, :], ALU.add))
            link(tt(xs[:, 1, :, :], x0[:, 1, :, :], p4r, ALU.mult))
            link(tt(xt[:, :, :], x0[:, 0, :, :], p4i, ALU.mult))
            link(tt(xs[:, 1, :, :], xs[:, 1, :, :], xt[:, :, :], ALU.add))
            tt(xs[:, 1, :, :], bs[:, 1], xs[:, 1, :, :], ALU.add).then_inc(S["s_fin"], 1)
            dve.memset(Tm[:, :, :, :], 0.0).then_inc(S["s_ttz"], 1)
            dve.wait_ge(S["s_setr"], 1)
            dve.tensor_copy(finrow[0:NJ, 0:2, :], bank[0][0:NJ, 0:2 * P].rearrange("p (c m) -> p c m", c=2)).then_inc(S["s_trot"], 1)
            dve.wait_ge(S["s_trot"], 1)
            dve.tensor_copy(finrow[:, 2:4, :], bank[0][:, 2 * P:4 * P].rearrange("p (c m) -> p c m", c=2)).then_inc(S["s_finc"], 1)
            for f in range(4):
                dve.wait_ge(S["s_sig"], 3 * f + 3)
                tt(e.ossmT[:, f, :], e.ossmT[:, f, :], zT[:, f, :], ALU.mult).then_inc(S["s_glc"], 1)


def stage_project(nc, e):
    with ExitStack() as c:
        sb = lambda n, s, d=F32: c.enter_context(nc.sbuf_tensor(n, s, d))
        sem = stage_semaphores(nc, c, "proj")
        wq = sb("wq", [P, KD, R, G, HD])
        wk = sb("wk", [P, KD, 6 * KVW + 3 * HQ])
        kv = sb("kv", [P, TB + 1, 6 * KVW])
        s_wq, s_wk, s_q, s_qc, s_kv, s_kvc, s_t, s_tc, s_v, s_ones = (sem(n) for n in (
            "s_wq", "s_wk", "s_q", "s_qc", "s_kv", "s_kvc", "s_t", "s_tc", "s_v", "s_ones"))
        block = c.enter_context(nc.Block())
        win = e.w_in[0].rearrange("(k p) n -> p k n", p=P)
        NQ = 3 * (R + 1)
        bank = e.bank
        rows = lambda tb: P if tb < TB else NS

        @block.sync
        def _(sp):
            for r in range(R):
                for g in range(G):
                    a = Q0 + (g * R + r) * HD
                    sp.dma_start(wq[:, :, r, g, :], win[:, :, a:a + HD]).then_inc(s_wq, 16)
            sp.dma_start(wk[:, :, :], win[:, :, KV0:U0]).then_inc(s_wk, 16)
            sp.wait_ge(s_kvc, 2 * TB)
            outs = (e.p_k_cmp, e.p_v_cmp, e.p_k_slc, e.p_v_slc)
            for i, o in enumerate(outs):
                sp.dma_start(o[0, 0].rearrange("(b p) g d -> p b (g d)", p=P), kv[:, 0:TB, i * KVW:(i + 1) * KVW]).then_inc(e.caches_stored, 16)
            for i, o in enumerate((e.p_k_win, e.p_v_win)):
                sp.dma_start(o[0, 0].rearrange("(b p) g d -> p b (g d)", p=P),
                             kv[:, TB - WIN // P:TB, (4 + i) * KVW:(5 + i) * KVW]).then_inc(e.caches_stored, 16)
            sp.wait_ge(s_kvc, 2 * TB + 2)
            for i, o in enumerate((e.s_k_cmp, e.s_v_cmp, e.s_k_slc, e.s_v_slc)):
                sp.dma_start(o[0].rearrange("n t g d -> (n t) (g d)"), kv[0:NS, TB, i * KVW:(i + 1) * KVW]).then_inc(e.caches_stored, 16)
            for i, (o, b) in enumerate(((e.s_k_win, e.cache_k_win), (e.s_v_win, e.cache_v_win))):
                sp.dma_start(o[0, :, 0:WIN - TS].rearrange("n w g d -> n (w g d)"), b[0, :, TS:WIN].rearrange("n w g d -> n (w g d)"))\
                  .then_inc(e.caches_stored, 16)
                sp.dma_start(o[0, :, WIN - TS:WIN].rearrange("n t g d -> n t (g d)"),
                             kv[0:NS, TB, (4 + i) * KVW:(5 + i) * KVW]).then_inc(e.caches_stored, 16)
            load_wait(sp, e.caches_stored, 14)

        @block.gpsimd
        def _(pool):
            pool.memset(e.vslc[:, :, HD:2 * HD], 1.0).then_inc(s_ones, 1)
            pool.memset(e.vwin[:, :, HD:2 * HD], 1.0).then_inc(s_ones, 1)
            for tb in range(TB):
                pool.wait_ge(s_kvc, 2 * tb + 2)
                for dst, i in ((e.vslc, 3), (e.vwin, 5)):
                    for g in range(G):
                        pool.tensor_copy(dst[:, tb, 2 * g * HD:(2 * g + 1) * HD],
                                         kv[:, tb, i * KVW + g * HD:i * KVW + (g + 1) * HD]).then_inc(s_v, 1)
            pool.wait_ge(s_kvc, 2 * TB + 2)
            pool.tensor_copy(e.vnew[:, 0, :], kv[0:NS, TB, 3 * KVW:4 * KVW]).then_inc(s_v, 1)
            pool.tensor_copy(e.vnew[:, 1, :], kv[0:NS, TB, 5 * KVW:6 * KVW]).then_inc(s_v, 1)
            pool.wait_ge(s_v, 4 * TB + 2)

        @block.tensor
        def _(pe):
            load_wait(pe, s_wq, 8)
            load_wait(pe, s_wk, 1)
            for i in range(NQ):
                f, s = i // 3, i % 3
                if i >= 4:
                    pe.wait_ge(s_qc, i - 3)
                m = P if f < R else 3 * HQ
                for k in range(KD):
                    w = wq[:, k, f, :, :].rearrange("p g d -> p (g d)") if f < R else wk[:, k, 6 * KVW:6 * KVW + 3 * HQ]
                    mm = pe.matmul(bank[i % 4][0:m, 0:SL], w, e.hT[:, k, s * SL:(s + 1) * SL], start=(k == 0), stop=(k == KD - 1))
                mm.then_inc(s_q, 1)
            for tb in range(TB + 1):
                for h in range(2):
                    i = 2 * tb + h
                    if i >= 2:
                        pe.wait_ge(s_kvc, i - 1)
                    for k in range(KD):
                        mm = pe.matmul(bank[4 + h][0:rows(tb), 0:3 * KVW], e.hT[:, k, tb * P:tb * P + rows(tb)],
                                       wk[:, k, h * 3 * KVW:(h + 1) * 3 * KVW], start=(k == 0), stop=(k == KD - 1))
                    mm.then_inc(s_kv, 1)
            for tb in range(TB + 1):
                n = rows(tb)
                pe.wait_ge(s_kvc, 2 * tb + 2)
                if tb >= 2:
                    pe.wait_ge(s_tc, tb - 1)
                for q, i in enumerate((2, 4)):
                    mm = pe.transpose(bank[6 + tb % 2][:, q * P:q * P + n], kv[0:n, tb, i * KVW:(i + 1) * KVW], e.ident[0:n, 0:n])
                mm.then_inc(s_t, 1)

        @block.scalar
        def _(act):
            for i in range(NQ):
                f, s = i // 3, i % 3
                act.wait_ge(s_q, i + 1)
                if f < R:
                    act.activation(e.qT[:, f, s * SL:(s + 1) * SL], bank[i % 4][:, 0:SL], ACT.Copy, scale=HD ** -0.5).then_inc(s_qc, 1)
                else:
                    act.activation(e.gates[:, s * SL:(s + 1) * SL], bank[i % 4][0:3 * HQ, 0:SL], ACT.Sigmoid).then_inc(s_qc, 1)

        @block.vector
        def _(dve):
            for i in range(2 * (TB + 1)):
                tb, h = i // 2, i % 2
                dve.wait_ge(s_kv, i + 1)
                dve.tensor_copy(kv[0:rows(tb), tb, h * 3 * KVW:(h + 1) * 3 * KVW], bank[4 + h][0:rows(tb), 0:3 * KVW]).then_inc(s_kvc, 1)
            for tb in range(TB + 1):
                n = rows(tb)
                dve.wait_ge(s_t, tb + 1)
                dve.tensor_copy(e.kT[:, :, tb * P:tb * P + n],
                                bank[6 + tb % 2][:, 0:2 * P].rearrange("p (c n) -> p c n", c=2)[:, :, 0:n]).then_inc(s_tc, 1)


def stage_tables(nc, e):
    with ExitStack() as c:
        sb = lambda n, s, d=F32: c.enter_context(nc.sbuf_tensor(n, s, d))
        sem = stage_semaphores(nc, c, "tab")
        tab = sb("tab", [NB + 1, HQ])
        oh = sb("oh", [NB + 1, 2 * BW])
        line = sb("line", [HQ, BW])
        perow = sb("perow", [16, 2, P])
        peT = sb("peT", [P, 2, 16])
        b1row = sb("b1row", [1, 2, HD])
        ptab = sb("ptab", [P, NSEQ * 2], I32)
        pf = sb("pf", [P, NSEQ * 2])
        s_tab, s_neg, s_oh, s_line, s_linec, s_rb, s_bt, s_bnz, s_bc, s_w, s_pe, s_peT, s_peTc, s_bb, s_pt, s_pf, s_end = (sem(n) for n in (
            "s_tab", "s_neg", "s_oh", "s_line", "s_linec", "s_rb", "s_bt", "s_bnz", "s_bc", "s_w", "s_pe", "s_peT", "s_peTc", "s_bb",
            "s_pt", "s_pf", "s_end"))
        rb = nc.dram_tensor("bias_lines", (P, HQ, BW), F32, kind="Internal").ap()
        block = c.enter_context(nc.Block())
        bank = e.bank
        line_ap = lambda off, ap: bass.AP(tensor=rb.tensor, offset=off, ap=ap)

        @block.sync
        def _(sp):
            sp.dma_start(tab[0:NB, :], e.rel_bias).then_inc(s_tab, 16)
            sp.dma_start(oh[:, :], e.onehot_in).then_inc(s_oh, 16)
            for kv in range(2):
                for j in range(2):
                    sp.dma_start(e.w1T[:, kv, :, j, :], e.cmp_w1[0, kv, 16 * j:16 * j + 16].rearrange("(a s) d e -> (s d) a e", s=2))\
                      .then_inc(s_w, 16)
                sp.dma_start(e.w2[:, kv, :], e.cmp_w2[0, kv]).then_inc(s_w, 16)
                sp.dma_start(perow[:, kv, :], e.cmp_pe[0, kv].rearrange("(a s) d -> a (s d)", s=2)).then_inc(s_pe, 16)
                sp.dma_start(b1row[:, kv, :], e.cmp_b1[:, kv, :]).then_inc(s_pe, 16)
            for sub in range(8):
                sp.dma_start(ptab[sub:P:8, :], bass.AP(tensor=e.page_table.tensor, offset=0, ap=[[1, 16], [16, 2 * NSEQ]]),
                             allow_slow_non_contiguous=True).then_inc(s_pt, 16)
            sp.wait_ge(s_linec, 1)
            sp.dma_start(rb.rearrange("p h w -> h p w"), line[:, None, :].to_broadcast([HQ, P, BW])).then_inc(s_rb, 16)
            load_wait(sp, s_rb, 1)
            for i, dlt in enumerate((1, 0)):
                sp.dma_start(e.bt[:, :, i * P:(i + 1) * P], line_ap(255 - P * dlt, [[HQ * BW - 1, P], [BW, HQ], [1, P]])).then_inc(s_bt, 16)
            sp.wait_ge(s_bnz, 2)
            for m in range(4):
                r = slice(32 * m, 32 * m + 32)
                sp.dma_start(e.btail[r, :], line_ap(127, [[BW, HQ], [HQ * BW - 1, TS], [1, P]])).then_inc(s_bt, 16)
                for t in range(TS):
                    sp.dma_start(e.bcd[32 * m + t:32 * m + 32:TS, :], line_ap(142 - t, [[BW, HQ], [16, 8]]),
                                 allow_slow_non_contiguous=True).then_inc(s_bt, 16)
                for b in range(2):
                    a = TS * (4 * b + m)
                    sp.dma_start(e.bnew[r, b, a:a + TS], line_ap(255, [[BW, HQ], [HQ * BW - 1, TS], [1, TS]])).then_inc(s_bt, 16)
            load_wait(sp, s_bt, 2 + 4 * 7)
            load_wait(sp, s_w, 6)

        @block.gpsimd
        def _(pool):
            pool.memset(e.bnew[:, :, :], NEG).then_inc(s_bnz, 1)
            pool.memset(e.qbd[:, :, :], 0.0).then_inc(s_bnz, 1)
            pool.wait_ge(s_bnz, 2)
            for g in range(G):
                for r in range(R):
                    a = (g * R + r) * TS
                    ins = pool.tensor_copy(e.qbd[g * HD:(g + 1) * HD, :, a:a + TS],
                                           e.qT[g * HD:(g + 1) * HD, r, T:NT].rearrange("p (n t) -> p n t", t=TS))
                    ins.then_inc(s_end, 1)
                    pool.wait_ge(s_end, g * R + r + 1)

        @block.tensor
        def _(pe):
            load_wait(pe, s_tab, 1)
            load_wait(pe, s_oh, 1)
            pe.wait_ge(s_neg, 1)
            pe.matmul(bank[0][0:HQ, 0:BW], tab[:, :], oh[:, 0:BW], start=True, stop=True).then_inc(s_line, 1)
            for i in range(16):
                y0 = BW + 96 - 16 * (i - 9)
                mm = pe.matmul(bank[1][:, i * HQ:(i + 1) * HQ], oh[:, y0:y0 + P], tab[:, :], start=True, stop=True)
            mm.then_inc(s_line, 1)
            load_wait(pe, s_pe, 4)
            for kv in range(2):
                mm = pe.transpose(bank[2][:, kv * 16:kv * 16 + 16], perow[:, kv, :], e.ident[0:16, 0:16])
            mm.then_inc(s_peT, 1)
            pe.wait_ge(s_peTc, 1)
            load_wait(pe, s_w, 6)
            for kv in range(2):
                o = bank[3 + kv][0:HD, 0:1]
                for x in range(16):
                    pe.matmul(o, e.w1T[:, kv, x % 8, x // 8, :], peT[:, kv, x:x + 1], start=(x == 0), stop=False)
                mm = pe.matmul(o, b1row[:, kv, :], e.ones[0:1, 0:1], start=False, stop=True)
            mm.then_inc(s_bb, 1)

        @block.scalar
        def _(act):
            act.wait_ge(s_line, 2)
            act.activation(e.bc[:, :, :], bank[1][:, 0:16 * HQ].rearrange("p (c h) -> p h c", h=HQ), ACT.Copy).then_inc(s_bc, 1)

        @block.vector
        def _(dve):
            dve.memset(tab[NB:NB + 1, :], NEG).then_inc(s_neg, 1)
            dve.wait_ge(s_line, 1)
            dve.tensor_copy(line[:, :], bank[0][0:HQ, 0:BW]).then_inc(s_linec, 1)
            dve.wait_ge(s_peT, 1)
            dve.tensor_copy(peT[:, :, :], bank[2][:, 0:32].rearrange("p (c x) -> p c x", c=2)).then_inc(s_peTc, 1)
            dve.wait_ge(s_bb, 1)
            for kv in range(2):
                dve.tensor_copy(e.cbias[:, kv:kv + 1], bank[3 + kv][0:HD, 0:1]).then_inc(s_peTc, 1)
            load_wait(dve, s_pt, 8)
            dve.tensor_copy(pf[:, :], ptab[:, :]).then_inc(s_pf, 1)
            dve.wait_ge(s_pf, 1)
            dve.tensor_scalar(pf[:, :], pf[:, :], 8.0, e.consts[:, C_SUB:C_SUB + 1], ALU.mult, ALU.add).then_inc(s_pf, 1)
            dve.wait_ge(s_pf, 2)
            dve.tensor_copy(e.rowidx[:, :], pf[:, :]).then_inc(s_pf, 1)


def stage_compress(nc, e):
    NI = 2 + 2 * NSEQ
    NCK = [T // CHK] * 2 + [PAST // CHK] * (2 * NSEQ)
    NBT = [4] * 2 + [8] * (2 * NSEQ)
    first = [sum(NBT[:i]) for i in range(NI + 1)]
    with ExitStack() as c:
        sb = lambda n, s, d=F32: c.enter_context(nc.sbuf_tensor(n, s, d))
        sem = stage_semaphores(nc, c, "cmp")
        raw = sb("raw", [P, 2, 2, CHK * KVW])
        byg = sb("byg", [P, 2, G, CHK, HD])
        xT2 = sb("xT2", [P, 2, 8, 512])
        low = sb("low", [HD, 2, 512])
        hsum = sb("hsum", [HD, 2, 512])
        hid = sb("hid", [HD, 2, G, 256])
        s_raw = [sem(f"s_raw{i}") for i in range(2)]
        s_pl = [sem(f"s_pl{i}") for i in range(2)]
        s_by, s_tr, s_eva, s_evd, s_part, s_low, s_sum, s_hid, s_w2, s_out, s_z = (sem(n) for n in (
            "s_by", "s_tr", "s_eva", "s_evd", "s_part", "s_low", "s_sum", "s_hid", "s_w2o", "s_outc", "s_zc"))
        block = c.enter_context(nc.Block())
        bank = e.bank
        rows = [x.rearrange("a b (c s) g d -> (a b c) (s g d)", s=CHK) for x in (e.cache_k_cmp, e.cache_v_cmp)]

        @block.sync
        def _(sp):
            for i, src in enumerate((e.p_k_cmp, e.p_v_cmp)):
                if i:
                    sp.wait_ge(s_tr, first[1])
                for g in range(G):
                    sp.dma_start(byg[0:64, 0, g, :, :], src[0, 0].rearrange("(c s) g d -> c s g d", s=CHK)[:, :, g, :]).then_inc(s_pl[i], 16)

        @block.gpsimd
        def _(pool):
            for i in range(2, NI):
                n, kv = (i - 2) // 2, i % 2
                if i >= 4:
                    pool.wait_ge(s_by, i - 3)
                for half in range(2):
                    col = 2 * n + half
                    pool.indirect_dma_start(raw[:, i % 2, half, :], None, rows[kv],
                                            bass.IndirectOffsetOnAxis(ap=e.rowidx[:, col:col + 1], axis=0)).then_inc(s_raw[i % 2], 16)

        @block.tensor
        def _(pe):
            def second(i):
                n, kv, C = (i - 2) // 2, i % 2, NCK[i]
                pe.wait_ge(s_hid, i + 1)
                if i >= 2:
                    pe.wait_ge(s_out, i - 1)
                o = bank[6 + i % 2]
                if kv == 0:
                    for g in range(G):
                        mm = pe.matmul(o[g * HD:(g + 1) * HD, 0:C], e.w2[:, 0, :], hid[:, i % 2, g, 0:C], start=True, stop=True)
                else:
                    for half in range(max(C // P, 1)):
                        m = min(C, P)
                        for g in range(G):
                            a = half * P + g * HD
                            mm = pe.matmul(o[0:m, a:a + HD], hid[:, i % 2, g, half * P:half * P + m], e.w2[:, 1, :], start=True, stop=True)
                mm.then_inc(s_w2, 1)

            pe.wait_ge(s_z, 1)
            for i in range(NI):
                C, kv = NCK[i], i % 2
                m = min(C, P)
                if i < 2:
                    load_wait(pe, s_pl[i], 2)
                else:
                    pe.wait_ge(s_by, i - 1)
                for b in range(NBT[i]):
                    y = first[i] + b
                    if y >= 4:
                        pe.wait_ge((s_eva, s_evd)[y % 2], y // 2 - 1)
                    half, sp2 = b // 4, b % 4
                    for a in range(2):
                        for g in range(G):
                            s = 2 * (2 * sp2 + a)
                            o = (a * G + g) * m
                            mm = pe.transpose(bank[y % 4][:, o:o + m], byg[0:m, half, g, s:s + 2, :].rearrange("p s d -> p (s d)"),
                                              e.ident[0:m, 0:m])
                    mm.then_inc(s_tr, 1)
                if i >= 1:
                    second(i - 1)
                pe.wait_ge(s_eva, first[i + 1] // 2)
                pe.wait_ge(s_evd, first[i + 1] // 2)
                if i >= 2:
                    pe.wait_ge(s_sum, i - 1)
                for sp in range(8):
                    mm = pe.matmul(bank[4 + i % 2][:, 0:G * C], e.w1T[:, kv, sp, :, :].rearrange("p j e -> p (j e)"),
                                   xT2[:, i % 2, sp, 0:G * C], start=(sp == 0), stop=(sp == 7))
                mm.then_inc(s_part, 1)
            second(NI - 1)

        def move(i, b):
            m, half, sp2 = min(NCK[i], P), b // 4, b % 4
            src = bank[(first[i] + b) % 4][:, 0:4 * m].rearrange("p (a g c) -> p a g c", a=2, g=G)
            dst = xT2[:, i % 2, 2 * sp2:2 * sp2 + 2, 0:G * NCK[i]].rearrange("p a (g c) -> p a g c", g=G)[:, :, :, half * P:half * P + m]
            return src, dst

        def hidden(act, i):
            C = NCK[i]
            act.wait_ge(s_sum, i + 1)
            if i >= 2:
                act.wait_ge(s_w2, i - 1)
            act.activation(hid[:, i % 2, :, 0:C - 1], hsum[:, i % 2, 0:G * C].rearrange("p (g c) -> p g c", g=G)[:, :, 0:C - 1],
                           ACT.Silu, bias=e.cbias[:, i % 2:i % 2 + 1]).then_inc(s_hid, 1)

        @block.scalar
        def _(act):
            for i in range(NI):
                C = NCK[i]
                for b in range(NBT[i]):
                    if (first[i] + b) % 2 == 0:
                        act.wait_ge(s_tr, first[i] + b + 1)
                        if i >= 2:
                            act.wait_ge(s_part, i - 1)
                        src, dst = move(i, b)
                        act.activation(dst, src, ACT.Copy).then_inc(s_eva, 1)
                if i >= 1:
                    hidden(act, i - 1)
                act.wait_ge(s_part, i + 1)
                if i >= 2:
                    act.wait_ge(s_sum, i - 1)
                act.activation(low[:, i % 2, 0:G * C], bank[4 + i % 2][HD:P, 0:G * C], ACT.Copy).then_inc(s_low, 1)
            hidden(act, NI - 1)

        @block.vector
        def _(dve):
            dve.memset(hid[:, :, :, :], 0.0).then_inc(s_z, 1)

            def regroup(i):
                load_wait(dve, s_raw[i % 2], 2 * (i // 2))
                dve.wait_ge(s_tr, first[i])
                ins = None
                for half in range(2):
                    ins = dve.tensor_copy(byg[:, half, :, :, :].rearrange("p g s d -> p s g d"),
                                          raw[:, i % 2, half, :].rearrange("p (s g d) -> p s g d", g=G, d=HD))
                ins.then_inc(s_by, 1)

            def keep(i):
                n, kv, C = (i - 2) // 2, i % 2, NCK[i]
                dve.wait_ge(s_w2, i + 1)
                o = bank[6 + i % 2]
                if i == 0:
                    ins = dve.tensor_copy(e.kcp[:, :], o[:, 0:C])
                elif i == 1:
                    for g in range(G):
                        ins = dve.tensor_copy(e.vcp[:, 2 * g * HD:(2 * g + 1) * HD], o[0:C, g * HD:(g + 1) * HD])
                elif kv == 0:
                    ins = dve.tensor_copy(e.kcT[:, n, :], o[:, 0:C])
                else:
                    ins = dve.tensor_copy(e.vc[:, n, :, :], o[:, 0:2 * P].rearrange("p (h f) -> p h f", h=2))
                ins.then_inc(s_out, 1)

            for i in range(NI):
                C = NCK[i]
                if i >= 2:
                    regroup(i)
                for b in range(NBT[i]):
                    if (first[i] + b) % 2 == 1:
                        dve.wait_ge(s_tr, first[i] + b + 1)
                        if i >= 2:
                            dve.wait_ge(s_part, i - 1)
                        src, dst = move(i, b)
                        dve.tensor_copy(dst, src).then_inc(s_evd, 1)
                if i >= 1:
                    keep(i - 1)
                dve.wait_ge(s_low, i + 1)
                if i >= 2:
                    dve.wait_ge(s_hid, i - 1)
                v = lambda t, a, b: t.rearrange("p (g c) -> p g c", g=G)[:, :, a:b]
                dve.tensor_tensor(v(hsum[:, i % 2, 0:G * C], 0, C - 1), v(bank[4 + i % 2][0:HD, 0:G * C], 0, C - 1),
                                  v(low[:, i % 2, 0:G * C], 1, C), ALU.add).then_inc(s_sum, 1)
            keep(NI - 1)
            dve.memset(e.vcp[:, HD:2 * HD], 1.0)


CMP, SLC, WND = range(3)


def prompt_units():
    for qb in range(TB):
        for r in range(R):
            for br in (CMP, WND, SLC):
                for g in range(G):
                    lo = 0 if br != WND else max(0, qb - WIN // P) * P
                    hi = 8 * qb + 7 if br == CMP else (qb + 1) * P
                    yield qb, r, br, g, lo, hi - lo


def stage_prompt(nc, e):
    U = list(prompt_units())
    NU = len(U)
    tiles = [-(-u[5] // P) for u in U]
    ngrp = [-(-t // 4) for t in tiles]
    grp0 = [sum(ngrp[:i]) for i in range(NU + 1)]
    with ExitStack() as c:
        sb = lambda n, s, d=F32: c.enter_context(nc.sbuf_tensor(n, s, d))
        sem = stage_semaphores(nc, c, "prompt")
        gT = sb("gT", [P, TB, 3 * HQ])
        pr = sb("pr", [P, 2, T])
        pt = sb("pt", [P, 2, TB, P])
        nmax = sb("nmax", [P, 4])
        rsum = sb("rsum", [P, 4])
        s_g, s_gc, s_s, s_bias, s_max, s_e, s_sum, s_rc, s_p, s_t, s_pt, s_pv, s_o = (sem(n) for n in (
            "s_g", "s_gc", "s_s", "s_bias", "s_max", "s_e", "s_sum", "s_rc", "s_p", "s_t", "s_pt", "s_pv", "s_o"))
        block = c.enter_context(nc.Block())
        bank, ps = e.bank, e.ps
        score = lambda u: ps[:, 1024 * (u % 2):1024 * (u % 2) + U[u][5]]
        outp = lambda u: bank[6 + (u // 6) % 2]

        @block.tensor
        def _(pe):
            for tb in range(TB):
                mm = pe.transpose(bank[7][:, tb * 24:(tb + 1) * 24], e.gates[:, tb * P:(tb + 1) * P], e.ident[0:24, 0:24])
            mm.then_inc(s_g, 1)
            pe.wait_ge(s_gc, 1)

            def scores(u):
                qb, r, br, g, lo, n = U[u]
                if u >= 2:
                    pe.wait_ge(s_e, u - 1)
                h = slice(g * HD, (g + 1) * HD)
                keys = e.kcp if br == CMP else e.kT[:, br - 1, :]
                for a in range(0, n, 512):
                    m = min(512, n - a)
                    mm = pe.matmul(score(u)[:, a:a + m], e.qT[h, r, qb * P:(qb + 1) * P], keys[h, lo + a:lo + a + m],
                                   start=True, stop=True)
                mm.then_inc(s_s, 1)

            def turn(u):
                n = U[u][5]
                pe.wait_ge(s_p, u + 1)
                for y in range(ngrp[u]):
                    if grp0[u] + y >= 2:
                        pe.wait_ge(s_pt, grp0[u] + y - 1)
                    for t in range(4 * y, min(4 * y + 4, tiles[u])):
                        m = min(P, n - t * P)
                        mm = pe.transpose(bank[4 + (grp0[u] + y) % 2][0:m, (t % 4) * P:(t % 4 + 1) * P],
                                          pr[:, u % 2, t * P:t * P + m], e.ident)
                    mm.then_inc(s_t, 1)

            def values(u):
                qb, r, br, g, lo, n = U[u]
                pe.wait_ge(s_pt, grp0[u + 1])
                if u % 6 < 2 and u >= 12:
                    pe.wait_ge(s_o, u // 6 - 1)
                o = outp(u)[g * HD:(g + 1) * HD, 0:P]
                va = 2 * g * HD
                for t in range(tiles[u]):
                    m = min(P, n - t * P)
                    v = e.vcp[0:m, va:va + HD] if br == CMP else (e.vslc, e.vwin)[br - 1][:, lo // P + t, va:va + HD]
                    mm = pe.matmul(o, v, pt[0:m, u % 2, t, :], start=(br == CMP and t == 0), stop=(br == SLC and t == tiles[u] - 1),
                                   skip_group_check=True)
                mm.then_inc(s_pv, 1)

            for u in range(NU + 2):
                if u < NU:
                    scores(u)
                if 1 <= u <= NU:
                    turn(u - 1)
                if u >= 2:
                    values(u - 2)

        @block.scalar
        def _(act):
            def copies(u):
                for y in range(ngrp[u]):
                    t0, t1 = 4 * y, min(4 * y + 4, tiles[u])
                    m = min(P, U[u][5])
                    act.wait_ge(s_t, grp0[u] + y + 1)
                    if y == 0 and u >= 2:
                        act.wait_ge(s_pv, u - 1)
                    act.activation(pt[0:m, u % 2, t0:t1, :], bank[4 + (grp0[u] + y) % 2][0:m, 0:(t1 - t0) * P].rearrange("p (t q) -> p t q", q=P),
                                   ACT.Copy).then_inc(s_pt, 1)

            for u in range(NU + 1):
                if u < NU:
                    act.wait_ge(s_max, u + 1)
                    if u >= 2:
                        act.wait_ge(s_t, grp0[u - 1])
                    if u >= 4:
                        act.wait_ge(s_rc, u - 3)
                    act.activation(pr[:, u % 2, 0:U[u][5]], score(u), ACT.Exp, bias=nmax[:, u % 4:u % 4 + 1],
                                   accum_out=rsum[:, u % 4:u % 4 + 1]).then_inc(s_e, 1)
                if u >= 1:
                    copies(u - 1)

        @block.vector
        def _(dve):
            bias_n = [0]

            def bias(dst, src):
                bias_n[0] += 1
                dve.tensor_tensor(dst, dst, src, ALU.add).then_inc(s_bias, 1)

            dve.wait_ge(s_g, 1)
            dve.tensor_copy(gT[:, :, :], bank[7][:, 0:TB * 24].rearrange("p (b h) -> p b h", h=24)).then_inc(s_gc, 1)
            dve.wait_ge(s_gc, 1)

            def maxima(u):
                qb, r, br, g, lo, n = U[u]
                h = g * R + r
                dve.wait_ge(s_s, u + 1)
                s = score(u)
                if br == CMP:
                    c0 = max(0, 8 * qb - 9)
                    bias(s[:, c0:n], e.bc[:, h, c0 - (8 * qb - 9):16])
                else:
                    m = min(2 * P, n)
                    bias(s[:, n - m:n], e.bt[:, h, 2 * P - m:2 * P])
                    if br == WND and qb >= WIN // P:
                        bias(s[:, 0:P], e.winmask)
                dve.wait_ge(s_bias, bias_n[0])
                if u >= 4:
                    dve.wait_ge(s_e, u - 3)
                dve.tensor_reduce(nmax[:, u % 4:u % 4 + 1], s, AXX, ALU.max, negate=True).then_inc(s_max, 1)

            def scale(u):
                qb, r, br, g, lo, n = U[u]
                h = g * R + r
                x = rsum[:, u % 4:u % 4 + 1]
                dve.wait_ge(s_e, u + 1)
                dve.tensor_scalar(x, x, 1e-30, None, ALU.max).then_inc(s_sum, 1)
                dve.wait_ge(s_sum, u + 1)
                dve.reciprocal(x, x).then_inc(s_rc, 1)
                dve.wait_ge(s_rc, u + 1)
                p = pr[:, u % 2, 0:n]
                if br == CMP and qb == 0:
                    dve.tensor_scalar(p, p, e.cmprow, None, ALU.mult).then_inc(s_bias, 1)
                    bias_n[0] += 1
                    dve.wait_ge(s_bias, bias_n[0])
                dve.tensor_scalar(p, p, x, gT[:, qb, br * HQ + h:br * HQ + h + 1], ALU.mult, ALU.mult).then_inc(s_p, 1)

            def output(x):
                qb, r = U[6 * x][0], U[6 * x][1]
                dve.wait_ge(s_pv, 6 * x + 6)
                dve.tensor_copy(e.oT[:, r, qb * P:(qb + 1) * P], outp(6 * x)[:, 0:P]).then_inc(s_o, 1)

            for u in range(NU + 1):
                if u < NU:
                    maxima(u)
                if u >= 1:
                    scale(u - 1)
                if u % 6 == 3 and u >= 9:
                    output(u // 6 - 1)
            output(NU // 6 - 1)


def stage_decode(nc, e):
    NR = 6
    NBAT, M = 2, 4
    W = PAST + NS
    BLK = 64
    NBK = PAST // BLK
    KG = M + 8 * M
    TCMP, TWIN, TSLC = 0, 2, 7
    NTL = TSLC + 33
    with ExitStack() as c:
        sb = lambda n, s, d=F32: c.enter_context(nc.sbuf_tensor(n, s, d))
        sem = stage_semaphores(nc, c, "decode")
        ring = sb("ring", [P, NR, CHK, KVW])
        Ss = sb("Ss", [P, W])
        Sw = sb("Sw", [P, WIN + NS])
        Sc = sb("Sc", [P, 256])
        wt = sb("wt", [P, NTL, P])
        kt = e.bt[:, :, :].rearrange("p h x -> p (h x)").rearrange("p (s x) -> p s x", s=4)
        kwin = e.vslc[:, :, :].rearrange("p b x -> p (b x)")[:, 0:1024].rearrange("p (s j x) -> p s j x", s=2, j=4)
        vwin = e.vwin[:, :, :].rearrange("p b x -> p (b x)")[:, 0:1024].rearrange("p (s j x) -> p s j x", s=2, j=4)
        gd = sb("gd", [P, NBAT, 3])
        sc = sb("sc", [P, NBK + 1])
        scs = sb("scs", [P, NBK + 1])
        m8 = sb("m8", [P, 8])
        st = sb("st", [P, 8])
        gscr = nc.dram_tensor("gate_rows", (3 * HQ, NS), F32, kind="Internal").ap()
        s_ring = [sem(f"s_ring{i}") for i in range(NR)]
        s_kw = [sem(f"s_kw{i}") for i in range(2)]
        s_vw = [sem(f"s_vw{i}") for i in range(2)]
        s_gs, s_gd, s_used, s_wused, s_vused, s_cs, s_cse, s_blk, s_sel, s_kt, s_ktc, s_ks, s_ksc, s_x, s_e, s_w, s_t, s_tc, s_pv, s_o = (
            sem(n) for n in ("s_gs", "s_gd", "s_used", "s_wused", "s_vused", "s_cs", "s_cse", "s_blk", "s_sel", "s_kt", "s_ktc", "s_ks",
                             "s_ksc", "s_x", "s_ed", "s_wd", "s_td", "s_tcd", "s_pvd", "s_od"))
        c_chain = sem("s_chain_d")
        block = c.enter_context(nc.Block())
        bank = e.bank
        rows = [x.rearrange("a b (c s) g d -> (a b c) (s g d)", s=CHK) for x in (e.cache_k_slc, e.cache_v_slc)]
        NG = -(-NTL // 4)

        @block.sync
        def _(sp):
            sp.dma_start(gscr, e.gates[:, T:NT]).then_inc(s_gs, 16)
            load_wait(sp, s_gs, 1)
            for n in range(NSEQ):
                for br in range(3):
                    sp.dma_start(gd[32 * (n % M):32 * (n % M) + 32, n // M, br:br + 1],
                                 bass.AP(tensor=gscr.tensor, offset=br * HQ * NS + n * TS, ap=[[NS, HQ], [1, TS]]),
                                 allow_slow_non_contiguous=True).then_inc(s_gd, 16)
            def window(n, slots, free, landed, cache):
                if n >= 2:
                    sp.wait_ge(free, n - 1)
                sp.dma_start(slots[:, n % 2], cache[0, n].rearrange("(j p) g d -> p j (g d)", p=P)).then_inc(landed[n % 2], 16)

            for b in range(NBAT):
                for n in range(M * b, M * b + M):
                    window(n, kwin, s_wused, s_kw, e.cache_k_win)
                for n in range(M * b, M * b + M):
                    window(n, vwin, s_vused, s_vw, e.cache_v_win)

        @block.gpsimd
        def _(pool):
            for x in range(NBAT * 16):
                b, kv, m, half = x // 16, x // 8 % 2, x // 2 % 4, x % 2
                if x >= NR:
                    pool.wait_ge(s_used, x - NR + 1)
                col = 2 * (M * b + m) + half
                pool.indirect_dma_start(ring[:, x % NR].rearrange("p s x -> p (s x)"), None, rows[kv],
                                        bass.IndirectOffsetOnAxis(ap=e.rowidx[:, col:col + 1], axis=0)).then_inc(s_ring[x % NR], 16)

        @block.tensor
        def _(pe):
            def keys(b, y):
                z = KG * b + y
                if z >= 2:
                    pe.wait_ge(s_ktc, z - 1)
                if y < M:
                    n = M * b + y
                    load_wait(pe, s_kw[n % 2], n // 2 + 1)
                    for j in range(4):
                        mm = pe.transpose(bank[z % 2][:, j * P:(j + 1) * P], kwin[:, n % 2, j, :], e.ident)
                    mm.then_inc(s_kt, 1)
                    return
                v = y - M
                x = 16 * b + v // 4
                load_wait(pe, s_ring[x % NR], x // NR + 1)
                for j in range(4):
                    mm = pe.transpose(bank[z % 2][:, j * P:(j + 1) * P], ring[:, x % NR, 4 * (v % 4) + j, :], e.ident)
                mm.then_inc(s_kt, 1)

            def scores(b, y):
                z = KG * b + y
                m = y if y < M else (y - M) // 8
                pe.wait_ge(s_ktc, z + 1)
                if z >= 2:
                    pe.wait_ge(s_ksc, z - 1)
                pe.matmul(bank[2 + z % 2][32 * m:32 * m + 32, :], e.qbd[:, M * b + m, :], kt[:, z % 4, :], start=True, stop=True)\
                  .then_inc(s_ks, 1)

            def turn(b, y):
                z = NG * b + y
                if z >= 2:
                    pe.wait_ge(s_tc, z - 1)
                for t in range(4 * y, min(4 * y + 4, NTL)):
                    if t < TWIN:
                        pe.wait_ge(s_w, 3 * b + 1)
                        src = Sc[:, t * P:(t + 1) * P]
                    elif t < TSLC:
                        pe.wait_ge(s_w, 3 * b + 2)
                        a = (t - TWIN) * P
                        src = Sw[:, a:min(a + P, WIN + NS)]
                    else:
                        pe.wait_ge(s_w, 3 * b + 3)
                        a = (t - TSLC) * P
                        src = Ss[:, a:min(a + P, W)]
                    mm = pe.transpose(bank[(5, 7)[z % 2]][0:src.shape[1], (t % 4) * P:(t % 4 + 1) * P], src, e.ident)
                mm.then_inc(s_t, 1)

            for b in range(NBAT):
                if b:
                    pe.wait_ge(s_cse, b)
                    pe.wait_ge(s_sel, 4)
                for m in range(M):
                    n = M * b + m
                    pe.matmul(bank[4][32 * m:32 * m + 32, 0:256], e.qbd[:, n, :], e.kcT[:, n, :], start=True, stop=True)
                q4 = e.qbd[:, M * b:M * b + M, :].rearrange("p n x -> p (n x)")
                for i in range(2):
                    mm = pe.matmul(bank[4][:, 256 + 32 * i:288 + 32 * i], q4, e.kT[:, i, T:NT], start=True, stop=True)
                mm.then_inc(s_cs, 1)
                for y in range(KG + 1):
                    if y < KG:
                        keys(b, y)
                        if y < M:
                            pe.wait_ge(s_kt, KG * b + y + 1)
                            pe.sem_inc(s_wused, 1)
                        elif (y - M) % 4 == 3:
                            pe.wait_ge(s_kt, KG * b + y + 1)
                            pe.sem_inc(s_used, 1)
                    if y >= 1:
                        scores(b, y - 1)
                    if y == M + 2:
                        pe.wait_ge(s_blk, b + 1)
                        pe.matmul(bank[6][:, 256:256 + NBK], e.sumr, sc[:, 0:NBK], start=True, stop=True).then_inc(s_sel, 1)
                        pe.wait_ge(s_sel, 4 * b + 1)
                if b:
                    pe.wait_ge(s_o, 1)
                pe.wait_ge(s_sel, 4 * b + 4)
                for y in range(NG):
                    turn(b, y)
                pe.wait_ge(s_tc, NG * (b + 1))
                first = True
                for m in range(M):
                    n = M * b + m
                    o = bank[6][:, 32 * m:32 * m + 32]
                    col = slice(32 * m, 32 * m + 32)

                    def add(v, t, k=P):
                        nonlocal first
                        mm = pe.matmul(o, v, wt[0:k, t, col], start=first, stop=False, skip_group_check=True)
                        first = False
                        return mm

                    for half in range(2):
                        add(e.vc[:, n, half, :], TCMP + half)
                    load_wait(pe, s_vw[n % 2], n // 2 + 1)
                    for j in range(4):
                        mm = add(vwin[:, n % 2, j, :], TWIN + j)
                    mm.then_inc(s_vused, 1)
                    add(e.vnew[:, 1, :], TWIN + 4, NS)
                    for half in range(2):
                        x = 16 * b + 8 + 2 * m + half
                        load_wait(pe, s_ring[x % NR], x // NR + 1)
                        for s in range(CHK):
                            mm = add(ring[:, x % NR, s, :], TSLC + CHK * half + s)
                        mm.then_inc(s_used, 1)
                    mm = add(e.vnew[:, 0, :], TSLC + 32, NS)
                mm.then_inc(s_pv, 1)

        @block.scalar
        def _(act):
            for b in range(NBAT):
                def softmax(i, s):
                    act.wait_ge(s_x, 3 * b + i + 1)
                    act.activation(s, s, ACT.Exp, bias=st[:, i:i + 1], accum_out=st[:, 3 + i:4 + i]).then_inc(s_e, 1)

                for y in range(KG):
                    z = KG * b + y
                    act.wait_ge(s_kt, z + 1)
                    if z >= 4:
                        act.wait_ge(s_ks, z - 3)
                    act.activation(kt[:, z % 4, :], bank[z % 2][:, :], ACT.Copy).then_inc(s_ktc, 1)
                    if y == 0:
                        softmax(0, Sc[:, :])
                    if y == M + 4:
                        softmax(1, Sw[:, :])
                softmax(2, Ss[:, :])
                for y in range(NG):
                    z = NG * b + y
                    t0, t1 = 4 * y, min(4 * y + 4, NTL)
                    act.wait_ge(s_t, z + 1)
                    if b and y == 0:
                        act.wait_ge(s_pv, b)
                    for t in ([None] if not {TWIN + 4, TSLC + 32} & set(range(t0, t1)) else range(t0, t1)):
                        if t is None:
                            ins = act.activation(wt[:, t0:t1, :], bank[(5, 7)[z % 2]][:, 0:(t1 - t0) * P].rearrange("p (t x) -> p t x", x=P), ACT.Copy)
                        else:
                            k = NS if t in (TWIN + 4, TSLC + 32) else P
                            ins = act.activation(wt[0:k, t, :], bank[(5, 7)[z % 2]][0:k, (t - t0) * P:(t - t0 + 1) * P], ACT.Copy)
                    ins.then_inc(s_tc, 1)

        @block.vector
        def _(dve):
            tt = dve.tensor_tensor
            s_c = c_chain
            n_ = [0]

            def link(ins):
                n_[0] += 1
                ins.then_inc(s_c, 1)
                dve.wait_ge(s_c, n_[0])

            def weights(b, i, s):
                dve.wait_ge(s_e, 3 * b + i + 1)
                x = st[:, 3 + i:4 + i]
                link(dve.tensor_scalar(x, x, 1e-30, None, ALU.max))
                link(dve.reciprocal(x, x))
                if i:
                    dve.tensor_scalar(s, s, x, gd[:, b, (0, 2, 1)[i]:(0, 2, 1)[i] + 1], ALU.mult, ALU.mult).then_inc(s_w, 1)

            def top(i, s):
                dve.tensor_reduce(st[:, i:i + 1], s, AXX, ALU.max, negate=True).then_inc(s_x, 1)

            load_wait(dve, s_gd, 3 * NSEQ)
            for b in range(NBAT):
                if b:
                    dve.wait_ge(s_t, NG * b)
                dve.wait_ge(s_cs, b + 1)
                link(dve.tensor_copy(Sc[:, 0:255], bank[4][:, 0:255]))
                link(dve.memset(Sc[:, 255:256], NEG))
                link(tt(Sc[:, 247:255], Sc[:, 247:255], e.bcd[:, :], ALU.add))
                link(tt(Ss[:, PAST:W], bank[4][:, 256:288], e.bnew[:, b, :], ALU.add))
                tt(Sw[:, WIN:WIN + NS], bank[4][:, 288:320], e.bnew[:, b, :], ALU.add).then_inc(s_cse, 1)
                top(0, Sc[:, :])

                def evac(y):
                    z = KG * b + y
                    dve.wait_ge(s_ks, z + 1)
                    m = y if y < M else (y - M) // 8
                    r = slice(32 * m, 32 * m + 32)
                    a = (y - M) % 8 * 512
                    dst = Sw[r, 0:WIN] if y < M else Ss[r, a:a + 512]
                    dve.tensor_copy(dst, bank[2 + z % 2][r, :]).then_inc(s_ksc, 1)

                weights(b, 0, Sc[:, :])
                link(dve.tensor_scalar(Sc[:, :], Sc[:, :], st[:, 3:4], None, ALU.mult))
                p4 = Sc[:, :].rearrange("p (j c) -> p j c", c=4)
                link(tt(sc[:, 0:NBK], p4[:, :, 0], p4[:, :, 1], ALU.add))
                link(tt(sc[:, 0:NBK], sc[:, 0:NBK], p4[:, :, 2], ALU.add))
                link(dve.scalar_tensor_tensor(out=sc[:, 0:NBK], in0=sc[:, 0:NBK], scalar=2.0, in1=p4[:, :, 3], op0=ALU.mult, op1=ALU.add))
                link(tt(sc[:, 1:NBK], sc[:, 1:NBK], p4[:, 0:NBK - 1, 3], ALU.add))
                dve.sem_inc(s_blk, 1)
                dve.tensor_scalar(Sc[:, :], Sc[:, :], gd[:, b, 0:1], None, ALU.mult).then_inc(s_w, 1)
                for y in range(M):
                    evac(y)
                dve.wait_ge(s_ksc, KG * b + M)
                link(tt(Sw[:, 0:TS], Sw[:, 0:TS], e.winhead, ALU.add))
                link(tt(Sw[:, WIN - P:WIN], Sw[:, WIN - P:WIN], e.btail[:, :], ALU.add))
                top(1, Sw[:, :])
                evac(M)
                evac(M + 1)
                dve.wait_ge(s_sel, 4 * b + 1)
                link(dve.tensor_copy(scs[:, 0:NBK], bank[6][:, 256:256 + NBK]))
                link(dve.memset(scs[:, 0:1], BIG))
                dve.memset(scs[:, NBK - 1:NBK + 1], BIG).then_inc(s_sel, 1)
                dve.wait_ge(s_sel, 4 * b + 2)
                for i in range(2):
                    link(dve.max(m8[:, :], scs[:, :]))
                    link(dve.match_replace(scs[:, :], m8[:, :], scs[:, :], -1.0))
                dve.tensor_scalar(scs[:, :], scs[:, :], 0.0, NEG, ALU.is_ge, ALU.mult).then_inc(s_sel, 1)
                weights(b, 1, Sw[:, :])
                for y in range(M + 2, KG):
                    evac(y)
                dve.wait_ge(s_ksc, KG * (b + 1))
                dve.wait_ge(s_sel, 4 * b + 3)
                last = Ss[:, PAST // 2:PAST].rearrange("p (s c) -> p s c", c=P)[:, :, P - 8:P]
                link(tt(last, last, e.btail[:, :].rearrange("p (c s) -> p s c", s=CHK), ALU.add))
                for half in range(2):
                    v = Ss[:, half * PAST // 2:(half + 1) * PAST // 2].rearrange("p (s j c) -> p s j c", s=CHK, c=4)
                    k = scs[:, half * 32:half * 32 + 32].unsqueeze(1).unsqueeze(3).to_broadcast([P, CHK, 32, 4])
                    ins = tt(v, v, k, ALU.add)
                    link(ins)
                dve.sem_inc(s_sel, 1)
                top(2, Ss[:, :])
                weights(b, 2, Ss[:, :])
                dve.wait_ge(s_pv, b + 1)
                for g in range(G):
                    h = slice(g * HD, (g + 1) * HD)
                    dst = e.oT[h, :, T + 16 * b:T + 16 * b + 16].rearrange("p r (m t) -> p r m t", t=TS)
                    src = bank[6][h, 0:P].rearrange("p (m g r t) -> p g r m t", g=G, r=R, t=TS)[:, g]
                    ins = dve.tensor_copy(dst, src)
                ins.then_inc(s_o, 1)


def stage_merge(nc, e):
    WC = 2 * P
    NL = D // WC
    with ExitStack() as c:
        sb = lambda n, s, d=F32: c.enter_context(nc.sbuf_tensor(n, s, d))
        sem = stage_semaphores(nc, c, "merge")
        wg = sb("wg", [P, 2, 2, KD, WC])
        wb = sb("wb", [P, 2, 2, 4, WC])
        sig = sb("sig", [P, 2, 2, SL])
        s_h = sem("s_h")
        s_w = [sem(f"s_w{i}") for i in range(2)]
        s_mm, s_sig, s_pr, s_mx = sem("s_mm"), sem("s_sig"), sem("s_pr"), sem("s_mx")
        block = c.enter_context(nc.Block())
        win = e.w_in[0].rearrange("(k p) n -> p k n", p=P)
        NU = 3 * KD
        bank = e.bank

        @block.sync
        def _(sp):
            sp.dma_start(e.hT[:, :, :], e.h_keep).then_inc(s_h, 16)
            for l in range(NL):
                if l >= 2:
                    sp.wait_ge(s_mm, 6 * (l - 1))
                q = slice(l * WC, (l + 1) * WC)
                for i, a in enumerate((GA0, GS0)):
                    sp.dma_start(wg[:, l % 2, i], win[:, :, a + l * WC:a + (l + 1) * WC]).then_inc(s_w[l % 2], 16)
                for g in range(G):
                    sp.dma_start(wb[g * HD:(g + 1) * HD, l % 2, 0],
                                 e.w_br_attn[0].rearrange("(g r d) n -> g d r n", g=G, d=HD)[g, :, :, q]).then_inc(s_w[l % 2], 16)
                sp.dma_start(wb[:, l % 2, 1], e.w_br_ssm[0].rearrange("(k p) n -> p k n", p=P)[:, :, q]).then_inc(s_w[l % 2], 16)

        @block.tensor
        def _(pe):
            load_wait(pe, s_h, 1)
            for u in range(NU):
                f, s = u // 3, u % 3
                l, a = f // 2, f % 2 * P
                if u % 6 == 0:
                    load_wait(pe, s_w[l % 2], 5 * (l // 2 + 1))
                if u >= 2:
                    pe.wait_ge(s_pr, 2 * (u - 1))
                t = slice(s * SL, (s + 1) * SL)
                for i in range(2):
                    for k in range(KD):
                        pe.matmul(bank[4 * (u % 2) + i][:, 0:SL], wg[:, l % 2, i, k, a:a + P], e.hT[:, k, t], start=(k == 0), stop=(k == KD - 1))
                for i, o in enumerate((e.oT, e.ossmT)):
                    for k in range(4):
                        mm = pe.matmul(bank[4 * (u % 2) + 2 + i][:, 0:SL], wb[:, l % 2, i, k, a:a + P], o[:, k, t], start=(k == 0), stop=(k == 3))
                mm.then_inc(s_mm, 1)

        @block.scalar
        def _(act):
            for u in range(NU):
                act.wait_ge(s_mm, u + 1)
                if u >= 2:
                    act.wait_ge(s_mx, u - 1)
                for i in range(2):
                    act.activation(sig[:, u % 2, i, :], bank[4 * (u % 2) + i][:, 0:SL], ACT.Sigmoid).then_inc(s_sig, 1)

        @block.vector
        def _(dve):
            for u in range(NU):
                f, s = u // 3, u % 3
                for i in range(2):
                    dve.wait_ge(s_sig, 2 * u + i + 1)
                    dve.tensor_tensor(sig[:, u % 2, i, :], sig[:, u % 2, i, :], bank[4 * (u % 2) + 2 + i][:, 0:SL], ALU.mult).then_inc(s_pr, 1)
                dve.wait_ge(s_pr, 2 * u + 2)
                dve.tensor_tensor(e.mixT[:, f, s * SL:(s + 1) * SL], sig[:, u % 2, 0, :], sig[:, u % 2, 1, :], ALU.add).then_inc(s_mx, 1)


def add_gated(dve, e, chain, wait_done, psum, tmp, f, s, gate):
    m = min(SL, T - s * SL)
    a = s * SL
    gx = e.mod[:, gate * KD + f, :]
    ins = dve.scalar_tensor_tensor(out=e.xT[:, f, a:a + m], in0=psum[:, 0:m], scalar=gx[:, 0:1], in1=e.xT[:, f, a:a + m],
                                   op0=ALU.mult, op1=ALU.add)
    if m < SL:
        v = lambda x: x.rearrange("p (n t) -> p n t", t=TS)
        ins.then_inc(chain, 1)
        dve.tensor_tensor(v(tmp), v(psum[:, m:SL]), gx[:, 1:1 + NSEQ].unsqueeze(2).to_broadcast([P, NSEQ, TS]), ALU.mult).then_inc(chain, 1)
        dve.wait_ge(chain, wait_done)
        ins = dve.tensor_tensor(e.xT[:, f, a + m:a + SL], e.xT[:, f, a + m:a + SL], tmp, ALU.add)
    return ins


def stage_out(nc, e):
    with ExitStack() as c:
        sb = lambda n, s, d=F32: c.enter_context(nc.sbuf_tensor(n, s, d))
        sem = stage_semaphores(nc, c, "out")
        wo = sb("wo", [P, 2, KD, 2 * P])
        tmp = sb("tmp", [P, NS])
        s_x, s_w, s_mm, s_ev, s_c = sem("s_x"), [sem("s_w0"), sem("s_w1")], sem("s_mm"), sem("s_ev"), sem("s_c")
        block = c.enter_context(nc.Block())
        bank = e.bank

        @block.sync
        def _(sp):
            sp.dma_start(e.xT[:, :, :], e.x_keep).then_inc(s_x, 16)
            for l in range(KD // 2):
                if l >= 2:
                    sp.wait_ge(s_mm, 6 * (l - 1))
                sp.dma_start(wo[:, l % 2], e.w_out[0].rearrange("(k p) n -> p k n", p=P)[:, :, l * 2 * P:(l + 1) * 2 * P])\
                  .then_inc(s_w[l % 2], 16)

        @block.tensor
        def _(pe):
            for u in range(3 * KD):
                f, s = u // 3, u % 3
                l = f // 2
                if u % 6 == 0:
                    load_wait(pe, s_w[l % 2], l // 2 + 1)
                if u >= 4:
                    pe.wait_ge(s_ev, u - 3)
                for k in range(KD):
                    mm = pe.matmul(bank[u % 4][:, 0:SL], wo[:, l % 2, k, f % 2 * P:(f % 2 + 1) * P], e.mixT[:, k, s * SL:(s + 1) * SL],
                                   start=(k == 0), stop=(k == KD - 1))
                mm.then_inc(s_mm, 1)

        @block.vector
        def _(dve):
            load_wait(dve, s_x, 1)
            for u in range(3 * KD):
                f, s = u // 3, u % 3
                dve.wait_ge(s_mm, u + 1)
                if s == 2 and f:
                    dve.wait_ge(s_ev, u)
                add_gated(dve, e, s_c, 2 * (f + 1), bank[u % 4], tmp[:, :], f, s, 2).then_inc(s_ev, 1)


def stage_mlp(nc, e):
    NR = 4
    FH = F // 2 // P
    with ExitStack() as c:
        sb = lambda n, s, d=F32: c.enter_context(nc.sbuf_tensor(n, s, d))
        sem = stage_semaphores(nc, c, "mlp")
        act_ = sb("act_", [P, FH, NT])
        ring = sb("wring", [P, NR, FH * P])
        tmp = sb("tmp2", [P, NS])
        s_w = [sem(f"s_w{i}") for i in range(NR)]
        s_up, s_relu, s_sq, s_dn, s_ev, s_c, s_used = (sem(n) for n in ("s_up", "s_relu", "s_sq", "s_dn", "s_ev", "s_c", "s_used"))
        block = c.enter_context(nc.Block())
        bank = e.bank
        NL1, NL2 = FH // 2, KD
        w1v = e.w_ff1[0].rearrange("(k p) n -> p k n", p=P)
        w2v = e.w_ff2[0].rearrange("(k p) n -> p k n", p=P)
        NU1, NU2 = 3 * FH, 3 * KD

        @block.sync
        def _(sp):
            x = 0
            for half in range(2):
                for l in range(NL1 + NL2):
                    if x >= NR:
                        sp.wait_ge(s_used, x - NR + 1)
                    if l < NL1:
                        a = half * FH * P + l * 2 * P
                        sp.dma_start(ring[:, x % NR, :].rearrange("p (k n) -> p k n", k=KD), w1v[:, :, a:a + 2 * P]).then_inc(s_w[x % NR], 16)
                    else:
                        f = l - NL1
                        sp.dma_start(ring[:, x % NR, :].rearrange("p (k n) -> p k n", k=FH), w2v[:, half * FH:(half + 1) * FH, f * P:(f + 1) * P])\
                          .then_inc(s_w[x % NR], 16)
                    x += 1

        @block.tensor
        def _(pe):
            for half in range(2):
                x0 = half * (NL1 + NL2)
                for u in range(NU1):
                    f, s = u // 3, u % 3
                    x = x0 + f // 2
                    if u % 6 == 0:
                        load_wait(pe, s_w[x % NR], x // NR + 1)
                    v = half * NU1 + u
                    if v >= 4:
                        pe.wait_ge(s_relu, v - 3)
                    w = ring[:, x % NR, :].rearrange("p (k n) -> p k n", k=KD)
                    for k in range(KD):
                        mm = pe.matmul(bank[v % 4][:, 0:SL], w[:, k, f % 2 * P:(f % 2 + 1) * P], e.hT[:, k, s * SL:(s + 1) * SL],
                                       start=(k == 0), stop=(k == KD - 1))
                    mm.then_inc(s_up, 1)
                    if u % 6 == 5:
                        pe.wait_ge(s_up, v + 1)
                        pe.sem_inc(s_used, 1)
                pe.wait_ge(s_sq, NU1 * (half + 1))
                for u in range(NU2):
                    f, s = u // 3, u % 3
                    x = x0 + NL1 + f
                    if u % 3 == 0:
                        load_wait(pe, s_w[x % NR], x // NR + 1)
                    v = half * NU2 + u
                    if v >= 4:
                        pe.wait_ge(s_ev, v - 3)
                    w = ring[:, x % NR, :].rearrange("p (k n) -> p k n", k=FH)
                    for k in range(FH):
                        mm = pe.matmul(bank[4 + v % 4][:, 0:SL], w[:, k, :], act_[:, k, s * SL:(s + 1) * SL], start=(k == 0), stop=(k == FH - 1))
                    mm.then_inc(s_dn, 1)
                    if s == 2:
                        pe.wait_ge(s_dn, v + 1)
                        pe.sem_inc(s_used, 1)

        @block.scalar
        def _(act):
            for half in range(2):
                for u in range(NU1):
                    f, s = u // 3, u % 3
                    v = half * NU1 + u
                    act.wait_ge(s_up, v + 1)
                    if half and u == 0:
                        act.wait_ge(s_dn, NU2)
                    act.activation(act_[:, f, s * SL:(s + 1) * SL], bank[v % 4][:, 0:SL], ACT.Relu).then_inc(s_relu, 1)

        @block.vector
        def _(dve):
            for half in range(2):
                for u in range(NU1):
                    f, s = u // 3, u % 3
                    dve.wait_ge(s_relu, half * NU1 + u + 1)
                    a = act_[:, f, s * SL:(s + 1) * SL]
                    dve.tensor_tensor(a, a, a, ALU.mult).then_inc(s_sq, 1)
                for u in range(NU2):
                    f, s = u // 3, u % 3
                    v = half * NU2 + u
                    dve.wait_ge(s_dn, v + 1)
                    if s == 2 and v > 2:
                        dve.wait_ge(s_ev, v)
                    add_gated(dve, e, s_c, 2 * (half * KD + f + 1), bank[4 + v % 4], tmp[:, :], f, s, 5).then_inc(s_ev, 1)


def stage_store(nc, e):
    with ExitStack() as c:
        sb = lambda n, s, d=F32: c.enter_context(nc.sbuf_tensor(n, s, d))
        sem = stage_semaphores(nc, c, "store")
        yrow = sb("yrow", [P, 3, D])
        s_t, s_tc = sem("s_t"), sem("s_tc")
        block = c.enter_context(nc.Block())
        rows = lambda tb: P if tb < TB else NS
        bank = e.bank

        @block.tensor
        def _(pe):
            for tb in range(TB + 1):
                n = rows(tb)
                for h in range(2):
                    u = 2 * tb + h
                    if u >= 4:
                        pe.wait_ge(s_tc, u - 3)
                    for k in range(4):
                        mm = pe.transpose(bank[u % 4][0:n, k * P:(k + 1) * P], e.hT[:, 4 * h + k, tb * P:tb * P + n], e.ident)
                    mm.then_inc(s_t, 1)

        @block.scalar
        def _(act):
            for u in range(2 * (TB + 1)):
                tb, h = u // 2, u % 2
                n = rows(tb)
                act.wait_ge(s_t, u + 1)
                if h == 0 and tb >= 3:
                    load_wait(act, e.y_stored[tb % 3], tb // 3)
                act.activation(yrow[0:n, tb % 3, h * 512:(h + 1) * 512], bank[u % 4][0:n, :], ACT.Copy).then_inc(s_tc, 1)

        @block.sync
        def _(sp):
            for tb in range(TB + 1):
                n = rows(tb)
                sp.wait_ge(s_tc, 2 * tb + 2)
                dst = e.y_prompt[0, tb * P:(tb + 1) * P, :] if tb < TB else e.y_sample.rearrange("n t d -> (n t) d")
                sp.dma_start(dst, yrow[0:n, tb % 3, :]).then_inc(e.y_stored[tb % 3], 16)
            for i in range(3):
                load_wait(sp, e.y_stored[i], 3)


def stages(nc, e):
    with nc.sbuf_tensor("hT", [P, KD, NT], F32, side="right") as hT:
        e.hT = hT
        with nc.sbuf_tensor("xT", [P, KD, NT], F32, side="right") as xT:
            e.xT = xT
            stage_inputs(nc, e)
            stage_norm(nc, e, "_mix", e.xT, e.hT, 0, shift=0, scale=1)
            stage_keep(nc, e)
        stage_ssm(nc, e)
        outer = ExitStack()
        attn = ExitStack()
        sb = lambda n, s, d=F32: attn.enter_context(nc.sbuf_tensor(n, s, d))
        e.qT = sb("qT", [P, R, NT])
        e.kT = sb("kT", [P, 2, NT])
        e.vslc = sb("vslc", [P, TB, 3 * HD])
        e.vwin = sb("vwin", [P, TB, 3 * HD])
        e.vnew = sb("vnew", [NS, 2, KVW])
        e.gates = sb("gates", [3 * HQ, NT])
        stage_project(nc, e)
    with outer:
        with attn:
            e.bt = sb("bt", [P, HQ, 2 * P])
            e.bc = sb("bc", [P, HQ, 16])
            e.btail = sb("btail", [P, P])
            e.bcd = sb("bcd", [P, 8])
            e.bnew = sb("bnew", [P, 2, NS])
            e.qbd = sb("qbd", [P, NSEQ, 32])
            e.rowidx = sb("rowidx", [P, NSEQ * 2], U32)
            e.kcp = sb("kcp", [P, T // CHK])
            e.vcp = sb("vcp", [T // CHK, 3 * HD])
            e.kcT = sb("kcT", [P, NSEQ, 256])
            e.vc = sb("vc", [P, NSEQ, 2, KVW])
            with ExitStack() as c:
                sb2 = lambda n, s, d=F32: c.enter_context(nc.sbuf_tensor(n, s, d))
                e.w1T = sb2("w1T", [P, 2, 8, 2, HD])
                e.w2 = sb2("w2c", [HD, 2, HD])
                e.cbias = sb2("cbias", [HD, 2])
                stage_tables(nc, e)
                stage_compress(nc, e)
            e.oT = outer.enter_context(nc.sbuf_tensor("oT", [P, R, NT], F32, side="right"))
            stage_prompt(nc, e)
            stage_decode(nc, e)
        late = ExitStack()
        e.xT = late.enter_context(nc.sbuf_tensor("xT_late", [P, KD, NT], F32))
        e.hT = late.enter_context(nc.sbuf_tensor("hT_late", [P, KD, NT], F32))
        with nc.sbuf_tensor("mixT", [P, KD, NT], F32) as e.mixT:
            stage_merge(nc, e)
            stage_out(nc, e)
    with late:
        stage_norm(nc, e, "_mlp", e.xT, e.hT, 1, shift=3, scale=4)
        stage_mlp(nc, e)
        stage_norm(nc, e, "_fin", e.xT, e.hT, 2)
        stage_store(nc, e)


def stage_keep(nc, e):
    with nc.semaphore("s_keep") as s, nc.Block() as block:
        @block.sync
        def _(sp):
            sp.dma_start(e.x_keep, e.xT[:, :, :]).then_inc(s, 16)
            sp.dma_start(e.h_keep, e.hT[:, :, :]).then_inc(s, 16)
            sp.wait_ge(s, 32)


def build(nc, ins, outs):
    e = Env()
    (e.x_prompt, e.x_sample, e.cache_k_cmp, e.cache_v_cmp, e.cache_k_slc, e.cache_v_slc, e.cache_k_win, e.cache_v_win,
     e.state_re, e.state_im, e.page_table, e.c_prompt, e.c_sample, e.rel_bias, e.w_ada, e.b_ada, g_mix, g_mlp, e.w_in,
     e.cmp_pe, e.cmp_w1, e.cmp_b1, e.cmp_w2, e.lam_re, e.lam_im, e.log_dt, e.b_re, e.b_im, e.c_re, e.c_im, e.ssm_d,
     e.w_glu, e.w_br_attn, e.w_br_ssm, e.w_out, e.w_ff1, e.w_ff2, g_final, e.consts_in, e.onehot_in) = ins
    (e.y_prompt, e.y_sample, e.p_k_cmp, e.p_v_cmp, e.p_k_slc, e.p_v_slc, e.p_k_win, e.p_v_win, e.p_re, e.p_im,
     e.s_k_cmp, e.s_v_cmp, e.s_k_slc, e.s_v_slc, e.s_k_win, e.s_v_win, e.s_re, e.s_im) = outs
    e.g_norm_mix = g_mix.rearrange("a (k p) -> (a k) p", p=P)
    e.g_norm_mlp = g_mlp.rearrange("a (k p) -> (a k) p", p=P)
    e.g_final = g_final.rearrange("(k p) -> k p", p=P)

    with ExitStack() as c:
        sb = lambda n, s, d=F32: c.enter_context(nc.sbuf_tensor(n, s, d))
        e.ps = c.enter_context(nc.psum_tensor("ps", [P, 8 * 512], F32))
        e.bank = [e.ps[:, 512 * i:512 * (i + 1)] for i in range(8)]
        sem = lambda n: c.enter_context(nc.semaphore(n))
        e.states_stored, e.caches_stored = sem("states_stored"), sem("caches_stored")
        e.y_stored = [sem(f"y_stored{i}") for i in range(3)]
        e.consts = sb("consts", [P, NCONST])
        e.ident = e.consts[:, C_IDENT:C_IDENT + P]
        e.ones = e.consts[:, C_ONES:C_ONES + P]
        e.eps = e.consts[:, C_EPS:C_EPS + 1]
        e.winmask = e.consts[:, C_WINM:C_WINM + P]
        e.sumr = e.consts[:, C_SUMR:C_SUMR + P]
        e.winhead = e.consts[:, C_WINH:C_WINH + TS]
        e.cmprow = e.consts[:, C_CROW:C_CROW + 1]
        e.mod = sb("mod", [P, 6 * KD, 1 + NSEQ])
        e.vec = sb("vec", [P, 3 * KD])
        e.ossmT = sb("ossmT", [P, SSM // P, NT])
        e.h_keep = nc.dram_tensor("h_keep", (P, KD, NT), F32, kind="Internal").ap()
        e.x_keep = nc.dram_tensor("x_keep", (P, KD, NT), F32, kind="Internal").ap()
        stages(nc, e)


def plan_consts():
    parts, at = {}, 0
    def put(name, a):
        nonlocal at
        full = np.zeros((P, a.shape[1]), np.float32)
        full[0:a.shape[0]] = a
        parts[name] = (at, full)
        at += a.shape[1]
    put("ident", np.eye(P, dtype=np.float32))
    put("ones", np.ones((P, P), np.float32))
    put("eps", np.full((P, 1), EPS, np.float32))
    sel = np.zeros((3 * HQ, 3, R, P), np.float32)
    for b in range(3):
        for r in range(R):
            for p in range(P):
                sel[b * HQ + (p // HD) * R + r, b, r, p] = 1
    put("gatesel", sel.reshape(3 * HQ, -1))
    k = np.arange(P)
    put("winmask", np.where(k[None, :] >= k[:, None], 0.0, NEG).astype(np.float32))
    put("cmprow", (k[:, None] >= CHK * 2 - 1).astype(np.float32))
    i, t = np.arange(P)[:, None], np.arange(P)[None, :]
    same = (i // 32 == t // 32) & ((i // 16) % 2 == (t // 16) % 2) & (i % 4 == t % 4)
    put("sumr", same.astype(np.float32))
    put("winhead", np.where(np.arange(TS)[None, :] < (k % TS)[:, None], NEG, 0.0).astype(np.float32))
    put("pow", np.tile(np.concatenate([np.arange(LC + 1), np.arange(LC)[::-1]]).astype(np.float32)[None, :], (P, 1)))
    put("sub", (k % 8).astype(np.float32)[:, None])
    return parts, at


_PARTS, NCONST = plan_consts()
C_IDENT, C_ONES, C_EPS, C_GSEL, C_WINM, C_CROW, C_SUMR, C_WINH, C_POW, C_SUB = (
    _PARTS[n][0] for n in ("ident", "ones", "eps", "gatesel", "winmask", "cmprow", "sumr", "winhead", "pow", "sub"))
BW = 383


def one_hot():
    n = 255 - np.arange(BW)
    exact = NB // 2
    nf = np.maximum(n, exact).astype(np.float32)
    large = exact + (np.log(nf / exact) / np.float32(np.log(128 / exact)) * (NB - exact)).astype(np.int32)
    b = np.where(n < exact, np.maximum(n, 0), np.minimum(large, NB - 1))
    out = np.zeros((NB + 1, BW), np.float32)
    out[b, np.arange(BW)] += 1
    out[NB - 1, :] -= 1
    out[NB, :] = n < 0
    return np.concatenate([out, out[:, ::-1]], axis=1)


_INS = ['x_prompt', 'x_sample', 'cache_k_cmp', 'cache_v_cmp', 'cache_k_slc', 'cache_v_slc', 'cache_k_win', 'cache_v_win',
        'state_ssm_re', 'state_ssm_im', 'page_table', 'c_prompt', 'c_sample', 'rel_bias', 'w_ada', 'b_ada', 'g_norm_mix',
        'g_norm_mlp', 'w_in', 'cmp_pe', 'cmp_w1', 'cmp_b1', 'cmp_w2', 'ssm_lambda_re', 'ssm_lambda_im', 'ssm_log_dt',
        'ssm_b_re', 'ssm_b_im', 'ssm_c_re', 'ssm_c_im', 'ssm_d', 'w_glu', 'w_br_attn', 'w_br_ssm', 'w_out', 'w_ff1',
        'w_ff2', 'g_final']
_OUTS = [(1, T, D), (NSEQ, TS, D)] + [(1, 1, T, G, HD)] * 4 + [(1, 1, WIN, G, HD)] * 2 + [(1, 1, SG, SP)] * 2 \
    + [(1, NSEQ, TS, G, HD)] * 4 + [(1, NSEQ, WIN, G, HD)] * 2 + [(1, NSEQ, SG, SP)] * 2


def kernel(**inputs):
    import concourse.bacc as _bacc
    from concourse.bass_utils import run_bass_kernel_spmd as _run

    nc = _bacc.Bacc("TRN2", target_bir_lowering=False, num_devices=1)
    arrays, args = {}, []
    for name in _INS:
        arrays[f"in_{name}"] = np.ascontiguousarray(inputs[name])
    arrays["in_consts"] = np.concatenate([a for _, a in _PARTS.values()], axis=1)
    arrays["in_onehot"] = one_hot()
    for name, a in arrays.items():
        args.append(nc.dram_tensor(name, a.shape, mybir.dt.from_np(a.dtype), kind="ExternalInput").ap())
    outs = [nc.dram_tensor(f"out_{i}", s, F32, kind="ExternalOutput").ap() for i, s in enumerate(_OUTS)]
    build(nc, args, outs)
    r = _run(nc, [arrays], core_ids=[0])
    return tuple(r.results[0][f"out_{i}"] for i in range(len(_OUTS)))
```

```python
from contextlib import ExitStack

import numpy as np

import concourse.bass as bass
from concourse import mybir

ALU = mybir.AluOpType
ACT = mybir.ActivationFunctionType
F32 = mybir.dt.float32
F32R = mybir.dt.float32r
I32 = mybir.dt.int32
U32 = mybir.dt.uint32
AXX = mybir.AxisListType.X

P = 128
D = 1024
KD = D // P
T = 1024
TB = T // P
NSEQ, TS = 8, 4
NS = NSEQ * TS
NT = T + NS
SL = NT // 3
HQ, G, R, HD = 8, 2, 4, 64
KVW = G * HD
PAST, PAGE = 4096, 128
NPAGE = PAST // PAGE
NPHYS = 5 * NSEQ * NPAGE // 4
CHK = 16
WIN = 512
F = 4 * D
SSM = D // 2
SG, SI, SP = 32, 16, 64
LC = 8
NCH = T // LC
NB = 32
EPS = 1e-6
NEG = -1e30
BIG = 1e30
Q0 = 0
KV0 = HQ * HD
GN0 = KV0 + 6 * KVW
U0 = GN0 + 3 * HQ
GA0 = U0 + SSM
GS0 = GA0 + D
INW = GS0 + D
TWO_PI = 2.0 * np.pi


class Env:
    pass


def load_wait(eng, sem, n):
    eng.wait_ge(sem, 16 * n)


def stage_semaphores(nc, c, stage):
    taken = []

    def give_back():
        nc.clear_and_free_semaphores(taken)
        nc.all_engine_barrier()

    def sem(name):
        taken.append(nc.alloc_semaphore(name=f"{name}_{stage}"))
        return taken[-1]

    c.callback(give_back)
    return sem


def stage_inputs(nc, e):
    NC9 = 1 + NSEQ
    with ExitStack() as c:
        sb = lambda n, s, d=F32: c.enter_context(nc.sbuf_tensor(n, s, d))
        sem = stage_semaphores(nc, c, "in")
        xrow = sb("xrow", [P, 3, D])
        crow = sb("crow", [NC9, D])
        srow = sb("srow", [NC9, D])
        scT = sb("scT", [P, KD, NC9])
        vrow = sb("vrow", [3 * KD, P])
        brow = sb("brow", [1, 6 * D])
        one9 = sb("one9", [1, NC9])
        wada = sb("wada", [P, 2, KD, 512])
        modrow = sb("modrow", [NC9, 2, 512])
        s_const, s_cond, s_vec, s_bada = sem("s_const"), sem("s_cond"), sem("s_vec"), sem("s_bada")
        s_x = [sem(f"s_x{i}") for i in range(3)]
        s_wada = [sem(f"s_wada{i}") for i in range(2)]
        s_silu, s_one, s_cT, s_cTc, s_vT, s_vTc = (sem(n) for n in ("s_silu", "s_one", "s_cT", "s_cTc", "s_vT", "s_vTc"))
        s_xT, s_xTc, s_mod, s_modc, s_mT, s_mTc = (sem(n) for n in ("s_xT", "s_xTc", "s_mod", "s_modc", "s_mT", "s_mTc"))
        block = c.enter_context(nc.Block())
        wview = e.w_ada[0].rearrange("(k p) n -> p k n", p=P)
        NBLK = 6 * D // 512

        def tokens(tb):
            return P if tb < TB else NS

        @block.sync
        def _(sp):
            sp.dma_start(crow[0:1, :], e.c_prompt).then_inc(s_cond, 16)
            sp.dma_start(crow[1:NC9, :], e.c_sample).then_inc(s_cond, 16)
            sp.dma_start(e.consts[:, :], e.consts_in).then_inc(s_const, 16)
            sp.dma_start(brow[:, :], e.b_ada).then_inc(s_bada, 16)
            for i in range(NBLK):
                if i >= 2:
                    sp.wait_ge(s_mod, i - 1)
                sp.dma_start(wada[:, i % 2], wview[:, :, i * 512:(i + 1) * 512]).then_inc(s_wada[i % 2], 16)

        @block.gpsimd
        def _(pool):
            pool.memset(one9[:, :], 1.0).then_inc(s_one, 1)

        @block.scalar
        def _(act):
            for i, g in enumerate((e.g_norm_mix, e.g_norm_mlp, e.g_final)):
                act.dma_start(vrow[i * KD:(i + 1) * KD, :], g).then_inc(s_vec, 16)
            for tb in range(TB + 1):
                if tb >= 3:
                    act.wait_ge(s_xT, 2 * (tb - 2))
                n = tokens(tb)
                src = e.x_prompt[0, tb * P:(tb + 1) * P, :] if tb < TB else e.x_sample.rearrange("n t d -> (n t) d")
                act.dma_start(xrow[0:n, tb % 3, :], src).then_inc(s_x[tb % 3], 16)
                if tb == 2:
                    load_wait(act, s_cond, 2)
                    act.activation(srow[:, :], crow[:, :], ACT.Silu).then_inc(s_silu, 1)

        @block.tensor
        def _(pe):
            load_wait(pe, s_const, 1)
            pe.wait_ge(s_silu, 1)
            for k in range(KD):
                mm = pe.transpose(e.bank[0][:, k * NC9:(k + 1) * NC9], srow[:, k * P:(k + 1) * P], e.ident[0:NC9, 0:NC9])
            mm.then_inc(s_cT, 1)
            load_wait(pe, s_vec, 3)
            pe.transpose(e.bank[1][:, 0:3 * KD], vrow[:, :], e.ident[0:3 * KD, 0:3 * KD]).then_inc(s_vT, 1)
            for tb in range(TB + 1):
                n = tokens(tb)
                load_wait(pe, s_x[tb % 3], tb // 3 + 1)
                for h in range(2):
                    j = 2 * tb + h
                    if j >= 2:
                        pe.wait_ge(s_xTc, j - 1)
                    for k in range(4):
                        kk = 4 * h + k
                        mm = pe.transpose(e.bank[2 + h][:, k * P:k * P + n], xrow[0:n, tb % 3, kk * P:(kk + 1) * P],
                                          e.ident[0:n, 0:n])
                    mm.then_inc(s_xT, 1)
            pe.wait_ge(s_cTc, 1)
            pe.wait_ge(s_one, 1)
            load_wait(pe, s_bada, 1)

            def turn(i):
                pe.wait_ge(s_modc, i + 1)
                if i >= 2:
                    pe.wait_ge(s_mTc, i - 1)
                for q in range(4):
                    mm = pe.transpose(e.bank[6 + i % 2][:, q * NC9:(q + 1) * NC9], modrow[:, i % 2, q * P:(q + 1) * P],
                                      e.ident[0:NC9, 0:NC9])
                mm.then_inc(s_mT, 1)

            for i in range(NBLK):
                load_wait(pe, s_wada[i % 2], i // 2 + 1)
                if i >= 2:
                    pe.wait_ge(s_modc, i - 1)
                out = e.bank[4 + i % 2][0:NC9, :]
                for k in range(KD):
                    pe.matmul(out, scT[:, k, :], wada[:, i % 2, k, :], start=(k == 0), stop=False)
                pe.matmul(out, one9[:, :], brow[:, i * 512:(i + 1) * 512], start=False, stop=True).then_inc(s_mod, 1)
                if i >= 1:
                    turn(i - 1)
            turn(NBLK - 1)

        @block.vector
        def _(dve):
            dve.wait_ge(s_cT, 1)
            dve.tensor_copy(scT[:, :, :], e.bank[0][:, 0:KD * NC9].rearrange("p (k n) -> p k n", k=KD)).then_inc(s_cTc, 1)
            dve.wait_ge(s_vT, 1)
            dve.tensor_copy(e.vec[:, :], e.bank[1][:, 0:3 * KD]).then_inc(s_vTc, 1)
            for tb in range(TB + 1):
                n = tokens(tb)
                for h in range(2):
                    dve.wait_ge(s_xT, 2 * tb + h + 1)
                    dve.tensor_copy(e.xT[:, 4 * h:4 * h + 4, tb * P:tb * P + n],
                                    e.bank[2 + h][:, :].rearrange("p (k n) -> p k n", k=4)[:, :, 0:n]).then_inc(s_xTc, 1)

            def keep(i):
                dve.wait_ge(s_mT, i + 1)
                dve.tensor_copy(e.mod[:, 4 * i:4 * i + 4, :],
                                e.bank[6 + i % 2][:, 0:4 * NC9].rearrange("p (q n) -> p q n", q=4)).then_inc(s_mTc, 1)

            for i in range(NBLK):
                dve.wait_ge(s_mod, i + 1)
                if i >= 2:
                    dve.wait_ge(s_mT, i - 1)
                dve.tensor_copy(modrow[:, i % 2, :], e.bank[4 + i % 2][0:NC9, :]).then_inc(s_modc, 1)
                if i >= 1:
                    keep(i - 1)
            keep(NBLK - 1)


def stage_norm(nc, e, tag, src, dst, gain, shift=None, scale=None):
    NC9 = 1 + NSEQ
    with ExitStack() as c:
        sb = lambda n, s, d=F32: c.enter_context(nc.sbuf_tensor(n + tag, s, d))
        sem = stage_semaphores(nc, c, "norm" + tag)
        sq = sb("sq", [P, 4, SL])
        rstd = sb("rstd", [P, NT])
        amp = sb("amp", [P, KD, NC9])
        s_sq, s_ssq, s_sqrt, s_amp, s_r, s_n, s_h = (sem(n) for n in ("s_sq", "s_ssq", "s_sqrt", "s_amp", "s_r", "s_n", "s_h"))
        block = c.enter_context(nc.Block())
        NU = 3 * KD

        @block.scalar
        def _(act):
            for i in range(NU):
                s, k = i // KD, i % KD
                if i >= 4:
                    act.wait_ge(s_ssq, i - 3)
                act.activation(sq[:, i % 4, :], src[:, k, s * SL:(s + 1) * SL], ACT.Square).then_inc(s_sq, 1)
            act.wait_ge(s_ssq, NU)
            for s in range(3):
                act.activation(rstd[:, s * SL:(s + 1) * SL], e.bank[s][:, 0:SL], ACT.Sqrt, bias=e.eps, scale=1.0 / D)\
                   .then_inc(s_sqrt, 1)

        @block.tensor
        def _(pe):
            for i in range(NU):
                s, k = i // KD, i % KD
                pe.wait_ge(s_sq, i + 1)
                pe.matmul(e.bank[s][:, 0:SL], e.ones[:, :], sq[:, i % 4, :], start=(k == 0), stop=(k == KD - 1))\
                  .then_inc(s_ssq, 1)

        @block.vector
        def _(dve):
            g = e.vec[:, gain * KD:(gain + 1) * KD]
            if scale is not None:
                dve.tensor_scalar(amp[:, :, :], e.mod[:, scale * KD:(scale + 1) * KD, :], 1.0, None, ALU.add).then_inc(s_amp, 1)
                dve.wait_ge(s_amp, 1)
                dve.tensor_tensor(amp[:, :, :], amp[:, :, :], g.unsqueeze(2).to_broadcast([P, KD, NC9]), ALU.mult)\
                   .then_inc(s_amp, 1)
            for s in range(3):
                dve.wait_ge(s_sqrt, s + 1)
                dve.reciprocal(rstd[:, s * SL:(s + 1) * SL], rstd[:, s * SL:(s + 1) * SL]).then_inc(s_r, 1)
            dve.wait_ge(s_r, 3)
            if scale is not None:
                dve.wait_ge(s_amp, 2)
            for k in range(KD):
                dve.tensor_tensor(dst[:, k, :], src[:, k, :], rstd[:, :], ALU.mult).then_inc(s_n, 1)
                dve.wait_ge(s_n, k + 1)
                if scale is None:
                    dve.tensor_scalar(dst[:, k, :], dst[:, k, :], g[:, k:k + 1], None, ALU.mult).then_inc(s_h, 1)
                    continue
                dve.tensor_scalar(dst[:, k, 0:T], dst[:, k, 0:T], amp[:, k, 0:1], e.mod[:, shift * KD + k, 0:1],
                                  ALU.mult, ALU.add).then_inc(s_h, 1)
                ds = dst[:, k, T:NT].rearrange("p (n t) -> p n t", t=TS)
                dve.tensor_tensor(ds, ds, amp[:, k, 1:NC9].unsqueeze(2).to_broadcast([P, NSEQ, TS]), ALU.mult)\
                   .then_inc(s_h, 1)
                dve.wait_ge(s_h, 3 * k + 2)
                dve.tensor_tensor(ds, ds, e.mod[:, shift * KD + k, 1:NC9].unsqueeze(2).to_broadcast([P, NSEQ, TS]),
                                  ALU.add).then_inc(s_h, 1)


def stage_norm_split(nc, e, tag, src, gain, shift, scale):
    NC9 = 1 + NSEQ
    with ExitStack() as c:
        sb = lambda n, s, d=F32: c.enter_context(nc.sbuf_tensor(n + tag, s, d))
        sem = stage_semaphores(nc, c, "norm" + tag)
        sq = sb("sq", [P, 4, SL])
        rstd = sb("rstd", [P, 3, SL])
        amp = sb("amp", [P, KD, NC9])
        hn = sb("hn", [P, 4, SL])
        squared, summed, root, amp_set, rstd_set, scaled, moved, hi_set, lo_set = (sem(n) for n in (
            "squared", "summed", "root", "amp_set", "rstd_set", "scaled", "moved", "hi_set", "lo_set"))
        block = c.enter_context(nc.Block())
        NU = 3 * KD
        sl = lambda s: slice(s * SL, (s + 1) * SL)
        M = T - 2 * SL

        @block.scalar
        def _(act):
            def modulate(i):
                s, k = i // KD, i % KD
                act.wait_ge(scaled, i + 1)
                m = SL if s < 2 else M
                act.activation(hn[:, i % 4, 0:m], hn[:, i % 4, 0:m], ACT.Identity, bias=e.mod[:, shift * KD + k, 0:1], scale=amp[:, k, 0:1])\
                   .then_inc(moved, 1)
                act.wait_ge(moved, i + 1)
                act.activation(e.hhi[:, k, sl(s)], hn[:, i % 4, :], ACT.Copy).then_inc(hi_set, 1)

            for i in range(NU):
                s, k = i // KD, i % KD
                if i >= 4:
                    act.wait_ge(summed, i - 3)
                act.activation(sq[:, i % 4, :], src[:, k, sl(s)], ACT.Square).then_inc(squared, 1)
            for s in range(3):
                act.wait_ge(summed, KD * (s + 1))
                act.activation(rstd[:, s, :], e.bank[s][:, 0:SL], ACT.Sqrt, bias=e.eps, scale=1.0 / D).then_inc(root, 1)
            for i in range(NU):
                modulate(i)

        @block.tensor
        def _(pe):
            for i in range(NU):
                s, k = i // KD, i % KD
                pe.wait_ge(squared, i + 1)
                pe.matmul(e.bank[s][:, 0:SL], e.ones[:, :], sq[:, i % 4, :], start=(k == 0), stop=(k == KD - 1)).then_inc(summed, 1)

        @block.vector
        def _(dve):
            g = e.vec[:, gain * KD:(gain + 1) * KD]
            dve.tensor_scalar(amp[:, :, :], e.mod[:, scale * KD:(scale + 1) * KD, :], 1.0, None, ALU.add).then_inc(amp_set, 1)
            dve.wait_ge(amp_set, 1)
            dve.tensor_tensor(amp[:, :, :], amp[:, :, :], g.unsqueeze(2).to_broadcast([P, KD, NC9]), ALU.mult).then_inc(amp_set, 1)
            dve.wait_ge(amp_set, 2)
            for s in range(3):
                dve.wait_ge(root, s + 1)
                dve.reciprocal(rstd[:, s, :], rstd[:, s, :]).then_inc(rstd_set, 1)
                dve.wait_ge(rstd_set, s + 1)
                for k in range(KD):
                    i = s * KD + k
                    if i >= 4:
                        dve.wait_ge(lo_set, i - 3)
                    ins = dve.tensor_tensor(hn[:, i % 4, :], src[:, k, sl(s)], rstd[:, s, :], ALU.mult)
                    if s == 2:
                        ds = hn[:, i % 4, M:SL].rearrange("p (n t) -> p n t", t=TS)
                        ins.then_inc(amp_set, 1)
                        dve.wait_ge(amp_set, 3 + 2 * k)
                        dve.tensor_tensor(ds, ds, amp[:, k, 1:NC9].unsqueeze(2).to_broadcast([P, NSEQ, TS]), ALU.mult).then_inc(amp_set, 1)
                        dve.wait_ge(amp_set, 4 + 2 * k)
                        ins = dve.tensor_tensor(ds, ds, e.mod[:, shift * KD + k, 1:NC9].unsqueeze(2).to_broadcast([P, NSEQ, TS]), ALU.add)
                    ins.then_inc(scaled, 1)

        @block.gpsimd
        def _(pool):
            for i in range(NU):
                s, k = i // KD, i % KD
                pool.wait_ge(hi_set, i + 1)
                pool.tensor_tensor(e.hlo[:, k, sl(s)], hn[:, i % 4, :], e.hhi[:, k, sl(s)], ALU.subtract).then_inc(lo_set, 1)


NJ = SG // 2
E1 = NCH + 1


def stage_ssm(nc, e):
    MAGIC = float(1.5 * 2 ** 23)
    PI2 = float(np.nextafter(np.float32(TWO_PI), np.float32(0)))
    NP = 2 * LC + 1
    with ExitStack() as c:
        sb = lambda n, s, d=F32: c.enter_context(nc.sbuf_tensor(n, s, d))
        sem = stage_semaphores(nc, c, "ssm")
        U = sb("U", [P, SG, LC, SI])
        small = sb("small", [SI, SG * LC * SI])
        Us = small[0:NSEQ, :].rearrange("p (g k i) -> p g k i", g=SG, k=LC)
        hall = small[:, :].rearrange("p (g k i) -> p g k i", g=SG, k=LC)
        Y = U[:, :, :, :].rearrange("p g k i -> p (g k i)").rearrange("p (k g i) -> p k g i", k=LC, g=SG)
        Ys = small[0:NSEQ, 0:SG * TS * SI].rearrange("p (k g i) -> p k g i", g=SG, k=TS)
        UT = sb("UT", [P, SG, NCH + NSEQ])
        wu = sb("wu", [P, KD, SSM])
        Gre = wu[:, 0:4, :].rearrange("p a (b k i) -> p (a b) k i", b=4, k=LC)
        Gim = wu[:, 4:8, :].rearrange("p a (b k i) -> p (a b) k i", b=4, k=LC)
        wglu = wu[:, 0:4, :]
        big = sb("big", [P, 4 * NT])
        ET = big[:, 0:2 * NJ * P].rearrange("p (c j m) -> p c j m", c=2, j=NJ)
        Tm = big[:, 0:SG * P].rearrange("p (g k o) -> p g k o", g=SG, k=LC)
        zT = big[:, :].rearrange("p (q t) -> p q t", q=4)
        Fre = sb("Fre", [P, NJ, LC + 1, SI])
        Fim = sb("Fim", [P, NJ, LC + 1, SI])
        rtab = e.ossmT[:, :, :].rearrange("p q t -> p (q t)")
        Rre = rtab[:, 0:NJ * E1].rearrange("p (j n) -> p j n", j=NJ)
        Rim = rtab[:, NJ * E1:2 * NJ * E1].rearrange("p (j n) -> p j n", j=NJ)
        Sre = sb("Sre", [P, NJ, E1])
        Sim = sb("Sim", [P, NJ, E1])
        H8 = NJ // 2
        M = sb("M", [P, H8, E1])
        t0 = sb("t0", [P, H8, E1])
        t1 = sb("t1", [P, H8, E1])
        Bre = sb("Bre", [P, NJ, SI])
        Bim = sb("Bim", [P, NJ, SI])
        BBre = sb("BBre", [P, NJ, SI])
        BBim = sb("BBim", [P, NJ, SI])
        cdup = big[:, 0:16 * SP].rearrange("p (c q d s) -> p c q d s", c=2, q=4, d=2)
        CT = sb("CT", [P, 2, NJ, SI])
        lamrow = sb("lamrow", [NJ, 2, P])
        ldt = sb("ldt", [1, SG])
        x0 = sb("x0", [P, 2, NSEQ, NJ])
        xs = sb("xs", [P, 2, NSEQ, NJ])
        xt = sb("xt", [P, NSEQ, NJ])
        dtb = sb("dtb", [P, SG])
        dtj = sb("dtj", [P, NJ])
        lam = sb("lam", [P, 2, NJ])
        dT = sb("dT", [SI, SG])
        dI = sb("dI", [SI, SG, SI])
        v = sb("v", [P, 8, NJ])
        w1 = sb("w1", [P, 4, NJ])
        w2 = sb("w2", [P, 4, NJ])
        angles = lambda m: m[:, :, :].rearrange("p j n -> p (j n)")[:, 0:2 * NJ * NP].rearrange("p (c j n) -> p c j n", c=2, j=NJ)
        ang, rnd = angles(M), angles(t1)
        trig = sb("trig", [P, 2, NJ, NP])
        mag = sb("mag", [P, NJ, NP])
        pw = sb("pw", [P, 2, NJ, NP])
        finrow = sb("finrow", [P, 4, P])
        x0row = finrow[:, 0:2, :]
        names = ("s_wu s_lam s_ldt s_b s_c s_x0 s_d s_glu s_ut s_um s_uc s_uT s_uTc s_zero s_lamT s_dt s_x0T s_cT s_exp"
                 " s_mag s_trig s_ptr s_gT s_gTc s_h s_hc s_tm s_et s_bu s_sc s_y s_yc s_ys s_fin s_finc s_zT s_zTc"
                 " s_gl s_sig s_glc s_r s_pchain s_dchain s_ready s_ask s_ttz s_hz s_trot s_setr s_bs s_hall").split()
        S = {n: sem(n) for n in names}
        block = c.enter_context(nc.Block())
        ident = e.ident
        NU = LC + TS
        NG3 = -(-SG // 3)
        bank = e.bank

        @block.sync
        def _(sp):
            sp.dma_start(wu[:, :, :], e.w_in[0].rearrange("(k p) n -> p k n", p=P)[:, :, U0:U0 + SSM]).then_inc(S["s_wu"], 16)
            for i, l in enumerate((e.lam_re, e.lam_im)):
                sp.dma_start(lamrow[:, i, :], l[0].rearrange("(j g) p -> j (g p)", g=2)).then_inc(S["s_lam"], 16)
            sp.dma_start(ldt[:, :], e.log_dt).then_inc(S["s_ldt"], 16)
            for b, s in ((Bre, e.b_re), (Bim, e.b_im)):
                sp.dma_start(b[:, :, :], s[0].rearrange("(j g) p i -> (g p) j i", g=2)).then_inc(S["s_b"], 16)
            for i, s in enumerate((e.c_re, e.c_im)):
                for q in range(4):
                    for d in range(2):
                        sp.dma_start(cdup[:, i, q, d, :], s[0, 8 * q:8 * q + 8].rearrange("g o p -> (g o) p")).then_inc(S["s_c"], 16)
            for i, s in enumerate((e.state_re, e.state_im)):
                sp.dma_start(x0row[:, i, :], s[0].rearrange("n (j g) p -> (n j) (g p)", g=2)).then_inc(S["s_x0"], 16)
            sp.dma_start(dT[:, :], e.ssm_d[0].rearrange("(g i) -> i g", i=SI), allow_slow_non_contiguous=True).then_inc(S["s_d"], 16)
            sp.wait_ge(S["s_hall"], 1)
            sp.wait_ge(S["s_ttz"], 1)
            for k in range(LC):
                sp.dma_start(Tm[SI * k:SI * (k + 1), :, k:LC, :], hall[:, :, 0:LC - k, :]).then_inc(S["s_tm"], 16)
            sp.wait_ge(S["s_gT"], 8)
            sp.dma_start(wglu, e.w_glu[0].rearrange("(k p) n -> p k n", p=P)).then_inc(S["s_glu"], 16)
            sp.wait_ge(S["s_finc"], 1)
            for i, o in enumerate((e.p_re, e.p_im)):
                sp.dma_start(o[0, 0].rearrange("(j g) p -> j (g p)", g=2), finrow[0:NJ, i, :]).then_inc(e.states_stored, 16)
            for i, o in enumerate((e.s_re, e.s_im)):
                sp.dma_start(o[0].rearrange("n (j g) p -> (n j) (g p)", g=2), finrow[:, 2 + i, :]).then_inc(e.states_stored, 16)
            load_wait(sp, e.states_stored, 4)

        @block.gpsimd
        def _(pool):
            n = [0]

            def link(ins):
                n[0] += 1
                ins.then_inc(S["s_pchain"], 1)
                pool.wait_ge(S["s_pchain"], n[0])

            pool.memset(small[0:NSEQ, :], 0.0).then_inc(S["s_zero"], 1)
            link(pool.memset(Rre[:, :, 0:2], 1.0))
            link(pool.memset(Rim[:, :, 0:2], 0.0))
            pool.wait_ge(S["s_ptr"], 1)
            wr, wi, wr2, wi2 = w1[:, 0, :], w1[:, 1, :], w2[:, 0, :], w2[:, 1, :]
            link(pool.tensor_copy(wr, trig[:, 0, :, LC]))
            link(pool.tensor_copy(wi, trig[:, 1, :, LC]))
            m = 1
            while m < NCH:
                wrb = wr.unsqueeze(2).to_broadcast([P, NJ, m])
                wib = wi.unsqueeze(2).to_broadcast([P, NJ, m])
                ar, ai = Rre[:, :, 1:1 + m], Rim[:, :, 1:1 + m]
                br, bi = Rre[:, :, 1 + m:1 + 2 * m], Rim[:, :, 1 + m:1 + 2 * m]
                tt = Sre[:, :, 0:m]
                t2 = Sim[:, :, 0:m]
                link(pool.tensor_tensor(br, ar, wrb, ALU.mult))
                link(pool.tensor_tensor(tt, ai, wib, ALU.mult))
                link(pool.tensor_tensor(br, br, tt, ALU.subtract))
                link(pool.tensor_tensor(bi, ar, wib, ALU.mult))
                link(pool.tensor_tensor(t2, ai, wrb, ALU.mult))
                link(pool.tensor_tensor(bi, bi, t2, ALU.add))
                if 2 * m < NCH:
                    link(pool.tensor_tensor(wr2, wr, wr, ALU.mult))
                    link(pool.tensor_tensor(wi2, wi, wi, ALU.mult))
                    link(pool.tensor_tensor(wi, wr, wi, ALU.mult))
                    link(pool.tensor_tensor(wr, wr2, wi2, ALU.subtract))
                    link(pool.tensor_tensor(wi, wi, wi, ALU.add))
                m *= 2
            pool.sem_inc(S["s_r"], 1)

        @block.tensor
        def _(pe):
            load_wait(pe, S["s_lam"], 2)
            for i in range(2):
                mm = pe.transpose(bank[0][:, i * NJ:(i + 1) * NJ], lamrow[:, i, :], ident[0:NJ, 0:NJ])
            mm.then_inc(S["s_lamT"], 1)
            load_wait(pe, S["s_ldt"], 1)
            pe.matmul(bank[1][:, 0:SG], e.ones[0:1, :], ldt[:, :], start=True, stop=True).then_inc(S["s_dt"], 1)
            load_wait(pe, S["s_x0"], 2)
            for i in range(2):
                mm = pe.transpose(bank[2][:, i * P:(i + 1) * P], x0row[:, i, :], ident[:, :])
            mm.then_inc(S["s_x0T"], 1)
            load_wait(pe, S["s_c"], 16)
            for i in range(2):
                for q in range(4):
                    mm = pe.transpose(bank[3 + i][:, q * P:(q + 1) * P], cdup[:, i, q, :, :].rearrange("p d s -> p (d s)"), ident[:, :])
            mm.then_inc(S["s_cT"], 1)
            load_wait(pe, S["s_wu"], 1)
            for i in range(NU):
                m = P if i < LC else NSEQ
                if i >= 2:
                    pe.wait_ge(S["s_uc"], i - 1)
                for k in range(KD):
                    lhs = e.hT[:, k, 0:T].rearrange("p (c k) -> p c k", k=LC)[:, :, i] if i < LC else \
                        e.hT[:, k, T:NT].rearrange("p (n t) -> p n t", t=TS)[:, :, i - LC]
                    mm = pe.matmul(bank[6 + i % 2][0:m, :], lhs, wu[:, k, :], start=(k == 0), stop=(k == KD - 1))
                mm.then_inc(S["s_um"], 1)
            pe.wait_ge(S["s_uc"], NU)
            for b in range(NG3):
                if b >= 2:
                    pe.wait_ge(S["s_uTc"], b - 1)
                for g in range(3 * b, min(3 * b + 3, SG)):
                    o = (g - 3 * b) * (NCH + NSEQ)
                    pe.transpose(bank[6 + b % 2][:, o:o + NCH], U[:, g, :, :].rearrange("p k i -> p (k i)"), ident[:, :])
                    mm = pe.transpose(bank[6 + b % 2][:, o + NCH:o + NCH + NSEQ], Us[:, g, :, :].rearrange("p k i -> p (k i)"),
                                      ident[0:NSEQ, 0:NSEQ])
                mm.then_inc(S["s_uT"], 1)
            pe.wait_ge(S["s_ask"], 1)
            for b in range(8):
                if b >= 2:
                    pe.wait_ge(S["s_gTc"], b - 1)
                elif b == 0:
                    pe.wait_ge(S["s_uTc"], NG3)
                for q in range(4):
                    x = 4 * b + q
                    Gx = (Gre, Gim)[x // NJ]
                    mm = pe.transpose(bank[6 + b % 2][:, q * P:(q + 1) * P], Gx[:, x % NJ, :, :].rearrange("p k i -> p (k i)"), ident[:, :])
                    if q == 3:
                        mm.then_inc(S["s_gT"], 1)
            for b in range(4):
                pe.wait_ge(S["s_hc"], 2 * b - 2) if b >= 2 else pe.wait_ge(S["s_gTc"], 8)
                for q in range(8):
                    g = 8 * b + q
                    j, h = g // 2, 64 * (g % 2)
                    o = bank[4 + 2 * (b % 2) + g % 2][0:SI, q // 2 * P:(q // 2 + 1) * P]
                    pe.matmul(o, BBre[h:h + SP, j, :], Fre[h:h + SP, j, 0:LC, :].rearrange("p l o -> p (l o)"), start=True, stop=False)
                    mm = pe.matmul(o, BBim[h:h + SP, j, :], Fim[h:h + SP, j, 0:LC, :].rearrange("p l o -> p (l o)"), start=False, stop=True)
                    if q >= 6:
                        mm.then_inc(S["s_h"], 1)
            for half in range(2):
                if half:
                    pe.wait_ge(S["s_sc"], 1)
                else:
                    pe.wait_ge(S["s_gTc"], 8)
                for ci in range(2):
                    for jj in range(H8):
                        j = half * H8 + jj
                        for h in range(2):
                            mm = pe.matmul(bank[2 * ci + jj // 4][64 * h:64 * h + 64, (jj % 4) * P:(jj % 4 + 1) * P],
                                           ET[:, ci, j, 64 * h:64 * h + 64], UT[:, 2 * j + h, 0:NCH], start=True, stop=True)
                mm.then_inc(S["s_bu"], 1)
            for ci in range(2):
                for j in range(NJ):
                    for h in range(2):
                        o = ci * P + j * NSEQ
                        mm = pe.matmul(bank[4][64 * h:64 * h + 64, o:o + NSEQ], ET[:, ci, j, 64 * h:64 * h + 64],
                                       UT[:, 2 * j + h, NCH:NCH + NSEQ], start=True, stop=True)
            mm.then_inc(S["s_bs"], 1)
            pe.wait_ge(S["s_fin"], 1)
            for i, s in enumerate((Sre, Sim)):
                pe.transpose(bank[0][0:NJ, i * P:(i + 1) * P], s[:, :, NCH], ident[:, :])
            for i in range(2):
                mm = pe.transpose(bank[0][:, (2 + i) * P:(3 + i) * P], xs[:, i, :, :].rearrange("p n j -> p (n j)"), ident[:, :])
            mm.then_inc(S["s_setr"], 1)
            load_wait(pe, S["s_tm"], LC)
            pe.wait_ge(S["s_hc"], 8)
            for b in range(4):
                if b >= 2:
                    pe.wait_ge(S["s_yc"], 2 * b - 2)
                for q in range(8):
                    g = 8 * b + q
                    j, h = g // 2, 64 * (g % 2)
                    o = bank[4 + 2 * (b % 2) + g % 2][:, q // 2 * P:(q // 2 + 1) * P]
                    pe.matmul(o, UT[:, g, 0:NCH], Tm[:, g, :, :].rearrange("p k o -> p (k o)"), start=True, stop=False)
                    pe.matmul(o, Sre[h:h + SP, j, 0:NCH], Fre[h:h + SP, j, 1:LC + 1, :].rearrange("p l o -> p (l o)"), start=False, stop=False)
                    mm = pe.matmul(o, Sim[h:h + SP, j, 0:NCH], Fim[h:h + SP, j, 1:LC + 1, :].rearrange("p l o -> p (l o)"), start=False, stop=True)
                    if q >= 6:
                        mm.then_inc(S["s_y"], 1)
            for b in range(4):
                if b >= 2:
                    pe.wait_ge(S["s_ys"], 2 * b - 2)
                if b == 1:
                    pe.wait_ge(S["s_finc"], 1)
                for q in range(8):
                    g = 8 * b + q
                    j, h = g // 2, 64 * (g % 2)
                    o = bank[2 - 2 * (b % 2) + g % 2][0:NSEQ, q // 2 * 64:(q // 2 + 1) * 64]
                    pe.matmul(o, UT[:, g, NCH:NCH + NSEQ], Tm[:, g, TS:LC, :].rearrange("p k o -> p (k o)"), start=True, stop=False)
                    pe.matmul(o, x0[h:h + SP, 0, :, j], Fre[h:h + SP, j, 1:TS + 1, :].rearrange("p l o -> p (l o)"), start=False, stop=False)
                    mm = pe.matmul(o, x0[h:h + SP, 1, :, j], Fim[h:h + SP, j, 1:TS + 1, :].rearrange("p l o -> p (l o)"), start=False, stop=True)
                    if q >= 6:
                        mm.then_inc(S["s_y"], 1)
            pe.wait_ge(S["s_yc"], 8)
            pe.wait_ge(S["s_ys"], 8)
            for b in range(LC):
                if b >= 2:
                    pe.wait_ge(S["s_zTc"], b - 1)
                for q in range(4):
                    mm = pe.transpose(bank[6 + b % 2][:, q * P:(q + 1) * P], Y[:, b, 8 * q:8 * q + 8, :].rearrange("p g i -> p (g i)"), ident[:, :])
                mm.then_inc(S["s_zT"], 1)
            pe.wait_ge(S["s_zTc"], 7)
            for k in range(TS):
                for q in range(4):
                    o = (k * 4 + q) * NSEQ
                    mm = pe.transpose(bank[6][:, o:o + NSEQ], Ys[:, k, 8 * q:8 * q + 8, :].rearrange("p g i -> p (g i)"), ident[0:NSEQ, 0:NSEQ])
            mm.then_inc(S["s_zT"], 1)
            pe.wait_ge(S["s_zTc"], LC + 1)
            load_wait(pe, S["s_glu"], 1)
            for f in range(4):
                for s in range(3):
                    i = 3 * f + s
                    if i >= 4:
                        pe.wait_ge(S["s_sig"], i - 3)
                    for k in range(4):
                        mm = pe.matmul(bank[i % 4][:, 0:SL], wglu[:, k, f * P:(f + 1) * P], zT[:, k, s * SL:(s + 1) * SL],
                                       start=(k == 0), stop=(k == 3))
                    mm.then_inc(S["s_gl"], 1)

        @block.scalar
        def _(act):
            act.wait_ge(S["s_dt"], 1)
            act.activation(dtb[:, :], bank[1][:, 0:SG], ACT.Exp).then_inc(S["s_exp"], 1)
            act.wait_ge(S["s_zero"], 1)
            for i in range(NU):
                act.wait_ge(S["s_um"], i + 1)
                m, dst, k = (P, U, i) if i < LC else (NSEQ, Us, TS + i - LC)
                act.activation(dst[:, :, k, :], bank[6 + i % 2][0:m, :].rearrange("p (g i) -> p g i", g=SG), ACT.Copy)\
                   .then_inc(S["s_uc"], 1)
            for b in range(NG3):
                g0, g1 = 3 * b, min(3 * b + 3, SG)
                act.wait_ge(S["s_uT"], b + 1)
                act.activation(UT[:, g0:g1, :], bank[6 + b % 2][:, 0:(g1 - g0) * (NCH + NSEQ)].rearrange("p (g n) -> p g n", g=g1 - g0),
                               ACT.Copy).then_inc(S["s_uTc"], 1)
            act.wait_ge(S["s_mag"], 1)
            act.activation(mag[:, :, :], mag[:, :, :], ACT.Exp).then_inc(S["s_exp"], 1)
            act.wait_ge(S["s_trig"], 1)
            act.activation(trig[:, :, :, :], ang[:, :, :, :], ACT.Sin, scale=PI2).then_inc(S["s_ptr"], 1)
            for b in range(8):
                act.wait_ge(S["s_gT"], b + 1)
                x = 4 * b
                act.activation(ET[:, x // NJ, x % NJ:x % NJ + 4, :], bank[6 + b % 2][:, :].rearrange("p (q m) -> p q m", q=4), ACT.Copy)\
                   .then_inc(S["s_gTc"], 1)
            act.wait_ge(S["s_uT"], NG3)
            for x in range(8):
                b, h = x // 2, x % 2
                act.wait_ge(S["s_h"], x + 1)
                act.activation(hall[:, 8 * b + h:8 * b + 8:2, :, :], bank[4 + 2 * (b % 2) + h][0:SI, :].rearrange("p (g k o) -> p g k o", g=4, k=LC),
                               ACT.Copy).then_inc(S["s_hc"], 1)
            for x in range(8):
                b, h = x // 2, x % 2
                act.wait_ge(S["s_y"], x + 1)
                act.activation(Y[:, :, 8 * b + h:8 * b + 8:2, :], bank[4 + 2 * (b % 2) + h][:, :].rearrange("p (g k o) -> p k g o", g=4, k=LC),
                               ACT.Gelu_apprx_tanh).then_inc(S["s_yc"], 1)
            for x in range(8):
                b, h = x // 2, x % 2
                act.wait_ge(S["s_y"], 8 + x + 1)
                act.activation(Ys[:, :, 8 * b + h:8 * b + 8:2, :], bank[2 - 2 * (b % 2) + h][0:NSEQ, 0:256].rearrange("p (g k o) -> p k g o", g=4, k=TS),
                               ACT.Gelu_apprx_tanh).then_inc(S["s_ys"], 1)
            for b in range(LC):
                act.wait_ge(S["s_zT"], b + 1)
                act.activation(zT[:, :, 0:T].rearrange("p q (c k) -> p q c k", k=LC)[:, :, :, b],
                               bank[6 + b % 2][:, :].rearrange("p (q c) -> p q c", q=4), ACT.Copy).then_inc(S["s_zTc"], 1)
            act.wait_ge(S["s_zT"], LC + 1)
            for k in range(TS):
                ins = act.activation(zT[:, :, T:NT].rearrange("p q (n t) -> p q n t", t=TS)[:, :, :, k],
                                     bank[6][:, k * 32:(k + 1) * 32].rearrange("p (q n) -> p q n", q=4), ACT.Copy)
            ins.then_inc(S["s_zTc"], 1)
            for i in range(12):
                f, s = i // 3, i % 3
                act.wait_ge(S["s_gl"], i + 1)
                act.activation(e.ossmT[:, f, s * SL:(s + 1) * SL], bank[i % 4][:, 0:SL], ACT.Sigmoid).then_inc(S["s_sig"], 1)

        @block.vector
        def _(dve):
            n = [0]

            def link(ins):
                n[0] += 1
                ins.then_inc(S["s_dchain"], 1)
                dve.wait_ge(S["s_dchain"], n[0])

            tt, ts_ = dve.tensor_tensor, dve.tensor_scalar
            dve.wait_ge(S["s_exp"], 1)
            link(dve.tensor_copy(dtj[0:64, :], dtb[0:64, :].rearrange("p (j g) -> p j g", g=2)[:, :, 0]))
            link(dve.tensor_copy(dtj[64:128, :], dtb[64:128, :].rearrange("p (j g) -> p j g", g=2)[:, :, 1]))
            dve.wait_ge(S["s_lamT"], 1)
            link(ts_(lam[:, 0, :], bank[0][:, 0:NJ], -1e-4, None, ALU.min))
            link(dve.tensor_copy(lam[:, 1, :], bank[0][:, NJ:2 * NJ]))
            lr, li = lam[:, 0, :], lam[:, 1, :]
            a1, th = v[:, 0, :], v[:, 1, :]
            link(tt(a1, lr, dtj[:, :], ALU.mult))
            link(tt(th, li, dtj[:, :], ALU.mult))
            link(ts_(th, th, float(1.0 / TWO_PI), None, ALU.mult))
            pows = e.consts[:, C_POW:C_POW + NP].unsqueeze(1).to_broadcast([P, NJ, NP])
            wide = lambda a: a.unsqueeze(2).to_broadcast([P, NJ, NP])
            tt(mag[:, :, :], wide(a1), pows, ALU.mult).then_inc(S["s_mag"], 1)
            link(tt(ang[:, 1, :, :], wide(th), pows, ALU.mult))
            link(ts_(ang[:, 0, :, :], ang[:, 1, :, :], 0.25, None, ALU.add))
            link(ts_(rnd[:, :, :, :], ang[:, :, :, :], MAGIC, None, ALU.add))
            link(ts_(rnd[:, :, :, :], rnd[:, :, :, :], MAGIC, None, ALU.subtract))
            link(tt(ang[:, :, :, :], ang[:, :, :, :], rnd[:, :, :, :], ALU.subtract))
            dve.sem_inc(S["s_trig"], 1)
            dve.wait_ge(S["s_ptr"], 1)
            dve.wait_ge(S["s_exp"], 2)
            for i in range(2):
                link(tt(pw[:, i, :, :], mag[:, :, :], trig[:, i, :, :], ALU.mult))
            pr, pi = pw[:, 0, :, :], pw[:, 1, :, :]
            am, den, fr, fi, x = v[:, 2, :], v[:, 3, :], v[:, 4, :], v[:, 5, :], v[:, 6, :]
            link(ts_(am, pr[:, :, 1], -1.0, None, ALU.add))
            link(tt(den, lr, lr, ALU.mult))
            link(tt(x, li, li, ALU.mult))
            link(tt(den, den, x, ALU.add))
            link(dve.reciprocal(den, den))
            link(tt(fr, am, lr, ALU.mult))
            link(tt(x, pi[:, :, 1], li, ALU.mult))
            link(tt(fr, fr, x, ALU.add))
            link(tt(fr, fr, den, ALU.mult))
            link(tt(fi, pi[:, :, 1], lr, ALU.mult))
            link(tt(x, am, li, ALU.mult))
            link(tt(fi, fi, x, ALU.subtract))
            link(tt(fi, fi, den, ALU.mult))
            load_wait(dve, S["s_b"], 2)
            frb, fib = (a.unsqueeze(2).to_broadcast([P, NJ, SI]) for a in (fr, fi))
            tb = t0[:, :, :].rearrange("p j n -> p (j n)")[:, 0:NJ * SI].rearrange("p (j i) -> p j i", i=SI)
            link(tt(BBre[:, :, :], Bre[:, :, :], frb, ALU.mult))
            link(tt(tb, Bim[:, :, :], fib, ALU.mult))
            link(tt(BBre[:, :, :], BBre[:, :, :], tb, ALU.subtract))
            link(tt(BBim[:, :, :], Bim[:, :, :], frb, ALU.mult))
            link(tt(tb, Bre[:, :, :], fib, ALU.mult))
            link(tt(BBim[:, :, :], BBim[:, :, :], tb, ALU.add))
            dve.wait_ge(S["s_cT"], 1)
            for i in range(2):
                src = bank[3 + i][:, :].rearrange("p (j g o) -> p j g o", g=2, o=SI)
                for h in range(2):
                    link(dve.tensor_copy(CT[64 * h:64 * h + 64, i, :, :], src[64 * h:64 * h + 64, :, h, :]))
            dve.wait_ge(S["s_x0T"], 1)
            link(dve.tensor_copy(x0[:, :, :, :], bank[2][:, 0:2 * P].rearrange("p (c n j) -> p c n j", c=2, n=NSEQ)))
            dve.wait_ge(S["s_um"], NU)
            tG = lambda a, k, s: a[:, :, k].unsqueeze(2).to_broadcast([P, NJ, s])
            tg = t0[:, :, :].rearrange("p j n -> p (j n)")[:, 0:NJ * SI].rearrange("p (j i) -> p j i", i=SI)
            for k in range(LC):
                q = LC + 1 + k
                link(tt(Gre[:, :, k, :], BBre[:, :, :], tG(pr, q, SI), ALU.mult))
                link(tt(tg, BBim[:, :, :], tG(pi, q, SI), ALU.mult))
                link(tt(Gre[:, :, k, :], Gre[:, :, k, :], tg, ALU.subtract))
                link(tt(Gim[:, :, k, :], BBim[:, :, :], tG(pr, q, SI), ALU.mult))
                link(tt(tg, BBre[:, :, :], tG(pi, q, SI), ALU.mult))
                link(tt(Gim[:, :, k, :], Gim[:, :, k, :], tg, ALU.add))
            for l in range(LC + 1):
                cr, cim = CT[:, 0, :, :], CT[:, 1, :, :]
                link(tt(Fre[:, :, l, :], cr, tG(pr, l, SI), ALU.mult))
                link(tt(tg, cim, tG(pi, l, SI), ALU.mult))
                link(tt(Fre[:, :, l, :], Fre[:, :, l, :], tg, ALU.subtract))
                link(tt(Fim[:, :, l, :], cr, tG(pi, l, SI), ALU.mult))
                link(tt(tg, cim, tG(pr, l, SI), ALU.mult))
                link(dve.scalar_tensor_tensor(out=Fim[:, :, l, :], in0=Fim[:, :, l, :], scalar=-1.0, in1=tg,
                                              op0=ALU.mult, op1=ALU.subtract))
            dve.sem_inc(S["s_ask"], 1)
            load_wait(dve, S["s_d"], 1)
            link(tt(dI[:, :, :], dT[:, :].unsqueeze(2).to_broadcast([SI, SG, SI]),
                    ident[0:SI, 0:SI].unsqueeze(1).to_broadcast([SI, SG, SI]), ALU.mult))
            dve.wait_ge(S["s_hc"], 8)
            tt(hall[:, :, 0, :], hall[:, :, 0, :], dI[:, :, :], ALU.add).then_inc(S["s_hall"], 1)
            dve.wait_ge(S["s_r"], 1)
            for half in range(2):
                j0 = half * H8
                jj = slice(j0, j0 + H8)
                link(dve.tensor_copy(M[:, :, :], mag[:, jj, LC].unsqueeze(2).to_broadcast([P, H8, E1])))
                link(dve.memset(M[:, :, 0], 0.0))
                link(dve.memset(Sre[:, jj, 0], 0.0))
                link(dve.memset(Sim[:, jj, 0], 0.0))
                dve.wait_ge(S["s_bu"], half + 1)
                for q in range(2):
                    qq = slice(j0 + 4 * q, j0 + 4 * q + 4)
                    br = bank[q][:, :].rearrange("p (j n) -> p j n", j=4)
                    bi = bank[2 + q][:, :].rearrange("p (j n) -> p j n", j=4)
                    rr, ri = Rre[:, qq, 1:E1], Rim[:, qq, 1:E1]
                    sr, si = Sre[:, qq, 1:E1], Sim[:, qq, 1:E1]
                    a, b = t0[:, 0:4, 1:E1], t1[:, 0:4, 1:E1]
                    link(tt(sr, br, rr, ALU.mult))
                    link(tt(a, bi, ri, ALU.mult))
                    link(tt(si, bi, rr, ALU.mult))
                    link(tt(b, br, ri, ALU.mult))
                    link(tt(sr, sr, a, ALU.add))
                    link(tt(si, si, b, ALU.subtract))
                Mf = M[:, :, :].rearrange("p j n -> p (j n)")
                for s in (Sre, Sim):
                    f = s[:, jj, :].rearrange("p j n -> p (j n)")
                    link(dve.tensor_tensor_scan(f, Mf, f, 0.0, ALU.mult, ALU.add))
                rr, ri, sr, si = Rre[:, jj, :], Rim[:, jj, :], Sre[:, jj, :], Sim[:, jj, :]
                link(tt(t0[:, :, :], sr, ri, ALU.mult))
                link(tt(t1[:, :, :], si, ri, ALU.mult))
                link(tt(sr, sr, rr, ALU.mult))
                link(tt(si, si, rr, ALU.mult))
                link(tt(sr, sr, t1[:, :, :], ALU.subtract))
                tt(si, si, t0[:, :, :], ALU.add).then_inc(S["s_sc"], 1)
                dve.wait_ge(S["s_sc"], half + 1)
            dve.wait_ge(S["s_bs"], 1)
            p4r = pr[:, :, TS].unsqueeze(1).to_broadcast([P, NSEQ, NJ])
            p4i = pi[:, :, TS].unsqueeze(1).to_broadcast([P, NSEQ, NJ])
            bs = bank[4][:, 0:2 * P].rearrange("p (c j n) -> p c n j", c=2, n=NSEQ)
            link(tt(xs[:, 0, :, :], x0[:, 0, :, :], p4r, ALU.mult))
            link(tt(xt[:, :, :], x0[:, 1, :, :], p4i, ALU.mult))
            link(tt(xs[:, 0, :, :], xs[:, 0, :, :], xt[:, :, :], ALU.subtract))
            link(tt(xs[:, 0, :, :], bs[:, 0], xs[:, 0, :, :], ALU.add))
            link(tt(xs[:, 1, :, :], x0[:, 1, :, :], p4r, ALU.mult))
            link(tt(xt[:, :, :], x0[:, 0, :, :], p4i, ALU.mult))
            link(tt(xs[:, 1, :, :], xs[:, 1, :, :], xt[:, :, :], ALU.add))
            tt(xs[:, 1, :, :], bs[:, 1], xs[:, 1, :, :], ALU.add).then_inc(S["s_fin"], 1)
            dve.memset(Tm[:, :, :, :], 0.0).then_inc(S["s_ttz"], 1)
            dve.wait_ge(S["s_setr"], 1)
            dve.tensor_copy(finrow[0:NJ, 0:2, :], bank[0][0:NJ, 0:2 * P].rearrange("p (c m) -> p c m", c=2)).then_inc(S["s_trot"], 1)
            dve.wait_ge(S["s_trot"], 1)
            dve.tensor_copy(finrow[:, 2:4, :], bank[0][:, 2 * P:4 * P].rearrange("p (c m) -> p c m", c=2)).then_inc(S["s_finc"], 1)
            for f in range(4):
                dve.wait_ge(S["s_sig"], 3 * f + 3)
                tt(e.ossmT[:, f, :], e.ossmT[:, f, :], zT[:, f, :], ALU.mult).then_inc(S["s_glc"], 1)


def stage_project(nc, e):
    with ExitStack() as c:
        sb = lambda n, s, d=F32: c.enter_context(nc.sbuf_tensor(n, s, d))
        sem = stage_semaphores(nc, c, "proj")
        wq = sb("wq", [P, KD, R, G, HD])
        wk = sb("wk", [P, KD, 6 * KVW + 3 * HQ])
        kv = sb("kv", [P, TB + 1, 6 * KVW])
        s_wq, s_wk, s_q, s_qc, s_kv, s_kvc, s_t, s_tc, s_v, s_ones = (sem(n) for n in (
            "s_wq", "s_wk", "s_q", "s_qc", "s_kv", "s_kvc", "s_t", "s_tc", "s_v", "s_ones"))
        block = c.enter_context(nc.Block())
        win = e.w_in[0].rearrange("(k p) n -> p k n", p=P)
        NQ = 3 * (R + 1)
        bank = e.bank
        rows = lambda tb: P if tb < TB else NS

        @block.sync
        def _(sp):
            for r in range(R):
                for g in range(G):
                    a = Q0 + (g * R + r) * HD
                    sp.dma_start(wq[:, :, r, g, :], win[:, :, a:a + HD]).then_inc(s_wq, 16)
            sp.dma_start(wk[:, :, :], win[:, :, KV0:U0]).then_inc(s_wk, 16)
            sp.wait_ge(s_kvc, 2 * TB)
            outs = (e.p_k_cmp, e.p_v_cmp, e.p_k_slc, e.p_v_slc)
            for i, o in enumerate(outs):
                sp.dma_start(o[0, 0].rearrange("(b p) g d -> p b (g d)", p=P), kv[:, 0:TB, i * KVW:(i + 1) * KVW]).then_inc(e.caches_stored, 16)
            for i, o in enumerate((e.p_k_win, e.p_v_win)):
                sp.dma_start(o[0, 0].rearrange("(b p) g d -> p b (g d)", p=P),
                             kv[:, TB - WIN // P:TB, (4 + i) * KVW:(5 + i) * KVW]).then_inc(e.caches_stored, 16)
            sp.wait_ge(s_kvc, 2 * TB + 2)
            for i, o in enumerate((e.s_k_cmp, e.s_v_cmp, e.s_k_slc, e.s_v_slc)):
                sp.dma_start(o[0].rearrange("n t g d -> (n t) (g d)"), kv[0:NS, TB, i * KVW:(i + 1) * KVW]).then_inc(e.caches_stored, 16)
            for i, (o, b) in enumerate(((e.s_k_win, e.cache_k_win), (e.s_v_win, e.cache_v_win))):
                sp.dma_start(o[0, :, 0:WIN - TS].rearrange("n w g d -> n (w g d)"), b[0, :, TS:WIN].rearrange("n w g d -> n (w g d)"))\
                  .then_inc(e.caches_stored, 16)
                sp.dma_start(o[0, :, WIN - TS:WIN].rearrange("n t g d -> n t (g d)"),
                             kv[0:NS, TB, (4 + i) * KVW:(5 + i) * KVW]).then_inc(e.caches_stored, 16)
            load_wait(sp, e.caches_stored, 14)

        @block.gpsimd
        def _(pool):
            pool.memset(e.vslc[:, :, HD:2 * HD], 1.0).then_inc(s_ones, 1)
            pool.memset(e.vwin[:, :, HD:2 * HD], 1.0).then_inc(s_ones, 1)
            for tb in range(TB):
                pool.wait_ge(s_kvc, 2 * tb + 2)
                for dst, i in ((e.vslc, 3), (e.vwin, 5)):
                    for g in range(G):
                        pool.tensor_copy(dst[:, tb, 2 * g * HD:(2 * g + 1) * HD],
                                         kv[:, tb, i * KVW + g * HD:i * KVW + (g + 1) * HD]).then_inc(s_v, 1)
            pool.wait_ge(s_kvc, 2 * TB + 2)
            pool.tensor_copy(e.vnew[:, 0, :], kv[0:NS, TB, 3 * KVW:4 * KVW]).then_inc(s_v, 1)
            pool.tensor_copy(e.vnew[:, 1, :], kv[0:NS, TB, 5 * KVW:6 * KVW]).then_inc(s_v, 1)
            pool.wait_ge(s_v, 4 * TB + 2)

        @block.tensor
        def _(pe):
            load_wait(pe, s_wq, 8)
            load_wait(pe, s_wk, 1)
            for i in range(NQ):
                f, s = i // 3, i % 3
                if i >= 4:
                    pe.wait_ge(s_qc, i - 3)
                m = P if f < R else 3 * HQ
                for k in range(KD):
                    w = wq[:, k, f, :, :].rearrange("p g d -> p (g d)") if f < R else wk[:, k, 6 * KVW:6 * KVW + 3 * HQ]
                    mm = pe.matmul(bank[i % 4][0:m, 0:SL], w, e.hT[:, k, s * SL:(s + 1) * SL], start=(k == 0), stop=(k == KD - 1))
                mm.then_inc(s_q, 1)
            for tb in range(TB + 1):
                for h in range(2):
                    i = 2 * tb + h
                    if i >= 2:
                        pe.wait_ge(s_kvc, i - 1)
                    for k in range(KD):
                        mm = pe.matmul(bank[4 + h][0:rows(tb), 0:3 * KVW], e.hT[:, k, tb * P:tb * P + rows(tb)],
                                       wk[:, k, h * 3 * KVW:(h + 1) * 3 * KVW], start=(k == 0), stop=(k == KD - 1))
                    mm.then_inc(s_kv, 1)
            for tb in range(TB + 1):
                n = rows(tb)
                pe.wait_ge(s_kvc, 2 * tb + 2)
                if tb >= 2:
                    pe.wait_ge(s_tc, tb - 1)
                for q, i in enumerate((2, 4)):
                    mm = pe.transpose(bank[6 + tb % 2][:, q * P:q * P + n], kv[0:n, tb, i * KVW:(i + 1) * KVW], e.ident[0:n, 0:n])
                mm.then_inc(s_t, 1)

        @block.scalar
        def _(act):
            for i in range(NQ):
                f, s = i // 3, i % 3
                act.wait_ge(s_q, i + 1)
                if f < R:
                    act.activation(e.qT[:, f, s * SL:(s + 1) * SL], bank[i % 4][:, 0:SL], ACT.Copy, scale=HD ** -0.5).then_inc(s_qc, 1)
                else:
                    act.activation(e.gates[:, s * SL:(s + 1) * SL], bank[i % 4][0:3 * HQ, 0:SL], ACT.Sigmoid).then_inc(s_qc, 1)

        @block.vector
        def _(dve):
            for i in range(2 * (TB + 1)):
                tb, h = i // 2, i % 2
                dve.wait_ge(s_kv, i + 1)
                dve.tensor_copy(kv[0:rows(tb), tb, h * 3 * KVW:(h + 1) * 3 * KVW], bank[4 + h][0:rows(tb), 0:3 * KVW]).then_inc(s_kvc, 1)
            for tb in range(TB + 1):
                n = rows(tb)
                dve.wait_ge(s_t, tb + 1)
                dve.tensor_copy(e.kT[:, :, tb * P:tb * P + n],
                                bank[6 + tb % 2][:, 0:2 * P].rearrange("p (c n) -> p c n", c=2)[:, :, 0:n]).then_inc(s_tc, 1)


def stage_tables(nc, e):
    with ExitStack() as c:
        sb = lambda n, s, d=F32: c.enter_context(nc.sbuf_tensor(n, s, d))
        sem = stage_semaphores(nc, c, "tab")
        tab = sb("tab", [NB + 1, HQ])
        oh = sb("oh", [NB + 1, 2 * BW])
        line = sb("line", [HQ, BW])
        perow = sb("perow", [16, 2, P])
        peT = sb("peT", [P, 2, 16])
        b1row = sb("b1row", [1, 2, HD])
        ptab = sb("ptab", [P, NSEQ * 2], I32)
        pf = sb("pf", [P, NSEQ * 2])
        s_tab, s_neg, s_oh, s_line, s_linec, s_rb, s_bt, s_bnz, s_bc, s_w, s_pe, s_peT, s_peTc, s_bb, s_pt, s_pf, s_end = (sem(n) for n in (
            "s_tab", "s_neg", "s_oh", "s_line", "s_linec", "s_rb", "s_bt", "s_bnz", "s_bc", "s_w", "s_pe", "s_peT", "s_peTc", "s_bb",
            "s_pt", "s_pf", "s_end"))
        rb = nc.dram_tensor("bias_lines", (P, HQ, BW), F32, kind="Internal").ap()
        block = c.enter_context(nc.Block())
        bank = e.bank
        line_ap = lambda off, ap: bass.AP(tensor=rb.tensor, offset=off, ap=ap)

        @block.sync
        def _(sp):
            sp.dma_start(tab[0:NB, :], e.rel_bias).then_inc(s_tab, 16)
            sp.dma_start(oh[:, :], e.onehot_in).then_inc(s_oh, 16)
            for kv in range(2):
                for j in range(2):
                    sp.dma_start(e.w1T[:, kv, :, j, :], e.cmp_w1[0, kv, 16 * j:16 * j + 16].rearrange("(a s) d e -> (s d) a e", s=2))\
                      .then_inc(s_w, 16)
                sp.dma_start(e.w2[:, kv, :], e.cmp_w2[0, kv]).then_inc(s_w, 16)
                sp.dma_start(perow[:, kv, :], e.cmp_pe[0, kv].rearrange("(a s) d -> a (s d)", s=2)).then_inc(s_pe, 16)
                sp.dma_start(b1row[:, kv, :], e.cmp_b1[:, kv, :]).then_inc(s_pe, 16)
            for sub in range(8):
                sp.dma_start(ptab[sub:P:8, :], bass.AP(tensor=e.page_table.tensor, offset=0, ap=[[1, 16], [16, 2 * NSEQ]]),
                             allow_slow_non_contiguous=True).then_inc(s_pt, 16)
            sp.wait_ge(s_linec, 1)
            sp.dma_start(rb.rearrange("p h w -> h p w"), line[:, None, :].to_broadcast([HQ, P, BW])).then_inc(s_rb, 16)
            load_wait(sp, s_rb, 1)
            for i, dlt in enumerate((1, 0)):
                sp.dma_start(e.bt[:, :, i * P:(i + 1) * P], line_ap(255 - P * dlt, [[HQ * BW - 1, P], [BW, HQ], [1, P]])).then_inc(s_bt, 16)
            sp.wait_ge(s_bnz, 2)
            for m in range(4):
                r = slice(32 * m, 32 * m + 32)
                sp.dma_start(e.btail[r, :], line_ap(127, [[BW, HQ], [HQ * BW - 1, TS], [1, P]])).then_inc(s_bt, 16)
                for t in range(TS):
                    sp.dma_start(e.bcd[32 * m + t:32 * m + 32:TS, :], line_ap(142 - t, [[BW, HQ], [16, 8]]),
                                 allow_slow_non_contiguous=True).then_inc(s_bt, 16)
                for b in range(2):
                    a = TS * (4 * b + m)
                    sp.dma_start(e.bnew[r, b, a:a + TS], line_ap(255, [[BW, HQ], [HQ * BW - 1, TS], [1, TS]])).then_inc(s_bt, 16)
            load_wait(sp, s_bt, 2 + 4 * 7)
            load_wait(sp, s_w, 6)

        @block.gpsimd
        def _(pool):
            pool.memset(e.bnew[:, :, :], NEG).then_inc(s_bnz, 1)
            pool.memset(e.qbd[:, :, :], 0.0).then_inc(s_bnz, 1)
            pool.wait_ge(s_bnz, 2)
            for g in range(G):
                for r in range(R):
                    a = (g * R + r) * TS
                    ins = pool.tensor_copy(e.qbd[g * HD:(g + 1) * HD, :, a:a + TS],
                                           e.qT[g * HD:(g + 1) * HD, r, T:NT].rearrange("p (n t) -> p n t", t=TS))
                    ins.then_inc(s_end, 1)
                    pool.wait_ge(s_end, g * R + r + 1)

        @block.tensor
        def _(pe):
            load_wait(pe, s_tab, 1)
            load_wait(pe, s_oh, 1)
            pe.wait_ge(s_neg, 1)
            pe.matmul(bank[0][0:HQ, 0:BW], tab[:, :], oh[:, 0:BW], start=True, stop=True).then_inc(s_line, 1)
            for i in range(16):
                y0 = BW + 96 - 16 * (i - 9)
                mm = pe.matmul(bank[1][:, i * HQ:(i + 1) * HQ], oh[:, y0:y0 + P], tab[:, :], start=True, stop=True)
            mm.then_inc(s_line, 1)
            load_wait(pe, s_pe, 4)
            for kv in range(2):
                mm = pe.transpose(bank[2][:, kv * 16:kv * 16 + 16], perow[:, kv, :], e.ident[0:16, 0:16])
            mm.then_inc(s_peT, 1)
            pe.wait_ge(s_peTc, 1)
            load_wait(pe, s_w, 6)
            for kv in range(2):
                o = bank[3 + kv][0:HD, 0:1]
                for x in range(16):
                    pe.matmul(o, e.w1T[:, kv, x % 8, x // 8, :], peT[:, kv, x:x + 1], start=(x == 0), stop=False)
                mm = pe.matmul(o, b1row[:, kv, :], e.ones[0:1, 0:1], start=False, stop=True)
            mm.then_inc(s_bb, 1)

        @block.scalar
        def _(act):
            act.wait_ge(s_line, 2)
            act.activation(e.bc[:, :, :], bank[1][:, 0:16 * HQ].rearrange("p (c h) -> p h c", h=HQ), ACT.Copy).then_inc(s_bc, 1)

        @block.vector
        def _(dve):
            dve.memset(tab[NB:NB + 1, :], NEG).then_inc(s_neg, 1)
            dve.wait_ge(s_line, 1)
            dve.tensor_copy(line[:, :], bank[0][0:HQ, 0:BW]).then_inc(s_linec, 1)
            dve.wait_ge(s_peT, 1)
            dve.tensor_copy(peT[:, :, :], bank[2][:, 0:32].rearrange("p (c x) -> p c x", c=2)).then_inc(s_peTc, 1)
            dve.wait_ge(s_bb, 1)
            for kv in range(2):
                dve.tensor_copy(e.cbias[:, kv:kv + 1], bank[3 + kv][0:HD, 0:1]).then_inc(s_peTc, 1)
            load_wait(dve, s_pt, 8)
            dve.tensor_copy(pf[:, :], ptab[:, :]).then_inc(s_pf, 1)
            dve.wait_ge(s_pf, 1)
            dve.tensor_scalar(pf[:, :], pf[:, :], 8.0, e.consts[:, C_SUB:C_SUB + 1], ALU.mult, ALU.add).then_inc(s_pf, 1)
            dve.wait_ge(s_pf, 2)
            dve.tensor_copy(e.rowidx[:, :], pf[:, :]).then_inc(s_pf, 1)


def stage_compress(nc, e):
    NI = 2 + 2 * NSEQ
    NCK = [T // CHK] * 2 + [PAST // CHK] * (2 * NSEQ)
    NBT = [4] * 2 + [8] * (2 * NSEQ)
    first = [sum(NBT[:i]) for i in range(NI + 1)]
    with ExitStack() as c:
        sb = lambda n, s, d=F32: c.enter_context(nc.sbuf_tensor(n, s, d))
        sem = stage_semaphores(nc, c, "cmp")
        raw = sb("raw", [P, 2, 2, CHK * KVW])
        byg = sb("byg", [P, 2, G, CHK, HD])
        xT2 = sb("xT2", [P, 2, 8, 512])
        low = sb("low", [HD, 2, 512])
        hsum = sb("hsum", [HD, 2, 512])
        hid = sb("hid", [HD, 2, G, 256])
        s_raw = [sem(f"s_raw{i}") for i in range(2)]
        s_pl = [sem(f"s_pl{i}") for i in range(2)]
        s_by, s_tr, s_eva, s_evd, s_part, s_low, s_sum, s_hid, s_w2, s_out, s_z = (sem(n) for n in (
            "s_by", "s_tr", "s_eva", "s_evd", "s_part", "s_low", "s_sum", "s_hid", "s_w2o", "s_outc", "s_zc"))
        block = c.enter_context(nc.Block())
        bank = e.bank
        rows = [x.rearrange("a b (c s) g d -> (a b c) (s g d)", s=CHK) for x in (e.cache_k_cmp, e.cache_v_cmp)]

        @block.sync
        def _(sp):
            for i, src in enumerate((e.p_k_cmp, e.p_v_cmp)):
                if i:
                    sp.wait_ge(s_tr, first[1])
                for g in range(G):
                    sp.dma_start(byg[0:64, 0, g, :, :], src[0, 0].rearrange("(c s) g d -> c s g d", s=CHK)[:, :, g, :]).then_inc(s_pl[i], 16)

        @block.gpsimd
        def _(pool):
            for i in range(2, NI):
                n, kv = (i - 2) // 2, i % 2
                if i >= 4:
                    pool.wait_ge(s_by, i - 3)
                for half in range(2):
                    col = 2 * n + half
                    pool.indirect_dma_start(raw[:, i % 2, half, :], None, rows[kv],
                                            bass.IndirectOffsetOnAxis(ap=e.rowidx[:, col:col + 1], axis=0)).then_inc(s_raw[i % 2], 16)

        @block.tensor
        def _(pe):
            def second(i):
                n, kv, C = (i - 2) // 2, i % 2, NCK[i]
                pe.wait_ge(s_hid, i + 1)
                if i >= 2:
                    pe.wait_ge(s_out, i - 1)
                o = bank[6 + i % 2]
                if kv == 0:
                    for g in range(G):
                        mm = pe.matmul(o[g * HD:(g + 1) * HD, 0:C], e.w2[:, 0, :], hid[:, i % 2, g, 0:C], start=True, stop=True)
                else:
                    for half in range(max(C // P, 1)):
                        m = min(C, P)
                        for g in range(G):
                            a = half * P + g * HD
                            mm = pe.matmul(o[0:m, a:a + HD], hid[:, i % 2, g, half * P:half * P + m], e.w2[:, 1, :], start=True, stop=True)
                mm.then_inc(s_w2, 1)

            pe.wait_ge(s_z, 1)
            for i in range(NI):
                C, kv = NCK[i], i % 2
                m = min(C, P)
                if i < 2:
                    load_wait(pe, s_pl[i], 2)
                else:
                    pe.wait_ge(s_by, i - 1)
                for b in range(NBT[i]):
                    y = first[i] + b
                    if y >= 4:
                        pe.wait_ge((s_eva, s_evd)[y % 2], y // 2 - 1)
                    half, sp2 = b // 4, b % 4
                    for a in range(2):
                        for g in range(G):
                            s = 2 * (2 * sp2 + a)
                            o = (a * G + g) * m
                            mm = pe.transpose(bank[y % 4][:, o:o + m], byg[0:m, half, g, s:s + 2, :].rearrange("p s d -> p (s d)"),
                                              e.ident[0:m, 0:m])
                    mm.then_inc(s_tr, 1)
                if i >= 1:
                    second(i - 1)
                pe.wait_ge(s_eva, first[i + 1] // 2)
                pe.wait_ge(s_evd, first[i + 1] // 2)
                if i >= 2:
                    pe.wait_ge(s_sum, i - 1)
                for sp in range(8):
                    mm = pe.matmul(bank[4 + i % 2][:, 0:G * C], e.w1T[:, kv, sp, :, :].rearrange("p j e -> p (j e)"),
                                   xT2[:, i % 2, sp, 0:G * C], start=(sp == 0), stop=(sp == 7))
                mm.then_inc(s_part, 1)
            second(NI - 1)

        def move(i, b):
            m, half, sp2 = min(NCK[i], P), b // 4, b % 4
            src = bank[(first[i] + b) % 4][:, 0:4 * m].rearrange("p (a g c) -> p a g c", a=2, g=G)
            dst = xT2[:, i % 2, 2 * sp2:2 * sp2 + 2, 0:G * NCK[i]].rearrange("p a (g c) -> p a g c", g=G)[:, :, :, half * P:half * P + m]
            return src, dst

        def hidden(act, i):
            C = NCK[i]
            act.wait_ge(s_sum, i + 1)
            if i >= 2:
                act.wait_ge(s_w2, i - 1)
            act.activation(hid[:, i % 2, :, 0:C - 1], hsum[:, i % 2, 0:G * C].rearrange("p (g c) -> p g c", g=G)[:, :, 0:C - 1],
                           ACT.Silu, bias=e.cbias[:, i % 2:i % 2 + 1]).then_inc(s_hid, 1)

        @block.scalar
        def _(act):
            for i in range(NI):
                C = NCK[i]
                for b in range(NBT[i]):
                    if (first[i] + b) % 2 == 0:
                        act.wait_ge(s_tr, first[i] + b + 1)
                        if i >= 2:
                            act.wait_ge(s_part, i - 1)
                        src, dst = move(i, b)
                        act.activation(dst, src, ACT.Copy).then_inc(s_eva, 1)
                if i >= 1:
                    hidden(act, i - 1)
                act.wait_ge(s_part, i + 1)
                if i >= 2:
                    act.wait_ge(s_sum, i - 1)
                act.activation(low[:, i % 2, 0:G * C], bank[4 + i % 2][HD:P, 0:G * C], ACT.Copy).then_inc(s_low, 1)
            hidden(act, NI - 1)

        @block.vector
        def _(dve):
            dve.memset(hid[:, :, :, :], 0.0).then_inc(s_z, 1)

            def regroup(i):
                load_wait(dve, s_raw[i % 2], 2 * (i // 2))
                dve.wait_ge(s_tr, first[i])
                ins = None
                for half in range(2):
                    ins = dve.tensor_copy(byg[:, half, :, :, :].rearrange("p g s d -> p s g d"),
                                          raw[:, i % 2, half, :].rearrange("p (s g d) -> p s g d", g=G, d=HD))
                ins.then_inc(s_by, 1)

            def keep(i):
                n, kv, C = (i - 2) // 2, i % 2, NCK[i]
                dve.wait_ge(s_w2, i + 1)
                o = bank[6 + i % 2]
                if i == 0:
                    ins = dve.tensor_copy(e.kcp[:, :], o[:, 0:C])
                elif i == 1:
                    for g in range(G):
                        ins = dve.tensor_copy(e.vcp[:, 2 * g * HD:(2 * g + 1) * HD], o[0:C, g * HD:(g + 1) * HD])
                elif kv == 0:
                    ins = dve.tensor_copy(e.kcT[:, n, :], o[:, 0:C])
                else:
                    ins = dve.tensor_copy(e.vc[:, n, :, :], o[:, 0:2 * P].rearrange("p (h f) -> p h f", h=2))
                ins.then_inc(s_out, 1)

            for i in range(NI):
                C = NCK[i]
                if i >= 2:
                    regroup(i)
                for b in range(NBT[i]):
                    if (first[i] + b) % 2 == 1:
                        dve.wait_ge(s_tr, first[i] + b + 1)
                        if i >= 2:
                            dve.wait_ge(s_part, i - 1)
                        src, dst = move(i, b)
                        dve.tensor_copy(dst, src).then_inc(s_evd, 1)
                if i >= 1:
                    keep(i - 1)
                dve.wait_ge(s_low, i + 1)
                if i >= 2:
                    dve.wait_ge(s_hid, i - 1)
                v = lambda t, a, b: t.rearrange("p (g c) -> p g c", g=G)[:, :, a:b]
                dve.tensor_tensor(v(hsum[:, i % 2, 0:G * C], 0, C - 1), v(bank[4 + i % 2][0:HD, 0:G * C], 0, C - 1),
                                  v(low[:, i % 2, 0:G * C], 1, C), ALU.add).then_inc(s_sum, 1)
            keep(NI - 1)
            dve.memset(e.vcp[:, HD:2 * HD], 1.0)


CMP, SLC, WND = range(3)


def prompt_units():
    for qb in range(TB):
        for r in range(R):
            for br in (CMP, WND, SLC):
                for g in range(G):
                    lo = 0 if br != WND else max(0, qb - WIN // P) * P
                    hi = 8 * qb + 7 if br == CMP else (qb + 1) * P
                    yield qb, r, br, g, lo, hi - lo


def stage_prompt(nc, e):
    U = list(prompt_units())
    NU = len(U)
    tiles = [-(-u[5] // P) for u in U]
    ngrp = [-(-t // 4) for t in tiles]
    grp0 = [sum(ngrp[:i]) for i in range(NU + 1)]
    NPR, NPT = 3, 4
    with ExitStack() as c:
        sb = lambda n, s, d=F32: c.enter_context(nc.sbuf_tensor(n, s, d))
        sem = stage_semaphores(nc, c, "prompt")
        gT = sb("gT", [P, TB, 3 * HQ])
        pr = sb("pr", [P, NPR, T])
        pt = sb("pt", [P, NPT, TB, P])
        nmax = sb("nmax", [P, 4])
        rsum = sb("rsum", [P, 4])
        s_g, s_gc, s_s, s_bias, s_max, s_e, s_sum, s_rc, s_p, s_t, s_pt, s_pv, s_o = (sem(n) for n in (
            "s_g", "s_gc", "s_s", "s_bias", "s_max", "s_e", "s_sum", "s_rc", "s_p", "s_t", "s_pt", "s_pv", "s_o"))
        block = c.enter_context(nc.Block())
        bank, ps = e.bank, e.ps
        score = lambda u: ps[:, 1024 * (u % 2):1024 * (u % 2) + U[u][5]]
        outp = lambda u: bank[6 + (u // 6) % 2]

        @block.tensor
        def _(pe):
            for tb in range(TB):
                mm = pe.transpose(bank[7][:, tb * 24:(tb + 1) * 24], e.gates[:, tb * P:(tb + 1) * P], e.ident[0:24, 0:24])
            mm.then_inc(s_g, 1)
            pe.wait_ge(s_gc, 1)

            def scores(u):
                qb, r, br, g, lo, n = U[u]
                if u >= 2:
                    pe.wait_ge(s_e, u - 1)
                h = slice(g * HD, (g + 1) * HD)
                keys = e.kcp if br == CMP else e.kT[:, br - 1, :]
                for a in range(0, n, 512):
                    m = min(512, n - a)
                    mm = pe.matmul(score(u)[:, a:a + m], e.qT[h, r, qb * P:(qb + 1) * P], keys[h, lo + a:lo + a + m],
                                   start=True, stop=True)
                mm.then_inc(s_s, 1)

            def turn(u):
                n = U[u][5]
                pe.wait_ge(s_p, u + 1)
                for y in range(ngrp[u]):
                    if grp0[u] + y >= 2:
                        pe.wait_ge(s_pt, grp0[u] + y - 1)
                    for t in range(4 * y, min(4 * y + 4, tiles[u])):
                        m = min(P, n - t * P)
                        mm = pe.transpose(bank[4 + (grp0[u] + y) % 2][0:m, (t % 4) * P:(t % 4 + 1) * P],
                                          pr[:, u % NPR, t * P:t * P + m], e.ident)
                    mm.then_inc(s_t, 1)

            def values(u):
                qb, r, br, _, lo, n = U[u]
                pe.wait_ge(s_pt, grp0[u + 1])
                if u % 6 == 1 and u >= 12:
                    pe.wait_ge(s_o, u // 6 - 1)
                for t in range(tiles[u]):
                    m = min(P, n - t * P)
                    for g in range(G):
                        va = 2 * g * HD
                        v = e.vcp[0:m, va:va + HD] if br == CMP else (e.vslc, e.vwin)[br - 1][:, lo // P + t, va:va + HD]
                        mm = pe.matmul(outp(u)[g * HD:(g + 1) * HD, 0:P], v, pt[0:m, (u - 1 + g) % NPT, t, :],
                                       start=(br == CMP and t == 0), stop=(br == SLC and t == tiles[u] - 1), skip_group_check=True)
                        if t == tiles[u] - 1:
                            mm.then_inc(s_pv, 1)

            for u in range(NU + 4):
                if u < NU:
                    scores(u)
                if 2 <= u < NU + 2:
                    turn(u - 2)
                if u % 2 == 0 and u >= 4:
                    values(u - 3)

        @block.scalar
        def _(act):
            def copies(u):
                for y in range(ngrp[u]):
                    t0, t1 = 4 * y, min(4 * y + 4, tiles[u])
                    m = min(P, U[u][5])
                    act.wait_ge(s_t, grp0[u] + y + 1)
                    if y == 0 and u >= NPT:
                        act.wait_ge(s_pv, u - NPT + 1)
                    act.activation(pt[0:m, u % NPT, t0:t1, :], bank[4 + (grp0[u] + y) % 2][0:m, 0:(t1 - t0) * P].rearrange("p (t q) -> p t q", q=P),
                                   ACT.Copy).then_inc(s_pt, 1)

            for u in range(NU + 2):
                if u < NU:
                    act.wait_ge(s_max, u + 1)
                    if u >= NPR:
                        act.wait_ge(s_t, grp0[u - NPR + 1])
                    if u >= 4:
                        act.wait_ge(s_rc, u - 3)
                    act.activation(pr[:, u % NPR, 0:U[u][5]], score(u), ACT.Exp, bias=nmax[:, u % 4:u % 4 + 1],
                                   accum_out=rsum[:, u % 4:u % 4 + 1]).then_inc(s_e, 1)
                if u >= 2:
                    copies(u - 2)

        @block.vector
        def _(dve):
            bias_n = [0]

            def bias(dst, src):
                bias_n[0] += 1
                dve.tensor_tensor(dst, dst, src, ALU.add).then_inc(s_bias, 1)

            dve.wait_ge(s_g, 1)
            dve.tensor_copy(gT[:, :, :], bank[7][:, 0:TB * 24].rearrange("p (b h) -> p b h", h=24)).then_inc(s_gc, 1)
            dve.wait_ge(s_gc, 1)

            def maxima(u):
                qb, r, br, g, lo, n = U[u]
                h = g * R + r
                dve.wait_ge(s_s, u + 1)
                s = score(u)
                if br == CMP:
                    c0 = max(0, 8 * qb - 9)
                    bias(s[:, c0:n], e.bc[:, h, c0 - (8 * qb - 9):16])
                else:
                    m = min(2 * P, n)
                    bias(s[:, n - m:n], e.bt[:, h, 2 * P - m:2 * P])
                    if br == WND and qb >= WIN // P:
                        bias(s[:, 0:P], e.winmask)
                dve.wait_ge(s_bias, bias_n[0])
                if u >= 4:
                    dve.wait_ge(s_e, u - 3)
                dve.tensor_reduce(nmax[:, u % 4:u % 4 + 1], s, AXX, ALU.max, negate=True).then_inc(s_max, 1)

            def scale(u):
                qb, r, br, g, lo, n = U[u]
                h = g * R + r
                x = rsum[:, u % 4:u % 4 + 1]
                dve.wait_ge(s_e, u + 1)
                dve.tensor_scalar(x, x, 1e-30, None, ALU.max).then_inc(s_sum, 1)
                dve.wait_ge(s_sum, u + 1)
                dve.reciprocal(x, x).then_inc(s_rc, 1)
                dve.wait_ge(s_rc, u + 1)
                p = pr[:, u % NPR, 0:n]
                if br == CMP and qb == 0:
                    dve.tensor_scalar(p, p, e.cmprow, None, ALU.mult).then_inc(s_bias, 1)
                    bias_n[0] += 1
                    dve.wait_ge(s_bias, bias_n[0])
                dve.tensor_scalar(p, p, x, gT[:, qb, br * HQ + h:br * HQ + h + 1], ALU.mult, ALU.mult).then_inc(s_p, 1)

            def output(x):
                qb, r = U[6 * x][0], U[6 * x][1]
                dve.wait_ge(s_pv, 6 * x + 6)
                dve.tensor_copy(e.oT[:, r, qb * P:(qb + 1) * P], outp(6 * x)[:, 0:P]).then_inc(s_o, 1)

            for u in range(NU + 1):
                if u < NU:
                    maxima(u)
                if u >= 1:
                    scale(u - 1)
                if u % 6 == 3 and u >= 9:
                    output(u // 6 - 1)
            output(NU // 6 - 1)


def stage_decode(nc, e):
    NR = 6
    NBAT, M = 2, 4
    W = PAST + NS
    BLK = 64
    NBK = PAST // BLK
    KG = M + 8 * M
    TCMP, TWIN, TSLC = 0, 2, 7
    NTL = TSLC + 33
    with ExitStack() as c:
        sb = lambda n, s, d=F32: c.enter_context(nc.sbuf_tensor(n, s, d))
        sem = stage_semaphores(nc, c, "decode")
        ring = sb("ring", [P, NR, CHK, KVW])
        Ss = sb("Ss", [P, W])
        Sw = sb("Sw", [P, WIN + NS])
        Sc = sb("Sc", [P, 256])
        wt = sb("wt", [P, NTL, P])
        kt = e.bt[:, :, :].rearrange("p h x -> p (h x)").rearrange("p (s x) -> p s x", s=4)
        kwin = e.vslc[:, :, :].rearrange("p b x -> p (b x)")[:, 0:1024].rearrange("p (s j x) -> p s j x", s=2, j=4)
        vwin = e.vwin[:, :, :].rearrange("p b x -> p (b x)")[:, 0:1024].rearrange("p (s j x) -> p s j x", s=2, j=4)
        gd = sb("gd", [P, NBAT, 3])
        sc = sb("sc", [P, NBK + 1])
        scs = sb("scs", [P, NBK + 1])
        m8 = sb("m8", [P, 8])
        st = sb("st", [P, 8])
        gscr = nc.dram_tensor("gate_rows", (3 * HQ, NS), F32, kind="Internal").ap()
        s_ring = [sem(f"s_ring{i}") for i in range(NR)]
        s_kw = [sem(f"s_kw{i}") for i in range(2)]
        s_vw = [sem(f"s_vw{i}") for i in range(2)]
        s_gs, s_gd, s_used, s_wused, s_vused, s_cs, s_cse, s_blk, s_sel, s_kt, s_ktc, s_ks, s_ksc, s_x, s_e, s_w, s_t, s_tc, s_pv, s_o = (
            sem(n) for n in ("s_gs", "s_gd", "s_used", "s_wused", "s_vused", "s_cs", "s_cse", "s_blk", "s_sel", "s_kt", "s_ktc", "s_ks",
                             "s_ksc", "s_x", "s_ed", "s_wd", "s_td", "s_tcd", "s_pvd", "s_od"))
        c_chain = sem("s_chain_d")
        block = c.enter_context(nc.Block())
        bank = e.bank
        rows = [x.rearrange("a b (c s) g d -> (a b c) (s g d)", s=CHK) for x in (e.cache_k_slc, e.cache_v_slc)]
        NG = -(-NTL // 4)

        @block.sync
        def _(sp):
            sp.dma_start(gscr, e.gates[:, T:NT]).then_inc(s_gs, 16)
            load_wait(sp, s_gs, 1)
            for n in range(NSEQ):
                for br in range(3):
                    sp.dma_start(gd[32 * (n % M):32 * (n % M) + 32, n // M, br:br + 1],
                                 bass.AP(tensor=gscr.tensor, offset=br * HQ * NS + n * TS, ap=[[NS, HQ], [1, TS]]),
                                 allow_slow_non_contiguous=True).then_inc(s_gd, 16)
            def window(n, slots, free, landed, cache):
                if n >= 2:
                    sp.wait_ge(free, n - 1)
                sp.dma_start(slots[:, n % 2], cache[0, n].rearrange("(j p) g d -> p j (g d)", p=P)).then_inc(landed[n % 2], 16)

            for b in range(NBAT):
                for n in range(M * b, M * b + M):
                    window(n, kwin, s_wused, s_kw, e.cache_k_win)
                for n in range(M * b, M * b + M):
                    window(n, vwin, s_vused, s_vw, e.cache_v_win)

        @block.gpsimd
        def _(pool):
            for x in range(NBAT * 16):
                b, kv, m, half = x // 16, x // 8 % 2, x // 2 % 4, x % 2
                if x >= NR:
                    pool.wait_ge(s_used, x - NR + 1)
                col = 2 * (M * b + m) + half
                pool.indirect_dma_start(ring[:, x % NR].rearrange("p s x -> p (s x)"), None, rows[kv],
                                        bass.IndirectOffsetOnAxis(ap=e.rowidx[:, col:col + 1], axis=0)).then_inc(s_ring[x % NR], 16)

        @block.tensor
        def _(pe):
            def keys(b, y):
                z = KG * b + y
                if z >= 2:
                    pe.wait_ge(s_ktc, z - 1)
                if y < M:
                    n = M * b + y
                    load_wait(pe, s_kw[n % 2], n // 2 + 1)
                    for j in range(4):
                        mm = pe.transpose(bank[z % 2][:, j * P:(j + 1) * P], kwin[:, n % 2, j, :], e.ident)
                    mm.then_inc(s_kt, 1)
                    return
                v = y - M
                x = 16 * b + v // 4
                load_wait(pe, s_ring[x % NR], x // NR + 1)
                for j in range(4):
                    mm = pe.transpose(bank[z % 2][:, j * P:(j + 1) * P], ring[:, x % NR, 4 * (v % 4) + j, :], e.ident)
                mm.then_inc(s_kt, 1)

            def scores(b, y):
                z = KG * b + y
                m = y if y < M else (y - M) // 8
                pe.wait_ge(s_ktc, z + 1)
                if z >= 2:
                    pe.wait_ge(s_ksc, z - 1)
                pe.matmul(bank[2 + z % 2][32 * m:32 * m + 32, :], e.qbd[:, M * b + m, :], kt[:, z % 4, :], start=True, stop=True)\
                  .then_inc(s_ks, 1)

            def turn(b, y):
                z = NG * b + y
                if z >= 2:
                    pe.wait_ge(s_tc, z - 1)
                for t in range(4 * y, min(4 * y + 4, NTL)):
                    if t < TWIN:
                        pe.wait_ge(s_w, 3 * b + 1)
                        src = Sc[:, t * P:(t + 1) * P]
                    elif t < TSLC:
                        pe.wait_ge(s_w, 3 * b + 2)
                        a = (t - TWIN) * P
                        src = Sw[:, a:min(a + P, WIN + NS)]
                    else:
                        pe.wait_ge(s_w, 3 * b + 3)
                        a = (t - TSLC) * P
                        src = Ss[:, a:min(a + P, W)]
                    mm = pe.transpose(bank[(5, 7)[z % 2]][0:src.shape[1], (t % 4) * P:(t % 4 + 1) * P], src, e.ident)
                mm.then_inc(s_t, 1)

            for b in range(NBAT):
                if b:
                    pe.wait_ge(s_cse, b)
                    pe.wait_ge(s_sel, 4)
                for m in range(M):
                    n = M * b + m
                    pe.matmul(bank[4][32 * m:32 * m + 32, 0:256], e.qbd[:, n, :], e.kcT[:, n, :], start=True, stop=True)
                q4 = e.qbd[:, M * b:M * b + M, :].rearrange("p n x -> p (n x)")
                for i in range(2):
                    mm = pe.matmul(bank[4][:, 256 + 32 * i:288 + 32 * i], q4, e.kT[:, i, T:NT], start=True, stop=True)
                mm.then_inc(s_cs, 1)
                for y in range(KG + 1):
                    if y < KG:
                        keys(b, y)
                        if y < M:
                            pe.wait_ge(s_kt, KG * b + y + 1)
                            pe.sem_inc(s_wused, 1)
                        elif (y - M) % 4 == 3:
                            pe.wait_ge(s_kt, KG * b + y + 1)
                            pe.sem_inc(s_used, 1)
                    if y >= 1:
                        scores(b, y - 1)
                    if y == M + 2:
                        pe.wait_ge(s_blk, b + 1)
                        pe.matmul(bank[6][:, 256:256 + NBK], e.sumr, sc[:, 0:NBK], start=True, stop=True).then_inc(s_sel, 1)
                        pe.wait_ge(s_sel, 4 * b + 1)
                if b:
                    pe.wait_ge(s_o, 1)
                pe.wait_ge(s_sel, 4 * b + 4)
                for y in range(NG):
                    turn(b, y)
                pe.wait_ge(s_tc, NG * (b + 1))
                first = True
                for m in range(M):
                    n = M * b + m
                    o = bank[6][:, 32 * m:32 * m + 32]
                    col = slice(32 * m, 32 * m + 32)

                    def add(v, t, k=P):
                        nonlocal first
                        mm = pe.matmul(o, v, wt[0:k, t, col], start=first, stop=False, skip_group_check=True)
                        first = False
                        return mm

                    for half in range(2):
                        add(e.vc[:, n, half, :], TCMP + half)
                    load_wait(pe, s_vw[n % 2], n // 2 + 1)
                    for j in range(4):
                        mm = add(vwin[:, n % 2, j, :], TWIN + j)
                    mm.then_inc(s_vused, 1)
                    add(e.vnew[:, 1, :], TWIN + 4, NS)
                    for half in range(2):
                        x = 16 * b + 8 + 2 * m + half
                        load_wait(pe, s_ring[x % NR], x // NR + 1)
                        for s in range(CHK):
                            mm = add(ring[:, x % NR, s, :], TSLC + CHK * half + s)
                        mm.then_inc(s_used, 1)
                    mm = add(e.vnew[:, 0, :], TSLC + 32, NS)
                mm.then_inc(s_pv, 1)

        @block.scalar
        def _(act):
            for b in range(NBAT):
                def softmax(i, s):
                    act.wait_ge(s_x, 3 * b + i + 1)
                    act.activation(s, s, ACT.Exp, bias=st[:, i:i + 1], accum_out=st[:, 3 + i:4 + i]).then_inc(s_e, 1)

                for y in range(KG):
                    z = KG * b + y
                    act.wait_ge(s_kt, z + 1)
                    if z >= 4:
                        act.wait_ge(s_ks, z - 3)
                    act.activation(kt[:, z % 4, :], bank[z % 2][:, :], ACT.Copy).then_inc(s_ktc, 1)
                    if y == 0:
                        softmax(0, Sc[:, :])
                    if y == M + 4:
                        softmax(1, Sw[:, :])
                softmax(2, Ss[:, :])
                for y in range(NG):
                    z = NG * b + y
                    t0, t1 = 4 * y, min(4 * y + 4, NTL)
                    act.wait_ge(s_t, z + 1)
                    if b and y == 0:
                        act.wait_ge(s_pv, b)
                    for t in ([None] if not {TWIN + 4, TSLC + 32} & set(range(t0, t1)) else range(t0, t1)):
                        if t is None:
                            ins = act.activation(wt[:, t0:t1, :], bank[(5, 7)[z % 2]][:, 0:(t1 - t0) * P].rearrange("p (t x) -> p t x", x=P), ACT.Copy)
                        else:
                            k = NS if t in (TWIN + 4, TSLC + 32) else P
                            ins = act.activation(wt[0:k, t, :], bank[(5, 7)[z % 2]][0:k, (t - t0) * P:(t - t0 + 1) * P], ACT.Copy)
                    ins.then_inc(s_tc, 1)

        @block.vector
        def _(dve):
            tt = dve.tensor_tensor
            s_c = c_chain
            n_ = [0]

            def link(ins):
                n_[0] += 1
                ins.then_inc(s_c, 1)
                dve.wait_ge(s_c, n_[0])

            def weights(b, i, s):
                dve.wait_ge(s_e, 3 * b + i + 1)
                x = st[:, 3 + i:4 + i]
                link(dve.tensor_scalar(x, x, 1e-30, None, ALU.max))
                link(dve.reciprocal(x, x))
                if i:
                    dve.tensor_scalar(s, s, x, gd[:, b, (0, 2, 1)[i]:(0, 2, 1)[i] + 1], ALU.mult, ALU.mult).then_inc(s_w, 1)

            def top(i, s):
                dve.tensor_reduce(st[:, i:i + 1], s, AXX, ALU.max, negate=True).then_inc(s_x, 1)

            load_wait(dve, s_gd, 3 * NSEQ)
            for b in range(NBAT):
                if b:
                    dve.wait_ge(s_t, NG * b)
                dve.wait_ge(s_cs, b + 1)
                link(dve.tensor_copy(Sc[:, 0:255], bank[4][:, 0:255]))
                link(dve.memset(Sc[:, 255:256], NEG))
                link(tt(Sc[:, 247:255], Sc[:, 247:255], e.bcd[:, :], ALU.add))
                link(tt(Ss[:, PAST:W], bank[4][:, 256:288], e.bnew[:, b, :], ALU.add))
                tt(Sw[:, WIN:WIN + NS], bank[4][:, 288:320], e.bnew[:, b, :], ALU.add).then_inc(s_cse, 1)
                top(0, Sc[:, :])

                def evac(y):
                    z = KG * b + y
                    dve.wait_ge(s_ks, z + 1)
                    m = y if y < M else (y - M) // 8
                    r = slice(32 * m, 32 * m + 32)
                    a = (y - M) % 8 * 512
                    dst = Sw[r, 0:WIN] if y < M else Ss[r, a:a + 512]
                    dve.tensor_copy(dst, bank[2 + z % 2][r, :]).then_inc(s_ksc, 1)

                weights(b, 0, Sc[:, :])
                link(dve.tensor_scalar(Sc[:, :], Sc[:, :], st[:, 3:4], None, ALU.mult))
                p4 = Sc[:, :].rearrange("p (j c) -> p j c", c=4)
                link(tt(sc[:, 0:NBK], p4[:, :, 0], p4[:, :, 1], ALU.add))
                link(tt(sc[:, 0:NBK], sc[:, 0:NBK], p4[:, :, 2], ALU.add))
                link(dve.scalar_tensor_tensor(out=sc[:, 0:NBK], in0=sc[:, 0:NBK], scalar=2.0, in1=p4[:, :, 3], op0=ALU.mult, op1=ALU.add))
                link(tt(sc[:, 1:NBK], sc[:, 1:NBK], p4[:, 0:NBK - 1, 3], ALU.add))
                dve.sem_inc(s_blk, 1)
                dve.tensor_scalar(Sc[:, :], Sc[:, :], gd[:, b, 0:1], None, ALU.mult).then_inc(s_w, 1)
                for y in range(M):
                    evac(y)
                dve.wait_ge(s_ksc, KG * b + M)
                link(tt(Sw[:, 0:TS], Sw[:, 0:TS], e.winhead, ALU.add))
                link(tt(Sw[:, WIN - P:WIN], Sw[:, WIN - P:WIN], e.btail[:, :], ALU.add))
                top(1, Sw[:, :])
                evac(M)
                evac(M + 1)
                dve.wait_ge(s_sel, 4 * b + 1)
                link(dve.tensor_copy(scs[:, 0:NBK], bank[6][:, 256:256 + NBK]))
                link(dve.memset(scs[:, 0:1], BIG))
                dve.memset(scs[:, NBK - 1:NBK + 1], BIG).then_inc(s_sel, 1)
                dve.wait_ge(s_sel, 4 * b + 2)
                for i in range(2):
                    link(dve.max(m8[:, :], scs[:, :]))
                    link(dve.match_replace(scs[:, :], m8[:, :], scs[:, :], -1.0))
                dve.tensor_scalar(scs[:, :], scs[:, :], 0.0, NEG, ALU.is_ge, ALU.mult).then_inc(s_sel, 1)
                weights(b, 1, Sw[:, :])
                for y in range(M + 2, KG):
                    evac(y)
                dve.wait_ge(s_ksc, KG * (b + 1))
                dve.wait_ge(s_sel, 4 * b + 3)
                last = Ss[:, PAST // 2:PAST].rearrange("p (s c) -> p s c", c=P)[:, :, P - 8:P]
                link(tt(last, last, e.btail[:, :].rearrange("p (c s) -> p s c", s=CHK), ALU.add))
                for half in range(2):
                    v = Ss[:, half * PAST // 2:(half + 1) * PAST // 2].rearrange("p (s j c) -> p s j c", s=CHK, c=4)
                    k = scs[:, half * 32:half * 32 + 32].unsqueeze(1).unsqueeze(3).to_broadcast([P, CHK, 32, 4])
                    ins = tt(v, v, k, ALU.add)
                    link(ins)
                dve.sem_inc(s_sel, 1)
                top(2, Ss[:, :])
                weights(b, 2, Ss[:, :])
                dve.wait_ge(s_pv, b + 1)
                for g in range(G):
                    h = slice(g * HD, (g + 1) * HD)
                    dst = e.oT[h, :, T + 16 * b:T + 16 * b + 16].rearrange("p r (m t) -> p r m t", t=TS)
                    src = bank[6][h, 0:P].rearrange("p (m g r t) -> p g r m t", g=G, r=R, t=TS)[:, g]
                    ins = dve.tensor_copy(dst, src)
                ins.then_inc(s_o, 1)


NRAW, NSPLIT = 2, 2
WK = 8


def weight_slots(sb, sem, tag):
    return (sb("wraw" + tag, [P, NRAW, WK, P]), sb("whi" + tag, [P, NSPLIT, WK, P], F32R), sb("wlo" + tag, [P, NSPLIT, WK, P], F32R),
            [sem(f"w_loaded{i}") for i in range(NRAW)], sem("w_hi"), sem("w_split"), sem("w_used"))


def split_weights_hi(act, x, wraw, whi, w_loaded, w_hi, w_used):
    load_wait(act, w_loaded[x % NRAW], x // NRAW + 1)
    if x >= NSPLIT:
        act.wait_ge(w_used, x - NSPLIT + 1)
    act.activation(whi[:, x % NSPLIT], wraw[:, x % NRAW], ACT.Copy).then_inc(w_hi, 1)


def split_weights_lo(pool, x, wraw, whi, wlo, w_hi, w_split):
    pool.wait_ge(w_hi, x + 1)
    pool.tensor_tensor(wlo[:, x % NSPLIT], wraw[:, x % NRAW], whi[:, x % NSPLIT], ALU.subtract).then_inc(w_split, 1)


def split_products(pe, out, whi, wlo, xhi, xlo, chunks):
    n = len(chunks)
    for i, (kw, kx) in enumerate(chunks):
        pe.matmul(out, whi[:, kw, :], xlo(kx), start=(i == 0), stop=False)
        pe.matmul(out, wlo[:, kw, :], xhi(kx), start=False, stop=False)
        mm = pe.matmul(out, whi[:, kw, :], xhi(kx), start=False, stop=(i == n - 1))
    return mm


def stage_split(nc, e):
    with ExitStack() as c:
        sem = stage_semaphores(nc, c, "split")
        h_loaded, hi_set, lo_set = sem("h_loaded"), sem("hi_set"), sem("lo_set")
        block = c.enter_context(nc.Block())
        pairs = ((e.oT, e.ohi, e.olo), (e.ossmT, e.shi, e.slo))

        @block.sync
        def _(sp):
            sp.dma_start(e.mixT[:, :, :], e.h_keep).then_inc(h_loaded, 16)
            load_wait(sp, h_loaded, 1)

        @block.scalar
        def _(act):
            for raw, hi, _ in pairs:
                for k in range(4):
                    act.activation(hi[:, k, :], raw[:, k, :], ACT.Copy).then_inc(hi_set, 1)

        @block.vector
        def _(dve):
            for i, (raw, hi, lo) in enumerate(pairs):
                for k in range(4):
                    dve.wait_ge(hi_set, 4 * i + k + 1)
                    dve.tensor_tensor(lo[:, k, :], raw[:, k, :], hi[:, k, :], ALU.subtract).then_inc(lo_set, 1)


def stage_merge(nc, e):
    with ExitStack() as c:
        sb = lambda n, s, d=F32: c.enter_context(nc.sbuf_tensor(n, s, d))
        sem = stage_semaphores(nc, c, "merge")
        hhi, hlo = sb("hhi", [P, KD, NT], F32R), sb("hlo", [P, KD, NT], F32R)
        wraw, whi, wlo, w_loaded, w_hi, w_split, w_used = weight_slots(sb, sem, "_merge")
        sig = sb("sig", [P, 2, 3, SL])
        prod = sb("prod", [P, 2, SL])
        h_hi, h_split = sem("h_hi"), sem("h_split")
        products, sigmoids, scaled, mixed = sem("products"), sem("sigmoids"), sem("scaled"), sem("mixed")
        block = c.enter_context(nc.Block())
        win = e.w_in[0].rearrange("(k p) n -> p k n", p=P)
        NLOAD = 3 * KD
        bank = e.bank
        sl = lambda s: slice(s * SL, (s + 1) * SL)

        @block.sync
        def _(sp):
            for x in range(NLOAD):
                f, j = x // 3, x % 3
                a = f * P
                if x >= NRAW:
                    sp.wait_ge(w_split, x - NRAW + 1)
                if j < 2:
                    sp.dma_start(wraw[:, x % NRAW], win[:, :, (GA0, GS0)[j] + a:(GA0, GS0)[j] + a + P]).then_inc(w_loaded[x % NRAW], 16)
                    continue
                for g in range(G):
                    sp.dma_start(wraw[g * HD:(g + 1) * HD, x % NRAW, 0:4],
                                 e.w_br_attn[0].rearrange("(g r d) n -> g d r n", g=G, d=HD)[g, :, :, a:a + P]).then_inc(w_loaded[x % NRAW], 16)
                sp.dma_start(wraw[:, x % NRAW, 4:8], e.w_br_ssm[0].rearrange("(k p) n -> p k n", p=P)[:, :, a:a + P])\
                  .then_inc(w_loaded[x % NRAW], 16)

        def dmas(x):
            return sum(3 if y % 3 == 2 else 1 for y in range(x % NRAW, x + 1, NRAW))

        @block.tensor
        def _(pe):
            for x in range(NLOAD):
                j = x % 3
                w, v = whi[:, x % NSPLIT], wlo[:, x % NSPLIT]
                pe.wait_ge(w_split, x + 1)
                for s in range(3):
                    if x == 0:
                        pe.wait_ge(h_split, s + 1)
                    if j < 2:
                        if x >= 3:
                            pe.wait_ge(sigmoids, 6 * (x // 3 - 1) + 3 * j + s + 1)
                        mm = split_products(pe, bank[3 * j + s][:, 0:SL], w, v, lambda k: hhi[:, k, sl(s)], lambda k: hlo[:, k, sl(s)],
                                            [(k, k) for k in range(KD)])
                    else:
                        for i, (hi, low) in enumerate(((e.ohi, e.olo), (e.shi, e.slo))):
                            n = 6 * (x // 3) + 2 * s + i
                            if n >= 2:
                                pe.wait_ge(scaled, n - 1)
                            mm = split_products(pe, bank[6 + i][:, 0:SL], w, v, lambda k: hi[:, k, sl(s)], lambda k: low[:, k, sl(s)],
                                                [(4 * i + k, k) for k in range(4)])
                            if i == 0:
                                mm.then_inc(products, 1)
                    mm.then_inc(products, 1)
                pe.wait_ge(products, 12 * (x // 3) + 3 * j + (3 if j < 2 else 6))
                pe.sem_inc(w_used, 1)

        @block.scalar
        def _(act):
            def weights_hi(x):
                act.wait_ge(w_loaded[x % NRAW], 16 * dmas(x))
                if x >= NSPLIT:
                    act.wait_ge(w_used, x - NSPLIT + 1)
                act.activation(whi[:, x % NSPLIT], wraw[:, x % NRAW], ACT.Copy).then_inc(w_hi, 1)

            weights_hi(0)
            for s in range(3):
                act.activation(hhi[:, :, sl(s)], e.mixT[:, :, sl(s)], ACT.Copy).then_inc(h_hi, 1)
            weights_hi(1)
            for x in range(NLOAD):
                f, j = x // 3, x % 3
                for s in range(3 if j < 2 else 0):
                    act.wait_ge(products, 12 * f + 3 * j + s + 1)
                    if f:
                        act.wait_ge(scaled, 6 * (f - 1) + 2 * s + j + 1)
                    act.activation(sig[:, j, s, :], bank[3 * j + s][:, 0:SL], ACT.Sigmoid).then_inc(sigmoids, 1)
                if x + 2 < NLOAD:
                    weights_hi(x + 2)

        @block.gpsimd
        def _(pool):
            for x in range(NLOAD):
                split_weights_lo(pool, x, wraw, whi, wlo, w_hi, w_split)

        @block.vector
        def _(dve):
            for s in range(3):
                dve.wait_ge(h_hi, s + 1)
                dve.tensor_tensor(hlo[:, :, sl(s)], e.mixT[:, :, sl(s)], hhi[:, :, sl(s)], ALU.subtract).then_inc(h_split, 1)
            dve.wait_ge(h_split, 3)
            for f in range(KD):
                for s in range(3):
                    u = 3 * f + s
                    if u >= 1:
                        dve.wait_ge(mixed, u)
                    for i in range(2):
                        dve.wait_ge(products, 12 * f + 6 + 2 * s + i + 1)
                        if i == 0:
                            dve.wait_ge(sigmoids, 6 * (f + 1))
                        dve.tensor_tensor(prod[:, i, :], sig[:, i, s, :], bank[6 + i][:, 0:SL], ALU.mult).then_inc(scaled, 1)
                    dve.wait_ge(scaled, 2 * u + 2)
                    dve.tensor_tensor(e.mixT[:, f, sl(s)], prod[:, 0, :], prod[:, 1, :], ALU.add).then_inc(mixed, 1)


def add_gated(dve, e, chain, wait_done, psum, tmp, f, s, gate):
    m = min(SL, T - s * SL)
    a = s * SL
    gx = e.mod[:, gate * KD + f, :]
    ins = dve.scalar_tensor_tensor(out=e.xT[:, f, a:a + m], in0=psum[:, 0:m], scalar=gx[:, 0:1], in1=e.xT[:, f, a:a + m],
                                   op0=ALU.mult, op1=ALU.add)
    if m < SL:
        v = lambda x: x.rearrange("p (n t) -> p n t", t=TS)
        ins.then_inc(chain, 1)
        dve.tensor_tensor(v(tmp), v(psum[:, m:SL]), gx[:, 1:1 + NSEQ].unsqueeze(2).to_broadcast([P, NSEQ, TS]), ALU.mult).then_inc(chain, 1)
        dve.wait_ge(chain, wait_done)
        ins = dve.tensor_tensor(e.xT[:, f, a + m:a + SL], e.xT[:, f, a + m:a + SL], tmp, ALU.add)
    return ins


def stage_out(nc, e):
    with ExitStack() as c:
        sb = lambda n, s, d=F32: c.enter_context(nc.sbuf_tensor(n, s, d))
        sem = stage_semaphores(nc, c, "out")
        mhi, mlo = sb("mhi", [P, KD, NT], F32R), sb("mlo", [P, KD, NT], F32R)
        wraw, whi, wlo, w_loaded, w_hi, w_split, w_used = weight_slots(sb, sem, "_out")
        tmp = sb("tmp", [P, NS])
        x_loaded, m_hi, m_split, products, added, chain = (sem(n) for n in ("x_loaded", "m_hi", "m_split", "products", "added", "chain"))
        block = c.enter_context(nc.Block())
        bank = e.bank
        sl = lambda s: slice(s * SL, (s + 1) * SL)

        @block.sync
        def _(sp):
            for x in range(KD):
                if x >= NRAW:
                    sp.wait_ge(w_split, x - NRAW + 1)
                sp.dma_start(wraw[:, x % NRAW], e.w_out[0].rearrange("(k p) n -> p k n", p=P)[:, :, x * P:(x + 1) * P])\
                  .then_inc(w_loaded[x % NRAW], 16)
                if x == 0:
                    sp.dma_start(e.xT[:, :, :], e.x_keep).then_inc(x_loaded, 16)

        @block.tensor
        def _(pe):
            for f in range(KD):
                pe.wait_ge(w_split, f + 1)
                for s in range(3):
                    u = 3 * f + s
                    if f == 0:
                        pe.wait_ge(m_split, s + 1)
                    if u >= 8:
                        pe.wait_ge(added, u - 7)
                    split_products(pe, bank[u % 8][:, 0:SL], whi[:, f % NSPLIT], wlo[:, f % NSPLIT], lambda k: mhi[:, k, sl(s)],
                                   lambda k: mlo[:, k, sl(s)], [(k, k) for k in range(KD)]).then_inc(products, 1)
                pe.wait_ge(products, 3 * f + 3)
                pe.sem_inc(w_used, 1)

        @block.scalar
        def _(act):
            for s in range(3):
                act.activation(mhi[:, :, sl(s)], e.mixT[:, :, sl(s)], ACT.Copy).then_inc(m_hi, 1)
                if s == 0:
                    split_weights_hi(act, 0, wraw, whi, w_loaded, w_hi, w_used)
            for x in range(1, KD):
                split_weights_hi(act, x, wraw, whi, w_loaded, w_hi, w_used)

        @block.gpsimd
        def _(pool):
            for x in range(KD):
                split_weights_lo(pool, x, wraw, whi, wlo, w_hi, w_split)

        @block.vector
        def _(dve):
            for s in range(3):
                dve.wait_ge(m_hi, s + 1)
                dve.tensor_tensor(mlo[:, :, sl(s)], e.mixT[:, :, sl(s)], mhi[:, :, sl(s)], ALU.subtract).then_inc(m_split, 1)
            load_wait(dve, x_loaded, 1)
            for u in range(3 * KD):
                f, s = u // 3, u % 3
                dve.wait_ge(products, u + 1)
                if s == 2 and f:
                    dve.wait_ge(added, u)
                add_gated(dve, e, chain, 2 * (f + 1), bank[u % 8], tmp[:, :], f, s, 2).then_inc(added, 1)


def stage_mlp(nc, e):
    FH = WK
    NQ = F // P // FH
    with ExitStack() as c:
        sb = lambda n, s, d=F32: c.enter_context(nc.sbuf_tensor(n, s, d))
        sem = stage_semaphores(nc, c, "mlp")
        ahi, alo = sb("ahi", [P, FH, NT], F32R), sb("alo", [P, FH, NT], F32R)
        wraw, whi, wlo, w_loaded, w_hi, w_split, w_used = weight_slots(sb, sem, "_mlp")
        sq = sb("sqr", [P, 3, SL])
        tmp = sb("tmp2", [P, NS])
        ups, relus, squares, a_hi, a_split, downs, added, chain = (sem(n) for n in ("ups", "relus", "squares", "a_hi", "a_split", "downs", "added", "chain"))
        block = c.enter_context(nc.Block())
        bank = e.bank
        w1 = e.w_ff1[0].rearrange("(k p) n -> p k n", p=P)
        w2 = e.w_ff2[0].rearrange("(k p) n -> p k n", p=P)
        NU1, NU2 = 3 * FH, 3 * KD
        sl = lambda s: slice(s * SL, (s + 1) * SL)
        loads = NQ * (FH + KD)

        @block.sync
        def _(sp):
            for x in range(loads):
                q, l = divmod(x, FH + KD)
                if x >= NRAW:
                    sp.wait_ge(w_split, x - NRAW + 1)
                a = (q * FH + l) * P
                src = w1[:, :, a:a + P] if l < FH else w2[:, q * FH:(q + 1) * FH, (l - FH) * P:(l - FH + 1) * P]
                sp.dma_start(wraw[:, x % NRAW], src).then_inc(w_loaded[x % NRAW], 16)

        @block.tensor
        def _(pe):
            for x in range(loads):
                q, l = divmod(x, FH + KD)
                w, v = whi[:, x % NSPLIT], wlo[:, x % NSPLIT]
                pe.wait_ge(w_split, x + 1)
                for s in range(3):
                    if l < FH:
                        u = q * NU1 + 3 * l + s
                        if u >= 4:
                            pe.wait_ge(relus, u - 3)
                        split_products(pe, bank[u % 4][:, 0:SL], w, v, lambda k: e.hhi[:, k, sl(s)], lambda k: e.hlo[:, k, sl(s)],
                                       [(k, k) for k in range(KD)]).then_inc(ups, 1)
                    else:
                        u = q * NU2 + 3 * (l - FH) + s
                        if l == FH:
                            pe.wait_ge(a_split, (q + 1) * NU1 - 2 + s)
                        if u >= 4:
                            pe.wait_ge(added, u - 3)
                        split_products(pe, bank[4 + u % 4][:, 0:SL], w, v, lambda k: ahi[:, k, sl(s)], lambda k: alo[:, k, sl(s)],
                                       [(k, k) for k in range(FH)]).then_inc(downs, 1)
                if l < FH:
                    pe.wait_ge(ups, q * NU1 + 3 * l + 3)
                else:
                    pe.wait_ge(downs, q * NU2 + 3 * (l - FH) + 3)
                pe.sem_inc(w_used, 1)

        @block.scalar
        def _(act):
            def hi(u):
                act.wait_ge(squares, u + 1)
                if u % NU1 == 0 and u:
                    act.wait_ge(downs, u // NU1 * NU2)
                act.activation(ahi[:, u % NU1 // 3, sl(u % 3)], sq[:, u % 3, :], ACT.Copy).then_inc(a_hi, 1)

            for x in range(NSPLIT):
                split_weights_hi(act, x, wraw, whi, w_loaded, w_hi, w_used)
            for x in range(loads):
                q, l = divmod(x, FH + KD)
                for s in range(3 if l < FH else 0):
                    u = q * NU1 + 3 * l + s
                    act.wait_ge(ups, u + 1)
                    if u >= 3:
                        act.wait_ge(a_split, u - 2)
                    act.activation(sq[:, u % 3, :], bank[u % 4][:, 0:SL], ACT.Relu).then_inc(relus, 1)
                    if u % NU1:
                        hi(u - 1)
                if l == FH - 1:
                    hi((q + 1) * NU1 - 1)
                if x + NSPLIT < loads:
                    split_weights_hi(act, x + NSPLIT, wraw, whi, w_loaded, w_hi, w_used)

        @block.gpsimd
        def _(pool):
            for x in range(loads):
                split_weights_lo(pool, x, wraw, whi, wlo, w_hi, w_split)

        @block.vector
        def _(dve):
            def low(u):
                l, s = u % NU1 // 3, u % 3
                dve.wait_ge(a_hi, u + 1)
                dve.tensor_tensor(alo[:, l, sl(s)], sq[:, u % 3, :], ahi[:, l, sl(s)], ALU.subtract).then_inc(a_split, 1)

            for q in range(NQ):
                for v in range(NU1):
                    u = q * NU1 + v
                    dve.wait_ge(relus, u + 1)
                    r = sq[:, u % 3, :]
                    dve.tensor_tensor(r, r, r, ALU.mult).then_inc(squares, 1)
                    if v:
                        low(u - 1)
                low(q * NU1 + NU1 - 1)
                for v in range(NU2):
                    f, s = v // 3, v % 3
                    u = q * NU2 + v
                    dve.wait_ge(downs, u + 1)
                    if s == 2 and u > 2:
                        dve.wait_ge(added, u)
                    add_gated(dve, e, chain, 2 * (q * KD + f + 1), bank[4 + u % 4], tmp[:, :], f, s, 5).then_inc(added, 1)


def stage_store(nc, e):
    with ExitStack() as c:
        sb = lambda n, s, d=F32: c.enter_context(nc.sbuf_tensor(n, s, d))
        sem = stage_semaphores(nc, c, "store")
        yrow = sb("yrow", [P, 3, D])
        s_t, s_tc = sem("s_t"), sem("s_tc")
        block = c.enter_context(nc.Block())
        rows = lambda tb: P if tb < TB else NS
        bank = e.bank

        @block.tensor
        def _(pe):
            for tb in range(TB + 1):
                n = rows(tb)
                for h in range(2):
                    u = 2 * tb + h
                    if u >= 4:
                        pe.wait_ge(s_tc, u - 3)
                    for k in range(4):
                        mm = pe.transpose(bank[u % 4][0:n, k * P:(k + 1) * P], e.hT[:, 4 * h + k, tb * P:tb * P + n], e.ident)
                    mm.then_inc(s_t, 1)

        @block.scalar
        def _(act):
            for u in range(2 * (TB + 1)):
                tb, h = u // 2, u % 2
                n = rows(tb)
                act.wait_ge(s_t, u + 1)
                if h == 0 and tb >= 3:
                    load_wait(act, e.y_stored[tb % 3], tb // 3)
                act.activation(yrow[0:n, tb % 3, h * 512:(h + 1) * 512], bank[u % 4][0:n, :], ACT.Copy).then_inc(s_tc, 1)

        @block.sync
        def _(sp):
            for tb in range(TB + 1):
                n = rows(tb)
                sp.wait_ge(s_tc, 2 * tb + 2)
                dst = e.y_prompt[0, tb * P:(tb + 1) * P, :] if tb < TB else e.y_sample.rearrange("n t d -> (n t) d")
                sp.dma_start(dst, yrow[0:n, tb % 3, :]).then_inc(e.y_stored[tb % 3], 16)
            for i in range(3):
                load_wait(sp, e.y_stored[i], 3)


def stages(nc, e):
    kept, mix, parts, late, last = (ExitStack() for _ in range(5))
    e.ossmT = kept.enter_context(nc.sbuf_tensor("ossmT", [P, SSM // P, NT], F32, side="right"))
    with nc.sbuf_tensor("hT", [P, KD, NT], F32, side="right") as hT:
        e.hT = hT
        with nc.sbuf_tensor("xT", [P, KD, NT], F32, side="right") as xT:
            e.xT = xT
            stage_inputs(nc, e)
            stage_norm(nc, e, "_mix", e.xT, e.hT, 0, shift=0, scale=1)
            stage_keep(nc, e)
        stage_ssm(nc, e)
        outer = ExitStack()
        attn = ExitStack()
        sb = lambda n, s, d=F32: attn.enter_context(nc.sbuf_tensor(n, s, d))
        e.qT = sb("qT", [P, R, NT])
        e.kT = sb("kT", [P, 2, NT])
        e.vslc = sb("vslc", [P, TB, 3 * HD])
        e.vwin = sb("vwin", [P, TB, 3 * HD])
        e.vnew = sb("vnew", [NS, 2, KVW])
        e.gates = sb("gates", [3 * HQ, NT])
        stage_project(nc, e)
    with outer:
        with attn:
            e.bt = sb("bt", [P, HQ, 2 * P])
            e.bc = sb("bc", [P, HQ, 16])
            e.btail = sb("btail", [P, P])
            e.bcd = sb("bcd", [P, 8])
            e.bnew = sb("bnew", [P, 2, NS])
            e.qbd = sb("qbd", [P, NSEQ, 32])
            e.rowidx = sb("rowidx", [P, NSEQ * 2], U32)
            e.kcp = sb("kcp", [P, T // CHK])
            e.vcp = sb("vcp", [T // CHK, 3 * HD])
            e.kcT = sb("kcT", [P, NSEQ, 256])
            e.vc = sb("vc", [P, NSEQ, 2, KVW])
            with ExitStack() as c:
                sb2 = lambda n, s, d=F32: c.enter_context(nc.sbuf_tensor(n, s, d))
                e.w1T = sb2("w1T", [P, 2, 8, 2, HD])
                e.w2 = sb2("w2c", [HD, 2, HD])
                e.cbias = sb2("cbias", [HD, 2])
                stage_tables(nc, e)
                stage_compress(nc, e)
            e.oT = outer.enter_context(nc.sbuf_tensor("oT", [P, R, NT], F32, side="right"))
            stage_prompt(nc, e)
            stage_decode(nc, e)
        e.mixT = mix.enter_context(nc.sbuf_tensor("mixT", [P, KD, NT], F32))
        e.ohi, e.olo, e.shi, e.slo = (parts.enter_context(nc.sbuf_tensor(n, [P, 4, NT], F32R)) for n in ("ohi", "olo", "shi", "slo"))
        stage_split(nc, e)
    kept.close()
    with parts:
        stage_merge(nc, e)
    late.enter_context(mix)
    with late:
        e.xT = last.enter_context(nc.sbuf_tensor("xT_late", [P, KD, NT], F32, side="right"))
        stage_out(nc, e)
    with last:
        with nc.sbuf_tensor("hhi_mlp", [P, KD, NT], F32R) as e.hhi, nc.sbuf_tensor("hlo_mlp", [P, KD, NT], F32R) as e.hlo:
            stage_norm_split(nc, e, "_mlp", e.xT, 1, shift=3, scale=4)
            stage_mlp(nc, e)
        with nc.sbuf_tensor("yT", [P, KD, NT], F32) as yT:
            e.hT = yT
            stage_norm(nc, e, "_fin", e.xT, e.hT, 2)
            stage_store(nc, e)


def stage_keep(nc, e):
    with nc.semaphore("s_keep") as s, nc.Block() as block:
        @block.sync
        def _(sp):
            sp.dma_start(e.x_keep, e.xT[:, :, :]).then_inc(s, 16)
            sp.dma_start(e.h_keep, e.hT[:, :, :]).then_inc(s, 16)
            sp.wait_ge(s, 32)


def build(nc, ins, outs):
    e = Env()
    (e.x_prompt, e.x_sample, e.cache_k_cmp, e.cache_v_cmp, e.cache_k_slc, e.cache_v_slc, e.cache_k_win, e.cache_v_win,
     e.state_re, e.state_im, e.page_table, e.c_prompt, e.c_sample, e.rel_bias, e.w_ada, e.b_ada, g_mix, g_mlp, e.w_in,
     e.cmp_pe, e.cmp_w1, e.cmp_b1, e.cmp_w2, e.lam_re, e.lam_im, e.log_dt, e.b_re, e.b_im, e.c_re, e.c_im, e.ssm_d,
     e.w_glu, e.w_br_attn, e.w_br_ssm, e.w_out, e.w_ff1, e.w_ff2, g_final, e.consts_in, e.onehot_in) = ins
    (e.y_prompt, e.y_sample, e.p_k_cmp, e.p_v_cmp, e.p_k_slc, e.p_v_slc, e.p_k_win, e.p_v_win, e.p_re, e.p_im,
     e.s_k_cmp, e.s_v_cmp, e.s_k_slc, e.s_v_slc, e.s_k_win, e.s_v_win, e.s_re, e.s_im) = outs
    e.g_norm_mix = g_mix.rearrange("a (k p) -> (a k) p", p=P)
    e.g_norm_mlp = g_mlp.rearrange("a (k p) -> (a k) p", p=P)
    e.g_final = g_final.rearrange("(k p) -> k p", p=P)

    with ExitStack() as c:
        sb = lambda n, s, d=F32: c.enter_context(nc.sbuf_tensor(n, s, d))
        e.ps = c.enter_context(nc.psum_tensor("ps", [P, 8 * 512], F32))
        e.bank = [e.ps[:, 512 * i:512 * (i + 1)] for i in range(8)]
        sem = lambda n: c.enter_context(nc.semaphore(n))
        e.states_stored, e.caches_stored = sem("states_stored"), sem("caches_stored")
        e.y_stored = [sem(f"y_stored{i}") for i in range(3)]
        e.consts = sb("consts", [P, NCONST])
        e.ident = e.consts[:, C_IDENT:C_IDENT + P]
        e.ones = e.consts[:, C_ONES:C_ONES + P]
        e.eps = e.consts[:, C_EPS:C_EPS + 1]
        e.winmask = e.consts[:, C_WINM:C_WINM + P]
        e.sumr = e.consts[:, C_SUMR:C_SUMR + P]
        e.winhead = e.consts[:, C_WINH:C_WINH + TS]
        e.cmprow = e.consts[:, C_CROW:C_CROW + 1]
        e.mod = sb("mod", [P, 6 * KD, 1 + NSEQ])
        e.vec = sb("vec", [P, 3 * KD])
        e.h_keep = nc.dram_tensor("h_keep", (P, KD, NT), F32, kind="Internal").ap()
        e.x_keep = nc.dram_tensor("x_keep", (P, KD, NT), F32, kind="Internal").ap()
        stages(nc, e)


def plan_consts():
    parts, at = {}, 0
    def put(name, a):
        nonlocal at
        full = np.zeros((P, a.shape[1]), np.float32)
        full[0:a.shape[0]] = a
        parts[name] = (at, full)
        at += a.shape[1]
    put("ident", np.eye(P, dtype=np.float32))
    put("ones", np.ones((P, P), np.float32))
    put("eps", np.full((P, 1), EPS, np.float32))
    k = np.arange(P)
    put("winmask", np.where(k[None, :] >= k[:, None], 0.0, NEG).astype(np.float32))
    put("cmprow", (k[:, None] >= CHK * 2 - 1).astype(np.float32))
    i, t = np.arange(P)[:, None], np.arange(P)[None, :]
    same = (i // 32 == t // 32) & ((i // 16) % 2 == (t // 16) % 2) & (i % 4 == t % 4)
    put("sumr", same.astype(np.float32))
    put("winhead", np.where(np.arange(TS)[None, :] < (k % TS)[:, None], NEG, 0.0).astype(np.float32))
    put("pow", np.tile(np.concatenate([np.arange(LC + 1), np.arange(LC)[::-1]]).astype(np.float32)[None, :], (P, 1)))
    put("sub", (k % 8).astype(np.float32)[:, None])
    return parts, at


_PARTS, NCONST = plan_consts()
C_IDENT, C_ONES, C_EPS, C_WINM, C_CROW, C_SUMR, C_WINH, C_POW, C_SUB = (
    _PARTS[n][0] for n in ("ident", "ones", "eps", "winmask", "cmprow", "sumr", "winhead", "pow", "sub"))
BW = 383


def one_hot():
    n = 255 - np.arange(BW)
    exact = NB // 2
    nf = np.maximum(n, exact).astype(np.float32)
    large = exact + (np.log(nf / exact) / np.float32(np.log(128 / exact)) * (NB - exact)).astype(np.int32)
    b = np.where(n < exact, np.maximum(n, 0), np.minimum(large, NB - 1))
    out = np.zeros((NB + 1, BW), np.float32)
    out[b, np.arange(BW)] += 1
    out[NB - 1, :] -= 1
    out[NB, :] = n < 0
    return np.concatenate([out, out[:, ::-1]], axis=1)


_INS = ['x_prompt', 'x_sample', 'cache_k_cmp', 'cache_v_cmp', 'cache_k_slc', 'cache_v_slc', 'cache_k_win', 'cache_v_win',
        'state_ssm_re', 'state_ssm_im', 'page_table', 'c_prompt', 'c_sample', 'rel_bias', 'w_ada', 'b_ada', 'g_norm_mix',
        'g_norm_mlp', 'w_in', 'cmp_pe', 'cmp_w1', 'cmp_b1', 'cmp_w2', 'ssm_lambda_re', 'ssm_lambda_im', 'ssm_log_dt',
        'ssm_b_re', 'ssm_b_im', 'ssm_c_re', 'ssm_c_im', 'ssm_d', 'w_glu', 'w_br_attn', 'w_br_ssm', 'w_out', 'w_ff1',
        'w_ff2', 'g_final']
_OUTS = [(1, T, D), (NSEQ, TS, D)] + [(1, 1, T, G, HD)] * 4 + [(1, 1, WIN, G, HD)] * 2 + [(1, 1, SG, SP)] * 2 \
    + [(1, NSEQ, TS, G, HD)] * 4 + [(1, NSEQ, WIN, G, HD)] * 2 + [(1, NSEQ, SG, SP)] * 2


def kernel(**inputs):
    import concourse.bacc as _bacc
    from concourse.bass_utils import run_bass_kernel_spmd as _run

    nc = _bacc.Bacc("TRN2", target_bir_lowering=False, num_devices=1)
    arrays, args = {}, []
    for name in _INS:
        arrays[f"in_{name}"] = np.ascontiguousarray(inputs[name])
    arrays["in_consts"] = np.concatenate([a for _, a in _PARTS.values()], axis=1)
    arrays["in_onehot"] = one_hot()
    for name, a in arrays.items():
        args.append(nc.dram_tensor(name, a.shape, mybir.dt.from_np(a.dtype), kind="ExternalInput").ap())
    outs = [nc.dram_tensor(f"out_{i}", s, F32, kind="ExternalOutput").ap() for i, s in enumerate(_OUTS)]
    build(nc, args, outs)
    r = _run(nc, [arrays], core_ids=[0])
    return tuple(r.results[0][f"out_{i}"] for i in range(len(_OUTS)))
```

```python
from contextlib import ExitStack

import numpy as np

import concourse.bass as bass
from concourse import mybir

ALU = mybir.AluOpType
ACT = mybir.ActivationFunctionType
F32 = mybir.dt.float32
F32R = mybir.dt.float32r
I32 = mybir.dt.int32
U32 = mybir.dt.uint32
AXX = mybir.AxisListType.X

P = 128
D = 1024
KD = D // P
T = 1024
TB = T // P
NSEQ, TS = 8, 4
NS = NSEQ * TS
NT = T + NS
SL = NT // 3
HQ, G, R, HD = 8, 2, 4, 64
KVW = G * HD
PAST, PAGE = 4096, 128
NPAGE = PAST // PAGE
NPHYS = 5 * NSEQ * NPAGE // 4
CHK = 16
WIN = 512
F = 4 * D
SSM = D // 2
SG, SI, SP = 32, 16, 64
LC = 8
NCH = T // LC
NB = 32
EPS = 1e-6
NEG = -1e30
BIG = 1e30
Q0 = 0
KV0 = HQ * HD
GN0 = KV0 + 6 * KVW
U0 = GN0 + 3 * HQ
GA0 = U0 + SSM
GS0 = GA0 + D
INW = GS0 + D
TWO_PI = 2.0 * np.pi


class Env:
    pass


def load_wait(eng, sem, n):
    eng.wait_ge(sem, 16 * n)


def stage_semaphores(nc, c, stage):
    taken = []

    def give_back():
        nc.clear_and_free_semaphores(taken)
        nc.all_engine_barrier()

    def sem(name):
        taken.append(nc.alloc_semaphore(name=f"{name}_{stage}"))
        return taken[-1]

    c.callback(give_back)
    return sem


NC9 = 1 + NSEQ
ADA_EARLY = 2 * KD


def ada_products(pe, out, w, scT):
    for k in range(KD):
        g = 32 * (k % 4)
        mm = pe.matmul(out[g:g + 32, :], scT[:, k, :], w[:, k, :], start=(k < 4), stop=(k >= 4), skip_group_check=True)
    return mm


def ada_sums(pe, out, partial, e):
    return pe.matmul(out, partial, e.condsum, start=True, stop=True)


def stage_inputs(nc, e):
    NBLK = ADA_EARLY // 4
    with ExitStack() as c:
        sb = lambda n, s, d=F32: c.enter_context(nc.sbuf_tensor(n, s, d))
        sem = stage_semaphores(nc, c, "in")
        xrow = sb("xrow", [P, TB + 1, D])
        crow = sb("crow", [NC9, D])
        srow = sb("srow", [NC9, D])
        vrow = sb("vrow", [3 * KD, P])
        brow = sb("brow", [6 * KD, P])
        wada = sb("wada", [P, 2, KD, 512])
        modrow = sb("modrow", [P, 2, 512])
        const_loaded, cond_loaded, vec_loaded, bias_loaded = sem("const_loaded"), sem("cond_loaded"), sem("vec_loaded"), sem("bias_loaded")
        x_loaded = [sem(f"x_loaded{i}") for i in range(TB + 1)]
        w_loaded = [sem(f"w_loaded{i}") for i in range(2)]
        silu_done, cond_turned, cond_zero, cond_kept, vec_turned, vec_kept, x_turned, x_kept, partial_done, partial_kept, mod_done, mod_kept = (
            sem(n) for n in ("silu_done", "cond_turned", "cond_zero", "cond_kept", "vec_turned", "vec_kept", "x_turned", "x_kept0",
                             "partial_done", "partial_kept", "mod_done", "mod_kept"))
        x_kept = [x_kept, sem("x_kept1")]
        block = c.enter_context(nc.Block())
        wview = e.w_ada[0].rearrange("(k p) n -> p k n", p=P)

        def tokens(tb):
            return P if tb < TB else NS

        def copy_x(eng, tb):
            n = tokens(tb)
            for h in range(2):
                eng.wait_ge(x_turned, 2 * tb + h + 1)
                dst = e.xT[:, 4 * h:4 * h + 4, tb * P:tb * P + n]
                src = e.bank[2 * (tb % 2) + h][:, :].rearrange("p (k n) -> p k n", k=4)[:, :, 0:n]
                ins = eng.activation(dst, src, ACT.Copy) if tb % 2 else eng.tensor_copy(dst, src)
                ins.then_inc(x_kept[tb % 2], 1)

        @block.sync
        def _(sp):
            for tb in range(TB + 1):
                n = tokens(tb)
                src = e.x_prompt[0, tb * P:(tb + 1) * P, :] if tb < TB else e.x_sample.rearrange("n t d -> (n t) d")
                sp.dma_start(xrow[0:n, tb, :], src).then_inc(x_loaded[tb], 16)
            for i in range(NBLK):
                if i >= 2:
                    sp.wait_ge(partial_done, i - 1)
                sp.dma_start(wada[:, i % 2], wview[:, :, i * 512:(i + 1) * 512]).then_inc(w_loaded[i % 2], 16)
            sp.dma_start(e.wu[:, :, :], e.w_in[0].rearrange("(k p) n -> p k n", p=P)[:, :, U0:U0 + SSM]).then_inc(e.wu_loaded, 16)

        @block.scalar
        def _(act):
            act.dma_start(crow[0:1, :], e.c_prompt).then_inc(cond_loaded, 16)
            act.dma_start(crow[1:NC9, :], e.c_sample).then_inc(cond_loaded, 16)
            act.dma_start(e.consts[:, :], e.consts_in).then_inc(const_loaded, 16)
            act.dma_start(brow[:, :], e.b_ada.rearrange("a (k p) -> (a k) p", p=P)).then_inc(bias_loaded, 16)
            for i, g in enumerate((e.g_norm_mix, e.g_norm_mlp, e.g_final)):
                act.dma_start(vrow[i * KD:(i + 1) * KD, :], g).then_inc(vec_loaded, 16)
            load_wait(act, cond_loaded, 2)
            act.activation(srow[:, :], crow[:, :], ACT.Silu).then_inc(silu_done, 1)
            for tb in range(1, TB + 1, 2):
                copy_x(act, tb)

        @block.tensor
        def _(pe):
            load_wait(pe, const_loaded, 1)
            pe.wait_ge(silu_done, 1)
            for k in range(KD):
                mm = pe.transpose(e.bank[4][:, k * NC9:(k + 1) * NC9], srow[:, k * P:(k + 1) * P], e.ident[0:NC9, 0:NC9])
            mm.then_inc(cond_turned, 1)
            load_wait(pe, vec_loaded, 3)
            load_wait(pe, bias_loaded, 1)
            pe.transpose(e.bank[5][:, 0:3 * KD], vrow[:, :], e.ident[0:3 * KD, 0:3 * KD])
            pe.transpose(e.bank[5][:, 3 * KD:9 * KD], brow[:, :], e.ident[0:6 * KD, 0:6 * KD]).then_inc(vec_turned, 1)
            for tb in range(TB + 1):
                n = tokens(tb)
                load_wait(pe, x_loaded[tb], 1)
                for h in range(2):
                    if tb >= 2:
                        pe.wait_ge(x_kept[tb % 2], 2 * (tb // 2 - 1) + h + 1)
                    for k in range(4):
                        kk = 4 * h + k
                        mm = pe.transpose(e.bank[2 * (tb % 2) + h][:, k * P:k * P + n], xrow[0:n, tb, kk * P:(kk + 1) * P],
                                          e.ident[0:n, 0:n])
                    mm.then_inc(x_turned, 1)
            pe.wait_ge(cond_kept, 1)
            pe.wait_ge(vec_kept, 1)

            def sums(i):
                pe.wait_ge(partial_kept, i + 1)
                for q in range(4):
                    f = 4 * i + q
                    mm = ada_sums(pe, e.bank[6][:, f * NC9:(f + 1) * NC9], modrow[:, i % 2, q * P:(q + 1) * P], e)
                mm.then_inc(mod_done, 1)

            for i in range(NBLK):
                load_wait(pe, w_loaded[i % 2], i // 2 + 1)
                if i >= 2:
                    pe.wait_ge(partial_kept, i - 1)
                ada_products(pe, e.bank[4 + i % 2], wada[:, i % 2], e.scT).then_inc(partial_done, 1)
                if i:
                    sums(i - 1)
            sums(NBLK - 1)

        @block.vector
        def _(dve):
            dve.memset(e.scT[:, :, :], 0.0).then_inc(cond_zero, 1)
            dve.wait_ge(cond_zero, 1)
            dve.wait_ge(cond_turned, 1)
            dve.tensor_copy(e.scT[:, :, 0:NC9], e.bank[4][:, 0:KD * NC9].rearrange("p (k n) -> p k n", k=KD)).then_inc(cond_kept, 1)
            dve.wait_ge(vec_turned, 1)
            dve.tensor_copy(e.vec[:, :], e.bank[5][:, 0:9 * KD]).then_inc(vec_kept, 1)
            for tb in range(0, TB + 1, 2):
                copy_x(dve, tb)
            for i in range(NBLK):
                dve.wait_ge(partial_done, i + 1)
                if i >= 2:
                    dve.wait_ge(mod_done, i - 1)
                dve.tensor_copy(modrow[:, i % 2, :], e.bank[4 + i % 2]).then_inc(partial_kept, 1)
            dve.wait_ge(vec_kept, 1)
            dve.wait_ge(mod_done, NBLK)
            dve.tensor_tensor(e.mod[:, 0:ADA_EARLY, :], e.bank[6][:, 0:ADA_EARLY * NC9].rearrange("p (f n) -> p f n", n=NC9),
                              e.vec[:, 3 * KD:3 * KD + ADA_EARLY].unsqueeze(2).to_broadcast([P, ADA_EARLY, NC9]), ALU.add).then_inc(mod_kept, 1)


def stage_norm(nc, e, tag, src, gain, shift=None, scale=None, dst=None, keep=None, store=False):
    with ExitStack() as c:
        sb = lambda n, s, d=F32: c.enter_context(nc.sbuf_tensor(n + tag, s, d))
        sem = stage_semaphores(nc, c, "norm" + tag)
        sq = sb("sq", [P, 4, SL])
        rstd = sb("rstd", [P, 3, SL])
        amp = sb("amp", [P, KD, NC9])
        hn = sb("hn", [P, 4, SL])
        squared, summed, root, amp_set, rstd_set, scaled, moved, hi_set, lo_set, src_kept = (sem(n) for n in (
            "squared", "summed", "root", "amp_set", "rstd_set", "scaled", "moved", "hi_set", "lo_set", "src_kept"))
        block = c.enter_context(nc.Block())
        NU = 3 * KD
        sl = lambda s: slice(s * SL, (s + 1) * SL)
        M = T - 2 * SL
        freed = moved if dst is not None else lo_set

        rows = lambda tb: P if tb < TB else NS
        if store:
            yrow = sb("yrow", [P, 3, D])
            y_turned, y_kept = sem("y_turned"), sem("y_kept")

            @block.sync
            def _(sp):
                for tb in range(TB + 1):
                    sp.wait_ge(y_kept, 2 * tb + 2)
                    out = e.y_prompt[0, tb * P:(tb + 1) * P, :] if tb < TB else e.y_sample.rearrange("n t d -> (n t) d")
                    sp.dma_start(out, yrow[0:rows(tb), tb % 3, :]).then_inc(e.y_stored[tb % 3], 16)
                for i in range(3):
                    load_wait(sp, e.y_stored[i], 3)

        if keep is not None:
            @block.sync
            def _(sp):
                sp.dma_start(keep, src[:, :, :]).then_inc(src_kept, 16)
                load_wait(sp, src_kept, 1)

        @block.scalar
        def _(act):
            def modulate(i):
                s, k = i // KD, i % KD
                act.wait_ge(scaled, i + 1)
                h = hn[:, i % 4, :]
                out = h if dst is None else dst[:, k, sl(s)]
                if scale is None:
                    act.activation(out, h, ACT.Copy, scale=e.vec[:, gain * KD + k:gain * KD + k + 1]).then_inc(moved, 1)
                    return
                m = SL if s < 2 else M
                ins = act.activation(out[:, 0:m], h[:, 0:m], ACT.Identity, bias=e.mod[:, shift * KD + k, 0:1], scale=amp[:, k, 0:1])
                if s == 2 and dst is not None:
                    ins = act.activation(out[:, m:SL], h[:, m:SL], ACT.Copy)
                ins.then_inc(moved, 1)

            def squares(s):
                for k in range(KD):
                    i = s * KD + k
                    if i >= 4:
                        act.wait_ge(summed, i - 3)
                    act.activation(sq[:, i % 4, :], src[:, k, sl(s)], ACT.Square).then_inc(squared, 1)

            def roots(s):
                act.wait_ge(summed, KD * (s + 1))
                act.activation(rstd[:, s, :], e.bank[s][:, 0:SL], ACT.Sqrt, bias=e.eps, scale=1.0 / D).then_inc(root, 1)

            squares(0)
            squares(1)
            roots(0)
            squares(2)
            roots(1)
            for i in range(NU):
                if i == KD // 2:
                    roots(2)
                modulate(i)

        @block.tensor
        def _(pe):
            for i in range(NU):
                s, k = i // KD, i % KD
                pe.wait_ge(squared, i + 1)
                pe.matmul(e.bank[s][:, 0:SL], e.ones[:, :], sq[:, i % 4, :], start=(k == 0), stop=(k == KD - 1)).then_inc(summed, 1)
            for u in range(2 * (TB + 1) if store else 0):
                tb, h = u // 2, u % 2
                n = rows(tb)
                pe.wait_ge(moved, KD * ((tb * P + n - 1) // SL + 1))
                if u >= 4:
                    pe.wait_ge(y_kept, u - 3)
                for k in range(4):
                    mm = pe.transpose(e.bank[4 + u % 4][0:n, k * P:(k + 1) * P], dst[:, 4 * h + k, tb * P:tb * P + n], e.ident)
                mm.then_inc(y_turned, 1)

        @block.vector
        def _(dve):
            M0, M1 = SL // P, 2 * SL // P

            def copy_blocks(first, last):
                for tb in range(first, last):
                    for h in range(2):
                        u = 2 * tb + h
                        dve.wait_ge(y_turned, u + 1)
                        if h == 0 and tb >= 3:
                            load_wait(dve, e.y_stored[tb % 3], tb // 3)
                        dve.tensor_copy(yrow[0:rows(tb), tb % 3, h * 512:(h + 1) * 512], e.bank[4 + u % 4][0:rows(tb), :]).then_inc(y_kept, 1)

            def hi(i):
                dve.wait_ge(moved, i + 1)
                dve.tensor_copy(e.hhi[:, i % KD, sl(i // KD)], hn[:, i % 4, :]).then_inc(hi_set, 1)

            if scale is not None:
                g = e.vec[:, gain * KD:(gain + 1) * KD]
                dve.tensor_scalar(amp[:, :, :], e.mod[:, scale * KD:(scale + 1) * KD, :], 1.0, None, ALU.add).then_inc(amp_set, 1)
                dve.wait_ge(amp_set, 1)
                dve.tensor_tensor(amp[:, :, :], amp[:, :, :], g.unsqueeze(2).to_broadcast([P, KD, NC9]), ALU.mult).then_inc(amp_set, 1)
                dve.wait_ge(amp_set, 2)
            for s in range(3):
                dve.wait_ge(root, s + 1)
                dve.reciprocal(rstd[:, s, :], rstd[:, s, :]).then_inc(rstd_set, 1)
                dve.wait_ge(rstd_set, s + 1)
                for k in range(KD):
                    i = s * KD + k
                    if i >= 4:
                        dve.wait_ge(freed, i - 3)
                    ins = dve.tensor_tensor(hn[:, i % 4, :], src[:, k, sl(s)], rstd[:, s, :], ALU.mult)
                    if s == 2 and scale is not None:
                        ds = hn[:, i % 4, M:SL].rearrange("p (n t) -> p n t", t=TS)
                        ins.then_inc(amp_set, 1)
                        dve.wait_ge(amp_set, 3 + 2 * k)
                        dve.tensor_tensor(ds, ds, amp[:, k, 1:NC9].unsqueeze(2).to_broadcast([P, NSEQ, TS]), ALU.mult).then_inc(amp_set, 1)
                        dve.wait_ge(amp_set, 4 + 2 * k)
                        ins = dve.tensor_tensor(ds, ds, e.mod[:, shift * KD + k, 1:NC9].unsqueeze(2).to_broadcast([P, NSEQ, TS]), ALU.add)
                    ins.then_inc(scaled, 1)
                    if dst is None and i >= 2:
                        hi(i - 2)
                if store and s:
                    copy_blocks(*((0, M0) if s == 1 else (M0, M1)))
            if dst is None:
                hi(NU - 2)
                hi(NU - 1)
            if store:
                copy_blocks(M1, TB + 1)

        if dst is None:
            @block.gpsimd
            def _(pool):
                for i in range(NU):
                    s, k = i // KD, i % KD
                    pool.wait_ge(hi_set, i + 1)
                    pool.tensor_tensor(e.hlo[:, k, sl(s)], hn[:, i % 4, :], e.hhi[:, k, sl(s)], ALU.subtract).then_inc(lo_set, 1)


NJ = SG // 2
E1 = NCH + 1


def stage_ssm(nc, e):
    MAGIC = float(1.5 * 2 ** 23)
    PI2 = float(np.nextafter(np.float32(TWO_PI), np.float32(0)))
    NP = 2 * LC + 1
    with ExitStack() as c:
        sb = lambda n, s, d=F32: c.enter_context(nc.sbuf_tensor(n, s, d))
        sem = stage_semaphores(nc, c, "ssm")
        U = sb("U", [P, SG, LC, SI])
        small = sb("small", [SI, SG * LC * SI])
        Us = small[0:NSEQ, :].rearrange("p (g k i) -> p g k i", g=SG, k=LC)
        hall = small[:, :].rearrange("p (g k i) -> p g k i", g=SG, k=LC)
        Y = U[:, :, :, :].rearrange("p g k i -> p (g k i)").rearrange("p (k g i) -> p k g i", k=LC, g=SG)
        Ys = small[0:NSEQ, 0:SG * TS * SI].rearrange("p (k g i) -> p k g i", g=SG, k=TS)
        UT = sb("UT", [P, SG, NCH + NSEQ])
        wu = e.wu
        wglu = wu[:, 0:4, :]
        big = sb("big", [P, 4 * NT])
        ET = big[:, 0:2 * NJ * P].rearrange("p (c j m) -> p c j m", c=2, j=NJ)
        Tm = big[:, 0:SG * P].rearrange("p (g k o) -> p g k o", g=SG, k=LC)
        zT = big[:, :].rearrange("p (q t) -> p q t", q=4)
        Fre = sb("Fre", [P, NJ, LC + 1, SI])
        Fim = sb("Fim", [P, NJ, LC + 1, SI])
        rtab = e.ossmT[:, :, :].rearrange("p q t -> p (q t)")
        Rre = rtab[:, 0:NJ * E1].rearrange("p (j n) -> p j n", j=NJ)
        Rim = rtab[:, NJ * E1:2 * NJ * E1].rearrange("p (j n) -> p j n", j=NJ)
        Sre = sb("Sre", [P, NJ, E1])
        Sim = sb("Sim", [P, NJ, E1])
        Gre, Gim = (m[:, :, :].rearrange("p j n -> p (j n)")[:, 0:NJ * LC * SI].rearrange("p (j k i) -> p j k i", k=LC, i=SI)
                    for m in (Sre, Sim))
        H8 = NJ // 2
        M = sb("M", [P, H8, E1])
        t0 = sb("t0", [P, H8, E1])
        t1 = sb("t1", [P, H8, E1])
        Bre = sb("Bre", [P, NJ, SI])
        Bim = sb("Bim", [P, NJ, SI])
        BBre = sb("BBre", [P, NJ, SI])
        BBim = sb("BBim", [P, NJ, SI])
        cdup = big[:, 0:16 * SP].rearrange("p (c q d s) -> p c q d s", c=2, q=4, d=2)
        CT = sb("CT", [P, 2, NJ, SI])
        lamrow = sb("lamrow", [NJ, 2, P])
        ldt = sb("ldt", [1, SG])
        x0 = sb("x0", [P, 2, NSEQ, NJ])
        xs = sb("xs", [P, 2, NSEQ, NJ])
        xt = sb("xt", [P, NSEQ, NJ])
        dtb = sb("dtb", [P, SG])
        dtj = sb("dtj", [P, NJ])
        lam = sb("lam", [P, 2, NJ])
        dT = sb("dT", [SI, SG])
        dI = sb("dI", [SI, SG, SI])
        v = sb("v", [P, 8, NJ])
        w1 = sb("w1", [P, 4, NJ])
        w2 = sb("w2", [P, 4, NJ])
        angles = lambda m: m[:, :, :].rearrange("p j n -> p (j n)")[:, 0:2 * NJ * NP].rearrange("p (c j n) -> p c j n", c=2, j=NJ)
        ang, rnd = angles(M), angles(t1)
        trig = sb("trig", [P, 2, NJ, NP])
        mag = sb("mag", [P, NJ, NP])
        pw = sb("pw", [P, 2, NJ, NP])
        finrow = sb("finrow", [P, 4, P])
        x0row = finrow[:, 0:2, :]
        names = ("h_stored lam_loaded dt_loaded b_loaded c_loaded x0_loaded d_loaded glu_loaded u_products u_kept "
                 "u_turned u_turned_kept small_cleared lam_turned dt_spread x0_turned c_turned exp_done "
                 "magnitudes_ready angles_ready trig_done g_turned g_kept lags_done lags_kept toeplitz_loaded "
                 "inputs_done states_scanned y_done y_gelu_done sample_gelu_done last_states_ready last_states_kept "
                 "z_turned z_kept gate_products gate_sigmoids gated rotations_ready pool_chain dve_chain tables_ready "
                 "toeplitz_cleared prompt_rows_kept last_states_turned sample_inputs_done lags_ready ").split()
        S = {n: sem(n) for n in names}
        block = c.enter_context(nc.Block())
        ident = e.ident
        NU = LC + TS
        NG3 = -(-SG // 3)
        bank = e.bank

        @block.sync
        def _(sp):
            for i, l in enumerate((e.lam_re, e.lam_im)):
                sp.dma_start(lamrow[:, i, :], l[0].rearrange("(j g) p -> j (g p)", g=2)).then_inc(S["lam_loaded"], 16)
            sp.dma_start(ldt[:, :], e.log_dt).then_inc(S["dt_loaded"], 16)
            for b, s in ((Bre, e.b_re), (Bim, e.b_im)):
                sp.dma_start(b[:, :, :], s[0].rearrange("(j g) p i -> (g p) j i", g=2)).then_inc(S["b_loaded"], 16)
            for i, s in enumerate((e.state_re, e.state_im)):
                sp.dma_start(x0row[:, i, :], s[0].rearrange("n (j g) p -> (n j) (g p)", g=2)).then_inc(S["x0_loaded"], 16)
            sp.dma_start(dT[:, :], e.ssm_d[0].rearrange("(g i) -> i g", i=SI), allow_slow_non_contiguous=True).then_inc(S["d_loaded"], 16)
            sp.wait_ge(S["lags_ready"], 1)
            sp.wait_ge(S["toeplitz_cleared"], 1)
            for k in range(LC):
                sp.dma_start(Tm[SI * k:SI * (k + 1), :, k:LC, :], hall[:, :, 0:LC - k, :]).then_inc(S["toeplitz_loaded"], 16)
            sp.wait_ge(S["u_products"], NU)
            sp.dma_start(wglu, e.w_glu[0].rearrange("(k p) n -> p k n", p=P)).then_inc(S["glu_loaded"], 16)
            sp.wait_ge(S["last_states_kept"], 1)
            for i, o in enumerate((e.p_re, e.p_im)):
                sp.dma_start(o[0, 0].rearrange("(j g) p -> j (g p)", g=2), finrow[0:NJ, i, :]).then_inc(e.states_stored, 16)
            for i, o in enumerate((e.s_re, e.s_im)):
                sp.dma_start(o[0].rearrange("n (j g) p -> (n j) (g p)", g=2), finrow[:, 2 + i, :]).then_inc(e.states_stored, 16)
            sp.dma_start(e.h_keep, e.hT[:, :, :]).then_inc(S["h_stored"], 16)
            load_wait(sp, e.states_stored, 4)
            load_wait(sp, S["h_stored"], 1)

        @block.gpsimd
        def _(pool):
            n = [0]

            def link(ins):
                n[0] += 1
                ins.then_inc(S["pool_chain"], 1)
                pool.wait_ge(S["pool_chain"], n[0])

            pool.memset(small[0:NSEQ, :], 0.0).then_inc(S["small_cleared"], 1)
            link(pool.memset(Rre[:, :, 0:2], 1.0))
            link(pool.memset(Rim[:, :, 0:2], 0.0))
            pool.wait_ge(S["trig_done"], 1)
            wr, wi, wr2, wi2 = w1[:, 0, :], w1[:, 1, :], w2[:, 0, :], w2[:, 1, :]
            link(pool.tensor_copy(wr, trig[:, 0, :, LC]))
            link(pool.tensor_copy(wi, trig[:, 1, :, LC]))
            m = 1
            while m < NCH:
                wrb = wr.unsqueeze(2).to_broadcast([P, NJ, m])
                wib = wi.unsqueeze(2).to_broadcast([P, NJ, m])
                ar, ai = Rre[:, :, 1:1 + m], Rim[:, :, 1:1 + m]
                br, bi = Rre[:, :, 1 + m:1 + 2 * m], Rim[:, :, 1 + m:1 + 2 * m]
                tt, t2 = (a[:, :, :].rearrange("p j n -> p (j n)")[:, 0:NJ * m].rearrange("p (j n) -> p j n", j=NJ) for a in (M, t1))
                link(pool.tensor_tensor(br, ar, wrb, ALU.mult))
                link(pool.tensor_tensor(tt, ai, wib, ALU.mult))
                link(pool.tensor_tensor(br, br, tt, ALU.subtract))
                link(pool.tensor_tensor(bi, ar, wib, ALU.mult))
                link(pool.tensor_tensor(t2, ai, wrb, ALU.mult))
                link(pool.tensor_tensor(bi, bi, t2, ALU.add))
                if 2 * m < NCH:
                    link(pool.tensor_tensor(wr2, wr, wr, ALU.mult))
                    link(pool.tensor_tensor(wi2, wi, wi, ALU.mult))
                    link(pool.tensor_tensor(wi, wr, wi, ALU.mult))
                    link(pool.tensor_tensor(wr, wr2, wi2, ALU.subtract))
                    link(pool.tensor_tensor(wi, wi, wi, ALU.add))
                m *= 2
            pool.sem_inc(S["rotations_ready"], 1)
            pool.wait_ge(S["sample_inputs_done"], 1)
            pool.memset(Tm[:, :, :, :], 0.0).then_inc(S["toeplitz_cleared"], 1)

        @block.tensor
        def _(pe):
            def turn_parameters():
                load_wait(pe, S["lam_loaded"], 2)
                for i in range(2):
                    mm = pe.transpose(bank[0][:, i * NJ:(i + 1) * NJ], lamrow[:, i, :], ident[0:NJ, 0:NJ])
                mm.then_inc(S["lam_turned"], 1)
                load_wait(pe, S["dt_loaded"], 1)
                pe.matmul(bank[1][:, 0:SG], e.ones[0:1, :], ldt[:, :], start=True, stop=True).then_inc(S["dt_spread"], 1)
                load_wait(pe, S["x0_loaded"], 2)
                for i in range(2):
                    mm = pe.transpose(bank[2][:, i * P:(i + 1) * P], x0row[:, i, :], ident[:, :])
                mm.then_inc(S["x0_turned"], 1)
                load_wait(pe, S["c_loaded"], 16)
                for i in range(2):
                    for q in range(4):
                        mm = pe.transpose(bank[3 + i][:, q * P:(q + 1) * P], cdup[:, i, q, :, :].rearrange("p d s -> p (d s)"), ident[:, :])
                mm.then_inc(S["c_turned"], 1)

            load_wait(pe, e.wu_loaded, 1)
            for i in range(NU):
                m = P if i < LC else NSEQ
                if i >= 2:
                    pe.wait_ge(S["u_kept"], i - 1)
                for k in range(KD):
                    lhs = e.hT[:, k, 0:T].rearrange("p (c k) -> p c k", k=LC)[:, :, i] if i < LC else \
                        e.hT[:, k, T:NT].rearrange("p (n t) -> p n t", t=TS)[:, :, i - LC]
                    mm = pe.matmul(bank[6 + i % 2][0:m, :], lhs, wu[:, k, :], start=(k == 0), stop=(k == KD - 1))
                mm.then_inc(S["u_products"], 1)
                if i == 1:
                    turn_parameters()
            pe.wait_ge(S["u_kept"], NU)
            for b in range(NG3):
                if b >= 2:
                    pe.wait_ge(S["u_turned_kept"], b - 1)
                for g in range(3 * b, min(3 * b + 3, SG)):
                    o = (g - 3 * b) * (NCH + NSEQ)
                    pe.transpose(bank[6 + b % 2][:, o:o + NCH], U[:, g, :, :].rearrange("p k i -> p (k i)"), ident[:, :])
                    mm = pe.transpose(bank[6 + b % 2][:, o + NCH:o + NCH + NSEQ], Us[:, g, :, :].rearrange("p k i -> p (k i)"),
                                      ident[0:NSEQ, 0:NSEQ])
                mm.then_inc(S["u_turned"], 1)
            pe.wait_ge(S["tables_ready"], 1)
            for b in range(8):
                if b >= 2:
                    pe.wait_ge(S["g_kept"], b - 1)
                elif b == 0:
                    pe.wait_ge(S["u_turned_kept"], NG3)
                for q in range(4):
                    x = 4 * b + q
                    Gx = (Gre, Gim)[x // NJ]
                    mm = pe.transpose(bank[6 + b % 2][:, q * P:(q + 1) * P], Gx[:, x % NJ, :, :].rearrange("p k i -> p (k i)"), ident[:, :])
                    if q == 3:
                        mm.then_inc(S["g_turned"], 1)
            for b in range(4):
                pe.wait_ge(S["lags_kept"], 2 * b - 2) if b >= 2 else pe.wait_ge(S["g_kept"], 8)
                for q in range(8):
                    g = 8 * b + q
                    j, h = g // 2, 64 * (g % 2)
                    o = bank[4 + 2 * (b % 2) + g % 2][0:SI, q // 2 * P:(q // 2 + 1) * P]
                    pe.matmul(o, BBre[h:h + SP, j, :], Fre[h:h + SP, j, 0:LC, :].rearrange("p l o -> p (l o)"), start=True, stop=False)
                    mm = pe.matmul(o, BBim[h:h + SP, j, :], Fim[h:h + SP, j, 0:LC, :].rearrange("p l o -> p (l o)"), start=False, stop=True)
                    if q >= 6:
                        mm.then_inc(S["lags_done"], 1)
            for half in range(2):
                if half:
                    pe.wait_ge(S["states_scanned"], 1)
                else:
                    pe.wait_ge(S["g_kept"], 8)
                for ci in range(2):
                    for jj in range(H8):
                        j = half * H8 + jj
                        for h in range(2):
                            mm = pe.matmul(bank[2 * ci + jj // 4][64 * h:64 * h + 64, (jj % 4) * P:(jj % 4 + 1) * P],
                                           ET[:, ci, j, 64 * h:64 * h + 64], UT[:, 2 * j + h, 0:NCH], start=True, stop=True)
                mm.then_inc(S["inputs_done"], 1)
            for ci in range(2):
                for j in range(NJ):
                    for h in range(2):
                        o = ci * P + j * NSEQ
                        mm = pe.matmul(bank[4][64 * h:64 * h + 64, o:o + NSEQ], ET[:, ci, j, 64 * h:64 * h + 64],
                                       UT[:, 2 * j + h, NCH:NCH + NSEQ], start=True, stop=True)
            mm.then_inc(S["sample_inputs_done"], 1)
            pe.wait_ge(S["last_states_ready"], 1)
            for i, s in enumerate((Sre, Sim)):
                pe.transpose(bank[0][0:NJ, i * P:(i + 1) * P], s[:, :, NCH], ident[:, :])
            for i in range(2):
                mm = pe.transpose(bank[0][:, (2 + i) * P:(3 + i) * P], xs[:, i, :, :].rearrange("p n j -> p (n j)"), ident[:, :])
            mm.then_inc(S["last_states_turned"], 1)
            load_wait(pe, S["toeplitz_loaded"], LC)
            pe.wait_ge(S["lags_kept"], 8)
            for b in range(4):
                if b >= 2:
                    pe.wait_ge(S["y_gelu_done"], 2 * b - 2)
                for q in range(8):
                    g = 8 * b + q
                    j, h = g // 2, 64 * (g % 2)
                    o = bank[4 + 2 * (b % 2) + g % 2][:, q // 2 * P:(q // 2 + 1) * P]
                    pe.matmul(o, UT[:, g, 0:NCH], Tm[:, g, :, :].rearrange("p k o -> p (k o)"), start=True, stop=False)
                    pe.matmul(o, Sre[h:h + SP, j, 0:NCH], Fre[h:h + SP, j, 1:LC + 1, :].rearrange("p l o -> p (l o)"), start=False, stop=False)
                    mm = pe.matmul(o, Sim[h:h + SP, j, 0:NCH], Fim[h:h + SP, j, 1:LC + 1, :].rearrange("p l o -> p (l o)"), start=False, stop=True)
                    if q >= 6:
                        mm.then_inc(S["y_done"], 1)
            for b in range(4):
                if b >= 2:
                    pe.wait_ge(S["sample_gelu_done"], 2 * b - 2)
                if b == 1:
                    pe.wait_ge(S["last_states_kept"], 1)
                for q in range(8):
                    g = 8 * b + q
                    j, h = g // 2, 64 * (g % 2)
                    o = bank[2 - 2 * (b % 2) + g % 2][0:NSEQ, q // 2 * 64:(q // 2 + 1) * 64]
                    pe.matmul(o, UT[:, g, NCH:NCH + NSEQ], Tm[:, g, TS:LC, :].rearrange("p k o -> p (k o)"), start=True, stop=False)
                    pe.matmul(o, x0[h:h + SP, 0, :, j], Fre[h:h + SP, j, 1:TS + 1, :].rearrange("p l o -> p (l o)"), start=False, stop=False)
                    mm = pe.matmul(o, x0[h:h + SP, 1, :, j], Fim[h:h + SP, j, 1:TS + 1, :].rearrange("p l o -> p (l o)"), start=False, stop=True)
                    if q >= 6:
                        mm.then_inc(S["y_done"], 1)
            pe.wait_ge(S["y_gelu_done"], 8)
            pe.wait_ge(S["sample_gelu_done"], 8)
            for b in range(LC):
                if b >= 2:
                    pe.wait_ge(S["z_kept"], b - 1)
                for q in range(4):
                    mm = pe.transpose(bank[6 + b % 2][:, q * P:(q + 1) * P], Y[:, b, 8 * q:8 * q + 8, :].rearrange("p g i -> p (g i)"), ident[:, :])
                mm.then_inc(S["z_turned"], 1)
            pe.wait_ge(S["z_kept"], 7)
            for k in range(TS):
                for q in range(4):
                    o = (k * 4 + q) * NSEQ
                    mm = pe.transpose(bank[6][:, o:o + NSEQ], Ys[:, k, 8 * q:8 * q + 8, :].rearrange("p g i -> p (g i)"), ident[0:NSEQ, 0:NSEQ])
            mm.then_inc(S["z_turned"], 1)
            pe.wait_ge(S["z_kept"], LC + 1)
            load_wait(pe, S["glu_loaded"], 1)
            for f in range(4):
                for s in range(3):
                    i = 3 * f + s
                    if i >= 4:
                        pe.wait_ge(S["gate_sigmoids"], i - 3)
                    for k in range(4):
                        mm = pe.matmul(bank[i % 4][:, 0:SL], wglu[:, k, f * P:(f + 1) * P], zT[:, k, s * SL:(s + 1) * SL],
                                       start=(k == 0), stop=(k == 3))
                    mm.then_inc(S["gate_products"], 1)

        @block.scalar
        def _(act):
            def keep_u(i):
                act.wait_ge(S["u_products"], i + 1)
                m, dst, k = (P, U, i) if i < LC else (NSEQ, Us, TS + i - LC)
                act.activation(dst[:, :, k, :], bank[6 + i % 2][0:m, :].rearrange("p (g i) -> p g i", g=SG), ACT.Copy)\
                   .then_inc(S["u_kept"], 1)

            for i, s in enumerate((e.c_re, e.c_im)):
                for q in range(4):
                    for d in range(2):
                        act.dma_start(cdup[:, i, q, d, :], s[0, 8 * q:8 * q + 8].rearrange("g o p -> (g o) p")).then_inc(S["c_loaded"], 16)
            act.wait_ge(S["small_cleared"], 1)
            for i in range(NU):
                keep_u(i)
                if i == 1:
                    act.wait_ge(S["dt_spread"], 1)
                    act.activation(dtb[:, :], bank[1][:, 0:SG], ACT.Exp).then_inc(S["exp_done"], 1)
                if i == 2:
                    act.wait_ge(S["magnitudes_ready"], 1)
                    act.activation(mag[:, :, :], mag[:, :, :], ACT.Exp).then_inc(S["exp_done"], 1)
                    act.wait_ge(S["angles_ready"], 1)
                    act.activation(trig[:, :, :, :], ang[:, :, :, :], ACT.Sin, scale=PI2).then_inc(S["trig_done"], 1)
            for b in range(NG3):
                g0, g1 = 3 * b, min(3 * b + 3, SG)
                act.wait_ge(S["u_turned"], b + 1)
                act.activation(UT[:, g0:g1, :], bank[6 + b % 2][:, 0:(g1 - g0) * (NCH + NSEQ)].rearrange("p (g n) -> p g n", g=g1 - g0),
                               ACT.Copy).then_inc(S["u_turned_kept"], 1)
            for b in range(8):
                act.wait_ge(S["g_turned"], b + 1)
                x = 4 * b
                act.activation(ET[:, x // NJ, x % NJ:x % NJ + 4, :], bank[6 + b % 2][:, :].rearrange("p (q m) -> p q m", q=4), ACT.Copy)\
                   .then_inc(S["g_kept"], 1)
            act.wait_ge(S["u_turned"], NG3)
            for x in range(8):
                b, h = x // 2, x % 2
                act.wait_ge(S["lags_done"], x + 1)
                act.activation(hall[:, 8 * b + h:8 * b + 8:2, :, :], bank[4 + 2 * (b % 2) + h][0:SI, :].rearrange("p (g k o) -> p g k o", g=4, k=LC),
                               ACT.Copy).then_inc(S["lags_kept"], 1)
            for x in range(8):
                b, h = x // 2, x % 2
                act.wait_ge(S["y_done"], x + 1)
                act.activation(Y[:, :, 8 * b + h:8 * b + 8:2, :], bank[4 + 2 * (b % 2) + h][:, :].rearrange("p (g k o) -> p k g o", g=4, k=LC),
                               ACT.Gelu_apprx_tanh).then_inc(S["y_gelu_done"], 1)
            for x in range(8):
                b, h = x // 2, x % 2
                act.wait_ge(S["y_done"], 8 + x + 1)
                act.activation(Ys[:, :, 8 * b + h:8 * b + 8:2, :], bank[2 - 2 * (b % 2) + h][0:NSEQ, 0:256].rearrange("p (g k o) -> p k g o", g=4, k=TS),
                               ACT.Gelu_apprx_tanh).then_inc(S["sample_gelu_done"], 1)
            for b in range(LC):
                act.wait_ge(S["z_turned"], b + 1)
                act.activation(zT[:, :, 0:T].rearrange("p q (c k) -> p q c k", k=LC)[:, :, :, b],
                               bank[6 + b % 2][:, :].rearrange("p (q c) -> p q c", q=4), ACT.Copy).then_inc(S["z_kept"], 1)
            act.wait_ge(S["z_turned"], LC + 1)
            for k in range(TS):
                ins = act.activation(zT[:, :, T:NT].rearrange("p q (n t) -> p q n t", t=TS)[:, :, :, k],
                                     bank[6][:, k * 32:(k + 1) * 32].rearrange("p (q n) -> p q n", q=4), ACT.Copy)
            ins.then_inc(S["z_kept"], 1)
            for i in range(12):
                f, s = i // 3, i % 3
                act.wait_ge(S["gate_products"], i + 1)
                act.activation(e.ossmT[:, f, s * SL:(s + 1) * SL], bank[i % 4][:, 0:SL], ACT.Sigmoid).then_inc(S["gate_sigmoids"], 1)

        @block.vector
        def _(dve):
            n = [0]

            def link(ins):
                n[0] += 1
                ins.then_inc(S["dve_chain"], 1)
                dve.wait_ge(S["dve_chain"], n[0])

            tt, ts_ = dve.tensor_tensor, dve.tensor_scalar
            dve.wait_ge(S["exp_done"], 1)
            link(dve.tensor_copy(dtj[0:64, :], dtb[0:64, :].rearrange("p (j g) -> p j g", g=2)[:, :, 0]))
            link(dve.tensor_copy(dtj[64:128, :], dtb[64:128, :].rearrange("p (j g) -> p j g", g=2)[:, :, 1]))
            dve.wait_ge(S["lam_turned"], 1)
            link(ts_(lam[:, 0, :], bank[0][:, 0:NJ], -1e-4, None, ALU.min))
            link(dve.tensor_copy(lam[:, 1, :], bank[0][:, NJ:2 * NJ]))
            lr, li = lam[:, 0, :], lam[:, 1, :]
            a1, th = v[:, 0, :], v[:, 1, :]
            link(tt(a1, lr, dtj[:, :], ALU.mult))
            link(tt(th, li, dtj[:, :], ALU.mult))
            link(ts_(th, th, float(1.0 / TWO_PI), None, ALU.mult))
            pows = e.consts[:, C_POW:C_POW + NP].unsqueeze(1).to_broadcast([P, NJ, NP])
            wide = lambda a: a.unsqueeze(2).to_broadcast([P, NJ, NP])
            tt(mag[:, :, :], wide(a1), pows, ALU.mult).then_inc(S["magnitudes_ready"], 1)
            link(tt(ang[:, 1, :, :], wide(th), pows, ALU.mult))
            link(ts_(ang[:, 0, :, :], ang[:, 1, :, :], 0.25, None, ALU.add))
            link(ts_(rnd[:, :, :, :], ang[:, :, :, :], MAGIC, None, ALU.add))
            link(ts_(rnd[:, :, :, :], rnd[:, :, :, :], MAGIC, None, ALU.subtract))
            link(tt(ang[:, :, :, :], ang[:, :, :, :], rnd[:, :, :, :], ALU.subtract))
            dve.sem_inc(S["angles_ready"], 1)
            dve.wait_ge(S["trig_done"], 1)
            dve.wait_ge(S["exp_done"], 2)
            for i in range(2):
                link(tt(pw[:, i, :, :], mag[:, :, :], trig[:, i, :, :], ALU.mult))
            pr, pi = pw[:, 0, :, :], pw[:, 1, :, :]
            am, den, fr, fi, x = v[:, 2, :], v[:, 3, :], v[:, 4, :], v[:, 5, :], v[:, 6, :]
            link(ts_(am, pr[:, :, 1], -1.0, None, ALU.add))
            link(tt(den, lr, lr, ALU.mult))
            link(tt(x, li, li, ALU.mult))
            link(tt(den, den, x, ALU.add))
            link(dve.reciprocal(den, den))
            link(tt(fr, am, lr, ALU.mult))
            link(tt(x, pi[:, :, 1], li, ALU.mult))
            link(tt(fr, fr, x, ALU.add))
            link(tt(fr, fr, den, ALU.mult))
            link(tt(fi, pi[:, :, 1], lr, ALU.mult))
            link(tt(x, am, li, ALU.mult))
            link(tt(fi, fi, x, ALU.subtract))
            link(tt(fi, fi, den, ALU.mult))
            load_wait(dve, S["b_loaded"], 2)
            frb, fib = (a.unsqueeze(2).to_broadcast([P, NJ, SI]) for a in (fr, fi))
            tb = t0[:, :, :].rearrange("p j n -> p (j n)")[:, 0:NJ * SI].rearrange("p (j i) -> p j i", i=SI)
            link(tt(BBre[:, :, :], Bre[:, :, :], frb, ALU.mult))
            link(tt(tb, Bim[:, :, :], fib, ALU.mult))
            link(tt(BBre[:, :, :], BBre[:, :, :], tb, ALU.subtract))
            link(tt(BBim[:, :, :], Bim[:, :, :], frb, ALU.mult))
            link(tt(tb, Bre[:, :, :], fib, ALU.mult))
            link(tt(BBim[:, :, :], BBim[:, :, :], tb, ALU.add))
            dve.wait_ge(S["c_turned"], 1)
            for i in range(2):
                src = bank[3 + i][:, :].rearrange("p (j g o) -> p j g o", g=2, o=SI)
                for h in range(2):
                    link(dve.tensor_copy(CT[64 * h:64 * h + 64, i, :, :], src[64 * h:64 * h + 64, :, h, :]))
            dve.wait_ge(S["x0_turned"], 1)
            link(dve.tensor_copy(x0[:, :, :, :], bank[2][:, 0:2 * P].rearrange("p (c n j) -> p c n j", c=2, n=NSEQ)))
            tG = lambda a, k, s: a[:, :, k].unsqueeze(2).to_broadcast([P, NJ, s])
            tg = t0[:, :, :].rearrange("p j n -> p (j n)")[:, 0:NJ * SI].rearrange("p (j i) -> p j i", i=SI)
            for k in range(LC):
                q = LC + 1 + k
                link(tt(Gre[:, :, k, :], BBre[:, :, :], tG(pr, q, SI), ALU.mult))
                link(tt(tg, BBim[:, :, :], tG(pi, q, SI), ALU.mult))
                link(tt(Gre[:, :, k, :], Gre[:, :, k, :], tg, ALU.subtract))
                link(tt(Gim[:, :, k, :], BBim[:, :, :], tG(pr, q, SI), ALU.mult))
                link(tt(tg, BBre[:, :, :], tG(pi, q, SI), ALU.mult))
                link(tt(Gim[:, :, k, :], Gim[:, :, k, :], tg, ALU.add))
            for l in range(LC + 1):
                cr, cim = CT[:, 0, :, :], CT[:, 1, :, :]
                link(tt(Fre[:, :, l, :], cr, tG(pr, l, SI), ALU.mult))
                link(tt(tg, cim, tG(pi, l, SI), ALU.mult))
                link(tt(Fre[:, :, l, :], Fre[:, :, l, :], tg, ALU.subtract))
                link(tt(Fim[:, :, l, :], cr, tG(pi, l, SI), ALU.mult))
                link(tt(tg, cim, tG(pr, l, SI), ALU.mult))
                link(dve.scalar_tensor_tensor(out=Fim[:, :, l, :], in0=Fim[:, :, l, :], scalar=-1.0, in1=tg,
                                              op0=ALU.mult, op1=ALU.subtract))
            dve.sem_inc(S["tables_ready"], 1)
            load_wait(dve, S["d_loaded"], 1)
            link(tt(dI[:, :, :], dT[:, :].unsqueeze(2).to_broadcast([SI, SG, SI]),
                    ident[0:SI, 0:SI].unsqueeze(1).to_broadcast([SI, SG, SI]), ALU.mult))
            dve.wait_ge(S["lags_kept"], 8)
            tt(hall[:, :, 0, :], hall[:, :, 0, :], dI[:, :, :], ALU.add).then_inc(S["lags_ready"], 1)
            dve.wait_ge(S["rotations_ready"], 1)
            dve.wait_ge(S["g_turned"], 8)
            for half in range(2):
                j0 = half * H8
                jj = slice(j0, j0 + H8)
                link(dve.tensor_copy(M[:, :, :], mag[:, jj, LC].unsqueeze(2).to_broadcast([P, H8, E1])))
                link(dve.memset(M[:, :, 0], 0.0))
                link(dve.memset(Sre[:, jj, 0], 0.0))
                link(dve.memset(Sim[:, jj, 0], 0.0))
                dve.wait_ge(S["inputs_done"], half + 1)
                for q in range(2):
                    qq = slice(j0 + 4 * q, j0 + 4 * q + 4)
                    br = bank[q][:, :].rearrange("p (j n) -> p j n", j=4)
                    bi = bank[2 + q][:, :].rearrange("p (j n) -> p j n", j=4)
                    rr, ri = Rre[:, qq, 1:E1], Rim[:, qq, 1:E1]
                    sr, si = Sre[:, qq, 1:E1], Sim[:, qq, 1:E1]
                    a, b = t0[:, 0:4, 1:E1], t1[:, 0:4, 1:E1]
                    link(tt(sr, br, rr, ALU.mult))
                    link(tt(a, bi, ri, ALU.mult))
                    link(tt(si, bi, rr, ALU.mult))
                    link(tt(b, br, ri, ALU.mult))
                    link(tt(sr, sr, a, ALU.add))
                    link(tt(si, si, b, ALU.subtract))
                Mf = M[:, :, :].rearrange("p j n -> p (j n)")
                for s in (Sre, Sim):
                    f = s[:, jj, :].rearrange("p j n -> p (j n)")
                    link(dve.tensor_tensor_scan(f, Mf, f, 0.0, ALU.mult, ALU.add))
                rr, ri, sr, si = Rre[:, jj, :], Rim[:, jj, :], Sre[:, jj, :], Sim[:, jj, :]
                link(tt(t0[:, :, :], sr, ri, ALU.mult))
                link(tt(t1[:, :, :], si, ri, ALU.mult))
                link(tt(sr, sr, rr, ALU.mult))
                link(tt(si, si, rr, ALU.mult))
                link(tt(sr, sr, t1[:, :, :], ALU.subtract))
                tt(si, si, t0[:, :, :], ALU.add).then_inc(S["states_scanned"], 1)
                dve.wait_ge(S["states_scanned"], half + 1)
            dve.wait_ge(S["sample_inputs_done"], 1)
            p4r = pr[:, :, TS].unsqueeze(1).to_broadcast([P, NSEQ, NJ])
            p4i = pi[:, :, TS].unsqueeze(1).to_broadcast([P, NSEQ, NJ])
            bs = bank[4][:, 0:2 * P].rearrange("p (c j n) -> p c n j", c=2, n=NSEQ)
            link(tt(xs[:, 0, :, :], x0[:, 0, :, :], p4r, ALU.mult))
            link(tt(xt[:, :, :], x0[:, 1, :, :], p4i, ALU.mult))
            link(tt(xs[:, 0, :, :], xs[:, 0, :, :], xt[:, :, :], ALU.subtract))
            link(tt(xs[:, 0, :, :], bs[:, 0], xs[:, 0, :, :], ALU.add))
            link(tt(xs[:, 1, :, :], x0[:, 1, :, :], p4r, ALU.mult))
            link(tt(xt[:, :, :], x0[:, 0, :, :], p4i, ALU.mult))
            link(tt(xs[:, 1, :, :], xs[:, 1, :, :], xt[:, :, :], ALU.add))
            tt(xs[:, 1, :, :], bs[:, 1], xs[:, 1, :, :], ALU.add).then_inc(S["last_states_ready"], 1)
            dve.wait_ge(S["last_states_turned"], 1)
            dve.tensor_copy(finrow[0:NJ, 0:2, :], bank[0][0:NJ, 0:2 * P].rearrange("p (c m) -> p c m", c=2)).then_inc(S["prompt_rows_kept"], 1)
            dve.wait_ge(S["prompt_rows_kept"], 1)
            dve.tensor_copy(finrow[:, 2:4, :], bank[0][:, 2 * P:4 * P].rearrange("p (c m) -> p c m", c=2)).then_inc(S["last_states_kept"], 1)
            for f in range(4):
                dve.wait_ge(S["gate_sigmoids"], 3 * f + 3)
                tt(e.ossmT[:, f, :], e.ossmT[:, f, :], zT[:, f, :], ALU.mult).then_inc(S["gated"], 1)


def table_steps(nc, e, sb, sem):
    tab = sb("tab", [NB + 1, HQ])
    oh = sb("oh", [NB + 1, 2 * BW])
    line = sb("line", [HQ, BW])
    perow = sb("perow", [16, 2, P])
    peT = sb("peT", [P, 2, 16])
    b1row = sb("b1row", [1, 2, HD])
    ptab = sb("ptab", [P, NSEQ * 2], I32)
    pf = sb("pf", [P, NSEQ * 2])
    bias_table_loaded, masked_row_set, onehot_loaded, bias_products, line_kept, lines_stored, bias_tiles_loaded, cleared, near_bias_kept, cmp_weights_loaded, cmp_rows_loaded, pe_turned, cmp_bias_kept, cmp_bias_products, pages_loaded, row_index_step, queries_laid = (sem(n) for n in (
        "bias_table_loaded", "masked_row_set", "onehot_loaded", "bias_products", "line_kept", "lines_stored", "bias_tiles_loaded", "cleared", "near_bias_kept", "cmp_weights_loaded", "cmp_rows_loaded", "pe_turned", "cmp_bias_kept", "cmp_bias_products",
        "pages_loaded", "row_index_step", "queries_laid"))
    rb = nc.dram_tensor("bias_lines", (P, HQ, BW), F32, kind="Internal").ap()
    bank = e.bank
    line_ap = lambda off, ap: bass.AP(tensor=rb.tensor, offset=off, ap=ap)

    def loads(sp):
        sp.dma_start(tab[0:NB, :], e.rel_bias).then_inc(bias_table_loaded, 16)
        sp.dma_start(oh[:, :], e.onehot_in).then_inc(onehot_loaded, 16)
        for kv in range(2):
            for j in range(2):
                sp.dma_start(e.w1T[:, kv, :, j, :], e.cmp_w1[0, kv, 16 * j:16 * j + 16].rearrange("(a s) d e -> (s d) a e", s=2))\
                  .then_inc(cmp_weights_loaded, 16)
            sp.dma_start(e.w2[:, kv, :], e.cmp_w2[0, kv]).then_inc(cmp_weights_loaded, 16)
            sp.dma_start(perow[:, kv, :], e.cmp_pe[0, kv].rearrange("(a s) d -> a (s d)", s=2)).then_inc(cmp_rows_loaded, 16)
            sp.dma_start(b1row[:, kv, :], e.cmp_b1[:, kv, :]).then_inc(cmp_rows_loaded, 16)
        for sub in range(8):
            sp.dma_start(ptab[sub:P:8, :], bass.AP(tensor=e.page_table.tensor, offset=0, ap=[[1, 16], [16, 2 * NSEQ]]),
                         allow_slow_non_contiguous=True).then_inc(pages_loaded, 16)

    def spread(sp):
        sp.wait_ge(line_kept, 1)
        sp.dma_start(rb.rearrange("p h w -> h p w"), line[:, None, :].to_broadcast([HQ, P, BW])).then_inc(lines_stored, 16)
        load_wait(sp, lines_stored, 1)
        for i, dlt in enumerate((1, 0)):
            sp.dma_start(e.bt[:, :, i * P:(i + 1) * P], line_ap(255 - P * dlt, [[HQ * BW - 1, P], [BW, HQ], [1, P]])).then_inc(bias_tiles_loaded, 16)
        sp.wait_ge(cleared, 2)
        for m in range(4):
            r = slice(32 * m, 32 * m + 32)
            sp.dma_start(e.btail[r, :], line_ap(127, [[BW, HQ], [HQ * BW - 1, TS], [1, P]])).then_inc(bias_tiles_loaded, 16)
            for t in range(TS):
                sp.dma_start(e.bcd[32 * m + t:32 * m + 32:TS, :], line_ap(142 - t, [[BW, HQ], [16, 8]]),
                             allow_slow_non_contiguous=True).then_inc(bias_tiles_loaded, 16)
            for b in range(2):
                a = TS * (4 * b + m)
                sp.dma_start(e.bnew[r, b, a:a + TS], line_ap(255, [[BW, HQ], [HQ * BW - 1, TS], [1, TS]])).then_inc(bias_tiles_loaded, 16)
        load_wait(sp, bias_tiles_loaded, 2 + 4 * 7)
        load_wait(sp, cmp_weights_loaded, 6)

    def clear(pool):
        pool.memset(e.bnew[:, :, :], NEG).then_inc(cleared, 1)
        pool.memset(e.qbd[:, :, :], 0.0).then_inc(cleared, 1)

    def queries(pool):
        pool.wait_ge(cleared, 2)
        for g in range(G):
            for r in range(R):
                a = (g * R + r) * TS
                ins = pool.tensor_copy(e.qbd[g * HD:(g + 1) * HD, :, a:a + TS],
                                       e.qT[g * HD:(g + 1) * HD, r, T:NT].rearrange("p (n t) -> p n t", t=TS))
                ins.then_inc(queries_laid, 1)
                pool.wait_ge(queries_laid, g * R + r + 1)

    def lines(pe):
        load_wait(pe, bias_table_loaded, 1)
        load_wait(pe, onehot_loaded, 1)
        pe.wait_ge(masked_row_set, 1)
        pe.matmul(bank[6][0:HQ, 0:BW], tab[:, :], oh[:, 0:BW], start=True, stop=True).then_inc(bias_products, 1)
        for i in range(16):
            y0 = BW + 96 - 16 * (i - 9)
            mm = pe.matmul(bank[7][:, i * HQ:(i + 1) * HQ], oh[:, y0:y0 + P], tab[:, :], start=True, stop=True)
        mm.then_inc(bias_products, 1)

    def compressor_bias(pe):
        load_wait(pe, cmp_rows_loaded, 4)
        for kv in range(2):
            mm = pe.transpose(bank[0][:, kv * 16:kv * 16 + 16], perow[:, kv, :], e.ident[0:16, 0:16])
        mm.then_inc(pe_turned, 1)
        pe.wait_ge(cmp_bias_kept, 1)
        load_wait(pe, cmp_weights_loaded, 6)
        for kv in range(2):
            o = bank[1][0:HD, kv:kv + 1]
            for x in range(16):
                pe.matmul(o, e.w1T[:, kv, x % 8, x // 8, :], peT[:, kv, x:x + 1], start=(x == 0), stop=False)
            mm = pe.matmul(o, b1row[:, kv, :], e.ones[0:1, 0:1], start=False, stop=True)
        mm.then_inc(cmp_bias_products, 1)

    def near_bias(act):
        act.wait_ge(bias_products, 2)
        act.activation(e.bc[:, :, :], bank[7][:, 0:16 * HQ].rearrange("p (c h) -> p h c", h=HQ), ACT.Copy).then_inc(near_bias_kept, 1)

    def keep_line(dve):
        dve.memset(tab[NB:NB + 1, :], NEG).then_inc(masked_row_set, 1)
        dve.wait_ge(bias_products, 1)
        dve.tensor_copy(line[:, :], bank[6][0:HQ, 0:BW]).then_inc(line_kept, 1)

    def keep_compressor_bias(dve):
        dve.wait_ge(pe_turned, 1)
        dve.tensor_copy(peT[:, :, :], bank[0][:, 0:32].rearrange("p (c x) -> p c x", c=2)).then_inc(cmp_bias_kept, 1)
        dve.wait_ge(cmp_bias_products, 1)
        for kv in range(2):
            dve.tensor_copy(e.cbias[:, kv:kv + 1], bank[1][0:HD, kv:kv + 1]).then_inc(cmp_bias_kept, 1)

    def rows(dve):
        load_wait(dve, pages_loaded, 8)
        dve.tensor_copy(pf[:, :], ptab[:, :]).then_inc(row_index_step, 1)
        dve.wait_ge(row_index_step, 1)
        dve.tensor_scalar(pf[:, :], pf[:, :], 8.0, e.consts[:, C_SUB:C_SUB + 1], ALU.mult, ALU.add).then_inc(row_index_step, 1)
        dve.wait_ge(row_index_step, 2)
        dve.tensor_copy(e.rowidx[:, :], pf[:, :]).then_inc(row_index_step, 1)

    kept = ((line_kept, 1), (near_bias_kept, 1), (cmp_bias_kept, 3))
    return loads, spread, clear, queries, lines, compressor_bias, near_bias, keep_line, keep_compressor_bias, rows, kept


def stage_project(nc, e):
    with ExitStack() as c:
        sb = lambda n, s, d=F32: c.enter_context(nc.sbuf_tensor(n, s, d))
        sem = stage_semaphores(nc, c, "proj")
        wq = sb("wq", [P, KD, R, G, HD])
        wk = sb("wk", [P, KD, 6 * KVW + 3 * HQ])
        kv = sb("kv", [P, TB + 1, 6 * KVW])
        wq_loaded, q_products, q_kept, kv_products, kv_kept, k_turned, kT_kept, values_laid, ones_set = (sem(n) for n in (
            "wq_loaded", "q_products", "q_kept", "kv_products", "kv_kept", "k_turned", "kT_kept", "values_laid", "ones_set"))
        (t_loads, t_spread, t_clear, t_queries, t_lines, t_compressor_bias, t_near_bias, t_keep_line, t_keep_compressor_bias, t_rows,
         t_kept) = table_steps(nc, e, sb, sem)
        wk_loaded = [sem(f"wk_loaded{i}") for i in range(4)]
        block = c.enter_context(nc.Block())
        win = e.w_in[0].rearrange("(k p) n -> p k n", p=P)
        NQ = 3 * (R + 1)
        bank = e.bank
        rows = lambda tb: P if tb < TB else NS

        @block.sync
        def _(sp):
            for i in range(4):
                sp.dma_start(wk[:, 2 * i:2 * i + 2, :], win[:, 2 * i:2 * i + 2, KV0:U0]).then_inc(wk_loaded[i], 16)
            for r in range(R):
                for g in range(G):
                    a = Q0 + (g * R + r) * HD
                    sp.dma_start(wq[:, :, r, g, :], win[:, :, a:a + HD]).then_inc(wq_loaded, 16)
            t_loads(sp)
            t_spread(sp)
            sp.wait_ge(kv_kept, 2 * TB)
            outs = (e.p_k_cmp, e.p_v_cmp, e.p_k_slc, e.p_v_slc)
            for i, o in enumerate(outs):
                sp.dma_start(o[0, 0].rearrange("(b p) g d -> p b (g d)", p=P), kv[:, 0:TB, i * KVW:(i + 1) * KVW]).then_inc(e.caches_stored, 16)
            for i, o in enumerate((e.p_k_win, e.p_v_win)):
                sp.dma_start(o[0, 0].rearrange("(b p) g d -> p b (g d)", p=P),
                             kv[:, TB - WIN // P:TB, (4 + i) * KVW:(5 + i) * KVW]).then_inc(e.caches_stored, 16)
            sp.wait_ge(kv_kept, 2 * TB + 2)
            for i, o in enumerate((e.s_k_cmp, e.s_v_cmp, e.s_k_slc, e.s_v_slc)):
                sp.dma_start(o[0].rearrange("n t g d -> (n t) (g d)"), kv[0:NS, TB, i * KVW:(i + 1) * KVW]).then_inc(e.caches_stored, 16)
            for i, (o, b) in enumerate(((e.s_k_win, e.cache_k_win), (e.s_v_win, e.cache_v_win))):
                sp.dma_start(o[0, :, 0:WIN - TS].rearrange("n w g d -> n (w g d)"), b[0, :, TS:WIN].rearrange("n w g d -> n (w g d)"))\
                  .then_inc(e.caches_stored, 16)
                sp.dma_start(o[0, :, WIN - TS:WIN].rearrange("n t g d -> n t (g d)"),
                             kv[0:NS, TB, (4 + i) * KVW:(5 + i) * KVW]).then_inc(e.caches_stored, 16)
            load_wait(sp, e.caches_stored, 14)

        @block.gpsimd
        def _(pool):
            t_clear(pool)
            pool.memset(e.vslc[:, :, HD:2 * HD], 1.0).then_inc(ones_set, 1)
            pool.memset(e.vwin[:, :, HD:2 * HD], 1.0).then_inc(ones_set, 1)
            pool.wait_ge(q_kept, 3 * R)
            t_queries(pool)
            for tb in range(TB):
                pool.wait_ge(kv_kept, 2 * tb + 2)
                for dst, i in ((e.vslc, 3), (e.vwin, 5)):
                    for g in range(G):
                        pool.tensor_copy(dst[:, tb, 2 * g * HD:(2 * g + 1) * HD],
                                         kv[:, tb, i * KVW + g * HD:i * KVW + (g + 1) * HD]).then_inc(values_laid, 1)
            pool.wait_ge(kv_kept, 2 * TB + 2)
            pool.tensor_copy(e.vnew[:, 0, :], kv[0:NS, TB, 3 * KVW:4 * KVW]).then_inc(values_laid, 1)
            pool.tensor_copy(e.vnew[:, 1, :], kv[0:NS, TB, 5 * KVW:6 * KVW]).then_inc(values_laid, 1)
            pool.wait_ge(values_laid, 4 * TB + 2)

        @block.tensor
        def _(pe):
            for tb in range(TB + 1):
                if tb == 1:
                    t_lines(pe)
                for h in range(2):
                    i = 2 * tb + h
                    if i >= 2:
                        pe.wait_ge(kv_kept, i - 1)
                    for k in range(KD):
                        if i == 0 and k % 2 == 0:
                            load_wait(pe, wk_loaded[k // 2], 1)
                        mm = pe.matmul(bank[4 + h][0:rows(tb), 0:3 * KVW], e.hT[:, k, tb * P:tb * P + rows(tb)],
                                       wk[:, k, h * 3 * KVW:(h + 1) * 3 * KVW], start=(k == 0), stop=(k == KD - 1))
                    mm.then_inc(kv_products, 1)
            t_compressor_bias(pe)
            for done, n in t_kept:
                pe.wait_ge(done, n)
            for tb in range(TB + 1):
                n = rows(tb)
                pe.wait_ge(kv_kept, 2 * tb + 2)
                if tb >= 2:
                    pe.wait_ge(kT_kept, tb - 1)
                for q, i in enumerate((2, 4)):
                    mm = pe.transpose(bank[6 + tb % 2][:, q * P:q * P + n], kv[0:n, tb, i * KVW:(i + 1) * KVW], e.ident[0:n, 0:n])
                mm.then_inc(k_turned, 1)
            load_wait(pe, wq_loaded, 8)
            for i in range(NQ):
                f, s = i // 3, i % 3
                if i >= 4:
                    pe.wait_ge(q_kept, i - 3)
                m = P if f < R else 3 * HQ
                for k in range(KD):
                    w = wq[:, k, f, :, :].rearrange("p g d -> p (g d)") if f < R else wk[:, k, 6 * KVW:6 * KVW + 3 * HQ]
                    mm = pe.matmul(bank[i % 4][0:m, 0:SL], w, e.hT[:, k, s * SL:(s + 1) * SL], start=(k == 0), stop=(k == KD - 1))
                mm.then_inc(q_products, 1)

        @block.scalar
        def _(act):
            t_near_bias(act)
            for i in range(NQ):
                f, s = i // 3, i % 3
                act.wait_ge(q_products, i + 1)
                if f < R:
                    act.activation(e.qT[:, f, s * SL:(s + 1) * SL], bank[i % 4][:, 0:SL], ACT.Copy, scale=HD ** -0.5).then_inc(q_kept, 1)
                else:
                    act.activation(e.gates[:, s * SL:(s + 1) * SL], bank[i % 4][0:3 * HQ, 0:SL], ACT.Sigmoid).then_inc(q_kept, 1)

        @block.vector
        def _(dve):
            t_rows(dve)
            for i in range(2 * (TB + 1)):
                tb, h = i // 2, i % 2
                if i == 2:
                    t_keep_line(dve)
                dve.wait_ge(kv_products, i + 1)
                dve.tensor_copy(kv[0:rows(tb), tb, h * 3 * KVW:(h + 1) * 3 * KVW], bank[4 + h][0:rows(tb), 0:3 * KVW]).then_inc(kv_kept, 1)
            t_keep_compressor_bias(dve)
            for tb in range(TB + 1):
                n = rows(tb)
                dve.wait_ge(k_turned, tb + 1)
                dve.tensor_copy(e.kT[:, :, tb * P:tb * P + n],
                                bank[6 + tb % 2][:, 0:2 * P].rearrange("p (c n) -> p c n", c=2)[:, :, 0:n]).then_inc(kT_kept, 1)




def stage_compress(nc, e):
    NI = 2 + 2 * NSEQ
    NCK = [T // CHK] * 2 + [PAST // CHK] * (2 * NSEQ)
    NBT = [4] * 2 + [8] * (2 * NSEQ)
    first = [sum(NBT[:i]) for i in range(NI + 1)]
    with ExitStack() as c:
        sb = lambda n, s, d=F32: c.enter_context(nc.sbuf_tensor(n, s, d))
        sem = stage_semaphores(nc, c, "cmp")
        raw = sb("raw", [P, 2, 2, CHK * KVW])
        byg = sb("byg", [P, 2, 2, G, CHK, HD])
        xT2 = sb("xT2", [P, 2, 8, 512])
        low = sb("low", [HD, 2, 512])
        hsum = sb("hsum", [HD, 2, 512])
        hid = sb("hid", [HD, 2, G, 256])
        pages_landed = [sem(f"pages_landed{i}") for i in range(2)]
        prompt_rows_landed = [sem(f"prompt_rows_landed{i}") for i in range(2)]
        regrouped, turned, even_kept, odd_kept, parts_done, low_kept, sums_done, hidden_done, outputs_done, outputs_kept, hidden_cleared = (sem(n) for n in (
            "regrouped", "turned", "even_kept", "odd_kept", "parts_done", "low_kept", "sums_done", "hidden_done", "outputs_done", "outputs_kept", "hidden_cleared"))
        block = c.enter_context(nc.Block())
        bank = e.bank
        rows = [x.rearrange("a b (c s) g d -> (a b c) (s g d)", s=CHK) for x in (e.cache_k_cmp, e.cache_v_cmp)]

        @block.sync
        def _(sp):
            for i, src in enumerate((e.p_k_cmp, e.p_v_cmp)):
                for g in range(G):
                    sp.dma_start(byg[0:64, i, 0, g, :, :], src[0, 0].rearrange("(c s) g d -> c s g d", s=CHK)[:, :, g, :]).then_inc(prompt_rows_landed[i], 16)

        @block.gpsimd
        def _(pool):
            for i in range(2, NI):
                n, kv = (i - 2) // 2, i % 2
                if i >= 4:
                    pool.wait_ge(regrouped, i - 3)
                for half in range(2):
                    col = 2 * n + half
                    pool.indirect_dma_start(raw[:, i % 2, half, :], None, rows[kv],
                                            bass.IndirectOffsetOnAxis(ap=e.rowidx[:, col:col + 1], axis=0)).then_inc(pages_landed[i % 2], 16)

        @block.tensor
        def _(pe):
            def second(i):
                n, kv, C = (i - 2) // 2, i % 2, NCK[i]
                pe.wait_ge(hidden_done, i + 1)
                if i >= 2:
                    pe.wait_ge(outputs_kept, i - 1)
                o = bank[6 + i % 2]
                if kv == 0:
                    for g in range(G):
                        mm = pe.matmul(o[g * HD:(g + 1) * HD, 0:C], e.w2[:, 0, :], hid[:, i % 2, g, 0:C], start=True, stop=True)
                else:
                    for half in range(max(C // P, 1)):
                        m = min(C, P)
                        for g in range(G):
                            a = half * P + g * HD
                            mm = pe.matmul(o[0:m, a:a + HD], hid[:, i % 2, g, half * P:half * P + m], e.w2[:, 1, :], start=True, stop=True)
                mm.then_inc(outputs_done, 1)

            def turn(i):
                m = min(NCK[i], P)
                if i < 2:
                    load_wait(pe, prompt_rows_landed[i], 2)
                else:
                    pe.wait_ge(regrouped, i - 1)
                for b in range(NBT[i]):
                    y = first[i] + b
                    if y >= 4:
                        pe.wait_ge((even_kept, odd_kept)[y % 2], y // 2 - 1)
                    half, sp2 = b // 4, b % 4
                    for a in range(2):
                        for g in range(G):
                            s = 2 * (2 * sp2 + a)
                            o = (a * G + g) * m
                            mm = pe.transpose(bank[y % 4][:, o:o + m], byg[0:m, i % 2, half, g, s:s + 2, :].rearrange("p s d -> p (s d)"),
                                              e.ident[0:m, 0:m])
                    mm.then_inc(turned, 1)

            pe.wait_ge(hidden_cleared, 1)
            turn(0)
            for i in range(NI):
                C, kv = NCK[i], i % 2
                if i + 1 < NI:
                    turn(i + 1)
                if i >= 1:
                    second(i - 1)
                pe.wait_ge(even_kept, first[i + 1] // 2)
                pe.wait_ge(odd_kept, first[i + 1] // 2)
                if i >= 2:
                    pe.wait_ge(sums_done, i - 1)
                for sp in range(8):
                    mm = pe.matmul(bank[4 + i % 2][:, 0:G * C], e.w1T[:, kv, sp, :, :].rearrange("p j e -> p (j e)"),
                                   xT2[:, i % 2, sp, 0:G * C], start=(sp == 0), stop=(sp == 7))
                mm.then_inc(parts_done, 1)
            second(NI - 1)

        def move(i, b):
            m, half, sp2 = min(NCK[i], P), b // 4, b % 4
            src = bank[(first[i] + b) % 4][:, 0:4 * m].rearrange("p (a g c) -> p a g c", a=2, g=G)
            dst = xT2[:, i % 2, 2 * sp2:2 * sp2 + 2, 0:G * NCK[i]].rearrange("p a (g c) -> p a g c", g=G)[:, :, :, half * P:half * P + m]
            return src, dst

        def hidden(act, i):
            C = NCK[i]
            act.wait_ge(sums_done, i + 1)
            if i >= 2:
                act.wait_ge(outputs_done, i - 1)
            act.activation(hid[:, i % 2, :, 0:C - 1], hsum[:, i % 2, 0:G * C].rearrange("p (g c) -> p g c", g=G)[:, :, 0:C - 1],
                           ACT.Silu, bias=e.cbias[:, i % 2:i % 2 + 1]).then_inc(hidden_done, 1)

        @block.scalar
        def _(act):
            def even(i):
                for b in range(NBT[i]):
                    if (first[i] + b) % 2 == 0:
                        act.wait_ge(turned, first[i] + b + 1)
                        if i >= 2:
                            act.wait_ge(parts_done, i - 1)
                        src, dst = move(i, b)
                        act.activation(dst, src, ACT.Copy).then_inc(even_kept, 1)

            even(0)
            for i in range(NI):
                C = NCK[i]
                if i + 1 < NI:
                    even(i + 1)
                if i >= 1:
                    hidden(act, i - 1)
                act.wait_ge(parts_done, i + 1)
                if i >= 2:
                    act.wait_ge(sums_done, i - 1)
                act.activation(low[:, i % 2, 0:G * C], bank[4 + i % 2][HD:P, 0:G * C], ACT.Copy).then_inc(low_kept, 1)
            hidden(act, NI - 1)

        @block.vector
        def _(dve):
            dve.memset(hid[:, :, :, :], 0.0).then_inc(hidden_cleared, 1)

            def regroup(i):
                load_wait(dve, pages_landed[i % 2], 2 * (i // 2))
                dve.wait_ge(turned, first[i - 1])
                ins = None
                for half in range(2):
                    ins = dve.tensor_copy(byg[:, i % 2, half, :, :, :].rearrange("p g s d -> p s g d"),
                                          raw[:, i % 2, half, :].rearrange("p (s g d) -> p s g d", g=G, d=HD))
                ins.then_inc(regrouped, 1)

            def keep(i):
                n, kv, C = (i - 2) // 2, i % 2, NCK[i]
                dve.wait_ge(outputs_done, i + 1)
                o = bank[6 + i % 2]
                if i == 0:
                    ins = dve.tensor_copy(e.kcp[:, :], o[:, 0:C])
                elif i == 1:
                    for g in range(G):
                        ins = dve.tensor_copy(e.vcp[:, 2 * g * HD:(2 * g + 1) * HD], o[0:C, g * HD:(g + 1) * HD])
                elif kv == 0:
                    ins = dve.tensor_copy(e.kcT[:, n, :], o[:, 0:C])
                else:
                    ins = dve.tensor_copy(e.vc[:, n, :, :], o[:, 0:2 * P].rearrange("p (h f) -> p h f", h=2))
                ins.then_inc(outputs_kept, 1)

            def odd(i):
                for b in range(NBT[i]):
                    if (first[i] + b) % 2 == 1:
                        dve.wait_ge(turned, first[i] + b + 1)
                        if i >= 2:
                            dve.wait_ge(parts_done, i - 1)
                        src, dst = move(i, b)
                        dve.tensor_copy(dst, src).then_inc(odd_kept, 1)

            odd(0)
            for i in range(NI):
                C = NCK[i]
                if i + 1 < NI:
                    odd(i + 1)
                if i + 2 < NI:
                    regroup(i + 2)
                if i >= 1:
                    keep(i - 1)
                dve.wait_ge(low_kept, i + 1)
                if i >= 2:
                    dve.wait_ge(hidden_done, i - 1)
                v = lambda t, a, b: t.rearrange("p (g c) -> p g c", g=G)[:, :, a:b]
                dve.tensor_tensor(v(hsum[:, i % 2, 0:G * C], 0, C - 1), v(bank[4 + i % 2][0:HD, 0:G * C], 0, C - 1),
                                  v(low[:, i % 2, 0:G * C], 1, C), ALU.add).then_inc(sums_done, 1)
            keep(NI - 1)
            dve.memset(e.vcp[:, HD:2 * HD], 1.0)


CMP, SLC, WND = range(3)


def prompt_units():
    for qb in range(TB):
        for r in range(R):
            for g in range(G):
                for br in (CMP, SLC, WND):
                    lo = 0 if br != WND else max(0, qb - WIN // P) * P
                    hi = 8 * qb + 7 if br == CMP else (qb + 1) * P
                    yield qb, r, br, g, lo, hi - lo


def stage_prompt(nc, e):
    U = list(prompt_units())
    NU = len(U)
    tiles = [-(-u[5] // P) for u in U]
    ngrp = [-(-t // 4) for t in tiles]
    grp0 = [sum(ngrp[:i]) for i in range(NU + 1)]
    NPR, NPT = 4, 4
    with ExitStack() as c:
        sb = lambda n, s, d=F32: c.enter_context(nc.sbuf_tensor(n, s, d))
        sem = stage_semaphores(nc, c, "prompt")
        gT = sb("gT", [P, TB, 3 * HQ])
        pr = sb("pr", [P, NPR, T])
        pt = sb("pt", [P, NPT, TB, P])
        nmax = sb("nmax", [P, 4])
        qhi, qlo = (sb(n, [P, 2, R, P], F32R) for n in ("q_hi", "q_lo"))
        khi, klo = (sb(n, [P, 2, T], F32R) for n in ("k_hi", "k_lo"))
        parts_hi, parts_ready = sem("parts_hi"), sem("parts_ready")
        rsum = sb("rsum", [P, 4])
        gates_turned, gates_kept, scores_done, bias_added, maxima_done, exps_done, sums_guarded, reciprocals_done, weights_scaled, weights_turned, turned_kept, values_done, outputs_kept = (sem(n) for n in (
            "gates_turned", "gates_kept", "scores_done", "bias_added", "maxima_done", "exps_done", "sums_guarded", "reciprocals_done", "weights_scaled", "weights_turned", "turned_kept", "values_done", "outputs_kept"))
        NADA = 6 * KD - ADA_EARLY
        assert NADA == NU // 6
        wada = sb("wada_late", [P, 3, KD, P])
        partial = sb("ada_partial", [P, NADA, P])
        ada_loaded, ada_done, ada_kept, mod_done, mod_kept = [sem(f"ada_loaded{i}") for i in range(3)], sem("ada_done"), sem("ada_kept"), sem("mod_done"), sem("mod_kept")
        ada_out = lambda j: bank[7 - j % 2][:, 2 * P:3 * P]
        block = c.enter_context(nc.Block())
        bank, ps = e.bank, e.ps

        @block.sync
        def _(sp):
            for j in range(NADA):
                if j >= 3:
                    sp.wait_ge(ada_done, j - 2)
                a = (ADA_EARLY + j) * P
                sp.dma_start(wada[:, j % 3], e.w_ada[0].rearrange("(k p) n -> p k n", p=P)[:, :, a:a + P]).then_inc(ada_loaded[j % 3], 16)

        score = lambda u: ps[:, 1024 * (u % 2):1024 * (u % 2) + U[u][5]]
        outp = lambda u: bank[6 + (u // 6) % 2]

        @block.tensor
        def _(pe):
            for tb in range(TB):
                mm = pe.transpose(bank[7][:, tb * 24:(tb + 1) * 24], e.gates[:, tb * P:(tb + 1) * P], e.ident[0:24, 0:24])
            mm.then_inc(gates_turned, 1)
            pe.wait_ge(gates_kept, 1)

            def scores(u):
                qb, r, br, g, lo, n = U[u]
                if u >= 2:
                    pe.wait_ge(exps_done, u - 1)
                h = slice(g * HD, (g + 1) * HD)
                if br == CMP:
                    pe.matmul(score(u), e.qT[h, r, qb * P:(qb + 1) * P], e.kcp[h, 0:n], start=True, stop=True).then_inc(scores_done, 1)
                    return
                if u % (6 * R) == 1:
                    pe.wait_ge(parts_ready, 2 * (qb + 1))
                kh, kl = khi[:, br - 1, :], klo[:, br - 1, :]
                qh, ql = qhi[h, qb % 2, r, :], qlo[h, qb % 2, r, :]
                for a in range(0, n, 512):
                    m = min(512, n - a)
                    o, keys = score(u)[:, a:a + m], slice(lo + a, lo + a + m)
                    pe.matmul(o, qh, kl[h, keys], start=True, stop=False)
                    pe.matmul(o, ql, kh[h, keys], start=False, stop=False)
                    mm = pe.matmul(o, qh, kh[h, keys], start=False, stop=True)
                mm.then_inc(scores_done, 1)

            def turn(u):
                n = U[u][5]
                pe.wait_ge(weights_scaled, u + 1)
                for y in range(ngrp[u]):
                    if grp0[u] + y >= 2:
                        pe.wait_ge(turned_kept, grp0[u] + y - 1)
                    for t in range(4 * y, min(4 * y + 4, tiles[u])):
                        m = min(P, n - t * P)
                        mm = pe.transpose(bank[4 + (grp0[u] + y) % 2][0:m, (t % 4) * P:(t % 4 + 1) * P],
                                          pr[:, u % NPR, t * P:t * P + m], e.ident)
                    mm.then_inc(weights_turned, 1)

            def values(u):
                qb, r, br, g, lo, n = U[u]
                pe.wait_ge(turned_kept, grp0[u + 1])
                if u % 6 == 0 and u >= 12:
                    pe.wait_ge(outputs_kept, u // 6 - 1)
                if u % 6 == 0 and u >= 6:
                    pe.wait_ge(ada_kept, u // 6)
                va = 2 * g * HD
                for t in range(tiles[u]):
                    m = min(P, n - t * P)
                    v = e.vcp[0:m, va:va + HD] if br == CMP else (e.vslc, e.vwin)[br - 1][:, lo // P + t, va:va + HD]
                    mm = pe.matmul(outp(u)[g * HD:(g + 1) * HD, 0:P], v, pt[0:m, u % NPT, t, :], start=(br == CMP and t == 0),
                                   stop=(br == WND and t == tiles[u] - 1), skip_group_check=True)
                mm.then_inc(values_done, 1)

            for u in range(NU + 4):
                if u < NU:
                    scores(u)
                if 3 <= u < NU + 3:
                    turn(u - 3)
                if u >= 4:
                    v = u - 4
                    values(v)
                    if v % 6 == 2:
                        j = v // 6
                        load_wait(pe, ada_loaded[j % 3], j // 3 + 1)
                        if j:
                            pe.wait_ge(outputs_kept, j)
                        ada_products(pe, ada_out(j), wada[:, j % 3], e.scT).then_inc(ada_done, 1)

            pe.wait_ge(ada_kept, NADA)
            pe.wait_ge(exps_done, NU)
            for j in range(NADA):
                mm = ada_sums(pe, bank[0][:, j * NC9:(j + 1) * NC9], partial[:, j, :], e)
            mm.then_inc(mod_done, 1)

        @block.gpsimd
        def _(pool):
            for qb in range(TB):
                if qb >= 2:
                    pool.wait_ge(scores_done, 6 * R * (qb - 1))
                q = slice(qb * P, (qb + 1) * P)
                split = ((e.qT[:, :, q], qhi[:, qb % 2], qlo[:, qb % 2]), (e.kT[:, :, q], khi[:, :, q], klo[:, :, q]))
                for i, (x, hi, lo) in enumerate(split):
                    pool.tensor_copy(hi, x).then_inc(parts_hi, 1)
                for i, (x, hi, lo) in enumerate(split):
                    pool.wait_ge(parts_hi, 2 * qb + i + 1)
                    pool.tensor_tensor(lo, x, hi, ALU.subtract).then_inc(parts_ready, 1)

        @block.scalar
        def _(act):
            def copies(u):
                for y in range(ngrp[u]):
                    t0, t1 = 4 * y, min(4 * y + 4, tiles[u])
                    m = min(P, U[u][5])
                    act.wait_ge(weights_turned, grp0[u] + y + 1)
                    if y == 0 and u >= NPT:
                        act.wait_ge(values_done, u - NPT + 1)
                    act.activation(pt[0:m, u % NPT, t0:t1, :], bank[4 + (grp0[u] + y) % 2][0:m, 0:(t1 - t0) * P].rearrange("p (t q) -> p t q", q=P),
                                   ACT.Copy).then_inc(turned_kept, 1)

            for u in range(NU + 3):
                if u < NU:
                    act.wait_ge(maxima_done, u + 1)
                    if u >= NPR:
                        act.wait_ge(weights_turned, grp0[u - NPR + 1])
                    if u >= 4:
                        act.wait_ge(reciprocals_done, u - 3)
                    act.activation(pr[:, u % NPR, 0:U[u][5]], score(u), ACT.Exp, bias=nmax[:, u % 4:u % 4 + 1],
                                   accum_out=rsum[:, u % 4:u % 4 + 1]).then_inc(exps_done, 1)
                if u >= 3:
                    copies(u - 3)

        @block.vector
        def _(dve):
            bias_n = [0]

            def bias(dst, src):
                bias_n[0] += 1
                dve.tensor_tensor(dst, dst, src, ALU.add).then_inc(bias_added, 1)

            dve.wait_ge(gates_turned, 1)
            dve.tensor_copy(gT[:, :, :], bank[7][:, 0:TB * 24].rearrange("p (b h) -> p b h", h=24)).then_inc(gates_kept, 1)
            dve.wait_ge(gates_kept, 1)

            def maxima(u):
                qb, r, br, g, lo, n = U[u]
                h = g * R + r
                dve.wait_ge(scores_done, u + 1)
                s = score(u)
                if br == CMP:
                    c0 = max(0, 8 * qb - 9)
                    bias(s[:, c0:n], e.bc[:, h, c0 - (8 * qb - 9):16])
                else:
                    m = min(2 * P, n)
                    bias(s[:, n - m:n], e.bt[:, h, 2 * P - m:2 * P])
                    if br == WND and qb >= WIN // P:
                        bias(s[:, 0:P], e.winmask)
                dve.wait_ge(bias_added, bias_n[0])
                if u >= 4:
                    dve.wait_ge(exps_done, u - 3)
                dve.tensor_reduce(nmax[:, u % 4:u % 4 + 1], s, AXX, ALU.max, negate=True).then_inc(maxima_done, 1)

            def scale(u):
                qb, r, br, g, lo, n = U[u]
                h = g * R + r
                x = rsum[:, u % 4:u % 4 + 1]
                dve.wait_ge(exps_done, u + 1)
                dve.tensor_scalar(x, x, 1e-30, None, ALU.max).then_inc(sums_guarded, 1)
                dve.wait_ge(sums_guarded, u + 1)
                dve.reciprocal(x, x).then_inc(reciprocals_done, 1)
                dve.wait_ge(reciprocals_done, u + 1)
                p = pr[:, u % NPR, 0:n]
                if br == CMP and qb == 0:
                    dve.tensor_scalar(p, p, e.cmprow, None, ALU.mult).then_inc(bias_added, 1)
                    bias_n[0] += 1
                    dve.wait_ge(bias_added, bias_n[0])
                dve.tensor_scalar(p, p, x, gT[:, qb, br * HQ + h:br * HQ + h + 1], ALU.mult, ALU.mult).then_inc(weights_scaled, 1)

            def output(x):
                qb, r = U[6 * x][0], U[6 * x][1]
                dve.wait_ge(values_done, 6 * x + 6)
                dve.tensor_copy(e.oT[:, r, qb * P:(qb + 1) * P], outp(6 * x)[:, 0:P]).then_inc(outputs_kept, 1)

            def modulation(j):
                dve.wait_ge(ada_done, j + 1)
                dve.tensor_copy(partial[:, j, :], ada_out(j)).then_inc(ada_kept, 1)

            for u in range(NU + 1):
                if u < NU:
                    maxima(u)
                if u >= 1:
                    scale(u - 1)
                if u % 6 == 2 and u >= 8:
                    modulation(u // 6 - 1)
                if u % 6 == 5 and u >= 11:
                    output(u // 6 - 1)
            modulation(NU // 6 - 1)
            output(NU // 6 - 1)
            dve.wait_ge(mod_done, 1)
            dve.tensor_tensor(e.mod[:, ADA_EARLY:6 * KD, :], bank[0][:, 0:NADA * NC9].rearrange("p (f n) -> p f n", n=NC9),
                              e.vec[:, 3 * KD + ADA_EARLY:9 * KD].unsqueeze(2).to_broadcast([P, NADA, NC9]), ALU.add).then_inc(mod_kept, 1)


def stage_decode(nc, e):
    NR = 6
    NBAT, M = 2, 4
    W = PAST + NS
    BLK = 64
    NBK = PAST // BLK
    KG = M + 8 * M
    TCMP, TWIN, TSLC = 0, 2, 7
    NTL = TSLC + 33
    with ExitStack() as c:
        sb = lambda n, s, d=F32: c.enter_context(nc.sbuf_tensor(n, s, d))
        sem = stage_semaphores(nc, c, "decode")
        ring = sb("ring", [P, NR, CHK, KVW])
        Ss = sb("Ss", [P, W])
        Sw = sb("Sw", [P, WIN + NS])
        Sc = sb("Sc", [P, 256])
        wt = sb("wt", [P, NTL, P])
        kt = e.bt[:, :, :].rearrange("p h x -> p (h x)").rearrange("p (s x) -> p s x", s=4)
        kwin = e.vslc[:, :, :].rearrange("p b x -> p (b x)")[:, 0:1024].rearrange("p (s j x) -> p s j x", s=2, j=4)
        vwin = e.vwin[:, :, :].rearrange("p b x -> p (b x)")[:, 0:1024].rearrange("p (s j x) -> p s j x", s=2, j=4)
        gd = sb("gd", [P, NBAT, 3])
        sc = sb("sc", [P, NBK + 1])
        scs = sb("scs", [P, NBK + 1])
        m8 = sb("m8", [P, 8])
        st = sb("st", [P, 8])
        gscr = nc.dram_tensor("gate_rows", (3 * HQ, NS), F32, kind="Internal").ap()
        ring_landed = [sem(f"ring_landed{i}") for i in range(NR)]
        window_keys_landed = [sem(f"window_keys_landed{i}") for i in range(2)]
        window_values_landed = [sem(f"window_values_landed{i}") for i in range(2)]
        gates_stored, gates_landed, ring_used, window_keys_used, window_values_used, first_scores_done, first_scores_kept, blocks_summed, selection_step, keys_turned, keys_kept, scores_done, scores_kept, maxima_done, exps_done, weights_scaled, weights_turned, turned_kept, values_done, outputs_kept = (
            sem(n) for n in ("gates_stored", "gates_landed", "ring_used", "window_keys_used", "window_values_used", "first_scores_done", "first_scores_kept", "blocks_summed", "selection_step", "keys_turned", "keys_kept", "scores_done",
                             "scores_kept", "maxima_done", "exps_done", "weights_scaled", "weights_turned", "turned_kept", "values_done", "outputs_kept"))
        rows_kept, rows_turned = sem("rows_kept"), sem("rows_turned")
        orow = sb("orow", [P, P])
        c_chain = sem("chain")
        block = c.enter_context(nc.Block())
        bank = e.bank
        rows = [x.rearrange("a b (c s) g d -> (a b c) (s g d)", s=CHK) for x in (e.cache_k_slc, e.cache_v_slc)]
        NG = -(-NTL // 4)

        @block.sync
        def _(sp):
            sp.dma_start(gscr, e.gates[:, T:NT]).then_inc(gates_stored, 16)
            load_wait(sp, gates_stored, 1)
            for n in range(NSEQ):
                for br in range(3):
                    sp.dma_start(gd[32 * (n % M):32 * (n % M) + 32, n // M, br:br + 1],
                                 bass.AP(tensor=gscr.tensor, offset=br * HQ * NS + n * TS, ap=[[NS, HQ], [1, TS]]),
                                 allow_slow_non_contiguous=True).then_inc(gates_landed, 16)
            def window(n, slots, free, landed, cache):
                if n >= 2:
                    sp.wait_ge(free, n - 1)
                sp.dma_start(slots[:, n % 2], cache[0, n].rearrange("(j p) g d -> p j (g d)", p=P)).then_inc(landed[n % 2], 16)

            for b in range(NBAT):
                for n in range(M * b, M * b + M):
                    window(n, kwin, window_keys_used, window_keys_landed, e.cache_k_win)
                for n in range(M * b, M * b + M):
                    window(n, vwin, window_values_used, window_values_landed, e.cache_v_win)

        @block.gpsimd
        def _(pool):
            for x in range(NBAT * 16):
                b, kv, m, half = x // 16, x // 8 % 2, x // 2 % 4, x % 2
                if x >= NR:
                    pool.wait_ge(ring_used, x - NR + 1)
                col = 2 * (M * b + m) + half
                pool.indirect_dma_start(ring[:, x % NR].rearrange("p s x -> p (s x)"), None, rows[kv],
                                        bass.IndirectOffsetOnAxis(ap=e.rowidx[:, col:col + 1], axis=0)).then_inc(ring_landed[x % NR], 16)

        @block.tensor
        def _(pe):
            def keys(b, y):
                z = KG * b + y
                if z >= 2:
                    pe.wait_ge(keys_kept, z - 1)
                if y < M:
                    n = M * b + y
                    load_wait(pe, window_keys_landed[n % 2], n // 2 + 1)
                    for j in range(4):
                        mm = pe.transpose(bank[z % 2][:, j * P:(j + 1) * P], kwin[:, n % 2, j, :], e.ident)
                    mm.then_inc(keys_turned, 1)
                    return
                v = y - M
                x = 16 * b + v // 4
                load_wait(pe, ring_landed[x % NR], x // NR + 1)
                for j in range(4):
                    mm = pe.transpose(bank[z % 2][:, j * P:(j + 1) * P], ring[:, x % NR, 4 * (v % 4) + j, :], e.ident)
                mm.then_inc(keys_turned, 1)

            def scores(b, y):
                z = KG * b + y
                m = y if y < M else (y - M) // 8
                pe.wait_ge(keys_kept, z + 1)
                if z >= 2:
                    pe.wait_ge(scores_kept, z - 1)
                pe.matmul(bank[2 + z % 2][32 * m:32 * m + 32, :], e.qbd[:, M * b + m, :], kt[:, z % 4, :], start=True, stop=True)\
                  .then_inc(scores_done, 1)

            def turn(b, y):
                z = NG * b + y
                if z >= 2:
                    pe.wait_ge(turned_kept, z - 1)
                for t in range(4 * y, min(4 * y + 4, NTL)):
                    if t < TWIN:
                        pe.wait_ge(weights_scaled, 3 * b + 1)
                        src = Sc[:, t * P:(t + 1) * P]
                    elif t < TSLC:
                        pe.wait_ge(weights_scaled, 3 * b + 2)
                        a = (t - TWIN) * P
                        src = Sw[:, a:min(a + P, WIN + NS)]
                    else:
                        pe.wait_ge(weights_scaled, 3 * b + 3)
                        a = (t - TSLC) * P
                        src = Ss[:, a:min(a + P, W)]
                    mm = pe.transpose(bank[(5, 7)[z % 2]][0:src.shape[1], (t % 4) * P:(t % 4 + 1) * P], src, e.ident)
                mm.then_inc(weights_turned, 1)

            for b in range(NBAT):
                if b:
                    pe.wait_ge(first_scores_kept, b)
                    pe.wait_ge(selection_step, 4)
                for m in range(M):
                    n = M * b + m
                    pe.matmul(bank[4][32 * m:32 * m + 32, 0:256], e.qbd[:, n, :], e.kcT[:, n, :], start=True, stop=True)
                q4 = e.qbd[:, M * b:M * b + M, :].rearrange("p n x -> p (n x)")
                for i in range(2):
                    mm = pe.matmul(bank[4][:, 256 + 32 * i:288 + 32 * i], q4, e.kT[:, i, T:NT], start=True, stop=True)
                mm.then_inc(first_scores_done, 1)
                for y in range(KG + 1):
                    if y < KG:
                        keys(b, y)
                        if y < M:
                            pe.wait_ge(keys_turned, KG * b + y + 1)
                            pe.sem_inc(window_keys_used, 1)
                        elif (y - M) % 4 == 3:
                            pe.wait_ge(keys_turned, KG * b + y + 1)
                            pe.sem_inc(ring_used, 1)
                    if y >= 1:
                        scores(b, y - 1)
                    if y == M + 2:
                        pe.wait_ge(blocks_summed, b + 1)
                        pe.matmul(bank[6][:, 256:256 + NBK], e.sumr, sc[:, 0:NBK], start=True, stop=True).then_inc(selection_step, 1)
                        pe.wait_ge(selection_step, 4 * b + 1)
                if b:
                    pe.wait_ge(outputs_kept, 1)
                pe.wait_ge(selection_step, 4 * b + 4)
                for y in range(NG):
                    turn(b, y)
                pe.wait_ge(turned_kept, NG * (b + 1))
                for m in range(M):
                    n = M * b + m
                    o = bank[6][32 * m:32 * m + 32, 0:P]
                    col = slice(32 * m, 32 * m + 32)
                    first = True

                    def add(v, t, k=P):
                        nonlocal first
                        mm = pe.matmul(o, wt[0:k, t, col], v, start=first, stop=False, skip_group_check=True)
                        first = False
                        return mm

                    for half in range(2):
                        add(e.vc[:, n, half, :], TCMP + half)
                    load_wait(pe, window_values_landed[n % 2], n // 2 + 1)
                    for j in range(4):
                        mm = add(vwin[:, n % 2, j, :], TWIN + j)
                    mm.then_inc(window_values_used, 1)
                    add(e.vnew[:, 1, :], TWIN + 4, NS)
                    for half in range(2):
                        x = 16 * b + 8 + 2 * m + half
                        load_wait(pe, ring_landed[x % NR], x // NR + 1)
                        for s in range(CHK):
                            mm = add(ring[:, x % NR, s, :], TSLC + CHK * half + s)
                        mm.then_inc(ring_used, 1)
                    mm = add(e.vnew[:, 0, :], TSLC + 32, NS)
                mm.then_inc(values_done, 1)
                pe.wait_ge(rows_kept, b + 1)
                pe.transpose(bank[6][:, 0:P], orow[:, :], e.ident).then_inc(rows_turned, 1)

        @block.scalar
        def _(act):
            for b in range(NBAT):
                def softmax(i, s):
                    act.wait_ge(maxima_done, 3 * b + i + 1)
                    act.activation(s, s, ACT.Exp, bias=st[:, i:i + 1], accum_out=st[:, 3 + i:4 + i]).then_inc(exps_done, 1)

                for y in range(KG):
                    z = KG * b + y
                    act.wait_ge(keys_turned, z + 1)
                    if z >= 4:
                        act.wait_ge(scores_done, z - 3)
                    act.activation(kt[:, z % 4, :], bank[z % 2][:, :], ACT.Copy).then_inc(keys_kept, 1)
                    if y == 0:
                        softmax(0, Sc[:, :])
                    if y == M + 4:
                        softmax(1, Sw[:, :])
                softmax(2, Ss[:, :])
                for y in range(NG):
                    z = NG * b + y
                    t0, t1 = 4 * y, min(4 * y + 4, NTL)
                    act.wait_ge(weights_turned, z + 1)
                    if b and y == 0:
                        act.wait_ge(values_done, b)
                    for t in ([None] if not {TWIN + 4, TSLC + 32} & set(range(t0, t1)) else range(t0, t1)):
                        if t is None:
                            ins = act.activation(wt[:, t0:t1, :], bank[(5, 7)[z % 2]][:, 0:(t1 - t0) * P].rearrange("p (t x) -> p t x", x=P), ACT.Copy)
                        else:
                            k = NS if t in (TWIN + 4, TSLC + 32) else P
                            ins = act.activation(wt[0:k, t, :], bank[(5, 7)[z % 2]][0:k, (t - t0) * P:(t - t0 + 1) * P], ACT.Copy)
                    ins.then_inc(turned_kept, 1)

        @block.vector
        def _(dve):
            tt = dve.tensor_tensor
            chain_ = c_chain
            n_ = [0]

            def link(ins):
                n_[0] += 1
                ins.then_inc(chain_, 1)
                dve.wait_ge(chain_, n_[0])

            def weights(b, i, s):
                dve.wait_ge(exps_done, 3 * b + i + 1)
                x = st[:, 3 + i:4 + i]
                link(dve.tensor_scalar(x, x, 1e-30, None, ALU.max))
                link(dve.reciprocal(x, x))
                if i:
                    dve.tensor_scalar(s, s, x, gd[:, b, (0, 2, 1)[i]:(0, 2, 1)[i] + 1], ALU.mult, ALU.mult).then_inc(weights_scaled, 1)

            def top(i, s):
                dve.tensor_reduce(st[:, i:i + 1], s, AXX, ALU.max, negate=True).then_inc(maxima_done, 1)

            load_wait(dve, gates_landed, 3 * NSEQ)
            for b in range(NBAT):
                if b:
                    dve.wait_ge(weights_turned, NG * b)
                dve.wait_ge(first_scores_done, b + 1)
                link(dve.tensor_copy(Sc[:, 0:255], bank[4][:, 0:255]))
                link(dve.memset(Sc[:, 255:256], NEG))
                link(tt(Sc[:, 247:255], Sc[:, 247:255], e.bcd[:, :], ALU.add))
                link(tt(Ss[:, PAST:W], bank[4][:, 256:288], e.bnew[:, b, :], ALU.add))
                tt(Sw[:, WIN:WIN + NS], bank[4][:, 288:320], e.bnew[:, b, :], ALU.add).then_inc(first_scores_kept, 1)
                top(0, Sc[:, :])

                def evac(y):
                    z = KG * b + y
                    dve.wait_ge(scores_done, z + 1)
                    m = y if y < M else (y - M) // 8
                    r = slice(32 * m, 32 * m + 32)
                    a = (y - M) % 8 * 512
                    dst = Sw[r, 0:WIN] if y < M else Ss[r, a:a + 512]
                    dve.tensor_copy(dst, bank[2 + z % 2][r, :]).then_inc(scores_kept, 1)

                weights(b, 0, Sc[:, :])
                link(dve.tensor_scalar(Sc[:, :], Sc[:, :], st[:, 3:4], None, ALU.mult))
                p4 = Sc[:, :].rearrange("p (j c) -> p j c", c=4)
                link(tt(sc[:, 0:NBK], p4[:, :, 0], p4[:, :, 1], ALU.add))
                link(tt(sc[:, 0:NBK], sc[:, 0:NBK], p4[:, :, 2], ALU.add))
                link(dve.scalar_tensor_tensor(out=sc[:, 0:NBK], in0=sc[:, 0:NBK], scalar=2.0, in1=p4[:, :, 3], op0=ALU.mult, op1=ALU.add))
                link(tt(sc[:, 1:NBK], sc[:, 1:NBK], p4[:, 0:NBK - 1, 3], ALU.add))
                dve.sem_inc(blocks_summed, 1)
                dve.tensor_scalar(Sc[:, :], Sc[:, :], gd[:, b, 0:1], None, ALU.mult).then_inc(weights_scaled, 1)
                for y in range(M):
                    evac(y)
                dve.wait_ge(scores_kept, KG * b + M)
                link(tt(Sw[:, 0:TS], Sw[:, 0:TS], e.winhead, ALU.add))
                link(tt(Sw[:, WIN - P:WIN], Sw[:, WIN - P:WIN], e.btail[:, :], ALU.add))
                top(1, Sw[:, :])
                evac(M)
                evac(M + 1)
                dve.wait_ge(selection_step, 4 * b + 1)
                link(dve.tensor_copy(scs[:, 0:NBK], bank[6][:, 256:256 + NBK]))
                link(dve.memset(scs[:, 0:1], BIG))
                dve.memset(scs[:, NBK - 1:NBK + 1], BIG).then_inc(selection_step, 1)
                dve.wait_ge(selection_step, 4 * b + 2)
                for i in range(2):
                    link(dve.max(m8[:, :], scs[:, :]))
                    link(dve.match_replace(scs[:, :], m8[:, :], scs[:, :], -1.0))
                dve.tensor_scalar(scs[:, :], scs[:, :], 0.0, NEG, ALU.is_ge, ALU.mult).then_inc(selection_step, 1)
                weights(b, 1, Sw[:, :])
                for y in range(M + 2, KG):
                    evac(y)
                dve.wait_ge(scores_kept, KG * (b + 1))
                dve.wait_ge(selection_step, 4 * b + 3)
                last = Ss[:, PAST // 2:PAST].rearrange("p (s c) -> p s c", c=P)[:, :, P - 8:P]
                link(tt(last, last, e.btail[:, :].rearrange("p (c s) -> p s c", s=CHK), ALU.add))
                for half in range(2):
                    v = Ss[:, half * PAST // 2:(half + 1) * PAST // 2].rearrange("p (s j c) -> p s j c", s=CHK, c=4)
                    k = scs[:, half * 32:half * 32 + 32].unsqueeze(1).unsqueeze(3).to_broadcast([P, CHK, 32, 4])
                    ins = tt(v, v, k, ALU.add)
                    link(ins)
                dve.sem_inc(selection_step, 1)
                top(2, Ss[:, :])
                weights(b, 2, Ss[:, :])
                dve.wait_ge(values_done, b + 1)
                dve.tensor_copy(orow[:, :], bank[6][:, 0:P]).then_inc(rows_kept, 1)
                dve.wait_ge(rows_turned, b + 1)
                for g in range(G):
                    h = slice(g * HD, (g + 1) * HD)
                    dst = e.oT[h, :, T + 16 * b:T + 16 * b + 16].rearrange("p r (m t) -> p r m t", t=TS)
                    src = bank[6][h, 0:P].rearrange("p (m g r t) -> p g r m t", g=G, r=R, t=TS)[:, g]
                    ins = dve.tensor_copy(dst, src)
                ins.then_inc(outputs_kept, 1)


NRAW, NSPLIT = 2, 2
WK = 8


def weight_slots(sb, sem, tag):
    return (sb("wraw" + tag, [P, NRAW, WK, P]), sb("whi" + tag, [P, NSPLIT, WK, P], F32R), sb("wlo" + tag, [P, NSPLIT, WK, P], F32R),
            [sem(f"w_loaded{i}") for i in range(NRAW)], sem("w_hi"), sem("w_split"))


def split_weights_hi(act, x, wraw, whi, w_loaded, w_hi, used):
    load_wait(act, w_loaded[x % NRAW], x // NRAW + 1)
    if x >= NSPLIT:
        act.wait_ge(*used(x - NSPLIT))
    act.activation(whi[:, x % NSPLIT], wraw[:, x % NRAW], ACT.Copy).then_inc(w_hi, 1)


def split_weights_lo(pool, x, wraw, whi, wlo, w_hi, w_split):
    pool.wait_ge(w_hi, x + 1)
    pool.tensor_tensor(wlo[:, x % NSPLIT], wraw[:, x % NRAW], whi[:, x % NSPLIT], ALU.subtract).then_inc(w_split, 1)


def split_products(pe, out, whi, wlo, xhi, xlo, chunks):
    n = len(chunks)
    for i, (kw, kx) in enumerate(chunks):
        pe.matmul(out, whi[:, kw, :], xlo(kx), start=(i == 0), stop=False)
        pe.matmul(out, wlo[:, kw, :], xhi(kx), start=False, stop=False)
        mm = pe.matmul(out, whi[:, kw, :], xhi(kx), start=False, stop=(i == n - 1))
    return mm


def stage_split(nc, e):
    with ExitStack() as c:
        sem = stage_semaphores(nc, c, "split")
        h_loaded, hi_set, lo_set = sem("h_loaded"), sem("hi_set"), sem("lo_set")
        block = c.enter_context(nc.Block())
        pairs = ((e.oT, e.ohi, e.olo), (e.ossmT, e.shi, e.slo))

        @block.sync
        def _(sp):
            sp.dma_start(e.mixT[:, :, :], e.h_keep).then_inc(h_loaded, 16)
            load_wait(sp, h_loaded, 1)

        @block.scalar
        def _(act):
            for raw, hi, _ in pairs:
                for k in range(4):
                    act.activation(hi[:, k, :], raw[:, k, :], ACT.Copy).then_inc(hi_set, 1)

        @block.vector
        def _(dve):
            for i, (raw, hi, lo) in enumerate(pairs):
                for k in range(4):
                    dve.wait_ge(hi_set, 4 * i + k + 1)
                    dve.tensor_tensor(lo[:, k, :], raw[:, k, :], hi[:, k, :], ALU.subtract).then_inc(lo_set, 1)


def stage_merge(nc, e):
    with ExitStack() as c:
        sb = lambda n, s, d=F32: c.enter_context(nc.sbuf_tensor(n, s, d))
        sem = stage_semaphores(nc, c, "merge")
        hhi, hlo = sb("hhi", [P, KD, NT], F32R), sb("hlo", [P, KD, NT], F32R)
        wraw, whi, wlo, w_loaded, w_hi, w_split = weight_slots(sb, sem, "_merge")
        sig = sb("sig", [P, 2, 3, SL])
        prod = sb("prod", [P, 2, SL])
        h_hi, h_split = sem("h_hi"), sem("h_split")
        products, sigmoids, scaled, mixed = sem("products"), sem("sigmoids"), sem("scaled"), sem("mixed")
        block = c.enter_context(nc.Block())
        win = e.w_in[0].rearrange("(k p) n -> p k n", p=P)
        NLOAD = 3 * KD
        bank = e.bank
        sl = lambda s: slice(s * SL, (s + 1) * SL)

        @block.sync
        def _(sp):
            for x in range(NLOAD):
                f, j = x // 3, x % 3
                a = f * P
                if x >= NRAW:
                    sp.wait_ge(w_split, x - NRAW + 1)
                if j < 2:
                    sp.dma_start(wraw[:, x % NRAW], win[:, :, (GA0, GS0)[j] + a:(GA0, GS0)[j] + a + P]).then_inc(w_loaded[x % NRAW], 16)
                    continue
                for g in range(G):
                    sp.dma_start(wraw[g * HD:(g + 1) * HD, x % NRAW, 0:4],
                                 e.w_br_attn[0].rearrange("(g r d) n -> g d r n", g=G, d=HD)[g, :, :, a:a + P]).then_inc(w_loaded[x % NRAW], 16)
                sp.dma_start(wraw[:, x % NRAW, 4:8], e.w_br_ssm[0].rearrange("(k p) n -> p k n", p=P)[:, :, a:a + P])\
                  .then_inc(w_loaded[x % NRAW], 16)

        def dmas(x):
            return sum(3 if y % 3 == 2 else 1 for y in range(x % NRAW, x + 1, NRAW))

        @block.tensor
        def _(pe):
            for x in range(NLOAD):
                j = x % 3
                w, v = whi[:, x % NSPLIT], wlo[:, x % NSPLIT]
                pe.wait_ge(w_split, x + 1)
                for s in range(3):
                    if x == 0:
                        pe.wait_ge(h_split, s + 1)
                    if j < 2:
                        if x >= 3:
                            pe.wait_ge(sigmoids, 6 * (x // 3 - 1) + 3 * j + s + 1)
                        mm = split_products(pe, bank[3 * j + s][:, 0:SL], w, v, lambda k: hhi[:, k, sl(s)], lambda k: hlo[:, k, sl(s)],
                                            [(k, k) for k in range(KD)])
                    else:
                        for i, (hi, low) in enumerate(((e.ohi, e.olo), (e.shi, e.slo))):
                            n = 6 * (x // 3) + 2 * s + i
                            if n >= 2:
                                pe.wait_ge(scaled, n - 1)
                            mm = split_products(pe, bank[6 + i][:, 0:SL], w, v, lambda k: hi[:, k, sl(s)], lambda k: low[:, k, sl(s)],
                                                [(4 * i + k, k) for k in range(4)])
                            if i == 0:
                                mm.then_inc(products, 1)
                    mm.then_inc(products, 1)

        @block.scalar
        def _(act):
            def weights_hi(x):
                act.wait_ge(w_loaded[x % NRAW], 16 * dmas(x))
                if x >= NSPLIT:
                    y = x - NSPLIT
                    act.wait_ge(products, 12 * (y // 3) + 3 * (y % 3) + (3 if y % 3 < 2 else 6))
                act.activation(whi[:, x % NSPLIT], wraw[:, x % NRAW], ACT.Copy).then_inc(w_hi, 1)

            weights_hi(0)
            for s in range(3):
                act.activation(hhi[:, :, sl(s)], e.mixT[:, :, sl(s)], ACT.Copy).then_inc(h_hi, 1)
            weights_hi(1)
            for x in range(NLOAD):
                f, j = x // 3, x % 3
                for s in range(3 if j < 2 else 0):
                    act.wait_ge(products, 12 * f + 3 * j + s + 1)
                    if f:
                        act.wait_ge(scaled, 6 * (f - 1) + 2 * s + j + 1)
                    act.activation(sig[:, j, s, :], bank[3 * j + s][:, 0:SL], ACT.Sigmoid).then_inc(sigmoids, 1)
                if x + 2 < NLOAD:
                    weights_hi(x + 2)

        @block.gpsimd
        def _(pool):
            for x in range(NLOAD):
                split_weights_lo(pool, x, wraw, whi, wlo, w_hi, w_split)

        @block.vector
        def _(dve):
            for s in range(3):
                dve.wait_ge(h_hi, s + 1)
                dve.tensor_tensor(hlo[:, :, sl(s)], e.mixT[:, :, sl(s)], hhi[:, :, sl(s)], ALU.subtract).then_inc(h_split, 1)
            dve.wait_ge(h_split, 3)
            for f in range(KD):
                for s in range(3):
                    u = 3 * f + s
                    if u >= 1:
                        dve.wait_ge(mixed, u)
                    for i in range(2):
                        dve.wait_ge(products, 12 * f + 6 + 2 * s + i + 1)
                        if i == 0:
                            dve.wait_ge(sigmoids, 6 * (f + 1))
                        dve.tensor_tensor(prod[:, i, :], sig[:, i, s, :], bank[6 + i][:, 0:SL], ALU.mult).then_inc(scaled, 1)
                    dve.wait_ge(scaled, 2 * u + 2)
                    dve.tensor_tensor(e.mixT[:, f, sl(s)], prod[:, 0, :], prod[:, 1, :], ALU.add).then_inc(mixed, 1)


def add_gated(dve, e, chain, wait_done, psum, tmp, f, s, gate):
    m = min(SL, T - s * SL)
    a = s * SL
    gx = e.mod[:, gate * KD + f, :]
    ins = dve.scalar_tensor_tensor(out=e.xT[:, f, a:a + m], in0=psum[:, 0:m], scalar=gx[:, 0:1], in1=e.xT[:, f, a:a + m],
                                   op0=ALU.mult, op1=ALU.add)
    if m < SL:
        v = lambda x: x.rearrange("p (n t) -> p n t", t=TS)
        ins.then_inc(chain, 1)
        dve.tensor_tensor(v(tmp), v(psum[:, m:SL]), gx[:, 1:1 + NSEQ].unsqueeze(2).to_broadcast([P, NSEQ, TS]), ALU.mult).then_inc(chain, 1)
        dve.wait_ge(chain, wait_done)
        ins = dve.tensor_tensor(e.xT[:, f, a + m:a + SL], e.xT[:, f, a + m:a + SL], tmp, ALU.add)
    return ins


def stage_out(nc, e):
    with ExitStack() as c:
        sb = lambda n, s, d=F32: c.enter_context(nc.sbuf_tensor(n, s, d))
        sem = stage_semaphores(nc, c, "out")
        mhi, mlo = sb("mhi", [P, KD, NT], F32R), sb("mlo", [P, KD, NT], F32R)
        wraw, whi, wlo, w_loaded, w_hi, w_split = weight_slots(sb, sem, "_out")
        tmp = sb("tmp", [P, NS])
        x_loaded, m_hi, m_split, products, added, chain = (sem(n) for n in ("x_loaded", "m_hi", "m_split", "products", "added", "chain"))
        block = c.enter_context(nc.Block())
        bank = e.bank
        sl = lambda s: slice(s * SL, (s + 1) * SL)

        def used(x):
            return products, 3 * x + 3

        @block.sync
        def _(sp):
            for x in range(KD):
                if x >= NRAW:
                    sp.wait_ge(w_split, x - NRAW + 1)
                sp.dma_start(wraw[:, x % NRAW], e.w_out[0].rearrange("(k p) n -> p k n", p=P)[:, :, x * P:(x + 1) * P])\
                  .then_inc(w_loaded[x % NRAW], 16)
                if x == 0:
                    sp.dma_start(e.xT[:, :, :], e.x_keep).then_inc(x_loaded, 16)

        @block.tensor
        def _(pe):
            for f in range(KD):
                pe.wait_ge(w_split, f + 1)
                for s in range(3):
                    u = 3 * f + s
                    if f == 0:
                        pe.wait_ge(m_split, s + 1)
                    if u >= 8:
                        pe.wait_ge(added, u - 7)
                    split_products(pe, bank[u % 8][:, 0:SL], whi[:, f % NSPLIT], wlo[:, f % NSPLIT], lambda k: mhi[:, k, sl(s)],
                                   lambda k: mlo[:, k, sl(s)], [(k, k) for k in range(KD)]).then_inc(products, 1)

        @block.scalar
        def _(act):
            for s in range(3):
                act.activation(mhi[:, :, sl(s)], e.mixT[:, :, sl(s)], ACT.Copy).then_inc(m_hi, 1)
                if s == 0:
                    split_weights_hi(act, 0, wraw, whi, w_loaded, w_hi, used)
            for x in range(1, KD):
                split_weights_hi(act, x, wraw, whi, w_loaded, w_hi, used)

        @block.gpsimd
        def _(pool):
            for x in range(KD):
                split_weights_lo(pool, x, wraw, whi, wlo, w_hi, w_split)

        @block.vector
        def _(dve):
            for s in range(3):
                dve.wait_ge(m_hi, s + 1)
                dve.tensor_tensor(mlo[:, :, sl(s)], e.mixT[:, :, sl(s)], mhi[:, :, sl(s)], ALU.subtract).then_inc(m_split, 1)
            load_wait(dve, x_loaded, 1)
            for u in range(3 * KD):
                f, s = u // 3, u % 3
                dve.wait_ge(products, u + 1)
                if s == 2 and f:
                    dve.wait_ge(added, u)
                add_gated(dve, e, chain, 2 * (f + 1), bank[u % 8], tmp[:, :], f, s, 2).then_inc(added, 1)


def stage_mlp(nc, e):
    FH = WK
    NQ = F // P // FH
    with ExitStack() as c:
        sb = lambda n, s, d=F32: c.enter_context(nc.sbuf_tensor(n, s, d))
        sem = stage_semaphores(nc, c, "mlp")
        ahi, alo = sb("ahi", [P, FH, NT], F32R), sb("alo", [P, FH, NT], F32R)
        wraw, whi, wlo, w_loaded, w_hi, w_split = weight_slots(sb, sem, "_mlp")
        sq = sb("sqr", [P, 3, SL])
        tmp = sb("tmp2", [P, NS])
        ups, relus, squares, a_hi, a_split, downs, added, chain = (sem(n) for n in ("ups", "relus", "squares", "a_hi", "a_split", "downs", "added", "chain"))
        block = c.enter_context(nc.Block())
        bank = e.bank
        w1 = e.w_ff1[0].rearrange("(k p) n -> p k n", p=P)
        w2 = e.w_ff2[0].rearrange("(k p) n -> p k n", p=P)
        NU1, NU2 = 3 * FH, 3 * KD
        sl = lambda s: slice(s * SL, (s + 1) * SL)
        loads = NQ * (FH + KD)

        def used(x):
            q, l = divmod(x, FH + KD)
            return (ups, q * NU1 + 3 * l + 3) if l < FH else (downs, q * NU2 + 3 * (l - FH) + 3)

        @block.sync
        def _(sp):
            for x in range(loads):
                q, l = divmod(x, FH + KD)
                if x >= NRAW:
                    sp.wait_ge(w_split, x - NRAW + 1)
                a = (q * FH + l) * P
                src = w1[:, :, a:a + P] if l < FH else w2[:, q * FH:(q + 1) * FH, (l - FH) * P:(l - FH + 1) * P]
                sp.dma_start(wraw[:, x % NRAW], src).then_inc(w_loaded[x % NRAW], 16)

        @block.tensor
        def _(pe):
            for x in range(loads):
                q, l = divmod(x, FH + KD)
                w, v = whi[:, x % NSPLIT], wlo[:, x % NSPLIT]
                pe.wait_ge(w_split, x + 1)
                for s in range(3):
                    if l < FH:
                        u = q * NU1 + 3 * l + s
                        if u >= 4:
                            pe.wait_ge(relus, u - 3)
                        split_products(pe, bank[u % 4][:, 0:SL], w, v, lambda k: e.hhi[:, k, sl(s)], lambda k: e.hlo[:, k, sl(s)],
                                       [(k, k) for k in range(KD)]).then_inc(ups, 1)
                    else:
                        u = q * NU2 + 3 * (l - FH) + s
                        if l == FH:
                            pe.wait_ge(a_split, (q + 1) * NU1 - 2 + s)
                        if u >= 4:
                            pe.wait_ge(added, u - 3)
                        split_products(pe, bank[4 + u % 4][:, 0:SL], w, v, lambda k: ahi[:, k, sl(s)], lambda k: alo[:, k, sl(s)],
                                       [(k, k) for k in range(FH)]).then_inc(downs, 1)

        @block.scalar
        def _(act):
            def hi(u):
                act.wait_ge(squares, u + 1)
                if u % NU1 == 0 and u:
                    act.wait_ge(downs, u // NU1 * NU2)
                act.activation(ahi[:, u % NU1 // 3, sl(u % 3)], sq[:, u % 3, :], ACT.Copy).then_inc(a_hi, 1)

            for x in range(NSPLIT):
                split_weights_hi(act, x, wraw, whi, w_loaded, w_hi, used)
            for x in range(loads):
                q, l = divmod(x, FH + KD)
                for s in range(3 if l < FH else 0):
                    u = q * NU1 + 3 * l + s
                    act.wait_ge(ups, u + 1)
                    if u >= 3:
                        act.wait_ge(a_split, u - 2)
                    act.activation(sq[:, u % 3, :], bank[u % 4][:, 0:SL], ACT.Relu).then_inc(relus, 1)
                    if u % NU1:
                        hi(u - 1)
                if l == FH - 1:
                    hi((q + 1) * NU1 - 1)
                if x + NSPLIT < loads:
                    split_weights_hi(act, x + NSPLIT, wraw, whi, w_loaded, w_hi, used)

        @block.gpsimd
        def _(pool):
            for x in range(loads):
                split_weights_lo(pool, x, wraw, whi, wlo, w_hi, w_split)

        @block.vector
        def _(dve):
            def low(u):
                l, s = u % NU1 // 3, u % 3
                dve.wait_ge(a_hi, u + 1)
                dve.tensor_tensor(alo[:, l, sl(s)], sq[:, u % 3, :], ahi[:, l, sl(s)], ALU.subtract).then_inc(a_split, 1)

            for q in range(NQ):
                for v in range(NU1):
                    u = q * NU1 + v
                    dve.wait_ge(relus, u + 1)
                    r = sq[:, u % 3, :]
                    dve.tensor_tensor(r, r, r, ALU.mult).then_inc(squares, 1)
                    if v:
                        low(u - 1)
                low(q * NU1 + NU1 - 1)
                for v in range(NU2):
                    f, s = v // 3, v % 3
                    u = q * NU2 + v
                    dve.wait_ge(downs, u + 1)
                    if s == 2 and u > 2:
                        dve.wait_ge(added, u)
                    add_gated(dve, e, chain, 2 * (q * KD + f + 1), bank[4 + u % 4], tmp[:, :], f, s, 5).then_inc(added, 1)


def stages(nc, e):
    kept, mix, parts, late, last = (ExitStack() for _ in range(5))
    e.ossmT = kept.enter_context(nc.sbuf_tensor("ossmT", [P, SSM // P, NT], F32, side="right"))
    with nc.sbuf_tensor("hT", [P, KD, NT], F32, side="right") as hT:
        e.hT = hT
        with nc.sbuf_tensor("wu", [P, KD, SSM], F32, side="right") as wu:
            e.wu = wu
            with nc.sbuf_tensor("xT", [P, KD, NT], F32, side="right") as xT:
                e.xT = xT
                stage_inputs(nc, e)
                stage_norm(nc, e, "_mix", e.xT, 0, shift=0, scale=1, dst=e.hT, keep=e.x_keep)
            stage_ssm(nc, e)
        outer = ExitStack()
        attn = ExitStack()
        sb = lambda n, s, d=F32: attn.enter_context(nc.sbuf_tensor(n, s, d))
        e.qT = sb("qT", [P, R, NT])
        e.kT = sb("kT", [P, 2, NT])
        e.vslc = sb("vslc", [P, TB, 3 * HD])
        e.vwin = sb("vwin", [P, TB, 3 * HD])
        e.vnew = sb("vnew", [NS, 2, KVW])
        e.gates = sb("gates", [3 * HQ, NT])
        e.bt = sb("bt", [P, HQ, 2 * P])
        e.bc = sb("bc", [P, HQ, 16])
        e.btail = sb("btail", [P, P])
        e.bcd = sb("bcd", [P, 8])
        e.bnew = sb("bnew", [P, 2, NS])
        e.qbd = sb("qbd", [P, NSEQ, 32])
        e.rowidx = sb("rowidx", [P, NSEQ * 2], U32)
        e.kcp = sb("kcp", [P, T // CHK])
        e.vcp = sb("vcp", [T // CHK, 3 * HD])
        e.kcT = sb("kcT", [P, NSEQ, 256])
        e.vc = sb("vc", [P, NSEQ, 2, KVW])
        weights = ExitStack()
        sb2 = lambda n, s, d=F32: weights.enter_context(nc.sbuf_tensor(n, s, d))
        e.w1T = sb2("w1T", [P, 2, 8, 2, HD])
        e.w2 = sb2("w2c", [HD, 2, HD])
        e.cbias = sb2("cbias", [HD, 2])
        stage_project(nc, e)
    with outer:
        with attn:
            with weights:
                stage_compress(nc, e)
            e.oT = outer.enter_context(nc.sbuf_tensor("oT", [P, R, NT], F32, side="right"))
            stage_prompt(nc, e)
            stage_decode(nc, e)
        e.mixT = mix.enter_context(nc.sbuf_tensor("mixT", [P, KD, NT], F32))
        e.ohi, e.olo, e.shi, e.slo = (parts.enter_context(nc.sbuf_tensor(n, [P, 4, NT], F32R)) for n in ("ohi", "olo", "shi", "slo"))
        stage_split(nc, e)
    kept.close()
    with parts:
        stage_merge(nc, e)
    late.enter_context(mix)
    with late:
        e.xT = last.enter_context(nc.sbuf_tensor("xT_late", [P, KD, NT], F32, side="right"))
        stage_out(nc, e)
    with last:
        with nc.sbuf_tensor("hhi_mlp", [P, KD, NT], F32R) as e.hhi, nc.sbuf_tensor("hlo_mlp", [P, KD, NT], F32R) as e.hlo:
            stage_norm(nc, e, "_mlp", e.xT, 1, shift=3, scale=4)
            stage_mlp(nc, e)
        with nc.sbuf_tensor("yT", [P, KD, NT], F32) as yT:
            stage_norm(nc, e, "_fin", e.xT, 2, dst=yT, store=True)


def build(nc, ins, outs):
    e = Env()
    (e.x_prompt, e.x_sample, e.cache_k_cmp, e.cache_v_cmp, e.cache_k_slc, e.cache_v_slc, e.cache_k_win, e.cache_v_win,
     e.state_re, e.state_im, e.page_table, e.c_prompt, e.c_sample, e.rel_bias, e.w_ada, e.b_ada, g_mix, g_mlp, e.w_in,
     e.cmp_pe, e.cmp_w1, e.cmp_b1, e.cmp_w2, e.lam_re, e.lam_im, e.log_dt, e.b_re, e.b_im, e.c_re, e.c_im, e.ssm_d,
     e.w_glu, e.w_br_attn, e.w_br_ssm, e.w_out, e.w_ff1, e.w_ff2, g_final, e.consts_in, e.onehot_in) = ins
    (e.y_prompt, e.y_sample, e.p_k_cmp, e.p_v_cmp, e.p_k_slc, e.p_v_slc, e.p_k_win, e.p_v_win, e.p_re, e.p_im,
     e.s_k_cmp, e.s_v_cmp, e.s_k_slc, e.s_v_slc, e.s_k_win, e.s_v_win, e.s_re, e.s_im) = outs
    e.g_norm_mix = g_mix.rearrange("a (k p) -> (a k) p", p=P)
    e.g_norm_mlp = g_mlp.rearrange("a (k p) -> (a k) p", p=P)
    e.g_final = g_final.rearrange("(k p) -> k p", p=P)

    with ExitStack() as c:
        sb = lambda n, s, d=F32: c.enter_context(nc.sbuf_tensor(n, s, d))
        e.ps = c.enter_context(nc.psum_tensor("ps", [P, 8 * 512], F32))
        e.bank = [e.ps[:, 512 * i:512 * (i + 1)] for i in range(8)]
        sem = lambda n: c.enter_context(nc.semaphore(n))
        e.states_stored, e.caches_stored = sem("states_stored"), sem("caches_stored")
        e.wu_loaded = sem("wu_loaded")
        e.y_stored = [sem(f"y_stored{i}") for i in range(3)]
        e.consts = sb("consts", [P, NCONST])
        e.ident = e.consts[:, C_IDENT:C_IDENT + P]
        e.ones = e.consts[:, C_ONES:C_ONES + P]
        e.condsum = e.consts[:, C_CSUM:C_CSUM + NC9]
        e.eps = e.consts[:, C_EPS:C_EPS + 1]
        e.winmask = e.consts[:, C_WINM:C_WINM + P]
        e.sumr = e.consts[:, C_SUMR:C_SUMR + P]
        e.winhead = e.consts[:, C_WINH:C_WINH + TS]
        e.cmprow = e.consts[:, C_CROW:C_CROW + 1]
        e.mod = sb("mod", [P, 6 * KD, 1 + NSEQ])
        e.vec = sb("vec", [P, 9 * KD])
        e.scT = sb("scT", [P, KD, 32])
        e.h_keep = nc.dram_tensor("h_keep", (P, KD, NT), F32, kind="Internal").ap()
        e.x_keep = nc.dram_tensor("x_keep", (P, KD, NT), F32, kind="Internal").ap()
        stages(nc, e)


def plan_consts():
    parts, at = {}, 0
    def put(name, a):
        nonlocal at
        full = np.zeros((P, a.shape[1]), np.float32)
        full[0:a.shape[0]] = a
        parts[name] = (at, full)
        at += a.shape[1]
    put("ident", np.eye(P, dtype=np.float32))
    put("ones", np.ones((P, P), np.float32))
    put("eps", np.full((P, 1), EPS, np.float32))
    k = np.arange(P)
    put("winmask", np.where(k[None, :] >= k[:, None], 0.0, NEG).astype(np.float32))
    put("cmprow", (k[:, None] >= CHK * 2 - 1).astype(np.float32))
    i, t = np.arange(P)[:, None], np.arange(P)[None, :]
    same = (i // 32 == t // 32) & ((i // 16) % 2 == (t // 16) % 2) & (i % 4 == t % 4)
    put("sumr", same.astype(np.float32))
    put("winhead", np.where(np.arange(TS)[None, :] < (k % TS)[:, None], NEG, 0.0).astype(np.float32))
    put("pow", np.tile(np.concatenate([np.arange(LC + 1), np.arange(LC)[::-1]]).astype(np.float32)[None, :], (P, 1)))
    put("condsum", (k[:, None] % 32 == np.arange(NC9)[None, :]).astype(np.float32))
    put("sub", (k % 8).astype(np.float32)[:, None])
    return parts, at


_PARTS, NCONST = plan_consts()
C_IDENT, C_ONES, C_EPS, C_WINM, C_CROW, C_SUMR, C_WINH, C_POW, C_CSUM, C_SUB = (
    _PARTS[n][0] for n in ("ident", "ones", "eps", "winmask", "cmprow", "sumr", "winhead", "pow", "condsum", "sub"))
BW = 383


def one_hot():
    n = 255 - np.arange(BW)
    exact = NB // 2
    nf = np.maximum(n, exact).astype(np.float32)
    large = exact + (np.log(nf / exact) / np.float32(np.log(128 / exact)) * (NB - exact)).astype(np.int32)
    b = np.where(n < exact, np.maximum(n, 0), np.minimum(large, NB - 1))
    out = np.zeros((NB + 1, BW), np.float32)
    out[b, np.arange(BW)] += 1
    out[NB - 1, :] -= 1
    out[NB, :] = n < 0
    return np.concatenate([out, out[:, ::-1]], axis=1)


_INS = ['x_prompt', 'x_sample', 'cache_k_cmp', 'cache_v_cmp', 'cache_k_slc', 'cache_v_slc', 'cache_k_win', 'cache_v_win',
        'state_ssm_re', 'state_ssm_im', 'page_table', 'c_prompt', 'c_sample', 'rel_bias', 'w_ada', 'b_ada', 'g_norm_mix',
        'g_norm_mlp', 'w_in', 'cmp_pe', 'cmp_w1', 'cmp_b1', 'cmp_w2', 'ssm_lambda_re', 'ssm_lambda_im', 'ssm_log_dt',
        'ssm_b_re', 'ssm_b_im', 'ssm_c_re', 'ssm_c_im', 'ssm_d', 'w_glu', 'w_br_attn', 'w_br_ssm', 'w_out', 'w_ff1',
        'w_ff2', 'g_final']
_OUTS = [(1, T, D), (NSEQ, TS, D)] + [(1, 1, T, G, HD)] * 4 + [(1, 1, WIN, G, HD)] * 2 + [(1, 1, SG, SP)] * 2 \
    + [(1, NSEQ, TS, G, HD)] * 4 + [(1, NSEQ, WIN, G, HD)] * 2 + [(1, NSEQ, SG, SP)] * 2


def kernel(**inputs):
    import concourse.bacc as _bacc
    from concourse.bass_utils import run_bass_kernel_spmd as _run

    nc = _bacc.Bacc("TRN2", target_bir_lowering=False, num_devices=1)
    arrays, args = {}, []
    for name in _INS:
        arrays[f"in_{name}"] = np.ascontiguousarray(inputs[name])
    arrays["in_consts"] = np.concatenate([a for _, a in _PARTS.values()], axis=1)
    arrays["in_onehot"] = one_hot()
    for name, a in arrays.items():
        args.append(nc.dram_tensor(name, a.shape, mybir.dt.from_np(a.dtype), kind="ExternalInput").ap())
    outs = [nc.dram_tensor(f"out_{i}", s, F32, kind="ExternalOutput").ap() for i, s in enumerate(_OUTS)]
    build(nc, args, outs)
    r = _run(nc, [arrays], core_ids=[0])
    return tuple(r.results[0][f"out_{i}"] for i in range(len(_OUTS)))
```
